# Optimizing a Trainium2 kernel written in Bass

```python
import jax, jax.numpy as jnp
from jax import lax
import numpy as np
import math

D_MODEL = 1024
BATCH = 1
SEQ = 256
DEPTH = 2

N_A = DEPTH // 2
N_B = DEPTH - N_A
N_META = 16
POOL_WINDOWS = (2, 4, 8, 16)
N_POOL_GROUPS = len(POOL_WINDOWS)
POOL_GROUP_DIM = D_MODEL // N_POOL_GROUPS
MAX_WINDOW = max(POOL_WINDOWS)
N_HEADS = 8
QK_NOPE_DIM = 128
QK_ROPE_DIM = 64
V_HEAD_DIM = 128
Q_LORA_RANK = 384
KV_LORA_RANK = 256
ROPE_THETA = 10000.0
ATTN_SCALE = (QK_NOPE_DIM + QK_ROPE_DIM) ** -0.5
Q_BLOCK = 128
N_EXPERT_GROUPS = 4
EXPERTS_PER_GROUP = 8
N_EXPERTS = N_EXPERT_GROUPS * EXPERTS_PER_GROUP
TOP_K_IN_GROUP = 2
D_EXPERT = 256
MOE_GROUP_ROWS = 256
RMS_EPS = 1e-6
NEG_INF = -1e30


def rmsnorm(x, g):
    xf = x.astype(jnp.float32)
    y = xf * lax.rsqrt(jnp.mean(xf * xf, axis=-1, keepdims=True) + RMS_EPS)
    return (y * g.astype(jnp.float32)).astype(x.dtype)

def rope_tables(length):
    pos = jnp.arange(length, dtype=jnp.float32)
    inv_freq = ROPE_THETA ** (-jnp.arange(0, QK_ROPE_DIM, 2, dtype=jnp.float32) / QK_ROPE_DIM)
    ang = pos[:, None] * inv_freq[None, :]
    return jnp.cos(ang), jnp.sin(ang)

def apply_rope(x, cos, sin):
    xf = x.astype(jnp.float32)
    half = xf.shape[-1] // 2
    x1, x2 = xf[..., :half], xf[..., half:]
    return jnp.concatenate([x1 * cos - x2 * sin, x1 * sin + x2 * cos], axis=-1).astype(x.dtype)

def pool_mixer(h, w_grp, scale):
    L_ = h.shape[1]
    hf = h.astype(jnp.float32)
    cs = jnp.pad(jnp.cumsum(hf, axis=1), ((0, 0), (MAX_WINDOW, 0), (0, 0)))
    t = jnp.arange(L_)
    outs = []
    for g, w in enumerate(POOL_WINDOWS):
        sl = slice(g * POOL_GROUP_DIM, (g + 1) * POOL_GROUP_DIM)
        win_sum = cs[:, MAX_WINDOW:, sl] - cs[:, MAX_WINDOW - w:MAX_WINDOW - w + L_, sl]
        cnt = jnp.minimum(t + 1, w).astype(jnp.float32)[None, :, None]
        pooled = (win_sum / cnt - hf[:, :, sl]).astype(h.dtype)
        outs.append(jnp.einsum('blc,cd->bld', pooled, w_grp[g]))
    return jnp.concatenate(outs, axis=-1) * scale

def shared_latent_kv(h, kv_norm, w_dkv, kv_lat_norm, w_uk, w_uv, cos, sin):
    c = jnp.einsum('bld,dr->blr', rmsnorm(h, kv_norm), w_dkv)
    c_kv = rmsnorm(c[..., :KV_LORA_RANK], kv_lat_norm)
    k_rope = apply_rope(c[..., KV_LORA_RANK:], cos, sin)
    k_nope = jnp.einsum('blr,rhd->blhd', c_kv, w_uk)
    v = jnp.einsum('blr,rhd->blhd', c_kv, w_uv)
    return k_nope, k_rope, v

def causal_block_attention(q_nope, q_rope, k_nope, k_rope, v):
    B_, L_, H_, _ = q_nope.shape
    nb = -(-L_ // Q_BLOCK)
    Lp = nb * Q_BLOCK
    pad = Lp - L_
    padf = lambda a: jnp.pad(a, [(0, 0), (0, pad)] + [(0, 0)] * (a.ndim - 2))
    qn, qr, kn, kr, vv = padf(q_nope), padf(q_rope), padf(k_nope), padf(k_rope), padf(v)
    to_blocks = lambda a: jnp.moveaxis(a.reshape((B_, nb, Q_BLOCK) + a.shape[2:]), 1, 0)
    kpos = jnp.arange(Lp)

    def one_block(args):
        qn_b, qr_b, b_idx = args
        s = (jnp.einsum('bqhd,bkhd->bhqk', qn_b, kn, preferred_element_type=jnp.float32)
             + jnp.einsum('bqhr,bkr->bhqk', qr_b, kr, preferred_element_type=jnp.float32)) * ATTN_SCALE
        qpos = b_idx * Q_BLOCK + jnp.arange(Q_BLOCK)
        s = jnp.where(kpos[None, :] <= qpos[:, None], s, NEG_INF)
        p = jax.nn.softmax(s, axis=-1)
        return jnp.einsum('bhqk,bkhd->bqhd', p.astype(vv.dtype), vv)

    o = lax.map(one_block, (to_blocks(qn), to_blocks(qr), jnp.arange(nb)))
    return jnp.moveaxis(o, 0, 1).reshape(B_, Lp, H_, V_HEAD_DIM)[:, :L_]

def mla_mixer(hn, w_dq, q_norm, w_uq, w_o, k_nope, k_rope, v, cos, sin):
    B_, L_, _ = hn.shape
    cq = rmsnorm(jnp.einsum('bld,dr->blr', hn, w_dq), q_norm)
    q = jnp.einsum('blr,rhd->blhd', cq, w_uq)
    q_nope = q[..., :QK_NOPE_DIM]
    q_rope = apply_rope(q[..., QK_NOPE_DIM:], cos[:, None, :], sin[:, None, :])
    o = causal_block_attention(q_nope, q_rope, k_nope, k_rope, v)
    return jnp.einsum('blf,fd->bld', o.reshape(B_, L_, N_HEADS * V_HEAD_DIM), w_o)

def hierarchical_moe(h, wr_g, br_g, wr_e, br_e, w_gate, w_up, w_down):
    B_, L_, D_ = h.shape
    xt = h.reshape(-1, D_)
    n_tok = xt.shape[0]
    xf = xt.astype(jnp.float32)
    p_g = jax.nn.softmax(xf @ wr_g.astype(jnp.float32) + br_g.astype(jnp.float32), axis=-1)
    g_sel = jnp.argmax(p_g, axis=-1)
    w_g = jnp.max(p_g, axis=-1)
    logit_e = (xf @ wr_e.astype(jnp.float32) + br_e.astype(jnp.float32)).reshape(n_tok, N_EXPERT_GROUPS, EXPERTS_PER_GROUP)
    sel = jnp.take_along_axis(logit_e, g_sel[:, None, None], axis=1)[:, 0]
    top_v, top_i = lax.top_k(sel, TOP_K_IN_GROUP)
    gate = w_g[:, None] * jax.nn.softmax(top_v, axis=-1)
    eid = (g_sel[:, None] * EXPERTS_PER_GROUP + top_i).reshape(-1).astype(jnp.int32)
    tid = jnp.repeat(jnp.arange(n_tok, dtype=jnp.int32), TOP_K_IN_GROUP)
    wt = gate.reshape(-1)
    n_assign = n_tok * TOP_K_IN_GROUP
    order = jnp.argsort(eid)
    e_sorted = eid[order]
    counts = jnp.bincount(eid, length=N_EXPERTS)
    starts = jnp.cumsum(counts) - counts
    padded = (counts + MOE_GROUP_ROWS - 1) // MOE_GROUP_ROWS * MOE_GROUP_ROWS
    pends = jnp.cumsum(padded)
    pstarts = pends - padded
    dest = pstarts[e_sorted] + (jnp.arange(n_assign) - starts[e_sorted])
    n_blocks = -(-(n_assign + N_EXPERTS * (MOE_GROUP_ROWS - 1)) // MOE_GROUP_ROWS)
    n_rows = n_blocks * MOE_GROUP_ROWS
    row_tok = jnp.full((n_rows,), n_tok, jnp.int32).at[dest].set(tid[order])
    row_w = jnp.zeros((n_rows,), h.dtype).at[dest].set(wt[order].astype(h.dtype))
    block_e = jnp.minimum(jnp.searchsorted(pends, jnp.arange(n_blocks) * MOE_GROUP_ROWS, side='right'), N_EXPERTS - 1)
    x_rows = jnp.concatenate([xt, jnp.zeros((1, D_), xt.dtype)], axis=0)[row_tok]
    x_rows = x_rows.reshape(n_blocks, MOE_GROUP_ROWS, D_)

    def expert_block(args):
        e, xb = args
        return (jax.nn.silu(xb @ w_gate[e]) * (xb @ w_up[e])) @ w_down[e]

    y = lax.map(expert_block, (block_e, x_rows)).reshape(n_rows, D_)
    out = jnp.zeros((n_tok + 1, D_), h.dtype).at[row_tok].add(y * row_w[:, None])[:n_tok]
    return out.reshape(B_, L_, D_)

def first_inputs(seed: int = 0) -> dict:
    key = jax.random.key(seed)
    ks = jax.random.split(key, 32)
    f32 = jnp.float32
    nrm = lambda k, shape, fan: jax.random.normal(k, shape, f32) * (fan ** -0.5)
    gain = lambda k, shape: 1.0 + 0.05 * jax.random.normal(k, shape, f32)
    return {
        "x": jax.random.normal(ks[0], (BATCH, SEQ, D_MODEL), f32),
        "meta_tokens": jax.random.normal(ks[1], (N_META, D_MODEL), f32),
        "a_norm": gain(ks[2], (N_A, D_MODEL)),
        "a_w": nrm(ks[3], (N_A, N_POOL_GROUPS, POOL_GROUP_DIM, POOL_GROUP_DIM), POOL_GROUP_DIM),
        "a_scale": gain(ks[4], (N_A, D_MODEL)),
        "b_norm": gain(ks[5], (N_B, D_MODEL)),
        "b_w_dq": nrm(ks[6], (N_B, D_MODEL, Q_LORA_RANK), D_MODEL),
        "b_q_norm": gain(ks[7], (N_B, Q_LORA_RANK)),
        "b_w_uq": nrm(ks[8], (N_B, Q_LORA_RANK, N_HEADS, QK_NOPE_DIM + QK_ROPE_DIM), Q_LORA_RANK),
        "b_w_o": nrm(ks[9], (N_B, N_HEADS * V_HEAD_DIM, D_MODEL), N_HEADS * V_HEAD_DIM),
        "kv_norm": gain(ks[10], (D_MODEL,)),
        "w_dkv": nrm(ks[11], (D_MODEL, KV_LORA_RANK + QK_ROPE_DIM), D_MODEL),
        "kv_lat_norm": gain(ks[12], (KV_LORA_RANK,)),
        "w_uk": nrm(ks[13], (KV_LORA_RANK, N_HEADS, QK_NOPE_DIM), KV_LORA_RANK),
        "w_uv": nrm(ks[14], (KV_LORA_RANK, N_HEADS, V_HEAD_DIM), KV_LORA_RANK),
        "ffn_norm": gain(ks[15], (DEPTH, D_MODEL)),
        "router_g": nrm(ks[16], (DEPTH, D_MODEL, N_EXPERT_GROUPS), D_MODEL),
        "router_g_bias": 0.01 * jax.random.normal(ks[17], (DEPTH, N_EXPERT_GROUPS), f32),
        "router_e": nrm(ks[18], (DEPTH, D_MODEL, N_EXPERTS), D_MODEL),
        "router_e_bias": 0.01 * jax.random.normal(ks[19], (DEPTH, N_EXPERTS), f32),
        "w_gate": nrm(ks[20], (DEPTH, N_EXPERTS, D_MODEL, D_EXPERT), D_MODEL),
        "w_up": nrm(ks[21], (DEPTH, N_EXPERTS, D_MODEL, D_EXPERT), D_MODEL),
        "w_down": nrm(ks[22], (DEPTH, N_EXPERTS, D_EXPERT, D_MODEL), D_EXPERT),
        "final_norm": gain(ks[23], (D_MODEL,)),
    }

def first_block(x, meta_tokens, a_norm, a_w, a_scale, b_norm, b_w_dq, b_q_norm, b_w_uq, b_w_o,
              kv_norm, w_dkv, kv_lat_norm, w_uk, w_uv, ffn_norm, router_g, router_g_bias,
              router_e, router_e_bias, w_gate, w_up, w_down, final_norm):
    B_, S_, D_ = x.shape
    h = jnp.concatenate([jnp.broadcast_to(meta_tokens[None].astype(x.dtype), (B_, N_META, D_)), x], axis=1)
    L_ = S_ + N_META
    cos, sin = rope_tables(L_)
    k_nope = k_rope = v = None
    for layer in range(DEPTH):
        if layer < N_A:
            i = layer
            h = h + pool_mixer(rmsnorm(h, a_norm[i]), a_w[i], a_scale[i])
        else:
            i = layer - N_A
            h = h + mla_mixer(rmsnorm(h, b_norm[i]), b_w_dq[i], b_q_norm[i], b_w_uq[i], b_w_o[i],
                              k_nope, k_rope, v, cos, sin)
        h = h + hierarchical_moe(rmsnorm(h, ffn_norm[layer]), router_g[layer], router_g_bias[layer],
                                 router_e[layer], router_e_bias[layer], w_gate[layer], w_up[layer], w_down[layer])
        if layer == N_A - 1:
            k_nope, k_rope, v = shared_latent_kv(h, kv_norm, w_dkv, kv_lat_norm, w_uk, w_uv, cos, sin)
    return rmsnorm(h, final_norm)[:, N_META:]


D_FF = 2816
NORM_EPS = 1e-6
NSA_HEADS = 8
NSA_KV_HEADS = 2
NSA_GROUP = NSA_HEADS // NSA_KV_HEADS
NSA_HEAD_DIM = 64
CMP_BLOCK = 32
CMP_STRIDE = 16
SEL_BLOCK = 64
SEL_TOPK = 16
WINDOW = 512
FORCE_SCORE = 1e4
SSD_HEADS = 16
SSD_HEAD_DIM = 64
SSD_D_INNER = SSD_HEADS * SSD_HEAD_DIM
SSD_GROUPS = 2
SSD_STATE = 128
SSD_CONV = 4
SSD_CHUNK = 128
SSD_NORM_EPS = 1e-5
RWKV_HEAD_DIM = 64
RWKV_HEADS = D_MODEL // RWKV_HEAD_DIM
DECAY_LORA = 64
AAA_LORA = 64
GATE_LORA = 160
RWKV_GN_EPS = 64e-5

N_EVEN = (DEPTH + 1) // 2
N_ODD = DEPTH // 2

NSA_Q_W = NSA_HEADS * NSA_HEAD_DIM
NSA_KV_W = NSA_KV_HEADS * NSA_HEAD_DIM
SSD_XBC = SSD_D_INNER + 2 * SSD_GROUPS * SSD_STATE
IN_SPLITS = (NSA_Q_W, NSA_KV_W, NSA_KV_W, NSA_KV_W, NSA_KV_W, NSA_KV_W, NSA_KV_W,
             NSA_HEADS * 3, SSD_D_INNER, SSD_XBC, SSD_HEADS)
IN_WIDTH = sum(IN_SPLITS)
MIX_OUT_WIDTH = NSA_Q_W + SSD_D_INNER


def rmsnorm_2(x, g, eps=NORM_EPS):
    xf = x.astype(jnp.float32)
    y = xf * lax.rsqrt(jnp.mean(xf * xf, -1, keepdims=True) + eps)
    return (y * g.astype(jnp.float32)).astype(x.dtype)

def swiglu(x, w_gate, w_up, w_down):
    return (jax.nn.silu(x @ w_gate) * (x @ w_up)) @ w_down

def rope_tables_2(seq, dim):
    inv = ROPE_THETA ** (-jnp.arange(0, dim, 2, dtype=jnp.float32) / dim)
    ang = jnp.arange(seq, dtype=jnp.float32)[:, None] * inv[None, :]
    return jnp.cos(ang), jnp.sin(ang)

def apply_rope_2(x, cos, sin):
    shape = (1, x.shape[1]) + (1,) * (x.ndim - 3) + (cos.shape[-1],)
    c = cos.reshape(shape).astype(x.dtype)
    s = sin.reshape(shape).astype(x.dtype)
    x1, x2 = jnp.split(x, 2, axis=-1)
    return jnp.concatenate([x1 * c - x2 * s, x2 * c + x1 * s], -1)

def masked_softmax(s, mask):
    s = jnp.where(mask, s.astype(jnp.float32), -1e30)
    p = jnp.where(mask, jnp.exp(s - jnp.max(s, -1, keepdims=True)), 0.0)
    return p / jnp.maximum(jnp.sum(p, -1, keepdims=True), 1e-30)

def compress_blocks(k, pe, w1, w2):
    b, s, h, d = k.shape
    n_cmp = (s - CMP_BLOCK) // CMP_STRIDE + 1
    idx = jnp.arange(n_cmp)[:, None] * CMP_STRIDE + jnp.arange(CMP_BLOCK)[None, :]
    blk = k[:, idx] + pe[None, None, :, None, :]
    blk = jnp.moveaxis(blk, 3, 2).reshape(b, n_cmp, h, CMP_BLOCK * d)
    return jax.nn.silu(blk @ w1) @ w2

def nsa_attention(q, k_cmp, v_cmp, k_sel, v_sel, k_win, v_win, gates,
                  pe_k, w1_k, w2_k, pe_v, w1_v, w2_v):
    b, s, hkv, g, d = q.shape
    kc = compress_blocks(k_cmp, pe_k, w1_k, w2_k)
    vc = compress_blocks(v_cmp, pe_v, w1_v, w2_v)
    n_cmp = kc.shape[1]
    n_sel = s // SEL_BLOCK
    topk = min(SEL_TOPK, n_sel)
    cmp_start = jnp.arange(n_cmp) * CMP_STRIDE
    cmp_end = cmp_start + CMP_BLOCK - 1
    sel_start = jnp.arange(n_sel) * SEL_BLOCK
    overlap = ((cmp_start[:, None] < sel_start[None, :] + SEL_BLOCK)
               & (cmp_end[:, None] >= sel_start[None, :])).astype(jnp.float32)
    ks_blk = jnp.moveaxis(k_sel, 2, 1).reshape(b, hkv, n_sel, SEL_BLOCK, d)
    vs_blk = jnp.moveaxis(v_sel, 2, 1).reshape(b, hkv, n_sel, SEL_BLOCK, d)
    pad = ((0, 0), (WINDOW, 0), (0, 0), (0, 0))
    kw_pad = jnp.pad(k_win, pad)
    vw_pad = jnp.pad(v_win, pad)
    bi = jnp.arange(b)[:, None, None, None]
    hi = jnp.arange(hkv)[None, :, None, None]
    blk_ids = jnp.arange(n_sel)

    def block(qi):
        s0 = qi * Q_BLOCK
        qb = lax.dynamic_slice_in_dim(q, s0, Q_BLOCK, 1)
        gb = lax.dynamic_slice_in_dim(gates, s0, Q_BLOCK, 1)
        t = s0 + jnp.arange(Q_BLOCK)
        p_c = masked_softmax(jnp.einsum('bqhgd,bchd->bhgqc', qb, kc),
                             cmp_end[None, :] <= t[:, None])
        o_c = jnp.einsum('bhgqc,bchd->bqhgd', p_c.astype(vc.dtype), vc)
        imp = jnp.einsum('bhgqc,cj->bhqj', p_c, overlap)
        cur = t // SEL_BLOCK
        forced = ((blk_ids[None, :] == 0) | (blk_ids[None, :] == cur[:, None])
                  | (blk_ids[None, :] == cur[:, None] - 1))
        valid = sel_start[None, :] <= t[:, None]
        imp = jnp.where(valid, jnp.where(forced, FORCE_SCORE, imp), -jnp.inf)
        _, sel = lax.top_k(imp, topk)
        kg = ks_blk[bi, hi, sel].reshape(b, hkv, Q_BLOCK, topk * SEL_BLOCK, d)
        vg = vs_blk[bi, hi, sel].reshape(b, hkv, Q_BLOCK, topk * SEL_BLOCK, d)
        tok = (sel[..., None] * SEL_BLOCK + jnp.arange(SEL_BLOCK)).reshape(
            b, hkv, Q_BLOCK, topk * SEL_BLOCK)
        p_s = masked_softmax(jnp.einsum('bqhgd,bhqnd->bhgqn', qb, kg),
                             (tok <= t[:, None])[:, :, None])
        o_s = jnp.einsum('bhgqn,bhqnd->bqhgd', p_s.astype(vg.dtype), vg)
        kw = lax.dynamic_slice_in_dim(kw_pad, s0, Q_BLOCK + WINDOW, 1)
        vw = lax.dynamic_slice_in_dim(vw_pad, s0, Q_BLOCK + WINDOW, 1)
        kp = s0 - WINDOW + jnp.arange(Q_BLOCK + WINDOW)
        mask_w = ((kp[None, :] <= t[:, None]) & (kp[None, :] > t[:, None] - WINDOW)
                  & (kp[None, :] >= 0))
        p_w = masked_softmax(jnp.einsum('bqhgd,bkhd->bhgqk', qb, kw), mask_w)
        o_w = jnp.einsum('bhgqk,bkhd->bqhgd', p_w.astype(vw.dtype), vw)
        return gb[..., 0:1] * o_c + gb[..., 1:2] * o_s + gb[..., 2:3] * o_w

    out = lax.map(block, jnp.arange(s // Q_BLOCK))
    return jnp.moveaxis(out, 0, 1).reshape(b, s, hkv * g * d)

def causal_depthwise_conv(x, w, bias):
    y = lax.conv_general_dilated(x, w, window_strides=(1,), padding=[(SSD_CONV - 1, 0)],
                                 dimension_numbers=('NWC', 'WIO', 'NWC'),
                                 feature_group_count=x.shape[-1])
    return y + bias

def ssd_chunked(x, dt, a, bmat, cmat):
    b, s, h, p = x.shape
    g, n = bmat.shape[2], bmat.shape[3]
    r = h // g
    l = SSD_CHUNK
    c = s // l
    xd = (x * dt[..., None]).reshape(b, c, l, g, r, p)
    a_cs = jnp.cumsum(jnp.moveaxis((dt * a).reshape(b, c, l, g, r), 2, -1), axis=-1)
    bm = bmat.reshape(b, c, l, g, n)
    cm = cmat.reshape(b, c, l, g, n)
    causal = jnp.tril(jnp.ones((l, l), bool))
    seg = jnp.exp(jnp.where(causal, a_cs[..., :, None] - a_cs[..., None, :], -jnp.inf))
    cb = jnp.einsum('bclgn,bcsgn->bcgls', cm, bm)
    y_diag = jnp.einsum('bcgrls,bcsgrp->bclgrp', cb[:, :, :, None] * seg, xd)
    decay_states = jnp.exp(a_cs[..., -1:] - a_cs)
    states = jnp.einsum('bclgn,bcgrl,bclgrp->bcgrpn', bm, decay_states, xd)
    chunk_decay = jnp.exp(a_cs[..., -1])

    def step(carry, inp):
        st, dec = inp
        return carry * dec[..., None, None] + st, carry

    _, states_in = lax.scan(step, jnp.zeros_like(states[:, 0]),
                            (jnp.moveaxis(states, 1, 0), jnp.moveaxis(chunk_decay, 1, 0)))
    states_in = jnp.moveaxis(states_in, 0, 1)
    y_off = jnp.einsum('bclgn,bcgrpn,bcgrl->bclgrp', cm, states_in, jnp.exp(a_cs))
    return (y_diag + y_off).reshape(b, s, h, p)

def mamba2_branch(z, xbc, dt_raw, conv_w, conv_b, dt_bias, a_log, d_skip, norm_w):
    b, s, _ = z.shape
    f32 = jnp.float32
    xbc = jax.nn.silu(causal_depthwise_conv(xbc, conv_w, conv_b))
    xs, bm, cm = jnp.split(xbc, [SSD_D_INNER, SSD_D_INNER + SSD_GROUPS * SSD_STATE], -1)
    xs = xs.reshape(b, s, SSD_HEADS, SSD_HEAD_DIM).astype(f32)
    dt = jax.nn.softplus(dt_raw.astype(f32) + dt_bias.astype(f32))
    a = -jnp.exp(a_log.astype(f32))
    y = ssd_chunked(xs, dt, a, bm.reshape(b, s, SSD_GROUPS, SSD_STATE).astype(f32),
                    cm.reshape(b, s, SSD_GROUPS, SSD_STATE).astype(f32))
    y = y + xs * d_skip.astype(f32)[:, None]
    y = y.reshape(b, s, SSD_D_INNER) * jax.nn.silu(z.astype(f32))
    yg = y.reshape(b, s, SSD_GROUPS, SSD_D_INNER // SSD_GROUPS)
    yg = yg * lax.rsqrt(jnp.mean(yg * yg, -1, keepdims=True) + SSD_NORM_EPS)
    return (yg.reshape(b, s, SSD_D_INNER) * norm_w.astype(f32)).astype(z.dtype)

def nsa_ssd_mixer(h, cos, sin, w_in, pe_k, w1_k, w2_k, pe_v, w1_v, w2_v,
                  conv_w, conv_b, dt_bias, a_log, d_skip, ssd_norm_w, w_out):
    b, s, _ = h.shape
    proj = h @ w_in
    offs = np.cumsum(IN_SPLITS)[:-1].tolist()
    q, kc, vc, ks, vs, kw, vw, gl, z, xbc, dt = jnp.split(proj, offs, -1)
    kvshape = (b, s, NSA_KV_HEADS, NSA_HEAD_DIM)
    q = apply_rope_2(q.reshape(b, s, NSA_KV_HEADS, NSA_GROUP, NSA_HEAD_DIM), cos, sin) * (NSA_HEAD_DIM ** -0.5)
    kc = apply_rope_2(kc.reshape(kvshape), cos, sin)
    ks = apply_rope_2(ks.reshape(kvshape), cos, sin)
    kw = apply_rope_2(kw.reshape(kvshape), cos, sin)
    gates = jax.nn.sigmoid(gl).reshape(b, s, NSA_KV_HEADS, NSA_GROUP, 3)
    o_a = nsa_attention(q, kc, vc.reshape(kvshape), ks, vs.reshape(kvshape), kw, vw.reshape(kvshape),
                        gates, pe_k, w1_k, w2_k, pe_v, w1_v, w2_v)
    o_b = mamba2_branch(z, xbc, dt, conv_w, conv_b, dt_bias, a_log, d_skip, ssd_norm_w)
    return jnp.concatenate([o_a, o_b], -1) @ w_out

def rwkv7_time_mix(h, mu, w_r, w_k, w_v, w_o, w0, w1, w2, a0, a1, a2, g1, g2,
                   k_k, k_a, r_k, ln_g, ln_b):
    b, s, d = h.shape
    f32 = jnp.float32
    xx = jnp.pad(h, ((0, 0), (1, 0), (0, 0)))[:, :-1] - h
    xr, xw, xk, xv, xa, xg = [h + xx * mu[i] for i in range(6)]
    r = xr @ w_r
    w = -jax.nn.softplus(-(w0 + jnp.tanh(xw @ w1) @ w2)) - 0.5
    k = xk @ w_k
    v = xv @ w_v
    a = jax.nn.sigmoid(a0 + (xa @ a1) @ a2)
    g = jax.nn.sigmoid(xg @ g1) @ g2
    heads = lambda t: t.reshape(b, s, RWKV_HEADS, RWKV_HEAD_DIM).astype(f32)
    kk = heads(k * k_k)
    kk = kk / jnp.maximum(jnp.sqrt(jnp.sum(kk * kk, -1, keepdims=True)), 1e-12)
    k = k * (1 + (a - 1) * k_a)
    r_, k_, v_, a_ = heads(r), heads(k), heads(v), heads(a)
    decay = jnp.exp(-jnp.exp(heads(w)))

    def step(state, inp):
        r_t, d_t, k_t, v_t, kk_t, a_t = inp
        sa = jnp.einsum('bhij,bhj->bhi', state, -kk_t)
        state = (state * d_t[:, :, None, :] + sa[..., None] * (kk_t * a_t)[:, :, None, :]
                 + v_t[..., None] * k_t[:, :, None, :])
        return state, jnp.einsum('bhij,bhj->bhi', state, r_t)

    xs = tuple(jnp.moveaxis(t, 1, 0) for t in (r_, decay, k_, v_, kk, a_))
    _, y = lax.scan(step, jnp.zeros((b, RWKV_HEADS, RWKV_HEAD_DIM, RWKV_HEAD_DIM), f32), xs)
    y = jnp.moveaxis(y, 0, 1)
    mean = jnp.mean(y, -1, keepdims=True)
    var = jnp.mean(jnp.square(y - mean), -1, keepdims=True)
    y = ((y - mean) * lax.rsqrt(var + RWKV_GN_EPS)).reshape(b, s, d)
    y = y * ln_g.astype(f32) + ln_b.astype(f32)
    bonus = jnp.sum(r_ * k_ * r_k.astype(f32), -1, keepdims=True) * v_
    y = y + bonus.reshape(b, s, d)
    return (y * g.astype(f32)).astype(h.dtype) @ w_o

def second_inputs(seed: int = 0) -> dict:
    key = jax.random.key(seed)
    ks = iter(jax.random.split(key, 48))
    nrm = lambda shape, scale: scale * jax.random.normal(next(ks), shape, jnp.float32)
    uni = lambda shape, lo, hi: jax.random.uniform(next(ks), shape, jnp.float32, lo, hi)
    D, F, E, O = D_MODEL, D_FF, N_EVEN, N_ODD
    L, KD = CMP_BLOCK, NSA_HEAD_DIM
    x = nrm((BATCH, SEQ, D), 1.0)
    norm_gains = 1.0 + nrm((DEPTH, 6, D), 0.05)
    ffn1_w_gate = nrm((DEPTH, D, F), D ** -0.5)
    ffn1_w_up = nrm((DEPTH, D, F), D ** -0.5)
    ffn1_w_down = nrm((DEPTH, F, D), F ** -0.5)
    ffn2_w_gate = nrm((DEPTH, D, F), D ** -0.5)
    ffn2_w_up = nrm((DEPTH, D, F), D ** -0.5)
    ffn2_w_down = nrm((DEPTH, F, D), F ** -0.5)
    ab_w_in = nrm((E, D, IN_WIDTH), D ** -0.5)
    a_cmp_pe_k = nrm((E, L, KD), 0.02)
    a_cmp_w1_k = nrm((E, L * KD, KD), (L * KD) ** -0.5)
    a_cmp_w2_k = nrm((E, KD, KD), KD ** -0.5)
    a_cmp_pe_v = nrm((E, L, KD), 0.02)
    a_cmp_w1_v = nrm((E, L * KD, KD), (L * KD) ** -0.5)
    a_cmp_w2_v = nrm((E, KD, KD), KD ** -0.5)
    b_conv_w = nrm((E, SSD_CONV, 1, SSD_XBC), SSD_CONV ** -0.5)
    b_conv_b = nrm((E, SSD_XBC), 0.02)
    dt0 = jnp.exp(uni((E, SSD_HEADS), math.log(1e-3), math.log(1e-1)))
    b_dt_bias = dt0 + jnp.log(-jnp.expm1(-dt0))
    b_a_log = jnp.log(uni((E, SSD_HEADS), 1.0, 16.0))
    b_d_skip = 1.0 + nrm((E, SSD_HEADS), 0.1)
    b_norm_w = 1.0 + nrm((E, SSD_D_INNER), 0.05)
    ab_w_out = nrm((E, MIX_OUT_WIDTH, D), MIX_OUT_WIDTH ** -0.5)
    c_mu = uni((O, 6, D), 0.0, 1.0)
    c_w_r = nrm((O, D, D), D ** -0.5)
    c_w_k = nrm((O, D, D), D ** -0.5)
    c_w_v = nrm((O, D, D), D ** -0.5)
    c_w_o = nrm((O, D, D), D ** -0.5)
    c_w0 = uni((O, D), -6.0, 1.0)
    c_w1 = nrm((O, D, DECAY_LORA), D ** -0.5)
    c_w2 = nrm((O, DECAY_LORA, D), 0.1 * DECAY_LORA ** -0.5)
    c_a0 = nrm((O, D), 0.1)
    c_a1 = nrm((O, D, AAA_LORA), D ** -0.5)
    c_a2 = nrm((O, AAA_LORA, D), 0.1 * AAA_LORA ** -0.5)
    c_g1 = nrm((O, D, GATE_LORA), D ** -0.5)
    c_g2 = nrm((O, GATE_LORA, D), GATE_LORA ** -0.5)
    c_k_k = 0.85 + nrm((O, D), 0.05)
    c_k_a = 1.0 + nrm((O, D), 0.05)
    c_r_k = nrm((O, RWKV_HEADS, RWKV_HEAD_DIM), 0.1)
    c_ln_g = 1.0 + nrm((O, D), 0.05)
    c_ln_b = nrm((O, D), 0.02)
    return {'x': x, 'norm_gains': norm_gains,
            'ffn1_w_gate': ffn1_w_gate, 'ffn1_w_up': ffn1_w_up, 'ffn1_w_down': ffn1_w_down,
            'ffn2_w_gate': ffn2_w_gate, 'ffn2_w_up': ffn2_w_up, 'ffn2_w_down': ffn2_w_down,
            'ab_w_in': ab_w_in, 'a_cmp_pe_k': a_cmp_pe_k, 'a_cmp_w1_k': a_cmp_w1_k,
            'a_cmp_w2_k': a_cmp_w2_k, 'a_cmp_pe_v': a_cmp_pe_v, 'a_cmp_w1_v': a_cmp_w1_v,
            'a_cmp_w2_v': a_cmp_w2_v, 'b_conv_w': b_conv_w, 'b_conv_b': b_conv_b,
            'b_dt_bias': b_dt_bias, 'b_a_log': b_a_log, 'b_d_skip': b_d_skip,
            'b_norm_w': b_norm_w, 'ab_w_out': ab_w_out,
            'c_mu': c_mu, 'c_w_r': c_w_r, 'c_w_k': c_w_k, 'c_w_v': c_w_v, 'c_w_o': c_w_o,
            'c_w0': c_w0, 'c_w1': c_w1, 'c_w2': c_w2, 'c_a0': c_a0, 'c_a1': c_a1, 'c_a2': c_a2,
            'c_g1': c_g1, 'c_g2': c_g2, 'c_k_k': c_k_k, 'c_k_a': c_k_a, 'c_r_k': c_r_k,
            'c_ln_g': c_ln_g, 'c_ln_b': c_ln_b}

def second_block(x, norm_gains, ffn1_w_gate, ffn1_w_up, ffn1_w_down, ffn2_w_gate, ffn2_w_up,
              ffn2_w_down, ab_w_in, a_cmp_pe_k, a_cmp_w1_k, a_cmp_w2_k, a_cmp_pe_v, a_cmp_w1_v,
              a_cmp_w2_v, b_conv_w, b_conv_b, b_dt_bias, b_a_log, b_d_skip, b_norm_w, ab_w_out,
              c_mu, c_w_r, c_w_k, c_w_v, c_w_o, c_w0, c_w1, c_w2, c_a0, c_a1, c_a2, c_g1, c_g2,
              c_k_k, c_k_a, c_r_k, c_ln_g, c_ln_b):
    cos, sin = rope_tables_2(x.shape[1], NSA_HEAD_DIM)
    for layer in range(DEPTH):
        ng = norm_gains[layer]
        hdn = swiglu(rmsnorm_2(x, ng[0]), ffn1_w_gate[layer], ffn1_w_up[layer], ffn1_w_down[layer])
        x = x + 0.5 * rmsnorm_2(hdn, ng[1])
        hdn = rmsnorm_2(x, ng[2])
        i = layer // 2
        if layer % 2 == 0:
            hdn = nsa_ssd_mixer(hdn, cos, sin, ab_w_in[i], a_cmp_pe_k[i], a_cmp_w1_k[i],
                                a_cmp_w2_k[i], a_cmp_pe_v[i], a_cmp_w1_v[i], a_cmp_w2_v[i],
                                b_conv_w[i], b_conv_b[i], b_dt_bias[i], b_a_log[i], b_d_skip[i],
                                b_norm_w[i], ab_w_out[i])
        else:
            hdn = rwkv7_time_mix(hdn, c_mu[i], c_w_r[i], c_w_k[i], c_w_v[i], c_w_o[i], c_w0[i],
                                 c_w1[i], c_w2[i], c_a0[i], c_a1[i], c_a2[i], c_g1[i], c_g2[i],
                                 c_k_k[i], c_k_a[i], c_r_k[i], c_ln_g[i], c_ln_b[i])
        x = x + rmsnorm_2(hdn, ng[3])
        hdn = swiglu(rmsnorm_2(x, ng[4]), ffn2_w_gate[layer], ffn2_w_up[layer], ffn2_w_down[layer])
        x = x + 0.5 * rmsnorm_2(hdn, ng[5])
    return x


def setup_inputs(seed=0):
    out = dict(first_inputs(seed))
    for name, value in second_inputs(seed + 1).items():
        if name != "x":
            out[name + "_2"] = value
    return out


def reference(
    x, meta_tokens, a_norm, a_w, a_scale, b_norm, b_w_dq, b_q_norm, b_w_uq, b_w_o, kv_norm,
    w_dkv, kv_lat_norm, w_uk, w_uv, ffn_norm, router_g, router_g_bias, router_e, router_e_bias,
    w_gate, w_up, w_down, final_norm, norm_gains_2, ffn1_w_gate_2, ffn1_w_up_2, ffn1_w_down_2,
    ffn2_w_gate_2, ffn2_w_up_2, ffn2_w_down_2, ab_w_in_2, a_cmp_pe_k_2, a_cmp_w1_k_2,
    a_cmp_w2_k_2, a_cmp_pe_v_2, a_cmp_w1_v_2, a_cmp_w2_v_2, b_conv_w_2, b_conv_b_2, b_dt_bias_2,
    b_a_log_2, b_d_skip_2, b_norm_w_2, ab_w_out_2, c_mu_2, c_w_r_2, c_w_k_2, c_w_v_2, c_w_o_2,
    c_w0_2, c_w1_2, c_w2_2, c_a0_2, c_a1_2, c_a2_2, c_g1_2, c_g2_2, c_k_k_2, c_k_a_2, c_r_k_2,
    c_ln_g_2, c_ln_b_2,
):
    x = first_block(
        x, meta_tokens, a_norm, a_w, a_scale, b_norm, b_w_dq, b_q_norm, b_w_uq, b_w_o, kv_norm,
        w_dkv, kv_lat_norm, w_uk, w_uv, ffn_norm, router_g, router_g_bias, router_e,
        router_e_bias, w_gate, w_up, w_down, final_norm,
    )
    return second_block(
        x, norm_gains_2, ffn1_w_gate_2, ffn1_w_up_2, ffn1_w_down_2, ffn2_w_gate_2, ffn2_w_up_2,
        ffn2_w_down_2, ab_w_in_2, a_cmp_pe_k_2, a_cmp_w1_k_2, a_cmp_w2_k_2, a_cmp_pe_v_2,
        a_cmp_w1_v_2, a_cmp_w2_v_2, b_conv_w_2, b_conv_b_2, b_dt_bias_2, b_a_log_2, b_d_skip_2,
        b_norm_w_2, ab_w_out_2, c_mu_2, c_w_r_2, c_w_k_2, c_w_v_2, c_w_o_2, c_w0_2, c_w1_2,
        c_w2_2, c_a0_2, c_a1_2, c_a2_2, c_g1_2, c_g2_2, c_k_k_2, c_k_a_2, c_r_k_2, c_ln_g_2,
        c_ln_b_2,
    )


_drawn_inputs = setup_inputs


def setup_inputs(seed=0):
    import zlib

    import numpy as np

    out = dict(_drawn_inputs(seed))
    spreads = {}
    factors = {'b_q_norm': 3.362,
     'router_g_bias': 3.202,
     'a_cmp_pe_k_2': 191.128,
     'a_cmp_pe_v_2': 8.0,
     'c_w1_2': 8.0,
     'c_w2_2': 8.0,
     'c_ln_b_2': 5.739,
     'c_k_k_2': 7.438}
    for name, (base, spread) in spreads.items():
        noise = np.random.default_rng([zlib.crc32(name.encode()), seed]).standard_normal(out[name].shape)
        drawn = base * np.exp(spread * noise) if base else spread * noise
        out[name] = __import__('jax').numpy.asarray(drawn.astype(out[name].dtype))
    for name, factor in factors.items():
        out[name] = (out[name] * factor).astype(out[name].dtype)
    return out
```

```python
import math
from contextlib import ExitStack

import numpy as np
import concourse.bass as bass
from concourse import mybir

F32 = mybir.dt.float32
ALU = mybir.AluOpType
ACT = mybir.ActivationFunctionType
AX = mybir.AxisListType.X

P = 128
D = 1024
KT = D // P
SEQ = 256
N_META = 16
L1 = SEQ + N_META
Q_TILES_1 = [(0, 128), (128, 128), (256, 16)]
NEG = -1e30
EPS = [1e-6, 1e-5, 64e-5]

POOL_G = 4
POOL_WINDOWS = (2, 4, 8, 16)
HEADS = 8
NOPE = 128
ROPE = 64
V_DIM = 128
Q_LORA = 384
KV_LORA = 256
MLA_SCALE = (NOPE + ROPE) ** -0.5
N_GROUPS = 4
PER_GROUP = 8
N_EXP = N_GROUPS * PER_GROUP
D_EXP = 256

D_FF = 2816
FF_T = D_FF // P
GU_COLS = 256
NSA_KV = 2
NSA_GROUP = 4
HD = 64
CMP_BLOCK = 32
CMP_STRIDE = 16
N_CMP = (SEQ - CMP_BLOCK) // CMP_STRIDE + 1
SSD_HEADS = 16
SSD_GROUPS = 2
SSD_STATE = 128
SSD_CONV = 4
SSD_INNER = 1024
XBC = SSD_INNER + 2 * SSD_GROUPS * SSD_STATE
SPLITS = (512, 128, 128, 128, 128, 128, 128, 24, SSD_INNER, XBC, SSD_HEADS)
OFF = [sum(SPLITS[:i]) for i in range(len(SPLITS) + 1)]
RW_HEADS = 16
RC = 32
N_RC = SEQ // RC
GATE_LORA = 160

C_ID, C_ONE, C_CAUSAL, C_TRI, C_ROT, C_HEAD = 0, 128, 256, 384, 512, 640
C_COS, C_SIN = 768, 768 + L1
C_CNT = C_SIN + L1
C_CMPM = C_CNT + 4 * L1
C_RWK = C_CMPM + 2 * (N_CMP + 1)
C_IOTA = C_RWK + 2 * RC
C_HSEL = C_IOTA + 8
C_END = C_HSEL + 2


def constants():
    c = np.zeros((P, C_END), np.float32)
    p = np.arange(P)
    c[:, C_ID:C_ID + P] = np.eye(P)
    c[:, C_ONE:C_ONE + P] = 1.0
    c[:, C_CAUSAL:C_CAUSAL + P] = np.where(p[None, :] <= p[:, None], 0.0, NEG)
    c[:, C_TRI:C_TRI + P] = p[:, None] <= p[None, :]
    for m in range(P):
        if m % 64 < 32:
            c[m + 32, C_ROT + m] = -1.0
        else:
            c[m - 32, C_ROT + m] = 1.0
    c[:, C_HEAD:C_HEAD + P] = (p[:, None] // 64) == (p[None, :] // 64)
    inv = (np.float32(10000.0) ** (-np.arange(0, ROPE, 2, dtype=np.float32) / np.float32(ROPE))).astype(np.float32)
    ang = (np.arange(L1, dtype=np.float32)[None, :] * inv[p % 32][:, None]).astype(np.float32)
    c[:, C_COS:C_COS + L1] = np.cos(ang)
    c[:, C_SIN:C_SIN + L1] = np.sin(ang)
    t = np.arange(L1)
    for g, w in enumerate(POOL_WINDOWS):
        c[:, C_CNT + g * L1:C_CNT + (g + 1) * L1] = 1.0 / np.minimum(t + 1, w).astype(np.float32)
    for i in range(2):
        for n in range(N_CMP):
            c[:, C_CMPM + i * (N_CMP + 1) + n] = (n * CMP_STRIDE + CMP_BLOCK - 1) <= (p + i * P)
    tc = np.arange(RC)
    c[:, C_RWK:C_RWK + RC] = (p[:, None] % RC) < tc[None, :]
    c[:, C_RWK + RC:C_RWK + 2 * RC] = (p[:, None] % RC) <= tc[None, :]
    c[:, C_IOTA:C_IOTA + 8] = 8.0 - np.arange(8)
    c[:, C_HSEL:C_HSEL + 2] = (p[:, None] // 64) == np.arange(2)[None, :]
    return c


VECTORS = [("a_norm", 8), ("a_scale", 8), ("b_norm", 8), ("kv_norm", 8), ("ffn_norm", 16), ("final_norm", 8),
           ("norm_gains_2", 96), ("c_mu_2", 48), ("c_w0_2", 8), ("c_a0_2", 8), ("c_k_k_2", 8), ("c_k_a_2", 8),
           ("c_r_k_2", 8), ("kv_lat_norm", 2), ("b_q_norm", 3), ("b_conv_w_2", 48), ("b_conv_b_2", 12)]
VEC_AT = {}
_n = 0
for _name, _rows in VECTORS:
    VEC_AT[_name] = _n
    _n += _rows
VEC_ROWS = _n
VEC_TILES = -(-VEC_ROWS // P)


class Signal:

    def __init__(self, nc, name):
        self.sem = nc.alloc_semaphore(name)
        self.given = self.base = 0

    def begin(self):
        self.base = self.given
        return self

    def at(self, n):
        return self.sem, self.base + n

    def one(self):
        self.given += 1
        return self.sem, 1

    def dma(self):
        self.given += 16
        return self.sem, 16

    def now(self):
        return self.sem, self.given


class Core:

    def __init__(self, nc, ins):
        self.nc, self.ins = nc, ins
        self.signals, self.stage = {}, 0
        self.h = nc.alloc_sbuf_tensor("h", [P, KT, L1], F32)
        self.xn = nc.alloc_sbuf_tensor("xn", [P, KT, L1], F32)
        self.sq = nc.alloc_sbuf_tensor("sq", [P, KT, L1], F32)
        self.rs = nc.alloc_sbuf_tensor("rs", [P, 3, L1], F32)
        self.cst = nc.alloc_sbuf_tensor("cst", [P, C_END], F32)
        self.vec = nc.alloc_sbuf_tensor("vec", [P, VEC_TILES * P], F32)
        self.w = nc.alloc_sbuf_tensor("w", [P, 2, 4096], F32)
        self.ps = nc.alloc_psum_tensor("ps", [P, 8, 512], F32)
        self.eps = nc.alloc_sbuf_tensor("eps", [P, len(EPS)], F32)
        self.dve_step, self.act_step = Signal(nc, "dve_step"), Signal(nc, "act_step")

    def sig(self, name):
        if name not in self.signals:
            self.signals[name] = Signal(self.nc, name)
        return self.signals[name].begin()

    def next(self):
        self.stage += 1
        return self.stage

    def con(self, at, n=P):
        return self.cst[:, at:at + n]

    def col(self, name, i=0, n=1):
        at = VEC_AT[name] + i
        return self.vec[:, at:at + n]


def link(eng, signal, instruction):
    instruction.then_inc(*signal.one())
    eng.wait_ge(*signal.now())


def rms_norm(K, src, dst, gain, eps=1e-6, add_to=None, factor=1.0):
    nc = K.nc
    n, T = src.shape[1], src.shape[2]
    squared, summed, rooted = K.sig("squared"), K.sig("summed"), K.sig("rooted")
    with nc.Block() as block:
        @block.tensor
        def _(pe):
            pe.wait_ge(*squared.at(1))
            for k in range(n):
                mm = nc.tensor.matmul(K.ps[:, 0, 0:T], K.con(C_ONE), K.sq[:, k, 0:T], start=k == 0, stop=k == n - 1)
            mm.then_inc(*summed.one())

        @block.scalar
        def _(act):
            nc.scalar.activation(K.sq[:, 0:n, 0:T], src, ACT.Square).then_inc(*squared.one())
            act.wait_ge(*summed.at(1))
            nc.scalar.activation(K.rs[:, 0, 0:T], K.ps[:, 0, 0:T], ACT.Sqrt, bias=K.eps[:, EPS.index(eps):EPS.index(eps) + 1],
                                 scale=1.0 / (n * P)).then_inc(*rooted.one())

        @block.vector
        def _(dve):
            dve.wait_ge(*rooted.at(1))
            link(dve, K.dve_step, nc.vector.reciprocal(K.rs[:, 1, 0:T], K.rs[:, 0, 0:T]))
            if factor != 1.0:
                link(dve, K.dve_step, nc.vector.tensor_scalar(K.rs[:, 1, 0:T], K.rs[:, 1, 0:T], factor, None, ALU.mult))
            for k in range(n):
                last = nc.vector.scalar_tensor_tensor(out=dst[:, k], in0=src[:, k], scalar=gain[:, k:k + 1],
                                                      in1=K.rs[:, 1, 0:T], op0=ALU.mult, op1=ALU.mult)
            if add_to is not None:
                link(dve, K.dve_step, last)
                nc.vector.tensor_tensor(add_to, add_to, dst, ALU.add)


def feature_linear(K, w, x, T, store, by="vector", pieces=None):
    nc = K.nc
    rows, N = w.shape
    kr = min(rows, P)
    nk = rows // kr
    wide = min(4096 // nk // P * P, -(-N // P) * P)
    mt = -(-N // P)
    per = wide // P
    loads = -(-N // wide)
    view = w.rearrange("(k p) n -> p k n", p=kr)
    loaded = [K.sig("w_loaded_0"), K.sig("w_loaded_1")]
    made, stored = K.sig("tile_made"), K.sig("tile_stored")

    with nc.Block() as block:
        @block.sync
        def _(sp):
            for b in range(loads):
                cw = min(wide, N - b * wide)
                if b >= 2:
                    sp.wait_ge(*made.at((b - 1) * per))
                slot = K.w[0:kr, b % 2, 0:nk * cw].rearrange("p (k n) -> p k n", k=nk)
                for to, at, n in pieces or [(0, b * wide, cw)]:
                    sp.dma_start(slot[:, :, to:to + n], view[:, :, at:at + n]).then_inc(*loaded[b % 2].dma())

        @block.tensor
        def _(pe):
            for m in range(mt):
                b = m // per
                cw = min(wide, N - b * wide)
                if m % per == 0:
                    pe.wait_ge(*loaded[b % 2].at(16 * (b // 2 + 1) * len(pieces or "1")))
                if m >= 8:
                    pe.wait_ge(*stored.at(m - 7))
                mw = min(P, N - m * P)
                at = m * P - b * wide
                for k in range(nk):
                    wk = K.w[0:kr, b % 2, k * cw:(k + 1) * cw]
                    mm = nc.tensor.matmul(K.ps[0:mw, m % 8, 0:T], wk[:, at:at + mw], x(k),
                                          start=k == 0, stop=k == nk - 1)
                mm.then_inc(*made.one())

        def take(eng):
            for m in range(mt):
                eng.wait_ge(*made.at(m + 1))
                store(m, K.ps[0:min(P, N - m * P), m % 8, 0:T]).then_inc(*stored.one())

        if by == "vector":
            @block.vector
            def _(dve):
                take(dve)
        else:
            @block.scalar
            def _(act):
                take(act)


def token_linear(K, w, x, nk, tiles, store, by="vector"):
    nc = K.nc
    rows, N = w.shape
    kr = min(rows, P)
    nk = rows // kr
    view = w.rearrange("(k p) n -> p k n", p=kr)
    blocks = [(c, min(512, N - c)) for c in range(0, N, 512)]
    nt = len(tiles)
    loaded = [K.sig("w_loaded_0"), K.sig("w_loaded_1")]
    made, stored = K.sig("tile_made"), K.sig("tile_stored")

    with nc.Block() as block:
        @block.sync
        def _(sp):
            for b, (c, cw) in enumerate(blocks):
                if b >= 2:
                    sp.wait_ge(*made.at((b - 1) * nt))
                sp.dma_start(K.w[0:kr, b % 2, 0:nk * cw].rearrange("p (k n) -> p k n", k=nk),
                             view[:, :, c:c + cw]).then_inc(*loaded[b % 2].dma())

        @block.tensor
        def _(pe):
            n = 0
            for b, (c, cw) in enumerate(blocks):
                pe.wait_ge(*loaded[b % 2].at(16 * (b // 2 + 1)))
                for t0, tn in tiles:
                    if n >= 8:
                        pe.wait_ge(*stored.at(n - 7))
                    for k in range(nk):
                        mm = nc.tensor.matmul(K.ps[0:tn, n % 8, 0:cw], x(k, t0, tn), K.w[0:kr, b % 2, k * cw:(k + 1) * cw],
                                              start=k == 0, stop=k == nk - 1)
                    mm.then_inc(*made.one())
                    n += 1

        def take(eng):
            n = 0
            for c, cw in blocks:
                for i, (t0, tn) in enumerate(tiles):
                    eng.wait_ge(*made.at(n + 1))
                    store(i, c, cw, K.ps[0:tn, n % 8, 0:cw]).then_inc(*stored.one())
                    n += 1

        if by == "vector":
            @block.vector
            def _(dve):
                take(dve)
        else:
            @block.scalar
            def _(act):
                take(act)


def load_all(K):
    nc, I = K.nc, K.ins
    with ExitStack() as ctx:
        rows = ctx.enter_context(nc.sbuf_tensor("vec_rows", [P, VEC_TILES, P], F32))
        tok = ctx.enter_context(nc.sbuf_tensor("tok_rows", [P, 3, D], F32))
        given, blank = K.sig("rows_given"), K.sig("rows_blank")
        made, stored = K.sig("tile_made"), K.sig("tile_stored")
        n_dma = 16 * (1 + 2 + len(VECTORS) + 2)
        pieces = []
        for name, n in VECTORS:
            flat = I[name]
            dims = " ".join(f"a{i}" for i in range(len(flat.shape)))
            flat = flat.rearrange(f"{dims} -> ({dims})").rearrange("(r c) -> r c", c=P)
            at, done = VEC_AT[name], 0
            while done < n:
                take = min(n - done, P - (at + done) % P)
                pieces.append(((at + done) // P, (at + done) % P, take, flat[done:done + take]))
                done += take
        block = ctx.enter_context(nc.Block())

        @block.sync
        def _(sp):
            sp.dma_start(K.cst[:], I["constants"]).then_inc(*given.dma())
            sp.dma_start(tok[0:N_META, 0], I["meta_tokens"]).then_inc(*given.dma())
            sp.dma_start(tok[N_META:P, 0], I["x"][0, 0:P - N_META]).then_inc(*given.dma())
            sp.dma_start(tok[:, 1], I["x"][0, P - N_META:2 * P - N_META]).then_inc(*given.dma())
            sp.dma_start(tok[0:N_META, 2], I["x"][0, 2 * P - N_META:SEQ]).then_inc(*given.dma())
            sp.wait_ge(*blank.at(1))
            for tile, row, n, src in pieces:
                sp.dma_start(rows[row:row + n, tile], src).then_inc(*given.dma())

        @block.vector
        def _(dve):
            for i, e in enumerate(EPS):
                nc.vector.memset(K.eps[:, i:i + 1], e)
            nc.vector.memset(rows[:], 0.0).then_inc(*blank.one())
            for n in range(VEC_TILES + 2 * 3):
                dve.wait_ge(*made.at(n + 1))
                if n < VEC_TILES:
                    last = nc.vector.tensor_copy(K.vec[:, n * P:(n + 1) * P], K.ps[:, n % 8, 0:P])
                else:
                    i, half = divmod(n - VEC_TILES, 2)
                    t0, tn = Q_TILES_1[i]
                    last = nc.vector.tensor_copy(K.h[:, 4 * half:4 * half + 4, t0:t0 + tn],
                                                 K.ps[:, n % 8, :].rearrange("p (k t) -> p k t", k=4)[:, :, 0:tn])
                last.then_inc(*stored.one())

        @block.tensor
        def _(pe):
            pe.wait_ge(*given.now())
            n = 0
            for i in range(VEC_TILES):
                nc.tensor.transpose(K.ps[:, n % 8, 0:P], rows[:, i], K.con(C_ID)).then_inc(*made.one())
                n += 1
            for i, (t0, tn) in enumerate(Q_TILES_1):
                for half in range(2):
                    if n >= 8:
                        pe.wait_ge(*stored.at(n - 7))
                    for k in range(4):
                        mm = nc.tensor.transpose(K.ps[:, n % 8, k * P:k * P + tn],
                                                 tok[0:tn, i, (4 * half + k) * P:(4 * half + k + 1) * P],
                                                 K.cst[0:tn, C_ID:C_ID + tn])
                    mm.then_inc(*made.one())
                    n += 1


def pool_mixer(K):
    nc, I = K.nc, K.ins
    gt = KT // POOL_G
    with ExitStack() as ctx:
        pad = max(POOL_WINDOWS)
        run = ctx.enter_context(nc.sbuf_tensor("run", [P, 2, KT, pad + L1], F32))
        wg = ctx.enter_context(nc.sbuf_tensor("pool_w", [P, POOL_G * gt, gt * P], F32))
        given, pooled = K.sig("rows_given"), K.sig("pooled")
        made, stored = K.sig("tile_made"), K.sig("tile_stored")
        block = ctx.enter_context(nc.Block())

        @block.sync
        def _(sp):
            sp.dma_start(wg[:], I["a_w"][0].rearrange("g (k p) n -> p (g k) n", p=P)).then_inc(*given.dma())

        @block.vector
        def _(dve):
            nc.vector.memset(run[:, :, :, 0:pad], 0.0)
            link(dve, K.dve_step, nc.vector.tensor_copy(run[:, 0, :, pad:], K.xn[:]))
            at = [0, 0, 0, 0]
            src, width = 0, 1
            for g, w in enumerate(POOL_WINDOWS):
                lo = g * gt
                link(dve, K.dve_step, nc.vector.tensor_tensor(
                    run[:, 1 - src, lo:, pad:], run[:, src, lo:, pad:], run[:, src, lo:, pad - width:pad - width + L1], ALU.add))
                src, width = 1 - src, w
                at[g] = src
                for k in range(lo, lo + gt):
                    link(dve, K.dve_step, nc.vector.tensor_tensor(K.sq[:, k], run[:, src, k, pad:],
                                                                  K.con(C_CNT + g * L1, L1), ALU.mult))
                last = nc.vector.tensor_tensor(K.sq[:, lo:lo + gt], K.sq[:, lo:lo + gt], K.xn[:, lo:lo + gt], ALU.subtract)
                last.then_inc(*pooled.one())
            for m in range(KT):
                dve.wait_ge(*made.at(m + 1))
                nc.vector.scalar_tensor_tensor(out=K.h[:, m], in0=K.ps[:, m, 0:L1], scalar=K.col("a_scale", m),
                                               in1=K.h[:, m], op0=ALU.mult, op1=ALU.add)

        @block.tensor
        def _(pe):
            pe.wait_ge(*given.at(16))
            for g in range(POOL_G):
                pe.wait_ge(*pooled.at(g + 1))
                for m in range(gt):
                    for k in range(gt):
                        mm = nc.tensor.matmul(K.ps[:, g * gt + m, 0:L1], wg[:, g * gt + k, m * P:(m + 1) * P], K.sq[:, g * gt + k],
                                              start=k == 0, stop=k == gt - 1)
                    mm.then_inc(*made.one())


def first_of(dve, K, mask, score, tmp, top):
    nc, n = K.nc, mask.shape[2]
    iota = K.con(C_IOTA + 8 - n, n).rearrange("p (a n) -> p a n", a=1).to_broadcast([P, 3, n])
    link(dve, K.dve_step, nc.vector.tensor_tensor(score, mask, iota, ALU.mult))
    link(dve, K.dve_step, nc.vector.reduce_max(top, score, AX))
    link(dve, K.dve_step, nc.vector.tensor_tensor(mask, score, top.to_broadcast([P, 3, n]), ALU.is_equal))


def moe(K, layer, gates_dram):
    nc, I = K.nc, K.ins
    nr = N_GROUPS + N_EXP
    with ExitStack() as ctx:
        def sb(name, shape):
            return ctx.enter_context(nc.sbuf_tensor(f"{name}_{layer}", shape, F32))
        wr = sb("wr", [P, KT, nr])
        bias = sb("rbias", [P, nr])
        lg = sb("lg", [P, 3, nr])
        small = sb("small", [P, 3, 64])
        gate = sb("gate", [P, 3, N_EXP])
        gT = sb("gT", [N_EXP, L1])
        given, logits, routed, turned = K.sig("rows_given"), K.sig("logits"), K.sig("routed"), K.sig("turned")
        copied, ex, exd, saved = K.sig("copied"), K.sig("exp_asked"), K.sig("exp_done"), K.sig("gates_saved")
        with nc.Block() as block:
            @block.sync
            def _(sp):
                with nc.allow_non_contiguous_dma(reason="router columns are narrow"):
                    sp.dma_start(wr[:, :, 0:N_GROUPS], I["router_g"][layer].rearrange("(k p) n -> p k n", p=P)).then_inc(*given.dma())
                    sp.dma_start(wr[:, :, N_GROUPS:], I["router_e"][layer].rearrange("(k p) n -> p k n", p=P)).then_inc(*given.dma())
                    sp.dma_start(bias[:, 0:N_GROUPS], I["router_g_bias"][layer:layer + 1].to_broadcast([P, N_GROUPS])).then_inc(*given.dma())
                    sp.dma_start(bias[:, N_GROUPS:], I["router_e_bias"][layer:layer + 1].to_broadcast([P, N_EXP])).then_inc(*given.dma())
                sp.wait_ge(*copied.at(1))
                sp.dma_start(gates_dram, gT[:]).then_inc(*saved.dma())
                sp.wait_ge(*saved.at(16))

            @block.tensor
            def _(pe):
                pe.wait_ge(*given.at(64))
                for i, (t0, tn) in enumerate(Q_TILES_1):
                    for k in range(KT):
                        mm = nc.tensor.matmul(K.ps[0:tn, i, 0:nr], K.xn[:, k, t0:t0 + tn], wr[:, k], start=k == 0, stop=k == KT - 1)
                mm.then_inc(*logits.one())
                pe.wait_ge(*routed.at(1))
                for i, (t0, tn) in enumerate(Q_TILES_1):
                    mm = nc.tensor.transpose(K.ps[0:N_EXP, 4, t0:t0 + tn], gate[0:tn, i], K.cst[0:tn, C_ID:C_ID + tn])
                mm.then_inc(*turned.one())

            @block.scalar
            def _(act):
                act.wait_ge(*ex.at(1))
                nc.scalar.activation(small[:, :, 4:8], small[:, :, 0:4], ACT.Exp).then_inc(*exd.one())
                act.wait_ge(*ex.at(2))
                nc.scalar.activation(small[:, :, 57:58], small[:, :, 56:57], ACT.Exp).then_inc(*exd.one())

            @block.vector
            def _(dve):
                def do(ins):
                    link(dve, K.dve_step, ins)
                v = nc.vector
                S = lambda a, b: small[:, :, a:b]
                do(v.memset(lg[:], 0.0))
                dve.wait_ge(*given.at(64))
                dve.wait_ge(*logits.at(1))
                for i, (t0, tn) in enumerate(Q_TILES_1):
                    do(v.tensor_tensor(lg[0:tn, i], K.ps[0:tn, i, 0:nr], bias[0:tn], ALU.add))
                G = lg[:, :, 0:N_GROUPS]
                do(v.reduce_max(S(8, 9), G, AX))
                do(v.tensor_tensor(S(0, 4), G, S(8, 9).to_broadcast([P, 3, 4]), ALU.subtract))
                v.tensor_tensor(S(12, 16), G, S(8, 9).to_broadcast([P, 3, 4]), ALU.is_equal).then_inc(*ex.one())
                dve.wait_ge(*ex.at(1))
                first_of(dve, K, S(12, 16), S(16, 20), None, S(9, 10))
                for g in range(N_GROUPS):
                    E = lg[:, :, N_GROUPS + g * PER_GROUP:N_GROUPS + (g + 1) * PER_GROUP]
                    m = S(12 + g, 13 + g).to_broadcast([P, 3, PER_GROUP])
                    if g == 0:
                        do(v.tensor_tensor(S(24, 32), E, m, ALU.mult))
                    else:
                        do(v.tensor_tensor(S(32, 40), E, m, ALU.mult))
                        do(v.tensor_tensor(S(24, 32), S(24, 32), S(32, 40), ALU.add))
                do(v.reduce_max(S(10, 11), S(24, 32), AX))
                do(v.tensor_tensor(S(40, 48), S(24, 32), S(10, 11).to_broadcast([P, 3, 8]), ALU.is_equal))
                first_of(dve, K, S(40, 48), S(32, 40), None, S(9, 10))
                do(v.scalar_tensor_tensor(out=S(24, 32), in0=S(40, 48), scalar=NEG, in1=S(24, 32), op0=ALU.mult, op1=ALU.add))
                do(v.reduce_max(S(11, 12), S(24, 32), AX))
                do(v.tensor_tensor(S(48, 56), S(24, 32), S(11, 12).to_broadcast([P, 3, 8]), ALU.is_equal))
                first_of(dve, K, S(48, 56), S(32, 40), None, S(9, 10))
                v.tensor_tensor(S(56, 57), S(11, 12), S(10, 11), ALU.subtract).then_inc(*ex.one())
                dve.wait_ge(*exd.at(2))
                do(v.reduce_sum(S(58, 59), S(4, 8), AX))
                do(v.tensor_scalar(S(59, 60), S(57, 58), 1.0, None, ALU.add))
                do(v.tensor_tensor(S(60, 61), S(58, 59), S(59, 60), ALU.mult))
                do(v.reciprocal(S(61, 62), S(60, 61)))
                do(v.tensor_tensor(S(62, 63), S(61, 62), S(57, 58), ALU.mult))
                do(v.tensor_tensor(S(32, 40), S(40, 48), S(61, 62).to_broadcast([P, 3, 8]), ALU.mult))
                do(v.tensor_tensor(S(24, 32), S(48, 56), S(62, 63).to_broadcast([P, 3, 8]), ALU.mult))
                do(v.tensor_tensor(S(32, 40), S(32, 40), S(24, 32), ALU.add))
                for g in range(N_GROUPS):
                    last = v.tensor_tensor(gate[:, :, g * PER_GROUP:(g + 1) * PER_GROUP], S(32, 40),
                                           S(12 + g, 13 + g).to_broadcast([P, 3, PER_GROUP]), ALU.mult)
                last.then_inc(*routed.one())
                dve.wait_ge(*turned.at(1))
                v.tensor_copy(gT[:], K.ps[0:N_EXP, 4, 0:L1]).then_inc(*copied.one())
    experts(K, layer, gates_dram)


def experts(K, layer, gates_dram):
    nc, I = K.nc, K.ins
    ET = D_EXP // P
    with ExitStack() as ctx:
        def sb(name, shape):
            return ctx.enter_context(nc.sbuf_tensor(f"{name}_{layer}", shape, F32))
        wgu = sb("wgu", [P, 2, 2, KT, D_EXP])
        wd = sb("wd", [P, 2, ET, D])
        gb = sb("gb", [P, 2, L1])
        sil = sb("sil", [P, 2, ET, L1])
        hid = sb("hid", [P, 2, ET, L1])
        gu_in = [K.sig("gu_in_0"), K.sig("gu_in_1")]
        d_in = [K.sig("d_in_0"), K.sig("d_in_1")]
        gu_made, hid_made, d_made, d_taken = K.sig("gu_made"), K.sig("hid_made"), K.sig("d_made"), K.sig("d_taken")
        silu_made, gated = K.sig("silu_made"), K.sig("gated")
        wg_v = I["w_gate"][layer].rearrange("e (k p) n -> p e k n", p=P)
        wu_v = I["w_up"][layer].rearrange("e (k p) n -> p e k n", p=P)
        wd_v = I["w_down"][layer].rearrange("e (k p) n -> p e k n", p=P)
        block = ctx.enter_context(nc.Block())

        @block.sync
        def _(sp):
            def load(e, s, i, first):
                if not first:
                    sp.wait_ge(gu_made.sem, gu_made.base + ET * (e - 1))
                    sp.wait_ge(hid_made.sem, hid_made.base + ET * (e - 1))
                one = bass.ds(e, 1)
                sp.dma_start(wgu[:, s, 0], wg_v[:, one]).then_inc(gu_in[s].sem, 16)
                sp.dma_start(wgu[:, s, 1], wu_v[:, one]).then_inc(gu_in[s].sem, 16)
                sp.dma_start(gb[:, s], gates_dram[one].to_broadcast([P, L1])).then_inc(gu_in[s].sem, 16)
                if not first:
                    sp.wait_ge(d_made.sem, d_made.base + KT * (e - 1))
                sp.dma_start(wd[:, s], wd_v[:, one]).then_inc(d_in[s].sem, 16)
            load(0, 0, 0, True)
            load(1, 1, 0, True)
            with sp.Fori(1, N_EXP // 2) as i:
                load(2 * i, 0, i, False)
                load(2 * i + 1, 1, i, False)

        @block.tensor
        def _(pe):
            def expert(e, s, i, first):
                pe.wait_ge(gu_in[s].sem, gu_in[s].base + 48 * i + 48)
                for m in range(ET):
                    if not first:
                        pe.wait_ge(hid_made.sem, hid_made.base + ET * (e - 1) + m + 1)
                    for j in range(2):
                        for k in range(KT):
                            mm = nc.tensor.matmul(K.ps[:, 2 * j + m, 0:L1], wgu[:, s, j, k, m * P:(m + 1) * P], K.xn[:, k],
                                                  start=k == 0, stop=k == KT - 1)
                    mm.then_inc(gu_made.sem, 1)
                pe.wait_ge(d_in[s].sem, d_in[s].base + 16 * i + 16)
                pe.wait_ge(hid_made.sem, hid_made.base + ET * e + ET)
                for m in range(KT):
                    if not (first and m < 4):
                        pe.wait_ge(d_taken.sem, d_taken.base + KT * e + m - 3)
                    for k in range(ET):
                        mm = nc.tensor.matmul(K.ps[:, 4 + m % 4, 0:L1], wd[:, s, k, m * P:(m + 1) * P], hid[:, s, k],
                                              start=k == 0, stop=k == ET - 1)
                    mm.then_inc(d_made.sem, 1)
            expert(0, 0, 0, True)
            expert(1, 1, 0, False)
            with pe.Fori(1, N_EXP // 2) as i:
                expert(2 * i, 0, i, False)
                expert(2 * i + 1, 1, i, False)

        @block.scalar
        def _(act):
            def expert(e, s):
                for m in range(ET):
                    act.wait_ge(gu_made.sem, gu_made.base + ET * e + m + 1)
                    nc.scalar.activation(sil[:, s, m], K.ps[:, m, 0:L1], ACT.Silu).then_inc(silu_made.sem, 1)
            with act.Fori(0, N_EXP // 2) as i:
                expert(2 * i, 0)
                expert(2 * i + 1, 1)

        @block.vector
        def _(dve):
            def expert(e, s, i):
                dve.wait_ge(gu_in[s].sem, gu_in[s].base + 48 * i + 48)
                for m in range(ET):
                    dve.wait_ge(silu_made.sem, silu_made.base + ET * e + m + 1)
                    nc.vector.tensor_tensor(sil[:, s, m], sil[:, s, m], gb[:, s], ALU.mult).then_inc(gated.sem, 1)
                    dve.wait_ge(gated.sem, gated.base + ET * e + m + 1)
                    nc.vector.tensor_tensor(hid[:, s, m], sil[:, s, m], K.ps[:, 2 + m, 0:L1], ALU.mult).then_inc(hid_made.sem, 1)
                for m in range(KT):
                    dve.wait_ge(d_made.sem, d_made.base + KT * e + m + 1)
                    nc.vector.tensor_tensor(K.h[:, m], K.h[:, m], K.ps[:, 4 + m % 4, 0:L1], ALU.add).then_inc(d_taken.sem, 1)
            with dve.Fori(0, N_EXP // 2) as i:
                expert(2 * i, 0, i)
                expert(2 * i + 1, 1, i)
        for s in range(2):
            gu_in[s].given += 48 * N_EXP // 2
            d_in[s].given += 16 * N_EXP // 2
        for sig, n in ((gu_made, ET), (hid_made, ET), (silu_made, ET), (gated, ET), (d_made, KT), (d_taken, KT)):
            sig.given += n * N_EXP


def store_tokens(K, out):
    nc = K.nc
    with ExitStack() as ctx:
        tok = ctx.enter_context(nc.sbuf_tensor("tok_out", [P, 2, D], F32))
        made, stored, saved = K.sig("tile_made"), K.sig("tile_stored"), K.sig("out_saved")
        block = ctx.enter_context(nc.Block())

        @block.tensor
        def _(pe):
            for n in range(4):
                for k in range(4):
                    mm = nc.tensor.transpose(K.ps[:, n, k * P:(k + 1) * P], K.h[:, 4 * (n % 2) + k, (n // 2) * P:(n // 2 + 1) * P],
                                             K.con(C_ID))
                mm.then_inc(*made.one())

        @block.vector
        def _(dve):
            for n in range(4):
                dve.wait_ge(*made.at(n + 1))
                nc.vector.tensor_copy(tok[:, n // 2, 512 * (n % 2):512 * (n % 2) + 512], K.ps[:, n]).then_inc(*stored.one())

        @block.sync
        def _(sp):
            for i in range(2):
                sp.wait_ge(*stored.at(2 * i + 2))
                sp.dma_start(out[0, i * P:(i + 1) * P], tok[:, i]).then_inc(*saved.dma())
            sp.wait_ge(*saved.now())


def rope(K, x, out, rows, T):
    nc = K.nc
    n = len(x)
    with ExitStack() as ctx:
        made, taken = K.sig("tile_made"), K.sig("tile_stored")
        block = ctx.enter_context(nc.Block())

        @block.tensor
        def _(pe):
            for i in range(n):
                if i >= 8:
                    pe.wait_ge(*taken.at(i - 7))
                nc.tensor.matmul(K.ps[0:rows, i % 8, 0:T], K.cst[0:rows, C_ROT:C_ROT + rows], x[i], start=True, stop=True).then_inc(*made.one())

        @block.vector
        def _(dve):
            for i in range(n):
                dve.wait_ge(*made.at(i + 1))
                rot = K.rs[0:rows, i % 2, 0:T]
                nc.vector.tensor_tensor(rot, K.ps[0:rows, i % 8, 0:T], K.cst[0:rows, C_SIN:C_SIN + T], ALU.mult).then_inc(*taken.one())
                link(dve, K.dve_step, nc.vector.tensor_tensor(out[i], x[i], K.cst[0:rows, C_COS:C_COS + T], ALU.mult))
                link(dve, K.dve_step, nc.vector.tensor_tensor(out[i], out[i], rot, ALU.add))


def latent_kv(K, ctx):
    nc, I = K.nc, K.ins
    kn = ctx.enter_context(nc.sbuf_tensor("mla_kn", [P, HEADS, L1], F32))
    kr = ctx.enter_context(nc.sbuf_tensor("mla_kr", [ROPE, L1], F32))
    v = ctx.enter_context(nc.sbuf_tensor("mla_v", [P, 3, HEADS * V_DIM], F32))
    rms_norm(K, K.h[:], K.xn, K.col("kv_norm", 0, KT))
    with ExitStack() as inner:
        c = inner.enter_context(nc.sbuf_tensor("lat_c", [P, 3, L1], F32))
        cn = inner.enter_context(nc.sbuf_tensor("lat_cn", [P, 2, L1], F32))
        feature_linear(K, I["w_dkv"], lambda k: K.xn[:, k], L1,
                       lambda m, ps: nc.vector.tensor_copy(c[0:ps.shape[0], m], ps))
        rms_norm(K, c[:, 0:2], cn, K.col("kv_lat_norm", 0, 2))
        rope(K, [c[0:ROPE, 2]], [kr[:]], ROPE, L1)
        feature_linear(K, I["w_uk"].rearrange("r h d -> r (h d)"), lambda k: cn[:, k], L1,
                       lambda m, ps: nc.vector.tensor_copy(kn[:, m], ps))
        token_linear(K, I["w_uv"].rearrange("r h d -> r (h d)"), lambda k, t0, tn: cn[:, k, t0:t0 + tn], 2, Q_TILES_1,
                     lambda i, at, n, ps: nc.scalar.copy(v[0:ps.shape[0], i, at:at + n], ps), by="scalar")
    return kn, kr, v


def mla(K, kv):
    nc, I = K.nc, K.ins
    kn, kr, v = kv
    rms_norm(K, K.h[:], K.xn, K.col("b_norm", 0, KT))
    with ExitStack() as ctx:
        def sb(name, shape):
            return ctx.enter_context(nc.sbuf_tensor(name, shape, F32))
        qn, qr = sb("mla_qn", [P, HEADS, L1]), sb("mla_qr", [ROPE, HEADS, L1])
        with ExitStack() as inner:
            cq = inner.enter_context(nc.sbuf_tensor("cq", [P, 3, L1], F32))
            cqn = inner.enter_context(nc.sbuf_tensor("cqn", [P, 3, L1], F32))
            feature_linear(K, I["b_w_dq"][0], lambda k: K.xn[:, k], L1,
                           lambda m, ps: nc.vector.tensor_copy(cq[:, m], ps))
            rms_norm(K, cq[:], cqn, K.col("b_q_norm", 0, 3))
            latent_queries(K, cqn, qn, qr)
        rope(K, [qr[:, h] for h in range(HEADS)], [K.xn[0:ROPE, h] for h in range(HEADS)], ROPE, L1)
        oT = sb("mla_oT", [P, HEADS, L1])
        mla_attention(K, qn, K.xn, kn, kr, v, oT)
        feature_linear(K, I["b_w_o"][0], lambda k: oT[:, k], L1,
                       lambda m, ps: nc.vector.tensor_tensor(K.h[:, m], K.h[:, m], ps, ALU.add))


def latent_queries(K, cqn, qn, qr):
    nc, I = K.nc, K.ins
    kq = Q_LORA // P
    w = NOPE + ROPE
    with ExitStack() as ctx:
        wq = ctx.enter_context(nc.sbuf_tensor("wq", [P, kq, HEADS * w], F32))
        given, made, taken = K.sig("rows_given"), K.sig("tile_made"), K.sig("tile_stored")
        block = ctx.enter_context(nc.Block())

        @block.sync
        def _(sp):
            sp.dma_start(wq[:], I["b_w_uq"][0].rearrange("(k p) h d -> p k (h d)", p=P)).then_inc(*given.dma())

        @block.tensor
        def _(pe):
            pe.wait_ge(*given.at(16))
            for n in range(2 * HEADS):
                h, r = divmod(n, 2)
                if n >= 8:
                    pe.wait_ge(*taken.at(n - 7))
                at, mw = h * w + NOPE * r, (NOPE, ROPE)[r]
                for k in range(kq):
                    mm = nc.tensor.matmul(K.ps[0:mw, n % 8, 0:L1], wq[:, k, at:at + mw], cqn[:, k], start=k == 0, stop=k == kq - 1)
                mm.then_inc(*made.one())

        @block.vector
        def _(dve):
            for n in range(2 * HEADS):
                h, r = divmod(n, 2)
                dve.wait_ge(*made.at(n + 1))
                nc.vector.tensor_copy((qn, qr)[r][:, h], K.ps[0:(NOPE, ROPE)[r], n % 8, 0:L1]).then_inc(*taken.one())


def mla_attention(K, qn, qr, kn, kr, v, oT):
    nc = K.nc
    units = [(h, i) for h in range(HEADS) for i in range(3)]
    n = len(units)
    keys = [t0 + tn for t0, tn in Q_TILES_1]
    with ExitStack() as ctx:
        def sb(name, shape):
            return ctx.enter_context(nc.sbuf_tensor(name, shape, F32))
        S, Pr, PT = sb("att_s", [P, 3, L1]), sb("att_p", [P, 3, L1]), sb("att_pt", [P, 2, 3, P])
        st = sb("att_stat", [P, 3, 4])
        s_made, s_ready, e_made, p_ready = K.sig("s_made"), K.sig("s_ready"), K.sig("e_made"), K.sig("p_ready")
        t_made, t_taken, pv_made, o_taken = K.sig("t_made"), K.sig("t_taken"), K.sig("pv_made"), K.sig("o_taken")
        block = ctx.enter_context(nc.Block())

        @block.tensor
        def _(pe):
            for u in range(n + 2):
                if u < n:
                    h, i = units[u]
                    t0, tn = Q_TILES_1[i]
                    if u >= 3:
                        pe.wait_ge(*s_ready.at(u - 2))
                    nc.tensor.matmul(K.ps[0:tn, u % 3, 0:keys[i]], qn[:, h, t0:t0 + tn], kn[:, h, 0:keys[i]], start=True, stop=False)
                    nc.tensor.matmul(K.ps[0:tn, u % 3, 0:keys[i]], qr[0:ROPE, h, t0:t0 + tn], kr[0:ROPE, 0:keys[i]],
                                     start=False, stop=True).then_inc(*s_made.one())
                if 1 <= u <= n:
                    w = u - 1
                    i = units[w][1]
                    tn = Q_TILES_1[i][1]
                    pe.wait_ge(*p_ready.at(w + 1))
                    if w >= 2:
                        pe.wait_ge(*t_taken.at(w - 1))
                    for j in range(i + 1):
                        k0, kn_ = Q_TILES_1[j]
                        mm = nc.tensor.transpose(K.ps[0:kn_, 3 + w % 2, j * P:j * P + tn], Pr[0:tn, w % 3, k0:k0 + kn_],
                                                 K.cst[0:tn, C_ID:C_ID + tn])
                    mm.then_inc(*t_made.one())
                if u >= 2:
                    w = u - 2
                    h, i = units[w]
                    t0, tn = Q_TILES_1[i]
                    pe.wait_ge(*t_taken.at(w + 1))
                    if i == 0 and h >= 2:
                        pe.wait_ge(*o_taken.at(h - 1))
                    for j in range(i + 1):
                        kn_ = Q_TILES_1[j][1]
                        mm = nc.tensor.matmul(K.ps[:, 5 + h % 2, t0:t0 + tn], v[0:kn_, j, h * V_DIM:(h + 1) * V_DIM],
                                              PT[0:kn_, w % 2, j, 0:tn], start=j == 0, stop=j == i)
                    mm.then_inc(*pv_made.one())

        @block.vector
        def _(dve):
            for u in range(n + 4):
                if u < n:
                    h, i = units[u]
                    t0, tn = Q_TILES_1[i]
                    dve.wait_ge(*s_made.at(u + 1))
                    if u >= 3:
                        dve.wait_ge(*e_made.at(u - 2))
                    if i:
                        nc.vector.tensor_scalar(S[0:tn, u % 3, 0:t0], K.ps[0:tn, u % 3, 0:t0], MLA_SCALE, None, ALU.mult)
                    link(dve, K.dve_step, nc.vector.scalar_tensor_tensor(
                        out=S[0:tn, u % 3, t0:t0 + tn], in0=K.ps[0:tn, u % 3, t0:t0 + tn], scalar=MLA_SCALE,
                        in1=K.cst[0:tn, C_CAUSAL:C_CAUSAL + tn], op0=ALU.mult, op1=ALU.add))
                    link(dve, K.dve_step, nc.vector.reduce_max(st[0:tn, u % 3, 3:4], S[0:tn, u % 3, 0:keys[i]], AX))
                    nc.vector.tensor_scalar(st[0:tn, u % 3, 0:1], st[0:tn, u % 3, 3:4], -1.0, None, ALU.mult).then_inc(*s_ready.one())
                if 1 <= u <= n:
                    w = u - 1
                    i = units[w][1]
                    tn = Q_TILES_1[i][1]
                    dve.wait_ge(*e_made.at(w + 1))
                    link(dve, K.dve_step, nc.vector.reciprocal(st[0:tn, w % 3, 2:3], st[0:tn, w % 3, 1:2]))
                    nc.vector.tensor_scalar(Pr[0:tn, w % 3, 0:keys[i]], Pr[0:tn, w % 3, 0:keys[i]], st[0:tn, w % 3, 2:3],
                                            None, ALU.mult).then_inc(*p_ready.one())
                if u >= 4 and units[u - 4][1] == 2:
                    h = units[u - 4][0]
                    dve.wait_ge(*pv_made.at(u - 3))
                    nc.vector.tensor_copy(oT[:, h], K.ps[:, 5 + h % 2, 0:L1]).then_inc(*o_taken.one())

        @block.scalar
        def _(act):
            for u in range(n + 1):
                if u < n:
                    i = units[u][1]
                    tn = Q_TILES_1[i][1]
                    act.wait_ge(*s_ready.at(u + 1))
                    if u >= 3:
                        act.wait_ge(*t_made.at(u - 2))
                    nc.scalar.activation(Pr[0:tn, u % 3, 0:keys[i]], S[0:tn, u % 3, 0:keys[i]], ACT.Exp, bias=st[0:tn, u % 3, 0:1],
                                         accum_out=st[0:tn, u % 3, 1:2]).then_inc(*e_made.one())
                if u >= 1:
                    w = u - 1
                    i = units[w][1]
                    tn = Q_TILES_1[i][1]
                    act.wait_ge(*t_made.at(w + 1))
                    if w >= 2:
                        act.wait_ge(*pv_made.at(w - 1))
                    full = min(i + 1, 2)
                    view = K.ps[:, 3 + w % 2, :].rearrange("p (j t) -> p j t", j=4)
                    last = nc.scalar.copy(PT[:, w % 2, 0:full, 0:tn], view[:, 0:full, 0:tn])
                    if i == 2:
                        kn_ = Q_TILES_1[2][1]
                        last = nc.scalar.copy(PT[0:kn_, w % 2, 2, 0:tn], K.ps[0:kn_, 3 + w % 2, 2 * P:2 * P + tn])
                    last.then_inc(*t_taken.one())


def final_norm(K):
    nc = K.nc
    rms_norm(K, K.h[:], K.xn, K.col("final_norm", 0, KT))
    with nc.Block() as block:
        @block.vector
        def _(dve):
            nc.vector.tensor_copy(K.h[:, :, 0:SEQ], K.xn[:, :, N_META:])


def ffn(K, w_gate, w_up, w_down, g_in, g_out):
    nc = K.nc
    H, X = K.h[:, :, 0:SEQ], K.xn[:, :, 0:SEQ]
    rms_norm(K, H, X, g_in)
    n_gu = D_FF // GU_COLS
    per = GU_COLS // P
    gu_len = KT * GU_COLS
    with ExitStack() as ctx:
        hid = ctx.enter_context(nc.sbuf_tensor(f"ffn_hid_{K.next()}", [P, FF_T, SEQ], F32))
        sil = ctx.enter_context(nc.sbuf_tensor(f"ffn_sil_{K.next()}", [P, 2, per, SEQ], F32))
        gu_in, dn_in = [K.sig("gu_in_0"), K.sig("gu_in_1")], [K.sig("d_in_0"), K.sig("d_in_1")]
        gu_made, silu_made, hid_made = K.sig("gu_made"), K.sig("silu_made"), K.sig("hid_made")
        dn_made, taken = K.sig("d_made"), K.sig("d_taken")
        wg, wu = (w.rearrange("(k p) n -> p k n", p=P) for w in (w_gate, w_up))
        wd = w_down.rearrange("(k p) n -> p k n", p=P)
        block = ctx.enter_context(nc.Block())
        assert n_gu % 2 == 1 and KT % 2 == 0

        @block.sync
        def _(sp):
            def gate_up(b, s, first=False):
                if not first:
                    sp.wait_ge(gu_made.sem, gu_made.base + per * (b - 1))
                sp.dma_start(K.w[:, s, 0:gu_len].rearrange("p (k n) -> p k n", k=KT),
                             wg[:, :, bass.ds(b * GU_COLS, GU_COLS)]).then_inc(gu_in[s].sem, 16)
                sp.dma_start(K.w[:, s, gu_len:2 * gu_len].rearrange("p (k n) -> p k n", k=KT),
                             wu[:, :, bass.ds(b * GU_COLS, GU_COLS)]).then_inc(gu_in[s].sem, 16)

            def down(j, s):
                sp.dma_start(K.w[:, s, 0:FF_T * P].rearrange("p (k n) -> p k n", k=FF_T),
                             wd[:, :, bass.ds(j * P, P)]).then_inc(dn_in[s].sem, 16)
            gate_up(0, 0, True)
            gate_up(1, 1, True)
            with sp.Fori(1, n_gu // 2) as i:
                gate_up(2 * i, 0)
                gate_up(2 * i + 1, 1)
            gate_up(n_gu - 1, 0)
            sp.wait_ge(*gu_made.at(per * (n_gu - 1)))
            down(0, 1)
            sp.wait_ge(*gu_made.at(per * n_gu))
            down(1, 0)
            with sp.Fori(1, KT // 2) as i:
                for s in range(2):
                    sp.wait_ge(dn_made.sem, dn_made.base + 2 * i + s - 1)
                    down(2 * i + s, 1 - s)

        @block.tensor
        def _(pe):
            def gate_up(b, s, turn, first=False):
                pe.wait_ge(gu_in[s].sem, gu_in[s].base + 32 * turn + 32)
                for m in range(per):
                    if not first:
                        pe.wait_ge(hid_made.sem, hid_made.base + per * (b - 2) + m + 1)
                    for j in range(2):
                        for k in range(KT):
                            at = j * gu_len + k * GU_COLS + m * P
                            mm = nc.tensor.matmul(K.ps[:, 4 * s + 2 * j + m, 0:SEQ], K.w[:, s, at:at + P], X[:, k],
                                                  start=k == 0, stop=k == KT - 1)
                    mm.then_inc(gu_made.sem, 1)

            def down(j, s, turn, first=False):
                pe.wait_ge(dn_in[1 - s].sem, dn_in[1 - s].base + 16 * turn + 16)
                if not first:
                    pe.wait_ge(taken.sem, taken.base + j - 1)
                for k in range(FF_T):
                    mm = nc.tensor.matmul(K.ps[:, s, 0:SEQ], K.w[:, 1 - s, k * P:(k + 1) * P], hid[:, k],
                                          start=k == 0, stop=k == FF_T - 1)
                mm.then_inc(dn_made.sem, 1)
            gate_up(0, 0, 0, True)
            gate_up(1, 1, 0, True)
            with pe.Fori(1, n_gu // 2) as i:
                gate_up(2 * i, 0, i)
                gate_up(2 * i + 1, 1, i)
            gate_up(n_gu - 1, 0, n_gu // 2)
            pe.wait_ge(*hid_made.at(FF_T))
            down(0, 0, 0, True)
            down(1, 1, 0, True)
            with pe.Fori(1, KT // 2) as i:
                down(2 * i, 0, i)
                down(2 * i + 1, 1, i)

        @block.scalar
        def _(act):
            def silu(b, s):
                for m in range(per):
                    act.wait_ge(gu_made.sem, gu_made.base + per * b + m + 1)
                    nc.scalar.activation(sil[:, s, m], K.ps[:, 4 * s + m, 0:SEQ], ACT.Silu).then_inc(silu_made.sem, 1)
            with act.Fori(0, n_gu // 2) as i:
                silu(2 * i, 0)
                silu(2 * i + 1, 1)
            silu(n_gu - 1, 0)

        @block.vector
        def _(dve):
            def times(b, s):
                for m in range(per):
                    dve.wait_ge(silu_made.sem, silu_made.base + per * b + m + 1)
                    nc.vector.tensor_tensor(hid[:, bass.ds(per * b + m, 1)], sil[:, s, m:m + 1],
                                            K.ps[:, 4 * s + 2 + m:4 * s + 3 + m, 0:SEQ], ALU.mult).then_inc(hid_made.sem, 1)
            with dve.Fori(0, n_gu // 2) as i:
                times(2 * i, 0)
                times(2 * i + 1, 1)
            times(n_gu - 1, 0)
            with dve.Fori(0, KT // 2) as i:
                for s in range(2):
                    dve.wait_ge(dn_made.sem, dn_made.base + 2 * i + s + 1)
                    nc.vector.tensor_copy(X[:, bass.ds(2 * i + s, 1)], K.ps[:, s:s + 1, 0:SEQ]).then_inc(taken.sem, 1)
        gu_in[0].given += 32 * (n_gu // 2 + 1)
        gu_in[1].given += 32 * (n_gu // 2)
        for s in range(2):
            dn_in[s].given += 16 * KT // 2
        for sig, n in ((gu_made, FF_T), (silu_made, FF_T), (hid_made, FF_T), (dn_made, KT), (taken, KT)):
            sig.given += n
    rms_norm(K, X, X, g_out, add_to=H, factor=0.5)


TT = [(0, P), (P, P)]


def nsa_ssd(K):
    nc, I = K.nc, K.ins
    X = K.xn[:, :, 0:SEQ]
    W = I["ab_w_in_2"][0]
    xk = lambda k: X[:, k]
    xt = lambda k, t0, tn: X[:, k, t0:t0 + tn]
    with ExitStack() as outer:
        joined = outer.enter_context(nc.sbuf_tensor("joined", [P, 2, 512 + SSD_INNER], F32))
        with ExitStack() as ctx:
            def sb(name, shape):
                return ctx.enter_context(nc.sbuf_tensor(name, shape, F32))
            q, kcv, kw = sb("q", [P, 4, SEQ]), sb("kcv", [P, 3, SEQ]), sb("kw", [P, 1, SEQ])
            vs, vg = sb("vs", [P, 2, 128]), sb("vg", [P, 2, 152])
            xbc, z, dt = sb("xbc", [P, 12, SEQ]), sb("z", [P, 2, SSD_INNER]), sb("dt", [P, 2, SSD_HEADS])
            copy = lambda dst: (lambda m, ps: nc.vector.tensor_copy(dst[:, m], ps))
            feature_linear(K, W[:, OFF[0]:OFF[1]], xk, SEQ, copy(q),
                           pieces=[((2 * g + v) * HD, (NSA_GROUP * v + g) * HD, HD) for g in range(NSA_GROUP) for v in range(NSA_KV)])
            feature_linear(K, W[:, OFF[1]:OFF[4]], xk, SEQ, copy(kcv))
            feature_linear(K, W[:, OFF[5]:OFF[6]], xk, SEQ, copy(kw))
            feature_linear(K, W[:, OFF[9]:OFF[10]], xk, SEQ, copy(xbc))

            def tcopy(dst):
                return lambda i, at, n, ps: nc.vector.tensor_copy(dst[:, i, at:at + n], ps)
            token_linear(K, W[:, OFF[4]:OFF[5]], xt, KT, TT, tcopy(vs))
            token_linear(K, W[:, OFF[6]:OFF[8]], xt, KT, TT, tcopy(vg))
            token_linear(K, W[:, OFF[8]:OFF[9]], xt, KT, TT, tcopy(z))
            with nc.allow_non_contiguous_dma(reason="16 columns"):
                token_linear(K, W[:, OFF[10]:OFF[11]], xt, KT, TT, tcopy(dt))
            rot = [q[:, g] for g in range(4)] + [kcv[:, 0], kcv[:, 2], kw[:, 0]]
            turned = K.sq[:, 0:7, 0:SEQ]
            rope(K, rot, [turned[:, i] for i in range(7)], P, SEQ)
            nsa(K, turned, kcv[:, 1], vs, vg, joined)
            ssd(K, xbc, z, dt, joined)
        project_joined(K, joined, (512 + SSD_INNER) // P, I["ab_w_out_2"][0])


def project_joined(K, tok, n, w):
    nc = K.nc
    with ExitStack() as ctx:
        feat = ctx.enter_context(nc.sbuf_tensor(f"feat_{K.next()}", [P, n, SEQ], F32))
        made, taken = K.sig("tile_made"), K.sig("tile_stored")
        with nc.Block() as block:
            @block.tensor
            def _(pe):
                for m in range(n // 2):
                    if m >= 8:
                        pe.wait_ge(*taken.at(m - 7))
                    for j in range(2):
                        for t in range(2):
                            at = (2 * m + j) * P
                            mm = nc.tensor.transpose(K.ps[:, m % 8, (2 * j + t) * P:(2 * j + t + 1) * P], tok[:, t, at:at + P], K.con(C_ID))
                    mm.then_inc(*made.one())

            @block.vector
            def _(dve):
                for m in range(n // 2):
                    dve.wait_ge(*made.at(m + 1))
                    nc.vector.tensor_copy(feat[:, 2 * m:2 * m + 2], K.ps[:, m % 8, :].rearrange("p (j t) -> p j t", j=2)).then_inc(*taken.one())
        feature_linear(K, w, lambda k: feat[:, k], SEQ, lambda m, ps: nc.vector.tensor_copy(K.xn[:, m, 0:SEQ], ps))


def nsa(K, roped, vc, vs, vg, joined):
    nc, I = K.nc, K.ins
    scale = HD ** -0.5
    with ExitStack() as ctx:
        def sb(name, shape):
            return ctx.enter_context(nc.sbuf_tensor(name, shape, F32))
        kC, vC = sb("kC", [P, N_CMP]), sb("vC", [N_CMP, 2, HD])
        gates = sb("nsa_gates", [P, 2, 24])
        compress(K, roped[:, 4], vc, kC, vC)
        pc = sb("pc", [P, 2, 8, N_CMP])
        stat = sb("pc_stat", [P, 2, 8, 2])
        madd = sb("pc_mask", [P, 2, N_CMP])
        pcT = sb("pcT", [N_CMP, 2, 8, P])
        made, e_in, e_done, ready = K.sig("tile_made"), K.sig("s_ready"), K.sig("e_made"), K.sig("p_ready")
        turned, copied, pv, gated = K.sig("t_made"), K.sig("t_taken"), K.sig("pv_made"), K.sig("gated")
        M = K.con(C_CMPM, 2 * (N_CMP + 1)).rearrange("p (t n) -> p t n", t=2)[:, :, 0:N_CMP]
        with nc.Block() as block:
            @block.tensor
            def _(pe):
                for t in range(2):
                    for v in range(NSA_KV):
                        for g in range(NSA_GROUP):
                            at = (t * NSA_GROUP + g) * 16
                            mm = nc.tensor.matmul(K.ps[:, v, at:at + N_CMP], roped[64 * v:64 * v + 64, g, t * P:(t + 1) * P],
                                                  kC[64 * v:64 * v + 64, :], start=True, stop=True)
                mm.then_inc(*made.one())
                pe.wait_ge(*ready.at(1))
                for t in range(2):
                    for h in range(8):
                        mm = nc.tensor.transpose(K.ps[0:N_CMP, 2 + 2 * t + h // 4, (h % 4) * P:(h % 4 + 1) * P], pc[:, t, h], K.con(C_ID))
                mm.then_inc(*turned.one())
                pe.wait_ge(*copied.at(1))
                for t in range(2):
                    for h in range(8):
                        mm = nc.tensor.matmul(K.ps[:, 6 + t, h * HD:(h + 1) * HD], pcT[:, t, h], vC[:, h // 4], start=True, stop=True)
                mm.then_inc(*pv.one())

            @block.scalar
            def _(act):
                nc.scalar.activation(gates[:], vg[:, :, 128:152], ACT.Sigmoid).then_inc(*gated.one())
                act.wait_ge(*e_in.at(1))
                nc.scalar.activation(pc[:], pc[:], ACT.Exp).then_inc(*e_done.one())

            @block.vector
            def _(dve):
                v = nc.vector
                do = lambda ins: link(dve, K.dve_step, ins)
                bc = lambda ap: ap.to_broadcast([P, 8, N_CMP])
                do(v.tensor_scalar(madd[:], M, 1.0, -NEG, ALU.subtract, ALU.mult))
                dve.wait_ge(*made.at(1))
                S = K.ps[:, 0:2, 0:128].rearrange("p v (t g n) -> p t v g n", t=2, g=NSA_GROUP)
                for t in range(2):
                    for kv in range(NSA_KV):
                        last = v.scalar_tensor_tensor(out=pc[:, t, 4 * kv:4 * kv + 4], in0=S[:, t, kv, :, 0:N_CMP], scalar=scale,
                                                      in1=madd[:, t:t + 1].to_broadcast([P, 4, N_CMP]), op0=ALU.mult, op1=ALU.add)
                    do(last)
                    do(v.reduce_max(stat[:, t, :, 0:1], pc[:, t], AX))
                    last = v.tensor_tensor(pc[:, t], pc[:, t], bc(stat[:, t, :, 0:1]), ALU.subtract)
                last.then_inc(*e_in.one())
                dve.wait_ge(*e_done.at(1))
                dve.wait_ge(*gated.at(1))
                for t in range(2):
                    do(v.tensor_tensor(pc[:, t], pc[:, t], bc(M[:, t:t + 1]), ALU.mult))
                    do(v.reduce_sum(stat[:, t, :, 0:1], pc[:, t], AX))
                    do(v.tensor_scalar(stat[:, t, :, 0:1], stat[:, t, :, 0:1], 1e-30, None, ALU.max))
                    do(v.reciprocal(stat[:, t, :, 1:2], stat[:, t, :, 0:1]))
                    gt = gates[:, t].rearrange("p (h c) -> p h c", c=3)
                    do(v.tensor_tensor(stat[:, t, :, 1:2], stat[:, t, :, 1:2], gt[:, :, 0:1], ALU.mult))
                    last = v.tensor_tensor(pc[:, t], pc[:, t], bc(stat[:, t, :, 1:2]), ALU.mult)
                last.then_inc(*ready.one())
                dve.wait_ge(*turned.at(1))
                for t in range(2):
                    last = v.tensor_copy(pcT[:, t].rearrange("c (a h) q -> c a (h q)", a=2), K.ps[0:N_CMP, 2 + 2 * t:4 + 2 * t, :])
                last.then_inc(*copied.one())
                dve.wait_ge(*pv.at(1))
                for t in range(2):
                    v.tensor_copy(joined[:, t, 0:512], K.ps[:, 6 + t])
        dense_branches(K, roped, vs, vg, gates, joined)


def compress(K, kc, vc, kC, vC):
    nc, I = K.nc, K.ins
    half = CMP_STRIDE
    with ExitStack() as ctx:
        def sb(name, shape):
            return ctx.enter_context(nc.sbuf_tensor(name, shape, F32))
        w1, w2 = sb("cw1", [P, 2, CMP_BLOCK, HD]), sb("cw2", [HD, 2, HD])
        pe_rows, peT = sb("pe_rows", [CMP_BLOCK, 2, 2, HD]), sb("peT", [P, 2, CMP_BLOCK])
        xs = sb("cmp_x", [P, 2, 2, SEQ])
        hidden = sb("cmp_h", [HD, 2, 2, N_CMP])
        given, turned, ready = K.sig("rows_given"), K.sig("t_made"), K.sig("p_ready")
        made, silu, out = K.sig("tile_made"), K.sig("silu_made"), K.sig("pv_made")
        block = ctx.enter_context(nc.Block())

        @block.sync
        def _(sp):
            for j, kind in enumerate("kv"):
                for v in range(2):
                    sp.dma_start(w1[64 * v:64 * v + 64, j], I[f"a_cmp_w1_{kind}_2"][0].rearrange("(l d) m -> d l m", d=HD)).then_inc(*given.dma())
                    sp.dma_start(pe_rows[:, j, v], I[f"a_cmp_pe_{kind}_2"][0]).then_inc(*given.dma())
                sp.dma_start(w2[:, j], I[f"a_cmp_w2_{kind}_2"][0]).then_inc(*given.dma())

        @block.tensor
        def _(pe):
            pe.wait_ge(*given.at(160))
            for j in range(2):
                mm = nc.tensor.transpose(K.ps[:, 0, j * CMP_BLOCK:(j + 1) * CMP_BLOCK], pe_rows[:, j].rearrange("l v d -> l (v d)"),
                                         K.cst[0:CMP_BLOCK, C_ID:C_ID + CMP_BLOCK])
            mm.then_inc(*turned.one())
            pe.wait_ge(*ready.at(1))
            for j in range(2):
                for v in range(2):
                    rows = slice(64 * v, 64 * v + 64)
                    for l in range(CMP_BLOCK):
                        x = xs[rows, j, l // half].rearrange("p (b r) -> p b r", r=half)[:, l // half:l // half + N_CMP, l % half]
                        mm = nc.tensor.matmul(K.ps[0:HD, 1 + 2 * j + v, 0:N_CMP], w1[rows, j, l], x,
                                              start=l == 0, stop=l == CMP_BLOCK - 1)
            mm.then_inc(*made.one())
            pe.wait_ge(*silu.at(1))
            for v in range(2):
                nc.tensor.matmul(K.ps[64 * v:64 * v + 64, 5, 0:N_CMP], w2[:, 0], hidden[:, 0, v], start=True, stop=True)
                mm = nc.tensor.matmul(K.ps[0:N_CMP, 6, v * HD:(v + 1) * HD], hidden[:, 1, v], w2[:, 1], start=True, stop=True)
            mm.then_inc(*out.one())

        @block.vector
        def _(dve):
            dve.wait_ge(*turned.at(1))
            link(dve, K.dve_step, nc.vector.tensor_copy(peT[:], K.ps[:, 0, 0:2 * CMP_BLOCK].rearrange("p (j l) -> p j l", j=2)))
            for j, x in enumerate((kc, vc)):
                for a in range(2):
                    last = nc.vector.tensor_tensor(xs[:, j, a].rearrange("p (b r) -> p b r", r=half), x.rearrange("p (b r) -> p b r", r=half),
                                                   peT[:, j:j + 1, a * half:(a + 1) * half].to_broadcast([P, SEQ // half, half]), ALU.add)
            last.then_inc(*ready.one())
            dve.wait_ge(*out.at(1))
            nc.vector.tensor_copy(kC[:], K.ps[:, 5, 0:N_CMP])
            nc.vector.tensor_copy(vC[:], K.ps[0:N_CMP, 6, 0:2 * HD].rearrange("n (v d) -> n v d", v=2))

        @block.scalar
        def _(act):
            act.wait_ge(*made.at(1))
            for j in range(2):
                last = nc.scalar.activation(hidden[:, j], K.ps[0:HD, 1 + 2 * j:3 + 2 * j, 0:N_CMP], ACT.Silu)
            last.then_inc(*silu.one())


def dense_branches(K, roped, vs, vg, gates, joined):
    nc = K.nc
    scale = HD ** -0.5
    units = [(b, v, g) for b in range(2) for v in range(NSA_KV) for g in range(NSA_GROUP)]
    n = len(units)
    W = 3 * P
    parts = [(0, 0, P), (1, P, W)]
    blocks = [(0, 0), (1, 0), (1, 1)]
    with ExitStack() as ctx:
        def sb(name, shape):
            return ctx.enter_context(nc.sbuf_tensor(name, shape, F32))
        S, Pr, PT = sb("nsa_s", [P, 3, W]), sb("nsa_p", [P, 3, W]), sb("nsa_pt", [P, 2, W])
        st = sb("nsa_stat", [P, 4, 2, 4])
        s_made, s_ready, e_made = K.sig("s_made"), K.sig("s_ready"), K.sig("e_made")
        t_made, t_taken, pv_made, o_taken = K.sig("t_made"), K.sig("t_taken"), K.sig("pv_made"), K.sig("o_taken")
        block = ctx.enter_context(nc.Block())

        @block.tensor
        def _(pe):
            for u in range(n + 2):
                if u < n:
                    b, v, g = units[u]
                    rows = slice(64 * v, 64 * v + 64)
                    if u >= 3:
                        pe.wait_ge(*s_ready.at(u - 2))
                    for t, lo, hi in parts:
                        mm = nc.tensor.matmul(K.ps[:, u % 3, lo:hi], roped[rows, g, t * P:(t + 1) * P], roped[rows, 5 + b, 0:hi - lo],
                                              start=True, stop=True)
                    mm.then_inc(*s_made.one())
                if 1 <= u <= n:
                    w = u - 1
                    pe.wait_ge(*e_made.at(w + 1))
                    if w >= 2:
                        pe.wait_ge(*t_taken.at(w - 1))
                    for j in range(3):
                        mm = nc.tensor.transpose(K.ps[:, 3 + w % 2, j * P:(j + 1) * P], Pr[:, w % 3, j * P:(j + 1) * P], K.con(C_ID))
                    mm.then_inc(*t_made.one())
                if u >= 2:
                    w = u - 2
                    b, v, g = units[w]
                    pe.wait_ge(*t_taken.at(w + 1))
                    if w >= 2:
                        pe.wait_ge(*o_taken.at(w - 1))
                    for j, (t, kt) in enumerate(blocks):
                        mm = nc.tensor.matmul(K.ps[:, 5 + w % 2, t * HD:(t + 1) * HD], PT[:, w % 2, j * P:(j + 1) * P],
                                              (vs, vg)[b][:, kt, v * HD:(v + 1) * HD], start=kt == 0, stop=kt == t)
                    mm.then_inc(*pv_made.one())

        @block.vector
        def _(dve):
            causal = K.cst[:, C_CAUSAL:C_CAUSAL + P]
            for u in range(n + 3):
                if u < n:
                    dve.wait_ge(*s_made.at(u + 1))
                    if u >= 3:
                        dve.wait_ge(*e_made.at(u - 2))
                    nc.vector.tensor_scalar(S[:, u % 3, P:2 * P], K.ps[:, u % 3, P:2 * P], scale, None, ALU.mult)
                    nc.vector.scalar_tensor_tensor(out=S[:, u % 3, 0:P], in0=K.ps[:, u % 3, 0:P], scalar=scale, in1=causal,
                                                   op0=ALU.mult, op1=ALU.add)
                    link(dve, K.dve_step, nc.vector.scalar_tensor_tensor(
                        out=S[:, u % 3, 2 * P:W], in0=K.ps[:, u % 3, 2 * P:W], scalar=scale, in1=causal, op0=ALU.mult, op1=ALU.add))
                    for t, lo, hi in parts:
                        last = nc.vector.reduce_max(st[:, u % 4, t, 3:4], S[:, u % 3, lo:hi], AX)
                    link(dve, K.dve_step, last)
                    nc.vector.tensor_scalar(st[:, u % 4, :, 0:1], st[:, u % 4, :, 3:4], -1.0, None, ALU.mult).then_inc(*s_ready.one())
                if u >= 3:
                    w = u - 3
                    b, v, g = units[w]
                    h = 4 * v + g
                    dve.wait_ge(*pv_made.at(w + 1))
                    link(dve, K.dve_step, nc.vector.reciprocal(st[:, w % 4, :, 2:3], st[:, w % 4, :, 1:2]))
                    link(dve, K.dve_step, nc.vector.tensor_tensor(st[:, w % 4, :, 2:3], st[:, w % 4, :, 2:3],
                                                                  gates[:, :, 3 * h + 1 + b:3 * h + 2 + b], ALU.mult))
                    for t in range(2):
                        o = joined[:, t, h * HD:(h + 1) * HD]
                        last = nc.vector.scalar_tensor_tensor(out=o, in0=K.ps[:, 5 + w % 2, t * HD:(t + 1) * HD], scalar=st[:, w % 4, t, 2:3],
                                                              in1=o, op0=ALU.mult, op1=ALU.add)
                    last.then_inc(*o_taken.one())

        @block.scalar
        def _(act):
            for u in range(n + 1):
                if u < n:
                    act.wait_ge(*s_ready.at(u + 1))
                    if u >= 3:
                        act.wait_ge(*t_made.at(u - 2))
                    for t, lo, hi in parts:
                        last = nc.scalar.activation(Pr[:, u % 3, lo:hi], S[:, u % 3, lo:hi], ACT.Exp, bias=st[:, u % 4, t, 0:1],
                                                    accum_out=st[:, u % 4, t, 1:2])
                    last.then_inc(*e_made.one())
                if u >= 1:
                    w = u - 1
                    act.wait_ge(*t_made.at(w + 1))
                    if w >= 2:
                        act.wait_ge(*pv_made.at(w - 1))
                    nc.scalar.copy(PT[:, w % 2], K.ps[:, 3 + w % 2, 0:W]).then_inc(*t_taken.one())


def ssd(K, xbc, z, dt, joined):
    nc, I = K.nc, K.ins
    NT = XBC // P
    with ExitStack() as ctx:
        def sb(name, shape):
            return ctx.enter_context(nc.sbuf_tensor(name, shape, F32))
        cv = sb("conv", [P, NT, SEQ])
        row = sb("ssd_rows", [P, 3, SSD_HEADS])
        normw = sb("ssd_normw", [P, SSD_INNER])
        sp_ = sb("softplus", [P, 2, 3, SSD_HEADS])
        dta, acs = sb("dta", [P, 2, SSD_HEADS]), sb("acs", [P, 2, 4, SSD_HEADS])
        given, conv_done = K.sig("rows_given"), K.sig("pooled")
        a_in, a_done = K.sig("exp_asked"), K.sig("exp_done")
        acs_made = K.sig("s_made")
        with nc.Block() as block:
            @block.sync
            def _(s):
                for j, name in enumerate(("b_dt_bias_2", "b_a_log_2", "b_d_skip_2")):
                    s.dma_start(row[:, j], I[name].to_broadcast([P, SSD_HEADS])).then_inc(*given.dma())
                s.dma_start(normw[:], I["b_norm_w_2"].to_broadcast([P, SSD_INNER])).then_inc(*given.dma())

            @block.vector
            def _(dve):
                v = nc.vector
                do = lambda ins: link(dve, K.dve_step, ins)
                dve.wait_ge(*given.at(64))
                for t in range(2):
                    do(v.tensor_tensor(sp_[:, t, 0], dt[:, t], row[:, 0], ALU.add))
                    do(v.tensor_scalar(sp_[:, t, 1], sp_[:, t, 0], -1.0, None, ALU.mult))
                    do(v.tensor_tensor(sp_[:, t, 1], sp_[:, t, 1], sp_[:, t, 0], ALU.min))
                    last = v.tensor_scalar(sp_[:, t, 0], sp_[:, t, 0], 0.0, None, ALU.max)
                last.then_inc(*a_in.one())
                cw = lambda tap, c: K.col("b_conv_w_2", tap * NT + c)
                for c in range(NT):
                    v.tensor_scalar(cv[:, c], xbc[:, c], cw(SSD_CONV - 1, c), K.col("b_conv_b_2", c), ALU.mult, ALU.add).then_inc(*K.dve_step.one())
                for s in range(1, SSD_CONV):
                    dve.wait_ge(*K.dve_step.now())
                    for c in range(NT):
                        last = v.scalar_tensor_tensor(out=cv[:, c, s:], in0=xbc[:, c, 0:SEQ - s], scalar=cw(SSD_CONV - 1 - s, c),
                                                      in1=cv[:, c, s:], op0=ALU.mult, op1=ALU.add)
                    last.then_inc(*K.dve_step.one())
                last2 = v.memset(acs[:], 0.0)
                last2.then_inc(*conv_done.one())
                dve.wait_ge(*a_done.at(1))
                for t in range(2):
                    do(v.tensor_tensor(dt[:, t], sp_[:, t, 0], sp_[:, t, 2], ALU.add))
                    last = v.scalar_tensor_tensor(out=dta[:, t], in0=dt[:, t], scalar=-1.0, in1=row[:, 1], op0=ALU.mult, op1=ALU.mult)
                last.then_inc(*a_in.one())
                dve.wait_ge(*acs_made.at(1))
                for t in range(2):
                    do(v.tensor_copy(acs[:, t, 0], K.ps[:, 0, t * 16:t * 16 + 16]))
                do(v.tensor_tensor(acs[:, 0, 1], K.ps[:, 0, 32:48], acs[:, 0, 0], ALU.subtract))

            @block.tensor
            def _(pe):
                pe.wait_ge(*a_in.at(2))
                for t in range(2):
                    nc.tensor.matmul(K.ps[:, 0, t * 16:t * 16 + 16], K.con(C_TRI), dta[:, t], start=True, stop=True)
                nc.tensor.matmul(K.ps[:, 0, 32:48], K.con(C_ONE), dta[:, 0], start=True, stop=True).then_inc(*acs_made.one())

            @block.scalar
            def _(act):
                act.wait_ge(*a_in.at(1))
                link(act, K.act_step, nc.scalar.activation(sp_[:, :, 1], sp_[:, :, 1], ACT.Exp))
                nc.scalar.activation(row[:, 1], row[:, 1], ACT.Exp)
                nc.scalar.activation(sp_[:, :, 2], sp_[:, :, 1], ACT.Ln, bias=1.0).then_inc(*a_done.one())
                act.wait_ge(*conv_done.at(1))
                nc.scalar.activation(cv[:], cv[:], ACT.Silu)
        ssd_chunks(K, cv, z, dt, dta, acs, row, normw, joined)


def ssd_chunks(K, cv, z, dt, dta, acs, row, normw, joined):
    nc = K.nc
    HG = SSD_HEADS // SSD_GROUPS
    hp = lambda ap: ap.rearrange("p (h d) -> p h d", d=HD)
    with ExitStack() as ctx:
        def sb(name, shape):
            return ctx.enter_context(nc.sbuf_tensor(name, shape, F32))
        xs, xd = sb("ssd_xs", [P, 2, SSD_INNER]), sb("ssd_xd", [P, 2, SSD_INNER])
        xdd = sb("ssd_xdd", [P, SSD_INNER])
        bt = sb("ssd_bt", [P, SSD_GROUPS, SSD_STATE])
        cb = sb("ssd_cb", [P, 2, SSD_GROUPS, P])
        state = sb("ssd_state", [P, SSD_GROUPS, HG * HD])
        ms = sb("ssd_ms", [P, 2, SSD_GROUPS, 2])
        made, taken = K.sig("tile_made"), K.sig("tile_stored")
        e_in, e_done = K.sig("exp_asked"), K.sig("exp_done")
        st_in, st_made, st_taken = K.sig("p_ready"), K.sig("pv_made"), K.sig("o_taken")
        with nc.Block() as block:
            @block.tensor
            def _(pe):
                for n in range(4):
                    for k in range(4):
                        mm = nc.tensor.transpose(K.ps[:, n, k * P:(k + 1) * P], cv[:, 4 * (n % 2) + k, (n // 2) * P:(n // 2 + 1) * P], K.con(C_ID))
                    mm.then_inc(*made.one())
                for g in range(SSD_GROUPS):
                    mm = nc.tensor.transpose(K.ps[:, 4, g * P:(g + 1) * P], cv[:, 8 + g, 0:P], K.con(C_ID))
                mm.then_inc(*made.one())
                for c in range(2):
                    for g in range(SSD_GROUPS):
                        t = slice(c * P, (c + 1) * P)
                        mm = nc.tensor.matmul(K.ps[:, 5, (2 * c + g) * P:(2 * c + g + 1) * P], cv[:, 8 + g, t], cv[:, 10 + g, t], start=True, stop=True)
                mm.then_inc(*made.one())
                pe.wait_ge(*st_in.at(1))
                for g in range(SSD_GROUPS):
                    mm = nc.tensor.matmul(K.ps[:, 6 + g], bt[:, g], xdd[:, g * 512:(g + 1) * 512], start=True, stop=True)
                mm.then_inc(*st_made.one())

            @block.scalar
            def _(act):
                nc.scalar.activation(acs[:, 0, 1], acs[:, 0, 1], ACT.Exp)
                nc.scalar.activation(acs[:, 1, 2], acs[:, 1, 0], ACT.Exp).then_inc(*e_done.one())
                nc.scalar.activation(z[:], z[:], ACT.Silu)

            @block.vector
            def _(dve):
                v = nc.vector
                do = lambda ins: link(dve, K.dve_step, ins)
                for n in range(4):
                    dve.wait_ge(*made.at(n + 1))
                    last = v.tensor_copy(xs[:, n // 2, 512 * (n % 2):512 * (n % 2) + 512], K.ps[:, n])
                do(last)
                for t in range(2):
                    do(v.tensor_tensor(hp(xd[:, t]), hp(xs[:, t]), dt[:, t].rearrange("p (h a) -> p h a", a=1).to_broadcast([P, 16, HD]), ALU.mult))
                dve.wait_ge(*e_done.at(1))
                do(v.tensor_tensor(hp(xdd[:]), hp(xd[:, 0]), acs[:, 0, 1].rearrange("p (h a) -> p h a", a=1).to_broadcast([P, 16, HD]), ALU.mult))
                dve.wait_ge(*made.at(5))
                v.tensor_copy(bt[:], K.ps[:, 4, 0:256].rearrange("p (g n) -> p g n", g=2)).then_inc(*st_in.one())
                dve.wait_ge(*made.at(6))
                v.tensor_tensor(cb[:].rearrange("p c g n -> p (c g) n"), K.ps[:, 5].rearrange("p (x n) -> p x n", x=4),
                                K.con(C_TRI).rearrange("p (a n) -> p a n", a=1).to_broadcast([P, 4, P]), ALU.mult)
                dve.wait_ge(*st_made.at(1))
                v.tensor_copy(state[:], K.ps[:, 6:8])
        units = [(c, g, q) for c in range(2) for g in range(SSD_GROUPS) for q in range(2)]
        n = len(units)
        seg = sb("ssd_seg", [P, 2, 4, P])
        made, s_ready, e_made, ready = K.sig("s_made"), K.sig("s_ready"), K.sig("e_made"), K.sig("p_ready")
        used, y_made, y_off = K.sig("t_made"), K.sig("pv_made"), K.sig("o_taken")
        with nc.Block() as block:
            @block.tensor
            def _(pe):
                for g in range(SSD_GROUPS):
                    mm = nc.tensor.matmul(K.ps[:, 6 + g], cv[:, 10 + g, P:2 * P], state[:, g], start=True, stop=True)
                mm.then_inc(*y_off.one())
                for u in range(n + 1):
                    if u < n:
                        c, g, q = units[u]
                        if u >= 2:
                            pe.wait_ge(*s_ready.at(u - 1))
                        for j in range(4):
                            h = g * HG + q * 4 + j
                            mm = nc.tensor.matmul(K.ps[:, u % 2, j * P:(j + 1) * P], dta[:, c, h:h + 1].to_broadcast([P, P]), K.con(C_TRI),
                                                  start=True, stop=True)
                        mm.then_inc(*made.one())
                    if u >= 1:
                        c, g, q = units[u - 1]
                        pe.wait_ge(*ready.at(u))
                        for j in range(4):
                            h = g * HG + q * 4 + j
                            at = (q * 4 + j) * HD
                            mm = nc.tensor.matmul(K.ps[:, 2 + 2 * c + g, at:at + HD], seg[:, (u - 1) % 2, j], xd[:, c, h * HD:(h + 1) * HD],
                                                  start=True, stop=True)
                        mm.then_inc(*y_made.one())

            @block.scalar
            def _(act):
                for u in range(n):
                    act.wait_ge(*s_ready.at(u + 1))
                    nc.scalar.activation(seg[:, u % 2], seg[:, u % 2], ACT.Exp).then_inc(*e_made.one())
                act.wait_ge(*used.at(1))
                for c in range(2):
                    for g in range(SSD_GROUPS):
                        last = nc.scalar.activation(xd[:, c, g * 512:(g + 1) * 512], xs[:, c, g * 512:(g + 1) * 512], ACT.Square,
                                                    accum_out=ms[:, c, g, 0:1])
                link(act, K.act_step, last)
                nc.scalar.activation(ms[:, :, :, 1:2], ms[:, :, :, 0:1], ACT.Sqrt, bias=K.eps[:, 1:2], scale=1.0 / (HG * HD)).then_inc(*used.one())

            @block.vector
            def _(dve):
                v = nc.vector
                do = lambda ins: link(dve, K.dve_step, ins)
                wide = lambda ap: ap.rearrange("p (h a) -> p h a", a=1)
                for u in range(n + 1):
                    if u < n:
                        c, g, q = units[u]
                        dve.wait_ge(*made.at(u + 1))
                        if u >= 2:
                            dve.wait_ge(*y_made.at(u - 1))
                        h = g * HG + q * 4
                        do(v.tensor_tensor(seg[:, u % 2], K.ps[:, u % 2].rearrange("p (j l) -> p j l", j=4),
                                           wide(acs[:, c, 0, h:h + 4]).to_broadcast([P, 4, P]), ALU.subtract))
                        v.tensor_scalar(seg[:, u % 2], seg[:, u % 2], 0.0, None, ALU.min).then_inc(*s_ready.one())
                    if u >= 1:
                        c, g, q = units[u - 1]
                        dve.wait_ge(*e_made.at(u))
                        v.tensor_tensor(seg[:, (u - 1) % 2], seg[:, (u - 1) % 2], cb[:, c, g:g + 1].to_broadcast([P, 4, P]), ALU.mult).then_inc(*ready.one())
                dve.wait_ge(*y_made.at(n))
                dve.wait_ge(*y_off.at(1))
                for c in range(2):
                    do(v.tensor_tensor(hp(xs[:, c]), hp(xs[:, c]), wide(row[:, 2]).to_broadcast([P, 16, HD]), ALU.mult))
                    for g in range(SSD_GROUPS):
                        part = xs[:, c, g * 512:(g + 1) * 512]
                        do(v.tensor_tensor(part, part, K.ps[:, 2 + 2 * c + g], ALU.add))
                        if c == 1:
                            tmp = xdd[:, g * 512:(g + 1) * 512]
                            do(v.tensor_tensor(hp(tmp), hp(K.ps[:, 6 + g]), wide(acs[:, 1, 2, g * HG:(g + 1) * HG]).to_broadcast([P, HG, HD]), ALU.mult))
                            do(v.tensor_tensor(part, part, tmp, ALU.add))
                last = v.tensor_tensor(xs[:], xs[:], z[:], ALU.mult)
                last.then_inc(*used.one())
                dve.wait_ge(*used.at(2))
                do(v.reciprocal(ms[:, :, :, 0:1], ms[:, :, :, 1:2]))
                for c in range(2):
                    for g in range(SSD_GROUPS):
                        at = g * 512
                        v.scalar_tensor_tensor(out=joined[:, c, 512 + at:1024 + at], in0=xs[:, c, at:at + 512], scalar=ms[:, c, g, 0:1],
                                               in1=normw[:, at:at + 512], op0=ALU.mult, op1=ALU.mult)


def rwkv(K, scratch):
    nc, I = K.nc, K.ins
    X = K.xn[:, :, 0:SEQ]
    with ExitStack() as ctx:
        def sb(name, shape):
            return ctx.enter_context(nc.sbuf_tensor(name, shape, F32))
        v, g = sb("rw_v", [P, 2, D]), sb("rw_g", [P, 2, D])
        y = sb("rw_y", [P, 2, D])
        with ExitStack() as inner:
            def sbi(name, shape):
                return inner.enter_context(nc.sbuf_tensor(name, shape, F32))
            r, k, sg, a = (sbi(f"rw_{n}", [P, KT, SEQ]) for n in ("r", "k", "sg", "a"))
            rwkv_projections(K, X, r, k, sg, a, v, g)
            ar = sbi("rw_ar", [P, KT, 2, SEQ])
            kk = sbi("rw_kk", [P, KT, SEQ])
            cl = sbi("rw_cl", [P, KT, N_RC])
            bon = sbi("rw_bonus", [P, 2, RW_HEADS])
            rwkv_factors(K, r, k, sg, a, kk, ar, cl)
            bp, kp = sbi("rw_bp", [P, 2, D]), sbi("rw_kp", [P, 2, D])
            sc = sbi("rw_sc", [P, 32, 4, RC])
            rwkv_scores(K, a, k, r, kk, ar, bp, kp, sc, bon)
            tm = sbi("rw_tm", [P, 32, RC])
            nv = sbi("rw_nv", [P, 2, 2, D])
            flat = lambda buf: buf[:].rearrange("p f t -> p (f t)")
            rwkv_inverse(K, sc, v, tm, nv, scratch, flat(sg), flat(kk))
            rwkv_chunks(K, ar, cl, bp, kp, sc, tm, nv, v, y, flat(a), flat(sg))
            rwkv_output(K, y, v, g, bon, flat(k).rearrange("p (j n) -> p j n", j=2), flat(r))
        project_joined(K, y, KT, I["c_w_o_2"][0])


def rwkv_projections(K, X, r, k, sg, a, v, g):
    nc, I = K.nc, K.ins
    with ExitStack() as ctx:
        def sb(name, shape):
            return ctx.enter_context(nc.sbuf_tensor(name, shape, F32))
        mix = sb("rw_mix", [P, 6, KT, SEQ])
        low = sb("rw_low", [P, 2, SEQ])
        xx = K.sq[:, :, 0:SEQ]
        with nc.Block() as block:
            @block.vector
            def _(dve):
                nc.vector.tensor_tensor(xx[:, :, 1:], X[:, :, 0:SEQ - 1], X[:, :, 1:], ALU.subtract)
                link(dve, K.dve_step, nc.vector.tensor_scalar(xx[:, :, 0:1], X[:, :, 0:1], -1.0, None, ALU.mult))
                for i in range(6):
                    for kt in range(KT):
                        nc.vector.scalar_tensor_tensor(out=mix[:, i, kt], in0=xx[:, kt], scalar=K.col("c_mu_2", 8 * i + kt),
                                                       in1=X[:, kt], op0=ALU.mult, op1=ALU.add)
        feat = lambda i: (lambda kt: mix[:, i, kt])
        tok = lambda i: (lambda kt, t0, tn: mix[:, i, kt, t0:t0 + tn])
        feature_linear(K, I["c_w_r_2"][0], feat(0), SEQ, lambda m, ps: nc.vector.tensor_copy(r[:, m], ps))
        feature_linear(K, I["c_w_k_2"][0], feat(2), SEQ, lambda m, ps: nc.vector.tensor_copy(k[:, m], ps))
        token_linear(K, I["c_w_v_2"][0], tok(3), KT, TT, lambda i, at, n, ps: nc.vector.tensor_copy(v[:, i, at:at + n], ps))
        feature_linear(K, I["c_w1_2"][0], feat(1), SEQ, lambda m, ps: nc.scalar.activation(low[0:64, 0], ps, ACT.Tanh), by="scalar")
        feature_linear(K, I["c_w2_2"][0], lambda kt: low[0:64, 0], SEQ,
                       lambda m, ps: nc.scalar.activation(sg[:, m], ps, ACT.Sigmoid, bias=K.col("c_w0_2", m)), by="scalar")
        feature_linear(K, I["c_a1_2"][0], feat(4), SEQ, lambda m, ps: nc.vector.tensor_copy(low[0:64, 1], ps))
        feature_linear(K, I["c_a2_2"][0], lambda kt: low[0:64, 1], SEQ,
                       lambda m, ps: nc.scalar.activation(a[:, m], ps, ACT.Sigmoid, bias=K.col("c_a0_2", m)), by="scalar")
        feature_linear(K, I["c_g1_2"][0], feat(5), SEQ,
                       lambda m, ps: nc.scalar.activation(low[0:ps.shape[0], m], ps, ACT.Sigmoid), by="scalar")
        token_linear(K, I["c_g2_2"][0, 0:P], lambda kt, t0, tn: low[:, 0, t0:t0 + tn], 1, TT,
                     lambda i, at, n, ps: nc.vector.tensor_copy(g[:, i, at:at + n], ps))
        token_linear(K, I["c_g2_2"][0, P:GATE_LORA], lambda kt, t0, tn: low[0:GATE_LORA - P, 1, t0:t0 + tn], 1, TT,
                     lambda i, at, n, ps: nc.vector.tensor_tensor(g[:, i, at:at + n], g[:, i, at:at + n], ps, ALU.add))


def rwkv_factors(K, r, k, sg, a, kk, ar, cl):
    nc = K.nc
    c1, c2 = K.sq[:, :, 0:SEQ], K.xn[:, :, 0:SEQ]
    ch = lambda ap: ap.rearrange("p f (c t) -> p f c t", t=RC)
    squared, made, rooted = K.sig("squared"), K.sig("tile_made"), K.sig("rooted")
    kk_in, cum, cum2, cexp = K.sig("s_ready"), K.sig("exp_asked"), K.sig("pooled"), K.sig("exp_done")
    with nc.Block() as block:
        @block.tensor
        def _(pe):
            pe.wait_ge(*squared.at(1))
            for f in range(KT):
                mm = nc.tensor.matmul(K.ps[:, f // 2, (f % 2) * SEQ:(f % 2 + 1) * SEQ], K.con(C_HEAD), ar[:, f, 0], start=True, stop=True)
            mm.then_inc(*made.one())

        @block.scalar
        def _(act):
            act.wait_ge(*kk_in.at(1))
            nc.scalar.activation(ar[:, :, 0], kk[:], ACT.Square).then_inc(*squared.one())
            act.wait_ge(*made.at(1))
            nc.scalar.activation(ar[:, :, 1], K.ps[:, 0:4].rearrange("p b (f t) -> p (b f) t", f=2), ACT.Sqrt).then_inc(*rooted.one())
            act.wait_ge(*cum.at(1))
            nc.scalar.activation(c2, c1, ACT.Exp).then_inc(*cexp.one())
            nc.scalar.activation(sg[:], sg[:], ACT.Exp).then_inc(*cexp.one())
            link(act, K.act_step, nc.scalar.activation(c1, c1, ACT.Exp, scale=-1.0))
            nc.scalar.copy(cl[:], ch(c2)[:, :, :, RC - 1]).then_inc(*cexp.one())

        @block.vector
        def _(dve):
            v = nc.vector
            do = lambda ins: link(dve, K.dve_step, ins)
            for f in range(KT):
                last = v.tensor_scalar(kk[:, f], k[:, f], K.col("c_k_k_2", f), None, ALU.mult)
            last.then_inc(*kk_in.one())
            for f in range(KT):
                last = v.tensor_scalar(c2[:, f], a[:, f], 1.0, K.col("c_k_a_2", f), ALU.subtract, ALU.mult)
            do(last)
            do(v.scalar_tensor_tensor(out=k[:], in0=c2, scalar=1.0, in1=k[:], op0=ALU.add, op1=ALU.mult))
            do(v.tensor_scalar(sg[:], sg[:], -math.exp(-0.5), None, ALU.mult))
            src, dst = sg[:], c1
            s = 1
            while s < RC:
                v.tensor_copy(ch(dst)[:, :, :, 0:s], ch(src)[:, :, :, 0:s])
                for f in range(KT):
                    last = v.tensor_tensor(ch(dst)[:, f, :, s:], ch(src)[:, f, :, s:], ch(src)[:, f, :, 0:RC - s], ALU.add)
                do(last)
                src, dst = dst, (c2 if dst is c1 else c1)
                s *= 2
            assert src is c1
            v.tensor_tensor(sg[:], c1, sg[:], ALU.subtract).then_inc(*cum.one())
            dve.wait_ge(*rooted.at(1))
            do(v.tensor_scalar(ar[:, :, 1], ar[:, :, 1], 1e-12, None, ALU.max))
            do(v.reciprocal(ar[:, :, 1], ar[:, :, 1]))
            do(v.tensor_tensor(kk[:], kk[:], ar[:, :, 1], ALU.mult))
            do(v.tensor_tensor(a[:], a[:], kk[:], ALU.mult))
            dve.wait_ge(*cexp.at(1))
            do(v.tensor_tensor(ar[:, :, 1], c2, r[:], ALU.mult))
            for f in range(KT):
                last = v.scalar_tensor_tensor(out=r[:, f], in0=r[:, f], scalar=K.col("c_r_k_2", f), in1=k[:, f], op0=ALU.mult, op1=ALU.mult)
            do(last)
            dve.wait_ge(*cexp.at(2))
            v.scalar_tensor_tensor(out=ar[:, :, 0], in0=sg[:], scalar=-1.0, in1=kk[:], op0=ALU.mult, op1=ALU.mult).then_inc(*K.dve_step.one())
            dve.wait_ge(*cexp.at(3))
            v.tensor_tensor(a[:], a[:], c1, ALU.mult).then_inc(*K.dve_step.one())
            do(v.tensor_tensor(k[:], k[:], c1, ALU.mult))
            for f in range(KT):
                end = cl[:, f].rearrange("p (c a) -> p c a", a=1).to_broadcast([P, N_RC, RC])
                v.tensor_tensor(ch(c2)[:, f], ch(a[:])[:, f], end, ALU.mult)
                v.tensor_tensor(ch(kk[:])[:, f], ch(k[:])[:, f], end, ALU.mult)


def rwkv_scores(K, bt, kt, rk, kend, ar, bp, kp, sc, bon):
    nc = K.nc
    bend = K.xn[:, :, 0:SEQ]
    made, taken = K.sig("tile_made"), K.sig("tile_stored")
    with nc.Block() as block:
        @block.tensor
        def _(pe):
            for n in range(8):
                src = (bend, kend)[n // 4]
                t, half = n // 2 % 2, n % 2
                for j in range(4):
                    mm = nc.tensor.transpose(K.ps[:, n, j * P:(j + 1) * P], src[:, 4 * half + j, t * P:(t + 1) * P], K.con(C_ID))
                mm.then_inc(*made.one())
            for u in range(32):
                par, t, f = u // 16, u // 8 % 2, u % 8
                rows = slice(64 * par, 64 * par + 64)
                if u % 4 == 0:
                    pe.wait_ge(*taken.at(u // 4 + 1))
                for c in range(4):
                    tok = slice(t * P + c * RC, t * P + (c + 1) * RC)
                    for j, src in enumerate((bt, kt)):
                        at = (u % 4) * P + j * 2 * RC
                        mm = nc.tensor.matmul(K.ps[RC * c:RC * c + RC, u // 4, at:at + 2 * RC], src[rows, f, tok], ar[rows, f, :, tok],
                                              start=True, stop=True)
                if u % 4 == 3:
                    mm.then_inc(*made.one())
            pe.wait_ge(*taken.at(9))
            for t in range(2):
                for f in range(KT):
                    at = t * RW_HEADS + 2 * f
                    mm = nc.tensor.matmul(K.ps[:, 0, at:at + 2], rk[:, f, t * P:(t + 1) * P], K.con(C_HSEL, 2), start=True, stop=True)
            mm.then_inc(*made.one())

        @block.vector
        def _(dve):
            v = nc.vector
            for n in range(8):
                dve.wait_ge(*made.at(n + 1))
                v.tensor_copy((bp, kp)[n // 4][:, n // 2 % 2, 512 * (n % 2):512 * (n % 2) + 512], K.ps[:, n]).then_inc(*taken.one())
            for b in range(8):
                dve.wait_ge(*made.at(9 + b))
                for j in range(2):
                    mask = sc_mask(K, j)
                    for w in range(2):
                        last = v.tensor_tensor(sc[:, 4 * b:4 * b + 4, 2 * w + j], K.ps[:, b].rearrange("p (u m t) -> p u m t", u=4, m=4)[:, :, 2 * w + j],
                                               mask, ALU.mult)
                last.then_inc(*taken.one())
            dve.wait_ge(*made.at(17))
            v.tensor_copy(bon[:], K.ps[:, 0, 0:2 * RW_HEADS].rearrange("p (t h) -> p t h", t=2))


def sc_mask(K, j):
    return K.con(C_RWK + j * RC, RC).rearrange("p (a t) -> p a t", a=1).to_broadcast([P, 4, RC])


def rwkv_inverse(K, sc, v, tm, nv, scratch, room, room2):
    nc = K.nc
    with ExitStack() as ctx:
        square = lambda ap: ap.rearrange("p (s t) -> p s t", s=RC)
        N, T = square(room[:, 0:RC * RC]), square(room[:, RC * RC:2 * RC * RC])
        prod = square(room2[:, 0:RC * RC])
        out, back = K.sig("inv_out"), K.sig("inv_back")
        solved, made = K.sig("p_ready"), K.sig("tile_made")
        block = ctx.enter_context(nc.Block())

        @block.sync
        def _(sp):
            for c in range(4):
                dst = scratch[0, c * 32:(c + 1) * 32].rearrange("u (s t) -> s u t", s=RC)
                sp.dma_start(dst, sc[c * RC:(c + 1) * RC, :, 0]).then_inc(*out.dma())
            sp.wait_ge(*out.now())
            sp.dma_start(N[:].rearrange("p s t -> p (s t)"), scratch[0]).then_inc(*back.dma())
            sp.wait_ge(*solved.at(1))
            sp.dma_start(scratch[1], prod[:].rearrange("p s t -> p (s t)")).then_inc(*out.dma())
            sp.wait_ge(*out.now())
            for c in range(4):
                src = scratch[1, c * 32:(c + 1) * 32].rearrange("u (s t) -> s u t", s=RC)
                sp.dma_start(tm[c * RC:(c + 1) * RC], src).then_inc(*back.dma())
            sp.wait_ge(*back.now())

        @block.tensor
        def _(pe):
            for t in range(2):
                for par in range(2):
                    for j in range(2):
                        for c in range(4):
                            R = slice(c * RC, (c + 1) * RC)
                            for f in range(KT):
                                h, u = 2 * f + par, par * 16 + t * 8 + f
                                mm = nc.tensor.matmul(K.ps[R, 4 * t + 2 * j + par, f * HD:(f + 1) * HD], sc[R, u, 2 + j],
                                                      v[R, t, h * HD:(h + 1) * HD], start=True, stop=True)
                        mm.then_inc(*made.one())

        @block.scalar
        def _(act):
            n = 0
            for t in range(2):
                for par in range(2):
                    for j in range(2):
                        act.wait_ge(*made.at(n + 1))
                        dst = nv[:, j, t].rearrange("p (f q i) -> p q f i", q=2, i=HD)[:, par]
                        nc.scalar.copy(dst, K.ps[:, 4 * t + 2 * j + par].rearrange("p (f i) -> p f i", i=HD))
                        n += 1

        @block.vector
        def _(dve):
            vv = nc.vector
            do = lambda ins: link(dve, K.dve_step, ins)
            do(vv.memset(T[:], 0.0))
            do(vv.memset(T[:].rearrange("p s t -> p (s t)")[:, 0:RC * RC:RC + 1], 1.0))
            dve.wait_ge(*back.at(16))
            for t in range(1, RC):
                coef = N[:, 0:t, t:t + 1].rearrange("p s a -> p a s").to_broadcast([P, t, t])
                pr = prod[:].rearrange("p s t -> p (s t)")[:, 0:t * t].rearrange("p (c s) -> p c s", s=t)
                do(vv.tensor_tensor(pr, T[:, 0:t, 0:t].rearrange("p s c -> p c s"), coef, ALU.mult))
                do(vv.reduce_sum(T[:, t, 0:t].rearrange("p (c a) -> p c a", a=1), pr, AX))
            vv.tensor_copy(prod[:], T[:].rearrange("p t s -> p s t")).then_inc(*solved.one())


def rwkv_chunks(K, ar, cl, bp, kp, sc, tm, nv, v, y, room, room2):
    nc = K.nc
    with ExitStack() as ctx:
        S, Sd = (room2[:, j * KT * HD:(j + 1) * KT * HD].rearrange("p (f i) -> p f i", i=HD) for j in range(2))
        W, SA = room[:, 0:D], room[:, D:2 * D]
        as_made, w_ready, sa_made, sa_ready = K.sig("s_made"), K.sig("s_ready"), K.sig("e_made"), K.sig("p_ready")
        st_made, st_ready, y_made, y_taken = K.sig("t_made"), K.sig("t_taken"), K.sig("pv_made"), K.sig("o_taken")
        by_par = lambda ap, par: ap.rearrange("p (f q i) -> p q f i", q=2, i=HD)[:, par]
        bank = lambda R, b: K.ps[R, b].rearrange("p (f i) -> p f i", i=HD)
        block = ctx.enter_context(nc.Block())

        @block.tensor
        def _(pe):
            for c in range(N_RC):
                t, R = c // 4, slice((c % 4) * RC, (c % 4 + 1) * RC)
                tok = slice(c * RC, (c + 1) * RC)
                if c:
                    pe.wait_ge(*st_ready.at(c))
                    pe.wait_ge(*y_taken.at(c))
                    for j in range(2):
                        for par in range(2):
                            rows = slice(64 * par, 64 * par + 64)
                            for f in range(KT):
                                mm = nc.tensor.matmul(K.ps[R, 5 * j + par, f * HD:(f + 1) * HD], ar[rows, f, j, tok], S[rows, f],
                                                      start=True, stop=True)
                        if j == 0:
                            mm.then_inc(*as_made.one())
                pe.wait_ge(*w_ready.at(c + 1))
                for par in range(2):
                    for f in range(KT):
                        h, u = 2 * f + par, par * 16 + t * 8 + f
                        mm = nc.tensor.matmul(K.ps[R, 2 + par, f * HD:(f + 1) * HD], tm[R, u], W[R, h * HD:(h + 1) * HD], start=True, stop=True)
                mm.then_inc(*sa_made.one())
                pe.wait_ge(*sa_ready.at(c + 1))
                if c < N_RC - 1:
                    for h in range(RW_HEADS):
                        o = K.ps[64 * (h % 2):64 * (h % 2) + 64, 4, (h // 2) * HD:(h // 2 + 1) * HD]
                        nc.tensor.matmul(o, bp[R, t, h * HD:(h + 1) * HD], SA[R, h * HD:(h + 1) * HD], start=True, stop=False)
                        mm = nc.tensor.matmul(o, kp[R, t, h * HD:(h + 1) * HD], v[R, t, h * HD:(h + 1) * HD], start=False, stop=True)
                    mm.then_inc(*st_made.one())
                for par in range(2):
                    for f in range(KT):
                        h, u = 2 * f + par, par * 16 + t * 8 + f
                        mm = nc.tensor.matmul(K.ps[R, par, f * HD:(f + 1) * HD], sc[R, u, 1], SA[R, h * HD:(h + 1) * HD], start=True, stop=True)
                mm.then_inc(*y_made.one())

        @block.vector
        def _(dve):
            vv = nc.vector
            do = lambda ins: link(dve, K.dve_step, ins)
            for c in range(N_RC):
                t, R = c // 4, slice((c % 4) * RC, (c % 4 + 1) * RC)
                if c:
                    dve.wait_ge(*as_made.at(c))
                    for par in range(2):
                        last = vv.tensor_tensor(by_par(W[R], par), bank(R, par), by_par(nv[R, 0, t], par), ALU.add)
                else:
                    last = vv.tensor_copy(W[R], nv[R, 0, t])
                last.then_inc(*w_ready.one())
                if c:
                    end = cl[:, :, c:c + 1].to_broadcast([P, KT, HD])
                    vv.tensor_tensor(Sd[:], S[:], end, ALU.mult).then_inc(*K.dve_step.one())
                dve.wait_ge(*sa_made.at(c + 1))
                for par in range(2):
                    last = vv.tensor_copy(by_par(SA[R], par), bank(R, 2 + par))
                last.then_inc(*sa_ready.one())
                if c < N_RC - 1:
                    dve.wait_ge(*st_made.at(c + 1))
                    if c:
                        dve.wait_ge(*K.dve_step.now())
                        vv.tensor_tensor(S[:], Sd[:], bank(slice(0, P), 4), ALU.add).then_inc(*st_ready.one())
                    else:
                        vv.tensor_copy(S[:], bank(slice(0, P), 4)).then_inc(*st_ready.one())
                dve.wait_ge(*y_made.at(c + 1))
                for par in range(2):
                    last = vv.tensor_tensor(by_par(y[R, t], par), bank(R, par), by_par(nv[R, 1, t], par), ALU.add)
                if c:
                    do(last)
                    for par in range(2):
                        last = vv.tensor_tensor(by_par(y[R, t], par), bank(R, 5 + par), by_par(y[R, t], par), ALU.add)
                last.then_inc(*y_taken.one())


def rwkv_output(K, y, v, g, bon, ln, tmp):
    nc, I = K.nc, K.ins
    n = 2 * RW_HEADS
    with ExitStack() as ctx:
        def sb(name, shape):
            return ctx.enter_context(nc.sbuf_tensor(name, shape, F32))
        st = sb("rw_st", [P, 4, n, 1])
        given, sq_in, sq_done = K.sig("rows_given"), K.sig("exp_asked"), K.sig("exp_done")
        block = ctx.enter_context(nc.Block())
        heads = lambda ap: ap.rearrange("p (h d) -> p h d", d=HD)
        Y = heads(y[:].rearrange("p t f -> p (t f)"))
        V = heads(v[:].rearrange("p t f -> p (t f)"))
        TMP = heads(tmp[:])
        wide = lambda i: st[:, i].to_broadcast([P, n, HD])

        @block.sync
        def _(sp):
            sp.dma_start(ln[:, 0], I["c_ln_g_2"].to_broadcast([P, D])).then_inc(*given.dma())
            sp.dma_start(ln[:, 1], I["c_ln_b_2"].to_broadcast([P, D])).then_inc(*given.dma())

        @block.scalar
        def _(act):
            act.wait_ge(*sq_in.at(1))
            nc.scalar.activation(TMP, Y, ACT.Square).then_inc(*sq_done.one())
            act.wait_ge(*sq_in.at(2))
            nc.scalar.activation(st[:, 2], st[:, 1], ACT.Sqrt, bias=K.eps[:, 2:3], scale=1.0 / HD).then_inc(*sq_done.one())

        @block.vector
        def _(dve):
            vv = nc.vector
            do = lambda ins: link(dve, K.dve_step, ins)
            do(vv.reduce_sum(st[:, 0], Y, AX))
            do(vv.tensor_scalar(st[:, 0], st[:, 0], 1.0 / HD, None, ALU.mult))
            vv.tensor_tensor(Y, Y, wide(0), ALU.subtract).then_inc(*sq_in.one())
            dve.wait_ge(*sq_done.at(1))
            vv.reduce_sum(st[:, 1], TMP, AX).then_inc(*sq_in.one())
            dve.wait_ge(*sq_done.at(2))
            do(vv.reciprocal(st[:, 3], st[:, 2]))
            do(vv.tensor_tensor(Y, Y, wide(3), ALU.mult))
            dve.wait_ge(*given.at(32))
            for j, op in ((0, ALU.mult), (1, ALU.add)):
                row = ln[:, j:j + 1].to_broadcast([P, 2, D])
                do(vv.tensor_tensor(y[:], y[:], row, op))
            do(vv.tensor_tensor(TMP, V, bon[:].rearrange("p t (h a) -> p (t h) a", a=1).to_broadcast([P, n, HD]), ALU.mult))
            do(vv.tensor_tensor(Y, Y, TMP, ALU.add))
            do(vv.tensor_tensor(y[:], y[:], g[:], ALU.mult))


def second_block(K, scratch):
    H, X = K.h[:, :, 0:SEQ], K.xn[:, :, 0:SEQ]
    for layer in range(2):
        gain = lambda j: K.col("norm_gains_2", (6 * layer + j) * KT, KT)
        ffn(K, *[K.ins[f"ffn1_w_{w}_2"][layer] for w in ("gate", "up", "down")], gain(0), gain(1))
        rms_norm(K, H, X, gain(2))
        if layer == 0:
            nsa_ssd(K)
        else:
            rwkv(K, scratch)
        rms_norm(K, X, X, gain(3), add_to=H)
        ffn(K, *[K.ins[f"ffn2_w_{w}_2"][layer] for w in ("gate", "up", "down")], gain(4), gain(5))


def token_model_kernel(nc, ins, out, gates_dram, scratch):
    K = Core(nc, ins)
    load_all(K)
    first_block(K, gates_dram)
    second_block(K, scratch)
    store_tokens(K, out)


def first_block(K, gates_dram):
    rms_norm(K, K.h[:], K.xn, K.col("a_norm", 0, KT))
    pool_mixer(K)
    rms_norm(K, K.h[:], K.xn, K.col("ffn_norm", 0, KT))
    moe(K, 0, gates_dram)
    with ExitStack() as ctx:
        kv = latent_kv(K, ctx)
        mla(K, kv)
    rms_norm(K, K.h[:], K.xn, K.col("ffn_norm", KT, KT))
    moe(K, 1, gates_dram)
    final_norm(K)


INS = ["x", "meta_tokens", "a_norm", "a_w", "a_scale", "b_norm", "b_w_dq", "b_q_norm", "b_w_uq", "b_w_o", "kv_norm",
       "w_dkv", "kv_lat_norm", "w_uk", "w_uv", "ffn_norm", "router_g", "router_g_bias", "router_e", "router_e_bias",
       "w_gate", "w_up", "w_down", "final_norm", "norm_gains_2", "ffn1_w_gate_2", "ffn1_w_up_2", "ffn1_w_down_2",
       "ffn2_w_gate_2", "ffn2_w_up_2", "ffn2_w_down_2", "ab_w_in_2", "a_cmp_pe_k_2", "a_cmp_w1_k_2", "a_cmp_w2_k_2",
       "a_cmp_pe_v_2", "a_cmp_w1_v_2", "a_cmp_w2_v_2", "b_conv_w_2", "b_conv_b_2", "b_dt_bias_2", "b_a_log_2",
       "b_d_skip_2", "b_norm_w_2", "ab_w_out_2", "c_mu_2", "c_w_r_2", "c_w_k_2", "c_w_v_2", "c_w_o_2", "c_w0_2",
       "c_w1_2", "c_w2_2", "c_a0_2", "c_a1_2", "c_a2_2", "c_g1_2", "c_g2_2", "c_k_k_2", "c_k_a_2", "c_r_k_2",
       "c_ln_g_2", "c_ln_b_2"]


def kernel(**inputs):
    import concourse.bacc as bacc
    from concourse.bass_utils import run_bass_kernel_spmd

    nc = bacc.Bacc("TRN2", target_bir_lowering=False, num_devices=1)
    arrays = {f"in_{n}": np.ascontiguousarray(inputs[n]) for n in INS}
    arrays["in_constants"] = constants()
    ins = {n[3:]: nc.dram_tensor(n, a.shape, F32, kind="ExternalInput").ap() for n, a in arrays.items()}
    out = nc.dram_tensor("out", (1, SEQ, D), F32, kind="ExternalOutput").ap()
    gates = nc.dram_tensor("gates", (N_EXP, L1), F32, kind="Internal").ap()
    scratch = nc.dram_tensor("scratch", (2, P, RC * RC), F32, kind="Internal").ap()
    token_model_kernel(nc, ins, out, gates, scratch)
    result = run_bass_kernel_spmd(nc, [arrays], core_ids=[0])
    return result.results[0]["out"]
```

```python
import math
from contextlib import ExitStack

import numpy as np
import concourse.bass as bass
from concourse import mybir

F32 = mybir.dt.float32
ALU = mybir.AluOpType
ACT = mybir.ActivationFunctionType
AX = mybir.AxisListType.X

P = 128
D = 1024
KT = D // P
SEQ = 256
N_META = 16
L1 = SEQ + N_META
Q_TILES_1 = [(0, 128), (128, 128), (256, 16)]
NEG = -1e30
EPS = [1e-6, 1e-5, 64e-5]

POOL_G = 4
POOL_WINDOWS = (2, 4, 8, 16)
HEADS = 8
NOPE = 128
ROPE = 64
V_DIM = 128
Q_LORA = 384
KV_LORA = 256
MLA_SCALE = (NOPE + ROPE) ** -0.5
N_GROUPS = 4
PER_GROUP = 8
N_EXP = N_GROUPS * PER_GROUP
D_EXP = 256
CAP = 32

D_FF = 2816
FF_T = D_FF // P
GU_COLS = 256
NSA_KV = 2
NSA_GROUP = 4
HD = 64
CMP_BLOCK = 32
CMP_STRIDE = 16
N_CMP = (SEQ - CMP_BLOCK) // CMP_STRIDE + 1
SSD_HEADS = 16
SSD_GROUPS = 2
SSD_STATE = 128
SSD_CONV = 4
SSD_INNER = 1024
XBC = SSD_INNER + 2 * SSD_GROUPS * SSD_STATE
SPLITS = (512, 128, 128, 128, 128, 128, 128, 24, SSD_INNER, XBC, SSD_HEADS)
OFF = [sum(SPLITS[:i]) for i in range(len(SPLITS) + 1)]
RW_HEADS = 16
RC = 32
N_RC = SEQ // RC
GATE_LORA = 160

C_ID, C_ONE, C_CAUSAL, C_TRI, C_ROT, C_HEAD = 0, 128, 256, 384, 512, 640
C_COS, C_SIN = 768, 768 + L1
C_CNT = C_SIN + L1
C_CMPM = C_CNT + 4 * L1
C_RWK = C_CMPM + 2 * (N_CMP + 1)
C_IOTA = C_RWK + 2 * RC
C_HSEL = C_IOTA + 8
C_TRI1 = C_HSEL + 2
C_SLOT = C_TRI1 + P
C_END = C_SLOT + CAP


def constants():
    c = np.zeros((P, C_END), np.float32)
    p = np.arange(P)
    c[:, C_ID:C_ID + P] = np.eye(P)
    c[:, C_ONE:C_ONE + P] = 1.0
    c[:, C_CAUSAL:C_CAUSAL + P] = np.where(p[None, :] <= p[:, None], 0.0, NEG)
    c[:, C_TRI:C_TRI + P] = p[:, None] <= p[None, :]
    for m in range(P):
        if m % 64 < 32:
            c[m + 32, C_ROT + m] = -1.0
        else:
            c[m - 32, C_ROT + m] = 1.0
    c[:, C_HEAD:C_HEAD + P] = (p[:, None] // 64) == (p[None, :] // 64)
    inv = (np.float32(10000.0) ** (-np.arange(0, ROPE, 2, dtype=np.float32) / np.float32(ROPE))).astype(np.float32)
    ang = (np.arange(L1, dtype=np.float32)[None, :] * inv[p % 32][:, None]).astype(np.float32)
    c[:, C_COS:C_COS + L1] = np.cos(ang)
    c[:, C_SIN:C_SIN + L1] = np.sin(ang)
    t = np.arange(L1)
    for g, w in enumerate(POOL_WINDOWS):
        c[:, C_CNT + g * L1:C_CNT + (g + 1) * L1] = 1.0 / np.minimum(t + 1, w).astype(np.float32)
    for i in range(2):
        for n in range(N_CMP):
            c[:, C_CMPM + i * (N_CMP + 1) + n] = (n * CMP_STRIDE + CMP_BLOCK - 1) <= (p + i * P)
    tc = np.arange(RC)
    c[:, C_RWK:C_RWK + RC] = (p[:, None] % RC) < tc[None, :]
    c[:, C_RWK + RC:C_RWK + 2 * RC] = (p[:, None] % RC) <= tc[None, :]
    c[:, C_IOTA:C_IOTA + 8] = 8.0 - np.arange(8)
    c[:, C_HSEL:C_HSEL + 2] = (p[:, None] // 64) == np.arange(2)[None, :]
    c[:, C_TRI1:C_TRI1 + P] = p[:, None] < p[None, :]
    c[:, C_SLOT:C_SLOT + CAP] = np.arange(CAP)
    return c


VECTORS = [("a_norm", 8), ("a_scale", 8), ("b_norm", 8), ("kv_norm", 8), ("ffn_norm", 16), ("final_norm", 8),
           ("norm_gains_2", 96), ("c_mu_2", 48), ("c_w0_2", 8), ("c_a0_2", 8), ("c_k_k_2", 8), ("c_k_a_2", 8),
           ("c_r_k_2", 8), ("kv_lat_norm", 2), ("b_q_norm", 3), ("b_conv_w_2", 48), ("b_conv_b_2", 12)]
VEC_AT = {}
_n = 0
for _name, _rows in VECTORS:
    VEC_AT[_name] = _n
    _n += _rows
VEC_ROWS = _n
VEC_TILES = -(-VEC_ROWS // P)


class Signal:

    def __init__(self, nc, name):
        self.sem = nc.alloc_semaphore(name)
        self.given = self.base = 0

    def begin(self):
        self.base = self.given
        return self

    def at(self, n):
        return self.sem, self.base + n

    def one(self):
        self.given += 1
        return self.sem, 1

    def dma(self):
        self.given += 16
        return self.sem, 16

    def now(self):
        return self.sem, self.given


class Core:

    def __init__(self, nc, ins):
        self.nc, self.ins = nc, ins
        self.signals, self.stage = {}, 0
        self.h = nc.alloc_sbuf_tensor("h", [P, KT, L1], F32)
        self.xn = nc.alloc_sbuf_tensor("xn", [P, KT, L1], F32)
        self.sq = nc.alloc_sbuf_tensor("sq", [P, KT, L1], F32)
        self.rs = nc.alloc_sbuf_tensor("rs", [P, 3, L1], F32)
        self.cst = nc.alloc_sbuf_tensor("cst", [P, C_END], F32)
        self.vec = nc.alloc_sbuf_tensor("vec", [P, VEC_TILES * P], F32)
        self.w = nc.alloc_sbuf_tensor("w", [P, 2, 4096], F32)
        self.ps = nc.alloc_psum_tensor("ps", [P, 8, 512], F32)
        self.eps = nc.alloc_sbuf_tensor("eps", [P, len(EPS)], F32)
        self.dve_step, self.act_step = Signal(nc, "dve_step"), Signal(nc, "act_step")

    def sig(self, name):
        if name not in self.signals:
            self.signals[name] = Signal(self.nc, name)
        return self.signals[name].begin()

    def next(self):
        self.stage += 1
        return self.stage

    def fullest(self, engine, count):
        return engine.value_load(count[0:1, 0:1], min_val=0, max_val=L1)

    def con(self, at, n=P):
        return self.cst[:, at:at + n]

    def col(self, name, i=0, n=1):
        at = VEC_AT[name] + i
        return self.vec[:, at:at + n]


def link(eng, signal, instruction):
    instruction.then_inc(*signal.one())
    eng.wait_ge(*signal.now())


def rms_norm(K, src, dst, gain, eps=1e-6, add_to=None, factor=1.0):
    nc = K.nc
    n, T = src.shape[1], src.shape[2]
    squared, summed, rooted = K.sig("squared"), K.sig("summed"), K.sig("rooted")
    with nc.Block() as block:
        @block.tensor
        def _(pe):
            pe.wait_ge(*squared.at(1))
            for k in range(n):
                mm = nc.tensor.matmul(K.ps[:, 0, 0:T], K.con(C_ONE), K.sq[:, k, 0:T], start=k == 0, stop=k == n - 1)
            mm.then_inc(*summed.one())

        @block.scalar
        def _(act):
            nc.scalar.activation(K.sq[:, 0:n, 0:T], src, ACT.Square).then_inc(*squared.one())
            act.wait_ge(*summed.at(1))
            nc.scalar.activation(K.rs[:, 0, 0:T], K.ps[:, 0, 0:T], ACT.Sqrt, bias=K.eps[:, EPS.index(eps):EPS.index(eps) + 1],
                                 scale=1.0 / (n * P)).then_inc(*rooted.one())

        @block.vector
        def _(dve):
            dve.wait_ge(*rooted.at(1))
            link(dve, K.dve_step, nc.vector.reciprocal(K.rs[:, 1, 0:T], K.rs[:, 0, 0:T]))
            if factor != 1.0:
                link(dve, K.dve_step, nc.vector.tensor_scalar(K.rs[:, 1, 0:T], K.rs[:, 1, 0:T], factor, None, ALU.mult))
            for k in range(n):
                last = nc.vector.scalar_tensor_tensor(out=dst[:, k], in0=src[:, k], scalar=gain[:, k:k + 1],
                                                      in1=K.rs[:, 1, 0:T], op0=ALU.mult, op1=ALU.mult)
            if add_to is not None:
                link(dve, K.dve_step, last)
                nc.vector.tensor_tensor(add_to, add_to, dst, ALU.add)


def feature_linear(K, w, x, T, store, by="vector", pieces=None):
    nc = K.nc
    rows, N = w.shape
    kr = min(rows, P)
    nk = rows // kr
    wide = min(4096 // nk // P * P, -(-N // P) * P)
    mt = -(-N // P)
    per = wide // P
    loads = -(-N // wide)
    view = w.rearrange("(k p) n -> p k n", p=kr)
    loaded = [K.sig("w_loaded_0"), K.sig("w_loaded_1")]
    made, stored = K.sig("tile_made"), K.sig("tile_stored")

    with nc.Block() as block:
        @block.sync
        def _(sp):
            for b in range(loads):
                cw = min(wide, N - b * wide)
                if b >= 2:
                    sp.wait_ge(*made.at((b - 1) * per))
                slot = K.w[0:kr, b % 2, 0:nk * cw].rearrange("p (k n) -> p k n", k=nk)
                for to, at, n in pieces or [(0, b * wide, cw)]:
                    sp.dma_start(slot[:, :, to:to + n], view[:, :, at:at + n]).then_inc(*loaded[b % 2].dma())

        @block.tensor
        def _(pe):
            for m in range(mt):
                b = m // per
                cw = min(wide, N - b * wide)
                if m % per == 0:
                    pe.wait_ge(*loaded[b % 2].at(16 * (b // 2 + 1) * len(pieces or "1")))
                if m >= 8:
                    pe.wait_ge(*stored.at(m - 7))
                mw = min(P, N - m * P)
                at = m * P - b * wide
                for k in range(nk):
                    wk = K.w[0:kr, b % 2, k * cw:(k + 1) * cw]
                    mm = nc.tensor.matmul(K.ps[0:mw, m % 8, 0:T], wk[:, at:at + mw], x(k),
                                          start=k == 0, stop=k == nk - 1)
                mm.then_inc(*made.one())

        def take(eng):
            for m in range(mt):
                eng.wait_ge(*made.at(m + 1))
                store(m, K.ps[0:min(P, N - m * P), m % 8, 0:T]).then_inc(*stored.one())

        if by == "vector":
            @block.vector
            def _(dve):
                take(dve)
        else:
            @block.scalar
            def _(act):
                take(act)


def token_linear(K, w, x, nk, tiles, store, by="vector"):
    nc = K.nc
    rows, N = w.shape
    kr = min(rows, P)
    nk = rows // kr
    view = w.rearrange("(k p) n -> p k n", p=kr)
    blocks = [(c, min(512, N - c)) for c in range(0, N, 512)]
    nt = len(tiles)
    loaded = [K.sig("w_loaded_0"), K.sig("w_loaded_1")]
    made, stored = K.sig("tile_made"), K.sig("tile_stored")

    with nc.Block() as block:
        @block.sync
        def _(sp):
            for b, (c, cw) in enumerate(blocks):
                if b >= 2:
                    sp.wait_ge(*made.at((b - 1) * nt))
                sp.dma_start(K.w[0:kr, b % 2, 0:nk * cw].rearrange("p (k n) -> p k n", k=nk),
                             view[:, :, c:c + cw]).then_inc(*loaded[b % 2].dma())

        @block.tensor
        def _(pe):
            n = 0
            for b, (c, cw) in enumerate(blocks):
                pe.wait_ge(*loaded[b % 2].at(16 * (b // 2 + 1)))
                for t0, tn in tiles:
                    if n >= 8:
                        pe.wait_ge(*stored.at(n - 7))
                    for k in range(nk):
                        mm = nc.tensor.matmul(K.ps[0:tn, n % 8, 0:cw], x(k, t0, tn), K.w[0:kr, b % 2, k * cw:(k + 1) * cw],
                                              start=k == 0, stop=k == nk - 1)
                    mm.then_inc(*made.one())
                    n += 1

        def take(eng):
            n = 0
            for c, cw in blocks:
                for i, (t0, tn) in enumerate(tiles):
                    eng.wait_ge(*made.at(n + 1))
                    store(i, c, cw, K.ps[0:tn, n % 8, 0:cw]).then_inc(*stored.one())
                    n += 1

        if by == "vector":
            @block.vector
            def _(dve):
                take(dve)
        else:
            @block.scalar
            def _(act):
                take(act)


def load_all(K):
    nc, I = K.nc, K.ins
    with ExitStack() as ctx:
        rows = ctx.enter_context(nc.sbuf_tensor("vec_rows", [P, VEC_TILES, P], F32))
        tok = ctx.enter_context(nc.sbuf_tensor("tok_rows", [P, 3, D], F32))
        given, blank = K.sig("rows_given"), K.sig("rows_blank")
        made, stored = K.sig("tile_made"), K.sig("tile_stored")
        n_dma = 16 * (1 + 2 + len(VECTORS) + 2)
        pieces = []
        for name, n in VECTORS:
            flat = I[name]
            dims = " ".join(f"a{i}" for i in range(len(flat.shape)))
            flat = flat.rearrange(f"{dims} -> ({dims})").rearrange("(r c) -> r c", c=P)
            at, done = VEC_AT[name], 0
            while done < n:
                take = min(n - done, P - (at + done) % P)
                pieces.append(((at + done) // P, (at + done) % P, take, flat[done:done + take]))
                done += take
        block = ctx.enter_context(nc.Block())

        @block.sync
        def _(sp):
            sp.dma_start(K.cst[:], I["constants"]).then_inc(*given.dma())
            sp.dma_start(tok[0:N_META, 0], I["meta_tokens"]).then_inc(*given.dma())
            sp.dma_start(tok[N_META:P, 0], I["x"][0, 0:P - N_META]).then_inc(*given.dma())
            sp.dma_start(tok[:, 1], I["x"][0, P - N_META:2 * P - N_META]).then_inc(*given.dma())
            sp.dma_start(tok[0:N_META, 2], I["x"][0, 2 * P - N_META:SEQ]).then_inc(*given.dma())
            sp.wait_ge(*blank.at(1))
            for tile, row, n, src in pieces:
                sp.dma_start(rows[row:row + n, tile], src).then_inc(*given.dma())

        @block.vector
        def _(dve):
            for i, e in enumerate(EPS):
                nc.vector.memset(K.eps[:, i:i + 1], e)
            nc.vector.memset(rows[:], 0.0).then_inc(*blank.one())
            for n in range(VEC_TILES + 2 * 3):
                dve.wait_ge(*made.at(n + 1))
                if n < VEC_TILES:
                    last = nc.vector.tensor_copy(K.vec[:, n * P:(n + 1) * P], K.ps[:, n % 8, 0:P])
                else:
                    i, half = divmod(n - VEC_TILES, 2)
                    t0, tn = Q_TILES_1[i]
                    last = nc.vector.tensor_copy(K.h[:, 4 * half:4 * half + 4, t0:t0 + tn],
                                                 K.ps[:, n % 8, :].rearrange("p (k t) -> p k t", k=4)[:, :, 0:tn])
                last.then_inc(*stored.one())

        @block.tensor
        def _(pe):
            pe.wait_ge(*given.now())
            n = 0
            for i in range(VEC_TILES):
                nc.tensor.transpose(K.ps[:, n % 8, 0:P], rows[:, i], K.con(C_ID)).then_inc(*made.one())
                n += 1
            for i, (t0, tn) in enumerate(Q_TILES_1):
                for half in range(2):
                    if n >= 8:
                        pe.wait_ge(*stored.at(n - 7))
                    for k in range(4):
                        mm = nc.tensor.transpose(K.ps[:, n % 8, k * P:k * P + tn],
                                                 tok[0:tn, i, (4 * half + k) * P:(4 * half + k + 1) * P],
                                                 K.cst[0:tn, C_ID:C_ID + tn])
                    mm.then_inc(*made.one())
                    n += 1


def pool_mixer(K):
    nc, I = K.nc, K.ins
    gt = KT // POOL_G
    with ExitStack() as ctx:
        pad = max(POOL_WINDOWS)
        run = ctx.enter_context(nc.sbuf_tensor("run", [P, 2, KT, pad + L1], F32))
        wg = ctx.enter_context(nc.sbuf_tensor("pool_w", [P, POOL_G * gt, gt * P], F32))
        given, pooled = K.sig("rows_given"), K.sig("pooled")
        made, stored = K.sig("tile_made"), K.sig("tile_stored")
        block = ctx.enter_context(nc.Block())

        @block.sync
        def _(sp):
            sp.dma_start(wg[:], I["a_w"][0].rearrange("g (k p) n -> p (g k) n", p=P)).then_inc(*given.dma())

        @block.vector
        def _(dve):
            nc.vector.memset(run[:, :, :, 0:pad], 0.0)
            link(dve, K.dve_step, nc.vector.tensor_copy(run[:, 0, :, pad:], K.xn[:]))
            at = [0, 0, 0, 0]
            src, width = 0, 1
            for g, w in enumerate(POOL_WINDOWS):
                lo = g * gt
                link(dve, K.dve_step, nc.vector.tensor_tensor(
                    run[:, 1 - src, lo:, pad:], run[:, src, lo:, pad:], run[:, src, lo:, pad - width:pad - width + L1], ALU.add))
                src, width = 1 - src, w
                at[g] = src
                for k in range(lo, lo + gt):
                    link(dve, K.dve_step, nc.vector.tensor_tensor(K.sq[:, k], run[:, src, k, pad:],
                                                                  K.con(C_CNT + g * L1, L1), ALU.mult))
                last = nc.vector.tensor_tensor(K.sq[:, lo:lo + gt], K.sq[:, lo:lo + gt], K.xn[:, lo:lo + gt], ALU.subtract)
                last.then_inc(*pooled.one())
            for m in range(KT):
                dve.wait_ge(*made.at(m + 1))
                nc.vector.scalar_tensor_tensor(out=K.h[:, m], in0=K.ps[:, m, 0:L1], scalar=K.col("a_scale", m),
                                               in1=K.h[:, m], op0=ALU.mult, op1=ALU.add)

        @block.tensor
        def _(pe):
            pe.wait_ge(*given.at(16))
            for g in range(POOL_G):
                pe.wait_ge(*pooled.at(g + 1))
                for m in range(gt):
                    for k in range(gt):
                        mm = nc.tensor.matmul(K.ps[:, g * gt + m, 0:L1], wg[:, g * gt + k, m * P:(m + 1) * P], K.sq[:, g * gt + k],
                                              start=k == 0, stop=k == gt - 1)
                    mm.then_inc(*made.one())


def first_of(dve, K, mask, score, top):
    nc, n = K.nc, mask.shape[2]
    iota = K.con(C_IOTA + 8 - n, n).rearrange("p (a n) -> p a n", a=1).to_broadcast([P, 3, n])
    link(dve, K.dve_step, nc.vector.tensor_tensor(score, mask, iota, ALU.mult))
    link(dve, K.dve_step, nc.vector.reduce_max(top, score, AX))
    link(dve, K.dve_step, nc.vector.tensor_tensor(mask, score, top.to_broadcast([P, 3, n]), ALU.is_equal))


def moe(K, layer, gates_dram):
    nc, I = K.nc, K.ins
    nr = N_GROUPS + N_EXP
    ET = D_EXP // P
    with ExitStack() as ctx:
        def sb(name, shape, dt=F32):
            return ctx.enter_context(nc.sbuf_tensor(f"{name}_{layer}", shape, dt))
        gate = sb("gate", [P, 3, N_EXP])
        count = sb("count", [1, 1], mybir.dt.int32)
        xg = sb("xg", [P, KT, N_EXP * CAP])
        spread = sb("spread", [P, N_EXP * CAP // P, L1])
        wd = sb("wd", [P, 4, ET, D])
        wgu = [K.w[:, j].rearrange("p (a k n) -> p a k n", a=2, k=KT) for j in range(2)]
        more = sb("wgu", [P, 2, 2, KT, D_EXP])
        wgu += [more[:, j] for j in range(2)]
        w_in = [K.sig(f"expert_w_{j}_{layer}") for j in range(4)]
        views = [I[n][layer].rearrange("e (k p) n -> p e k n", p=P) for n in ("w_gate", "w_up", "w_down")]

        def load_expert(sp, e, j):
            one = bass.ds(e, 1)
            sp.dma_start(wgu[j][:, 0], views[0][:, one]).then_inc(w_in[j].sem, 16)
            sp.dma_start(wgu[j][:, 1], views[1][:, one]).then_inc(w_in[j].sem, 16)
            sp.dma_start(wd[:, j], views[2][:, one]).then_inc(w_in[j].sem, 16)
        with ExitStack() as inner:
            route(K, layer, inner, gate, count, xg, spread, load_expert)
        with ExitStack() as inner:
            over_all = experts_over_all(K, layer, inner, gates_dram, gate, wgu, wd, w_in)
            in_slots = experts_in_slots(K, layer, inner, xg, spread, wgu, wd, w_in, load_expert)
            block = inner.enter_context(nc.Block())

            @block.sync
            def _(sp):
                with sp.If(K.fullest(sp, count) > CAP):
                    over_all["sync"](sp)
                with sp.Else():
                    in_slots["sync"](sp)

            @block.tensor
            def _(pe):
                with pe.If(K.fullest(pe, count) > CAP):
                    over_all["tensor"](pe)
                with pe.Else():
                    in_slots["tensor"](pe)

            @block.scalar
            def _(act):
                with act.If(K.fullest(act, count) > CAP):
                    over_all["scalar"](act)
                with act.Else():
                    in_slots["scalar"](act)

            @block.vector
            def _(dve):
                with dve.If(K.fullest(dve, count) > CAP):
                    over_all["vector"](dve)
                with dve.Else():
                    in_slots["vector"](dve)

            @block.gpsimd
            def _(pool):
                with pool.If(K.fullest(pool, count) <= CAP):
                    in_slots["gpsimd"](pool)


def route(K, layer, ctx, gate, count, xg, spread, load_expert):
    nc, I = K.nc, K.ins
    nr = N_GROUPS + N_EXP
    SG = N_EXP * CAP // P
    def sb(name, shape):
        return ctx.enter_context(nc.sbuf_tensor(f"{name}_{layer}", shape, F32))
    wr = sb("wr", [P, KT, nr])
    bias = sb("rbias", [P, nr])
    lg = sb("lg", [P, 3, nr])
    small = sb("small", [P, 3, 64])
    mask, pos = sb("mask", [P, 3, N_EXP]), sb("pos", [P, 3, N_EXP])
    xt = sb("xt", [P, 3, D])
    sel = sb("sel", [P, 3, N_EXP * CAP])
    given, logits, routed = K.sig("rows_given"), K.sig("logits"), K.sig("routed")
    ex, exd = K.sig("exp_asked"), K.sig("exp_done")
    x_turned, x_taken, placed = K.sig("t_made"), K.sig("t_taken"), K.sig("placed")
    chosen, sel_made, made, taken_v, taken_s = (K.sig(n) for n in ("chosen", "sel_made", "tile_made", "taken_v", "taken_s"))
    s_turned, gated = K.sig("s_turned"), K.sig("gated")
    with nc.Block() as block:
        @block.sync
        def _(sp):
            with nc.allow_non_contiguous_dma(reason="router columns are narrow"):
                sp.dma_start(wr[:, :, 0:N_GROUPS], I["router_g"][layer].rearrange("(k p) n -> p k n", p=P)).then_inc(*given.dma())
                sp.dma_start(wr[:, :, N_GROUPS:], I["router_e"][layer].rearrange("(k p) n -> p k n", p=P)).then_inc(*given.dma())
                sp.dma_start(bias[:, 0:N_GROUPS], I["router_g_bias"][layer:layer + 1].to_broadcast([P, N_GROUPS])).then_inc(*given.dma())
                sp.dma_start(bias[:, N_GROUPS:], I["router_e_bias"][layer:layer + 1].to_broadcast([P, N_EXP])).then_inc(*given.dma())
            for j in range(4):
                load_expert(sp, j, j)

        @block.tensor
        def _(pe):
            for n in range(6):
                i, half = divmod(n, 2)
                t0, tn = Q_TILES_1[i]
                for k in range(4):
                    mm = nc.tensor.transpose(K.ps[0:tn, n, k * P:(k + 1) * P], K.xn[:, 4 * half + k, t0:t0 + tn], K.con(C_ID))
                mm.then_inc(*x_turned.one())
            pe.wait_ge(*given.at(64))
            for i, (t0, tn) in enumerate(Q_TILES_1):
                for k in range(KT):
                    mm = nc.tensor.matmul(K.ps[0:tn, 6, i * nr:(i + 1) * nr], K.xn[:, k, t0:t0 + tn], wr[:, k], start=k == 0, stop=k == KT - 1)
            mm.then_inc(*logits.one())
            pe.wait_ge(*chosen.at(1))
            for i, (t0, tn) in enumerate(Q_TILES_1):
                for j in range(i + 1):
                    kn_ = Q_TILES_1[j][1]
                    before = K.cst[0:kn_, C_TRI1:C_TRI1 + tn] if j == i else K.cst[0:kn_, C_ONE:C_ONE + tn]
                    nc.tensor.matmul(K.ps[0:tn, 7, i * N_EXP:(i + 1) * N_EXP], before, mask[0:kn_, j], start=j == 0, stop=j == i)
            for j, (t0, kn_) in enumerate(Q_TILES_1):
                mm = nc.tensor.matmul(K.ps[0:1, 7, 3 * N_EXP:4 * N_EXP], K.cst[0:kn_, C_ONE:C_ONE + 1], mask[0:kn_, j], start=j == 0, stop=j == 2)
            mm.then_inc(*placed.one())
            pe.wait_ge(*x_taken.at(2))
            pe.wait_ge(*sel_made.at(1))
            for n in range(2 * KT):
                k, half = divmod(n, 2)
                if n >= 8:
                    pe.wait_ge(*(taken_v, taken_s)[n % 2].at((n - 8) // 2 + 1))
                for i, (t0, tn) in enumerate(Q_TILES_1):
                    mm = nc.tensor.matmul(K.ps[:, n % 8, :], xt[0:tn, i, k * P:(k + 1) * P], sel[0:tn, i, half * 512:(half + 1) * 512],
                                          start=i == 0, stop=i == 2)
                mm.then_inc(*made.one())
            pe.wait_ge(*gated.at(1))
            for s in range(SG):
                if s % 2 == 0:
                    pe.wait_ge(*taken_v.at(4 + s // 2 + 1))
                else:
                    pe.wait_ge(*taken_s.at(4 + s // 2 + 1))
                for i, (t0, tn) in enumerate(Q_TILES_1):
                    mm = nc.tensor.transpose(K.ps[:, s, t0:t0 + tn], sel[0:tn, i, s * P:(s + 1) * P], K.cst[0:tn, C_ID:C_ID + tn])
                mm.then_inc(*s_turned.one())

        @block.scalar
        def _(act):
            for i in range(3):
                act.wait_ge(*x_turned.at(2 * i + 2))
                tn = Q_TILES_1[i][1]
                last = nc.scalar.copy(xt[0:tn, i, 512:], K.ps[0:tn, 2 * i + 1])
            last.then_inc(*x_taken.one())
            act.wait_ge(*ex.at(1))
            nc.scalar.activation(small[:, :, 4:8], small[:, :, 0:4], ACT.Exp).then_inc(*exd.one())
            act.wait_ge(*ex.at(2))
            nc.scalar.activation(small[:, :, 57:58], small[:, :, 56:57], ACT.Exp).then_inc(*exd.one())
            for k in range(KT):
                act.wait_ge(*made.at(2 * k + 2))
                nc.scalar.copy(xg[:, k, 512:], K.ps[:, (2 * k + 1) % 8]).then_inc(*taken_s.one())
            for s in range(1, SG, 2):
                act.wait_ge(*s_turned.at(s + 1))
                nc.scalar.copy(spread[:, s], K.ps[:, s, 0:L1])

        @block.vector
        def _(dve):
            def do(ins):
                link(dve, K.dve_step, ins)
            v = nc.vector
            S = lambda a, b: small[:, :, a:b]
            v.memset(mask[:], 0.0)
            do(v.memset(lg[:], 0.0))
            for i in range(3):
                dve.wait_ge(*x_turned.at(2 * i + 1))
                tn = Q_TILES_1[i][1]
                last = v.tensor_copy(xt[0:tn, i, 0:512], K.ps[0:tn, 2 * i])
            last.then_inc(*x_taken.one())
            dve.wait_ge(*given.at(64))
            dve.wait_ge(*logits.at(1))
            for i, (t0, tn) in enumerate(Q_TILES_1):
                last = v.tensor_tensor(lg[0:tn, i], K.ps[0:tn, 6, i * nr:(i + 1) * nr], bias[0:tn], ALU.add)
            do(last)
            G = lg[:, :, 0:N_GROUPS]
            do(v.reduce_max(S(8, 9), G, AX))
            v.tensor_tensor(S(0, 4), G, S(8, 9).to_broadcast([P, 3, 4]), ALU.subtract).then_inc(*ex.one())
            do(v.tensor_tensor(S(12, 16), G, S(8, 9).to_broadcast([P, 3, 4]), ALU.is_equal))
            first_of(dve, K, S(12, 16), S(16, 20), S(9, 10))
            for g in range(N_GROUPS):
                E = lg[:, :, N_GROUPS + g * PER_GROUP:N_GROUPS + (g + 1) * PER_GROUP]
                m = S(12 + g, 13 + g).to_broadcast([P, 3, PER_GROUP])
                if g == 0:
                    do(v.tensor_tensor(S(24, 32), E, m, ALU.mult))
                else:
                    do(v.tensor_tensor(S(32, 40), E, m, ALU.mult))
                    do(v.tensor_tensor(S(24, 32), S(24, 32), S(32, 40), ALU.add))
            do(v.reduce_max(S(10, 11), S(24, 32), AX))
            do(v.tensor_tensor(S(40, 48), S(24, 32), S(10, 11).to_broadcast([P, 3, 8]), ALU.is_equal))
            first_of(dve, K, S(40, 48), S(32, 40), S(9, 10))
            do(v.scalar_tensor_tensor(out=S(24, 32), in0=S(40, 48), scalar=NEG, in1=S(24, 32), op0=ALU.mult, op1=ALU.add))
            do(v.reduce_max(S(11, 12), S(24, 32), AX))
            v.tensor_tensor(S(56, 57), S(11, 12), S(10, 11), ALU.subtract).then_inc(*ex.one())
            do(v.tensor_tensor(S(48, 56), S(24, 32), S(11, 12).to_broadcast([P, 3, 8]), ALU.is_equal))
            first_of(dve, K, S(48, 56), S(32, 40), S(9, 10))
            do(v.tensor_tensor(S(24, 32), S(40, 48), S(48, 56), ALU.add))
            for g in range(N_GROUPS):
                for i, (t0, tn) in enumerate(Q_TILES_1):
                    last = v.tensor_tensor(mask[0:tn, i, g * PER_GROUP:(g + 1) * PER_GROUP], small[0:tn, i, 24:32],
                                           small[0:tn, i, 12 + g:13 + g].to_broadcast([tn, PER_GROUP]), ALU.mult)
            last.then_inc(*chosen.one())
            dve.wait_ge(*exd.at(2))
            do(v.reduce_sum(S(58, 59), S(4, 8), AX))
            do(v.tensor_scalar(S(59, 60), S(57, 58), 1.0, None, ALU.add))
            do(v.tensor_tensor(S(60, 61), S(58, 59), S(59, 60), ALU.mult))
            do(v.reciprocal(S(61, 62), S(60, 61)))
            do(v.tensor_tensor(S(62, 63), S(61, 62), S(57, 58), ALU.mult))
            do(v.tensor_tensor(S(32, 40), S(40, 48), S(61, 62).to_broadcast([P, 3, 8]), ALU.mult))
            do(v.tensor_tensor(S(24, 32), S(48, 56), S(62, 63).to_broadcast([P, 3, 8]), ALU.mult))
            do(v.tensor_tensor(S(32, 40), S(32, 40), S(24, 32), ALU.add))
            for g in range(N_GROUPS):
                last = v.tensor_tensor(gate[:, :, g * PER_GROUP:(g + 1) * PER_GROUP], S(32, 40),
                                       S(12 + g, 13 + g).to_broadcast([P, 3, PER_GROUP]), ALU.mult)
            do(last)
            dve.wait_ge(*placed.at(1))
            do(v.reduce_max(small[0:1, 0, 63:64], K.ps[0:1, 7, 3 * N_EXP:4 * N_EXP], AX))
            v.tensor_copy(count[:], small[0:1, 0, 63:64])
            for i, (t0, tn) in enumerate(Q_TILES_1):
                do(v.scalar_tensor_tensor(out=pos[0:tn, i], in0=K.ps[0:tn, 7, i * N_EXP:(i + 1) * N_EXP], scalar=1.0, in1=mask[0:tn, i],
                                          op0=ALU.add, op1=ALU.mult))
                do(v.tensor_scalar(pos[0:tn, i], pos[0:tn, i], -1.0, None, ALU.add))
            slots = lambda ap: ap.rearrange("p (e c) -> p e c", c=CAP)
            for i, (t0, tn) in enumerate(Q_TILES_1):
                iota = K.cst[0:tn, C_SLOT:C_SLOT + CAP].rearrange("p (a c) -> p a c", a=1).to_broadcast([tn, N_EXP, CAP])
                last = v.tensor_tensor(slots(sel[0:tn, i]), iota, pos[0:tn, i].rearrange("p (e a) -> p e a", a=1).to_broadcast([tn, N_EXP, CAP]),
                                       ALU.is_equal)
            last.then_inc(*sel_made.one())
            for k in range(KT):
                dve.wait_ge(*made.at(2 * k + 1))
                v.tensor_copy(xg[:, k, 0:512], K.ps[:, (2 * k) % 8]).then_inc(*taken_v.one())
            dve.wait_ge(*made.at(2 * KT))
            for i, (t0, tn) in enumerate(Q_TILES_1):
                last = v.tensor_tensor(slots(sel[0:tn, i]), slots(sel[0:tn, i]),
                                       gate[0:tn, i].rearrange("p (e a) -> p e a", a=1).to_broadcast([tn, N_EXP, CAP]), ALU.mult)
            last.then_inc(*gated.one())
            for s in range(0, SG, 2):
                dve.wait_ge(*s_turned.at(s + 1))
                v.tensor_copy(spread[:, s], K.ps[:, s, 0:L1])


def experts_in_slots(K, layer, ctx, xg, spread, wgu, wd, w_in, load_expert):
    nc = K.nc
    ET = D_EXP // P
    turns = N_EXP // 4
    def sb(name, shape):
        return ctx.enter_context(nc.sbuf_tensor(f"{name}_{layer}", shape, F32))
    xe = sb("slot_x", [P, 2, KT, CAP])
    sil, hid = sb("slot_sil", [CAP, 2, D_EXP]), sb("slot_hid", [CAP, 2, D_EXP])
    hidT = sb("slot_hidT", [P, 2, ET, CAP])
    yt = sb("slot_y", [P, D])
    s = lambda name: K.sig(f"slot_{name}_{layer}")
    x_ready, gu_made, silu_made, hid_made, hid_turned, hidT_made = s("x_ready"), s("gu"), s("silu"), s("hid"), s("turn"), s("hidT")
    y_made, y_taken, back, added = s("y"), s("y_out"), s("back"), s("added")
    def sync(sp):
        with sp.Fori(1, turns) as i:
            for j in range(4):
                sp.wait_ge(y_made.sem, 4 * i + j - 3)
                load_expert(sp, 4 * i + j, j)

    def tensor(pe):
        def gate_up(j, k):
            return nc.tensor.matmul(K.ps[0:CAP, j % 2, :].rearrange("p (a n) -> p a n", a=2), xe[:, j % 2, k], wgu[j % 4][:, :, k],
                                    start=k == 0, stop=k == KT - 1)

        def expert(i, j, first=False, last=False):
            nj = (j + 1) % 4
            if not last:
                pe.wait_ge(w_in[nj].sem, 48 * (i + (j + 1) // 4) + 48)
                pe.wait_ge(x_ready.sem, 4 * i + j + 2)
                for k in range(KT // 2):
                    gate_up(nj, k)
            pe.wait_ge(hid_made.sem, 4 * i + j + 1)
            for m in range(ET):
                mm = nc.tensor.matmul(K.ps[:, 2 + j % 2, m * CAP:(m + 1) * CAP], hid[:, j % 2, m * P:(m + 1) * P],
                                      K.cst[0:CAP, C_ID:C_ID + CAP], start=True, stop=True)
            mm.then_inc(hid_turned.sem, 1)
            if not last:
                for k in range(KT // 2, KT):
                    mm = gate_up(nj, k)
                mm.then_inc(gu_made.sem, 1)
            pe.wait_ge(hidT_made.sem, 4 * i + j + 1)
            if not first:
                pe.wait_ge(y_taken.sem, 4 * i + j - 3)
            for half in range(2):
                for k in range(ET):
                    mm = nc.tensor.matmul(K.ps[j * CAP:(j + 1) * CAP, 4 + half, :], hidT[:, j % 2, k], wd[:, j, k, half * 512:(half + 1) * 512],
                                          start=k == 0, stop=k == ET - 1, tile_position=(0, j * CAP))
            mm.then_inc(y_made.sem, 1)

        def by_token(i, first=False):
            pe.wait_ge(y_taken.sem, 4 * i + 4)
            for m in range(KT):
                if not (first and m < 2):
                    pe.wait_ge(added.sem, KT * i + m - 1)
                nc.tensor.matmul(K.ps[:, 6 + m % 2, 0:L1], yt[:, m * P:(m + 1) * P], spread[:, bass.ds(i, 1)],
                                 start=True, stop=True).then_inc(back.sem, 1)
        pe.wait_ge(w_in[0].sem, 48)
        pe.wait_ge(x_ready.sem, 1)
        for k in range(KT):
            mm = gate_up(0, k)
        mm.then_inc(gu_made.sem, 1)
        for j in range(4):
            expert(0, j, first=True)
        expert(1, 0)
        by_token(0, first=True)
        for j in range(1, 4):
            expert(1, j)
        with pe.Fori(2, turns - 1) as i:
            expert(i, 0)
            by_token(i - 1)
            for j in range(1, 4):
                expert(i, j)
        expert(turns - 1, 0)
        by_token(turns - 2)
        for j in range(1, 4):
            expert(turns - 1, j, last=j == 3)
        by_token(turns - 1)

    def scalar(act):
        def silu(i, j):
            act.wait_ge(gu_made.sem, 4 * i + j + 1)
            nc.scalar.activation(sil[:, j % 2], K.ps[0:CAP, j % 2, 0:D_EXP], ACT.Silu).then_inc(silu_made.sem, 1)

        def output(i, j):
            act.wait_ge(y_made.sem, 4 * i + j + 1)
            nc.scalar.copy(yt[j * CAP:(j + 1) * CAP].rearrange("p (a n) -> p a n", a=2), K.ps[j * CAP:(j + 1) * CAP, 4:6, :]).then_inc(y_taken.sem, 1)

        def turn(i, last=False):
            for j in range(4):
                if not (last and j == 3):
                    silu(i, j + 1)
                if j == 0 and not (isinstance(i, int) and i == 0):
                    act.wait_ge(back.sem, KT * i)
                output(i, j)
        silu(0, 0)
        turn(0)
        with act.Fori(1, turns - 1) as i:
            turn(i)
        turn(turns - 1, True)

    def vector(dve):
        def hidden(i, j):
            dve.wait_ge(silu_made.sem, 4 * i + j + 1)
            nc.vector.tensor_tensor(hid[:, j % 2], sil[:, j % 2], K.ps[0:CAP, j % 2, D_EXP:2 * D_EXP], ALU.mult).then_inc(hid_made.sem, 1)

        def turned(i, j):
            dve.wait_ge(hid_turned.sem, 4 * i + j + 1)
            nc.vector.tensor_copy(hidT[:, j % 2], K.ps[:, 2 + j % 2, 0:ET * CAP].rearrange("p (m c) -> p m c", m=ET)).then_inc(hidT_made.sem, 1)

        def add(i):
            for m in range(KT):
                dve.wait_ge(back.sem, KT * i + m + 1)
                nc.vector.tensor_tensor(K.h[:, m], K.h[:, m], K.ps[:, 6 + m % 2, 0:L1], ALU.add).then_inc(added.sem, 1)

        def turn(i, first=False, last=False):
            for j in range(4):
                turned(i, j)
                if not (last and j == 3):
                    hidden(i, j + 1)
                if j == 0 and not first:
                    add(i - 1)
        hidden(0, 0)
        turn(0, first=True)
        with dve.Fori(1, turns - 1) as i:
            turn(i)
        turn(turns - 1, last=True)
        add(turns - 1)

    def gpsimd(pool):
        def tokens(e, j):
            nc.gpsimd.tensor_copy(xe[:, j % 2], xg[:, :, bass.ds(e * CAP, CAP)]).then_inc(x_ready.sem, 1)
        tokens(0, 0)
        tokens(1, 1)
        pool.wait_ge(gu_made.sem, 1)
        tokens(2, 0)
        pool.wait_ge(gu_made.sem, 2)
        tokens(3, 1)
        with pool.Fori(1, turns) as i:
            for j in range(4):
                pool.wait_ge(gu_made.sem, 4 * i + j - 1)
                tokens(4 * i + j, j)
    return {"sync": sync, "tensor": tensor, "scalar": scalar, "vector": vector, "gpsimd": gpsimd}


def experts_over_all(K, layer, ctx, gates_dram, gate, wgu, wd, w_in):
    nc, I = K.nc, K.ins
    ET = D_EXP // P
    def sb(name, shape):
        return ctx.enter_context(nc.sbuf_tensor(f"{name}_{layer}", shape, F32))
    gT = sb("gT", [N_EXP, L1])
    gb = sb("gb", [P, 2, L1])
    sil = sb("sil", [P, 2, ET, L1])
    hid = sb("hid", [P, 2, ET, L1])
    sg = lambda name: K.sig(f"all_{name}_{layer}")
    turned, copied, saved = sg("turned"), sg("copied"), sg("saved")
    gu_in, d_in = [sg("gu_in_0"), sg("gu_in_1")], [sg("d_in_0"), sg("d_in_1")]
    gu_made, hid_made, d_made, d_taken = sg("gu_made"), sg("hid_made"), sg("d_made"), sg("d_taken")
    silu_made, gated = sg("silu_made"), sg("gated")
    wg_v = I["w_gate"][layer].rearrange("e (k p) n -> p e k n", p=P)
    wu_v = I["w_up"][layer].rearrange("e (k p) n -> p e k n", p=P)
    wd_v = I["w_down"][layer].rearrange("e (k p) n -> p e k n", p=P)

    def sync(sp):
        def load(e, s, first=False):
            if not first:
                sp.wait_ge(gu_made.sem, ET * (e - 1))
                sp.wait_ge(hid_made.sem, ET * (e - 1))
            one = bass.ds(e, 1)
            sp.dma_start(wgu[s][:, 0], wg_v[:, one]).then_inc(gu_in[s].sem, 16)
            sp.dma_start(wgu[s][:, 1], wu_v[:, one]).then_inc(gu_in[s].sem, 16)
            sp.dma_start(gb[:, s], gates_dram[one].to_broadcast([P, L1])).then_inc(gu_in[s].sem, 16)
            if not first:
                sp.wait_ge(d_made.sem, KT * (e - 1))
            sp.dma_start(wd[:, s], wd_v[:, one]).then_inc(d_in[s].sem, 16)
        for j in range(4):
            sp.wait_ge(w_in[j].sem, 48)
        sp.wait_ge(copied.sem, 1)
        sp.dma_start(gates_dram, gT[:]).then_inc(saved.sem, 16)
        sp.wait_ge(saved.sem, 16)
        load(0, 0, True)
        load(1, 1, True)
        with sp.Fori(1, N_EXP // 2) as i:
            load(2 * i, 0)
            load(2 * i + 1, 1)

    def tensor(pe):
        for i, (t0, tn) in enumerate(Q_TILES_1):
            mm = nc.tensor.transpose(K.ps[0:N_EXP, 7, t0:t0 + tn], gate[0:tn, i], K.cst[0:tn, C_ID:C_ID + tn])
        mm.then_inc(turned.sem, 1)
        pe.wait_ge(copied.sem, 1)

        def expert(e, s, i, first=False):
            pe.wait_ge(gu_in[s].sem, 48 * i + 48)
            for m in range(ET):
                if not first:
                    pe.wait_ge(hid_made.sem, ET * (e - 1) + m + 1)
                for j in range(2):
                    for k in range(KT):
                        mm = nc.tensor.matmul(K.ps[:, 2 * j + m, 0:L1], wgu[s][:, j, k, m * P:(m + 1) * P], K.xn[:, k],
                                              start=k == 0, stop=k == KT - 1)
                mm.then_inc(gu_made.sem, 1)
            pe.wait_ge(d_in[s].sem, 16 * i + 16)
            pe.wait_ge(hid_made.sem, ET * e + ET)
            for m in range(KT):
                if not (first and m < 4):
                    pe.wait_ge(d_taken.sem, KT * e + m - 3)
                for k in range(ET):
                    mm = nc.tensor.matmul(K.ps[:, 4 + m % 4, 0:L1], wd[:, s, k, m * P:(m + 1) * P], hid[:, s, k],
                                          start=k == 0, stop=k == ET - 1)
                mm.then_inc(d_made.sem, 1)
        expert(0, 0, 0, True)
        expert(1, 1, 0)
        with pe.Fori(1, N_EXP // 2) as i:
            expert(2 * i, 0, i)
            expert(2 * i + 1, 1, i)

    def scalar(act):
        with act.Fori(0, N_EXP // 2) as i:
            for s in range(2):
                for m in range(ET):
                    act.wait_ge(gu_made.sem, ET * (2 * i + s) + m + 1)
                    nc.scalar.activation(sil[:, s, m], K.ps[:, m, 0:L1], ACT.Silu).then_inc(silu_made.sem, 1)

    def vector(dve):
        dve.wait_ge(turned.sem, 1)
        nc.vector.tensor_copy(gT[:], K.ps[0:N_EXP, 7, 0:L1]).then_inc(copied.sem, 1)
        with dve.Fori(0, N_EXP // 2) as i:
            for s in range(2):
                e = 2 * i + s
                dve.wait_ge(gu_in[s].sem, 48 * i + 48)
                for m in range(ET):
                    dve.wait_ge(silu_made.sem, ET * e + m + 1)
                    nc.vector.tensor_tensor(sil[:, s, m], sil[:, s, m], gb[:, s], ALU.mult).then_inc(gated.sem, 1)
                    dve.wait_ge(gated.sem, ET * e + m + 1)
                    nc.vector.tensor_tensor(hid[:, s, m], sil[:, s, m], K.ps[:, 2 + m, 0:L1], ALU.mult).then_inc(hid_made.sem, 1)
                for m in range(KT):
                    dve.wait_ge(d_made.sem, KT * e + m + 1)
                    nc.vector.tensor_tensor(K.h[:, m], K.h[:, m], K.ps[:, 4 + m % 4, 0:L1], ALU.add).then_inc(d_taken.sem, 1)
    return {"sync": sync, "tensor": tensor, "scalar": scalar, "vector": vector}


def store_tokens(K, out):
    nc = K.nc
    with ExitStack() as ctx:
        tok = ctx.enter_context(nc.sbuf_tensor("tok_out", [P, 2, D], F32))
        made, stored, saved = K.sig("tile_made"), K.sig("tile_stored"), K.sig("out_saved")
        block = ctx.enter_context(nc.Block())

        @block.tensor
        def _(pe):
            for n in range(4):
                for k in range(4):
                    mm = nc.tensor.transpose(K.ps[:, n, k * P:(k + 1) * P], K.h[:, 4 * (n % 2) + k, (n // 2) * P:(n // 2 + 1) * P],
                                             K.con(C_ID))
                mm.then_inc(*made.one())

        @block.vector
        def _(dve):
            for n in range(4):
                dve.wait_ge(*made.at(n + 1))
                nc.vector.tensor_copy(tok[:, n // 2, 512 * (n % 2):512 * (n % 2) + 512], K.ps[:, n]).then_inc(*stored.one())

        @block.sync
        def _(sp):
            for i in range(2):
                sp.wait_ge(*stored.at(2 * i + 2))
                sp.dma_start(out[0, i * P:(i + 1) * P], tok[:, i]).then_inc(*saved.dma())
            sp.wait_ge(*saved.now())


def rope(K, x, out, rows, T):
    nc = K.nc
    n = len(x)
    with ExitStack() as ctx:
        made, taken = K.sig("tile_made"), K.sig("tile_stored")
        block = ctx.enter_context(nc.Block())

        @block.tensor
        def _(pe):
            for i in range(n):
                if i >= 8:
                    pe.wait_ge(*taken.at(i - 7))
                nc.tensor.matmul(K.ps[0:rows, i % 8, 0:T], K.cst[0:rows, C_ROT:C_ROT + rows], x[i], start=True, stop=True).then_inc(*made.one())

        @block.vector
        def _(dve):
            for i in range(n):
                dve.wait_ge(*made.at(i + 1))
                rot = K.rs[0:rows, i % 2, 0:T]
                nc.vector.tensor_tensor(rot, K.ps[0:rows, i % 8, 0:T], K.cst[0:rows, C_SIN:C_SIN + T], ALU.mult).then_inc(*taken.one())
                link(dve, K.dve_step, nc.vector.tensor_tensor(out[i], x[i], K.cst[0:rows, C_COS:C_COS + T], ALU.mult))
                link(dve, K.dve_step, nc.vector.tensor_tensor(out[i], out[i], rot, ALU.add))


def latent_kv(K, ctx):
    nc, I = K.nc, K.ins
    kn = ctx.enter_context(nc.sbuf_tensor("mla_kn", [P, HEADS, L1], F32))
    kr = ctx.enter_context(nc.sbuf_tensor("mla_kr", [ROPE, L1], F32))
    v = ctx.enter_context(nc.sbuf_tensor("mla_v", [P, 3, HEADS * V_DIM], F32))
    rms_norm(K, K.h[:], K.xn, K.col("kv_norm", 0, KT))
    with ExitStack() as inner:
        c = inner.enter_context(nc.sbuf_tensor("lat_c", [P, 3, L1], F32))
        cn = inner.enter_context(nc.sbuf_tensor("lat_cn", [P, 2, L1], F32))
        feature_linear(K, I["w_dkv"], lambda k: K.xn[:, k], L1,
                       lambda m, ps: nc.vector.tensor_copy(c[0:ps.shape[0], m], ps))
        rms_norm(K, c[:, 0:2], cn, K.col("kv_lat_norm", 0, 2))
        rope(K, [c[0:ROPE, 2]], [kr[:]], ROPE, L1)
        feature_linear(K, I["w_uk"].rearrange("r h d -> r (h d)"), lambda k: cn[:, k], L1,
                       lambda m, ps: nc.vector.tensor_copy(kn[:, m], ps))
        token_linear(K, I["w_uv"].rearrange("r h d -> r (h d)"), lambda k, t0, tn: cn[:, k, t0:t0 + tn], 2, Q_TILES_1,
                     lambda i, at, n, ps: nc.scalar.copy(v[0:ps.shape[0], i, at:at + n], ps), by="scalar")
    return kn, kr, v


def mla(K, kv):
    nc, I = K.nc, K.ins
    kn, kr, v = kv
    rms_norm(K, K.h[:], K.xn, K.col("b_norm", 0, KT))
    with ExitStack() as ctx:
        def sb(name, shape):
            return ctx.enter_context(nc.sbuf_tensor(name, shape, F32))
        qn, qr = sb("mla_qn", [P, HEADS, L1]), sb("mla_qr", [ROPE, HEADS, L1])
        with ExitStack() as inner:
            cq = inner.enter_context(nc.sbuf_tensor("cq", [P, 3, L1], F32))
            cqn = inner.enter_context(nc.sbuf_tensor("cqn", [P, 3, L1], F32))
            feature_linear(K, I["b_w_dq"][0], lambda k: K.xn[:, k], L1,
                           lambda m, ps: nc.vector.tensor_copy(cq[:, m], ps))
            rms_norm(K, cq[:], cqn, K.col("b_q_norm", 0, 3))
            latent_queries(K, cqn, qn, qr)
        rope(K, [qr[:, h] for h in range(HEADS)], [K.xn[0:ROPE, h] for h in range(HEADS)], ROPE, L1)
        oT = sb("mla_oT", [P, HEADS, L1])
        mla_attention(K, qn, K.xn, kn, kr, v, oT)
        feature_linear(K, I["b_w_o"][0], lambda k: oT[:, k], L1,
                       lambda m, ps: nc.vector.tensor_tensor(K.h[:, m], K.h[:, m], ps, ALU.add))


def latent_queries(K, cqn, qn, qr):
    nc, I = K.nc, K.ins
    kq = Q_LORA // P
    w = NOPE + ROPE
    with ExitStack() as ctx:
        wq = ctx.enter_context(nc.sbuf_tensor("wq", [P, kq, HEADS * w], F32))
        given, made, taken = K.sig("rows_given"), K.sig("tile_made"), K.sig("tile_stored")
        block = ctx.enter_context(nc.Block())

        @block.sync
        def _(sp):
            sp.dma_start(wq[:], I["b_w_uq"][0].rearrange("(k p) h d -> p k (h d)", p=P)).then_inc(*given.dma())

        @block.tensor
        def _(pe):
            pe.wait_ge(*given.at(16))
            for n in range(2 * HEADS):
                h, r = divmod(n, 2)
                if n >= 8:
                    pe.wait_ge(*taken.at(n - 7))
                at, mw = h * w + NOPE * r, (NOPE, ROPE)[r]
                for k in range(kq):
                    mm = nc.tensor.matmul(K.ps[0:mw, n % 8, 0:L1], wq[:, k, at:at + mw], cqn[:, k], start=k == 0, stop=k == kq - 1)
                mm.then_inc(*made.one())

        @block.vector
        def _(dve):
            for n in range(2 * HEADS):
                h, r = divmod(n, 2)
                dve.wait_ge(*made.at(n + 1))
                nc.vector.tensor_copy((qn, qr)[r][:, h], K.ps[0:(NOPE, ROPE)[r], n % 8, 0:L1]).then_inc(*taken.one())


def mla_attention(K, qn, qr, kn, kr, v, oT):
    nc = K.nc
    units = [(h, i) for h in range(HEADS) for i in range(3)]
    n = len(units)
    keys = [t0 + tn for t0, tn in Q_TILES_1]
    with ExitStack() as ctx:
        def sb(name, shape):
            return ctx.enter_context(nc.sbuf_tensor(name, shape, F32))
        S, Pr, PT = sb("att_s", [P, 3, L1]), sb("att_p", [P, 3, L1]), sb("att_pt", [P, 2, 3, P])
        st = sb("att_stat", [P, 3, 4])
        s_made, s_ready, e_made, p_ready = K.sig("s_made"), K.sig("s_ready"), K.sig("e_made"), K.sig("p_ready")
        t_made, t_taken, pv_made, o_taken = K.sig("t_made"), K.sig("t_taken"), K.sig("pv_made"), K.sig("o_taken")
        block = ctx.enter_context(nc.Block())

        @block.tensor
        def _(pe):
            for u in range(n + 2):
                if u < n:
                    h, i = units[u]
                    t0, tn = Q_TILES_1[i]
                    if u >= 3:
                        pe.wait_ge(*s_ready.at(u - 2))
                    nc.tensor.matmul(K.ps[0:tn, u % 3, 0:keys[i]], qn[:, h, t0:t0 + tn], kn[:, h, 0:keys[i]], start=True, stop=False)
                    nc.tensor.matmul(K.ps[0:tn, u % 3, 0:keys[i]], qr[0:ROPE, h, t0:t0 + tn], kr[0:ROPE, 0:keys[i]],
                                     start=False, stop=True).then_inc(*s_made.one())
                if 1 <= u <= n:
                    w = u - 1
                    i = units[w][1]
                    tn = Q_TILES_1[i][1]
                    pe.wait_ge(*p_ready.at(w + 1))
                    if w >= 2:
                        pe.wait_ge(*t_taken.at(w - 1))
                    for j in range(i + 1):
                        k0, kn_ = Q_TILES_1[j]
                        mm = nc.tensor.transpose(K.ps[0:kn_, 3 + w % 2, j * P:j * P + tn], Pr[0:tn, w % 3, k0:k0 + kn_],
                                                 K.cst[0:tn, C_ID:C_ID + tn])
                    mm.then_inc(*t_made.one())
                if u >= 2:
                    w = u - 2
                    h, i = units[w]
                    t0, tn = Q_TILES_1[i]
                    pe.wait_ge(*t_taken.at(w + 1))
                    if i == 0 and h >= 2:
                        pe.wait_ge(*o_taken.at(h - 1))
                    for j in range(i + 1):
                        kn_ = Q_TILES_1[j][1]
                        mm = nc.tensor.matmul(K.ps[:, 5 + h % 2, t0:t0 + tn], v[0:kn_, j, h * V_DIM:(h + 1) * V_DIM],
                                              PT[0:kn_, w % 2, j, 0:tn], start=j == 0, stop=j == i)
                    mm.then_inc(*pv_made.one())

        @block.vector
        def _(dve):
            for u in range(n + 4):
                if u < n:
                    h, i = units[u]
                    t0, tn = Q_TILES_1[i]
                    dve.wait_ge(*s_made.at(u + 1))
                    if u >= 3:
                        dve.wait_ge(*e_made.at(u - 2))
                    if i:
                        nc.vector.tensor_scalar(S[0:tn, u % 3, 0:t0], K.ps[0:tn, u % 3, 0:t0], MLA_SCALE, None, ALU.mult)
                    link(dve, K.dve_step, nc.vector.scalar_tensor_tensor(
                        out=S[0:tn, u % 3, t0:t0 + tn], in0=K.ps[0:tn, u % 3, t0:t0 + tn], scalar=MLA_SCALE,
                        in1=K.cst[0:tn, C_CAUSAL:C_CAUSAL + tn], op0=ALU.mult, op1=ALU.add))
                    link(dve, K.dve_step, nc.vector.reduce_max(st[0:tn, u % 3, 3:4], S[0:tn, u % 3, 0:keys[i]], AX))
                    nc.vector.tensor_scalar(st[0:tn, u % 3, 0:1], st[0:tn, u % 3, 3:4], -1.0, None, ALU.mult).then_inc(*s_ready.one())
                if 1 <= u <= n:
                    w = u - 1
                    i = units[w][1]
                    tn = Q_TILES_1[i][1]
                    dve.wait_ge(*e_made.at(w + 1))
                    link(dve, K.dve_step, nc.vector.reciprocal(st[0:tn, w % 3, 2:3], st[0:tn, w % 3, 1:2]))
                    nc.vector.tensor_scalar(Pr[0:tn, w % 3, 0:keys[i]], Pr[0:tn, w % 3, 0:keys[i]], st[0:tn, w % 3, 2:3],
                                            None, ALU.mult).then_inc(*p_ready.one())
                if u >= 4 and units[u - 4][1] == 2:
                    h = units[u - 4][0]
                    dve.wait_ge(*pv_made.at(u - 3))
                    nc.vector.tensor_copy(oT[:, h], K.ps[:, 5 + h % 2, 0:L1]).then_inc(*o_taken.one())

        @block.scalar
        def _(act):
            for u in range(n + 1):
                if u < n:
                    i = units[u][1]
                    tn = Q_TILES_1[i][1]
                    act.wait_ge(*s_ready.at(u + 1))
                    if u >= 3:
                        act.wait_ge(*t_made.at(u - 2))
                    nc.scalar.activation(Pr[0:tn, u % 3, 0:keys[i]], S[0:tn, u % 3, 0:keys[i]], ACT.Exp, bias=st[0:tn, u % 3, 0:1],
                                         accum_out=st[0:tn, u % 3, 1:2]).then_inc(*e_made.one())
                if u >= 1:
                    w = u - 1
                    i = units[w][1]
                    tn = Q_TILES_1[i][1]
                    act.wait_ge(*t_made.at(w + 1))
                    if w >= 2:
                        act.wait_ge(*pv_made.at(w - 1))
                    full = min(i + 1, 2)
                    view = K.ps[:, 3 + w % 2, :].rearrange("p (j t) -> p j t", j=4)
                    last = nc.scalar.copy(PT[:, w % 2, 0:full, 0:tn], view[:, 0:full, 0:tn])
                    if i == 2:
                        kn_ = Q_TILES_1[2][1]
                        last = nc.scalar.copy(PT[0:kn_, w % 2, 2, 0:tn], K.ps[0:kn_, 3 + w % 2, 2 * P:2 * P + tn])
                    last.then_inc(*t_taken.one())


def final_norm(K):
    nc = K.nc
    rms_norm(K, K.h[:], K.xn, K.col("final_norm", 0, KT))
    with nc.Block() as block:
        @block.vector
        def _(dve):
            nc.vector.tensor_copy(K.h[:, :, 0:SEQ], K.xn[:, :, N_META:])


def ffn(K, w_gate, w_up, w_down, g_in, g_out):
    nc = K.nc
    H, X = K.h[:, :, 0:SEQ], K.xn[:, :, 0:SEQ]
    rms_norm(K, H, X, g_in)
    n_gu = D_FF // GU_COLS
    per = GU_COLS // P
    gu_len = KT * GU_COLS
    with ExitStack() as ctx:
        hid = ctx.enter_context(nc.sbuf_tensor(f"ffn_hid_{K.next()}", [P, FF_T, SEQ], F32))
        sil = ctx.enter_context(nc.sbuf_tensor(f"ffn_sil_{K.next()}", [P, 2, per, SEQ], F32))
        gu_in, dn_in = [K.sig("gu_in_0"), K.sig("gu_in_1")], [K.sig("d_in_0"), K.sig("d_in_1")]
        gu_made, silu_made, hid_made = K.sig("gu_made"), K.sig("silu_made"), K.sig("hid_made")
        dn_made, taken = K.sig("d_made"), K.sig("d_taken")
        wg, wu = (w.rearrange("(k p) n -> p k n", p=P) for w in (w_gate, w_up))
        wd = w_down.rearrange("(k p) n -> p k n", p=P)
        block = ctx.enter_context(nc.Block())
        assert n_gu % 2 == 1 and KT % 2 == 0

        @block.sync
        def _(sp):
            def gate_up(b, s, first=False):
                if not first:
                    sp.wait_ge(gu_made.sem, gu_made.base + per * (b - 1))
                sp.dma_start(K.w[:, s, 0:gu_len].rearrange("p (k n) -> p k n", k=KT),
                             wg[:, :, bass.ds(b * GU_COLS, GU_COLS)]).then_inc(gu_in[s].sem, 16)
                sp.dma_start(K.w[:, s, gu_len:2 * gu_len].rearrange("p (k n) -> p k n", k=KT),
                             wu[:, :, bass.ds(b * GU_COLS, GU_COLS)]).then_inc(gu_in[s].sem, 16)

            def down(j, s):
                sp.dma_start(K.w[:, s, 0:FF_T * P].rearrange("p (k n) -> p k n", k=FF_T),
                             wd[:, :, bass.ds(j * P, P)]).then_inc(dn_in[s].sem, 16)
            gate_up(0, 0, True)
            gate_up(1, 1, True)
            with sp.Fori(1, n_gu // 2) as i:
                gate_up(2 * i, 0)
                gate_up(2 * i + 1, 1)
            gate_up(n_gu - 1, 0)
            sp.wait_ge(*gu_made.at(per * (n_gu - 1)))
            down(0, 1)
            sp.wait_ge(*gu_made.at(per * n_gu))
            down(1, 0)
            with sp.Fori(1, KT // 2) as i:
                for s in range(2):
                    sp.wait_ge(dn_made.sem, dn_made.base + 2 * i + s - 1)
                    down(2 * i + s, 1 - s)

        @block.tensor
        def _(pe):
            def gate_up(b, s, turn, first=False):
                pe.wait_ge(gu_in[s].sem, gu_in[s].base + 32 * turn + 32)
                for m in range(per):
                    if not first:
                        pe.wait_ge(hid_made.sem, hid_made.base + per * (b - 2) + m + 1)
                    for j in range(2):
                        for k in range(KT):
                            at = j * gu_len + k * GU_COLS + m * P
                            mm = nc.tensor.matmul(K.ps[:, 4 * s + 2 * j + m, 0:SEQ], K.w[:, s, at:at + P], X[:, k],
                                                  start=k == 0, stop=k == KT - 1)
                    mm.then_inc(gu_made.sem, 1)

            def down(j, s, turn, first=False):
                pe.wait_ge(dn_in[1 - s].sem, dn_in[1 - s].base + 16 * turn + 16)
                if not first:
                    pe.wait_ge(taken.sem, taken.base + j - 1)
                for k in range(FF_T):
                    mm = nc.tensor.matmul(K.ps[:, s, 0:SEQ], K.w[:, 1 - s, k * P:(k + 1) * P], hid[:, k],
                                          start=k == 0, stop=k == FF_T - 1)
                mm.then_inc(dn_made.sem, 1)
            gate_up(0, 0, 0, True)
            gate_up(1, 1, 0, True)
            with pe.Fori(1, n_gu // 2) as i:
                gate_up(2 * i, 0, i)
                gate_up(2 * i + 1, 1, i)
            gate_up(n_gu - 1, 0, n_gu // 2)
            pe.wait_ge(*hid_made.at(FF_T))
            down(0, 0, 0, True)
            down(1, 1, 0, True)
            with pe.Fori(1, KT // 2) as i:
                down(2 * i, 0, i)
                down(2 * i + 1, 1, i)

        @block.scalar
        def _(act):
            def silu(b, s):
                for m in range(per):
                    act.wait_ge(gu_made.sem, gu_made.base + per * b + m + 1)
                    nc.scalar.activation(sil[:, s, m], K.ps[:, 4 * s + m, 0:SEQ], ACT.Silu).then_inc(silu_made.sem, 1)
            with act.Fori(0, n_gu // 2) as i:
                silu(2 * i, 0)
                silu(2 * i + 1, 1)
            silu(n_gu - 1, 0)

        @block.vector
        def _(dve):
            def times(b, s):
                for m in range(per):
                    dve.wait_ge(silu_made.sem, silu_made.base + per * b + m + 1)
                    nc.vector.tensor_tensor(hid[:, bass.ds(per * b + m, 1)], sil[:, s, m:m + 1],
                                            K.ps[:, 4 * s + 2 + m:4 * s + 3 + m, 0:SEQ], ALU.mult).then_inc(hid_made.sem, 1)
            with dve.Fori(0, n_gu // 2) as i:
                times(2 * i, 0)
                times(2 * i + 1, 1)
            times(n_gu - 1, 0)
            with dve.Fori(0, KT // 2) as i:
                for s in range(2):
                    dve.wait_ge(dn_made.sem, dn_made.base + 2 * i + s + 1)
                    nc.vector.tensor_copy(X[:, bass.ds(2 * i + s, 1)], K.ps[:, s:s + 1, 0:SEQ]).then_inc(taken.sem, 1)
        gu_in[0].given += 32 * (n_gu // 2 + 1)
        gu_in[1].given += 32 * (n_gu // 2)
        for s in range(2):
            dn_in[s].given += 16 * KT // 2
        for sig, n in ((gu_made, FF_T), (silu_made, FF_T), (hid_made, FF_T), (dn_made, KT), (taken, KT)):
            sig.given += n
    rms_norm(K, X, X, g_out, add_to=H, factor=0.5)


TT = [(0, P), (P, P)]


def nsa_ssd(K):
    nc, I = K.nc, K.ins
    X = K.xn[:, :, 0:SEQ]
    W = I["ab_w_in_2"][0]
    xk = lambda k: X[:, k]
    xt = lambda k, t0, tn: X[:, k, t0:t0 + tn]
    with ExitStack() as outer:
        joined = outer.enter_context(nc.sbuf_tensor("joined", [P, 2, 512 + SSD_INNER], F32))
        with ExitStack() as ctx:
            def sb(name, shape):
                return ctx.enter_context(nc.sbuf_tensor(name, shape, F32))
            q, kcv, kw = sb("q", [P, 4, SEQ]), sb("kcv", [P, 3, SEQ]), sb("kw", [P, 1, SEQ])
            vs, vg = sb("vs", [P, 2, 128]), sb("vg", [P, 2, 152])
            xbc, z, dt = sb("xbc", [P, 12, SEQ]), sb("z", [P, 2, SSD_INNER]), sb("dt", [P, 2, SSD_HEADS])
            copy = lambda dst: (lambda m, ps: nc.vector.tensor_copy(dst[:, m], ps))
            feature_linear(K, W[:, OFF[0]:OFF[1]], xk, SEQ, copy(q),
                           pieces=[((2 * g + v) * HD, (NSA_GROUP * v + g) * HD, HD) for g in range(NSA_GROUP) for v in range(NSA_KV)])
            feature_linear(K, W[:, OFF[1]:OFF[4]], xk, SEQ, copy(kcv))
            feature_linear(K, W[:, OFF[5]:OFF[6]], xk, SEQ, copy(kw))
            feature_linear(K, W[:, OFF[9]:OFF[10]], xk, SEQ, copy(xbc))

            def tcopy(dst):
                return lambda i, at, n, ps: nc.vector.tensor_copy(dst[:, i, at:at + n], ps)
            token_linear(K, W[:, OFF[4]:OFF[5]], xt, KT, TT, tcopy(vs))
            token_linear(K, W[:, OFF[6]:OFF[8]], xt, KT, TT, tcopy(vg))
            token_linear(K, W[:, OFF[8]:OFF[9]], xt, KT, TT, tcopy(z))
            with nc.allow_non_contiguous_dma(reason="16 columns"):
                token_linear(K, W[:, OFF[10]:OFF[11]], xt, KT, TT, tcopy(dt))
            rot = [q[:, g] for g in range(4)] + [kcv[:, 0], kcv[:, 2], kw[:, 0]]
            turned = K.sq[:, 0:7, 0:SEQ]
            rope(K, rot, [turned[:, i] for i in range(7)], P, SEQ)
            nsa(K, turned, kcv[:, 1], vs, vg, joined)
            ssd(K, xbc, z, dt, joined)
        project_joined(K, joined, (512 + SSD_INNER) // P, I["ab_w_out_2"][0])


def project_joined(K, tok, n, w):
    nc = K.nc
    with ExitStack() as ctx:
        feat = ctx.enter_context(nc.sbuf_tensor(f"feat_{K.next()}", [P, n, SEQ], F32))
        made, taken = K.sig("tile_made"), K.sig("tile_stored")
        with nc.Block() as block:
            @block.tensor
            def _(pe):
                for m in range(n // 2):
                    if m >= 8:
                        pe.wait_ge(*taken.at(m - 7))
                    for j in range(2):
                        for t in range(2):
                            at = (2 * m + j) * P
                            mm = nc.tensor.transpose(K.ps[:, m % 8, (2 * j + t) * P:(2 * j + t + 1) * P], tok[:, t, at:at + P], K.con(C_ID))
                    mm.then_inc(*made.one())

            @block.vector
            def _(dve):
                for m in range(n // 2):
                    dve.wait_ge(*made.at(m + 1))
                    nc.vector.tensor_copy(feat[:, 2 * m:2 * m + 2], K.ps[:, m % 8, :].rearrange("p (j t) -> p j t", j=2)).then_inc(*taken.one())
        feature_linear(K, w, lambda k: feat[:, k], SEQ, lambda m, ps: nc.vector.tensor_copy(K.xn[:, m, 0:SEQ], ps))


def nsa(K, roped, vc, vs, vg, joined):
    nc, I = K.nc, K.ins
    scale = HD ** -0.5
    with ExitStack() as ctx:
        def sb(name, shape):
            return ctx.enter_context(nc.sbuf_tensor(name, shape, F32))
        kC, vC = sb("kC", [P, N_CMP]), sb("vC", [N_CMP, 2, HD])
        gates = sb("nsa_gates", [P, 2, 24])
        compress(K, roped[:, 4], vc, kC, vC)
        pc = sb("pc", [P, 2, 8, N_CMP])
        stat = sb("pc_stat", [P, 2, 8, 2])
        madd = sb("pc_mask", [P, 2, N_CMP])
        pcT = sb("pcT", [N_CMP, 2, 8, P])
        made, e_in, e_done, ready = K.sig("tile_made"), K.sig("s_ready"), K.sig("e_made"), K.sig("p_ready")
        turned, copied, pv, gated = K.sig("t_made"), K.sig("t_taken"), K.sig("pv_made"), K.sig("gated")
        M = K.con(C_CMPM, 2 * (N_CMP + 1)).rearrange("p (t n) -> p t n", t=2)[:, :, 0:N_CMP]
        with nc.Block() as block:
            @block.tensor
            def _(pe):
                for t in range(2):
                    for v in range(NSA_KV):
                        for g in range(NSA_GROUP):
                            at = (t * NSA_GROUP + g) * 16
                            mm = nc.tensor.matmul(K.ps[:, v, at:at + N_CMP], roped[64 * v:64 * v + 64, g, t * P:(t + 1) * P],
                                                  kC[64 * v:64 * v + 64, :], start=True, stop=True)
                mm.then_inc(*made.one())
                pe.wait_ge(*ready.at(1))
                for t in range(2):
                    for h in range(8):
                        mm = nc.tensor.transpose(K.ps[0:N_CMP, 2 + 2 * t + h // 4, (h % 4) * P:(h % 4 + 1) * P], pc[:, t, h], K.con(C_ID))
                mm.then_inc(*turned.one())
                pe.wait_ge(*copied.at(1))
                for t in range(2):
                    for h in range(8):
                        mm = nc.tensor.matmul(K.ps[:, 6 + t, h * HD:(h + 1) * HD], pcT[:, t, h], vC[:, h // 4], start=True, stop=True)
                mm.then_inc(*pv.one())

            @block.scalar
            def _(act):
                nc.scalar.activation(gates[:], vg[:, :, 128:152], ACT.Sigmoid).then_inc(*gated.one())
                act.wait_ge(*e_in.at(1))
                nc.scalar.activation(pc[:], pc[:], ACT.Exp).then_inc(*e_done.one())

            @block.vector
            def _(dve):
                v = nc.vector
                do = lambda ins: link(dve, K.dve_step, ins)
                bc = lambda ap: ap.to_broadcast([P, 8, N_CMP])
                do(v.tensor_scalar(madd[:], M, 1.0, -NEG, ALU.subtract, ALU.mult))
                dve.wait_ge(*made.at(1))
                S = K.ps[:, 0:2, 0:128].rearrange("p v (t g n) -> p t v g n", t=2, g=NSA_GROUP)
                for t in range(2):
                    for kv in range(NSA_KV):
                        last = v.scalar_tensor_tensor(out=pc[:, t, 4 * kv:4 * kv + 4], in0=S[:, t, kv, :, 0:N_CMP], scalar=scale,
                                                      in1=madd[:, t:t + 1].to_broadcast([P, 4, N_CMP]), op0=ALU.mult, op1=ALU.add)
                    do(last)
                    do(v.reduce_max(stat[:, t, :, 0:1], pc[:, t], AX))
                    last = v.tensor_tensor(pc[:, t], pc[:, t], bc(stat[:, t, :, 0:1]), ALU.subtract)
                last.then_inc(*e_in.one())
                dve.wait_ge(*e_done.at(1))
                dve.wait_ge(*gated.at(1))
                for t in range(2):
                    do(v.tensor_tensor(pc[:, t], pc[:, t], bc(M[:, t:t + 1]), ALU.mult))
                    do(v.reduce_sum(stat[:, t, :, 0:1], pc[:, t], AX))
                    do(v.tensor_scalar(stat[:, t, :, 0:1], stat[:, t, :, 0:1], 1e-30, None, ALU.max))
                    do(v.reciprocal(stat[:, t, :, 1:2], stat[:, t, :, 0:1]))
                    gt = gates[:, t].rearrange("p (h c) -> p h c", c=3)
                    do(v.tensor_tensor(stat[:, t, :, 1:2], stat[:, t, :, 1:2], gt[:, :, 0:1], ALU.mult))
                    last = v.tensor_tensor(pc[:, t], pc[:, t], bc(stat[:, t, :, 1:2]), ALU.mult)
                last.then_inc(*ready.one())
                dve.wait_ge(*turned.at(1))
                for t in range(2):
                    last = v.tensor_copy(pcT[:, t].rearrange("c (a h) q -> c a (h q)", a=2), K.ps[0:N_CMP, 2 + 2 * t:4 + 2 * t, :])
                last.then_inc(*copied.one())
                dve.wait_ge(*pv.at(1))
                for t in range(2):
                    v.tensor_copy(joined[:, t, 0:512], K.ps[:, 6 + t])
        dense_branches(K, roped, vs, vg, gates, joined)


def compress(K, kc, vc, kC, vC):
    nc, I = K.nc, K.ins
    half = CMP_STRIDE
    with ExitStack() as ctx:
        def sb(name, shape):
            return ctx.enter_context(nc.sbuf_tensor(name, shape, F32))
        w1, w2 = sb("cw1", [P, 2, CMP_BLOCK, HD]), sb("cw2", [HD, 2, HD])
        pe_rows, peT = sb("pe_rows", [CMP_BLOCK, 2, 2, HD]), sb("peT", [P, 2, CMP_BLOCK])
        xs = sb("cmp_x", [P, 2, 2, SEQ])
        hidden = sb("cmp_h", [HD, 2, 2, N_CMP])
        given, turned, ready = K.sig("rows_given"), K.sig("t_made"), K.sig("p_ready")
        made, silu, out = K.sig("tile_made"), K.sig("silu_made"), K.sig("pv_made")
        block = ctx.enter_context(nc.Block())

        @block.sync
        def _(sp):
            for j, kind in enumerate("kv"):
                for v in range(2):
                    sp.dma_start(w1[64 * v:64 * v + 64, j], I[f"a_cmp_w1_{kind}_2"][0].rearrange("(l d) m -> d l m", d=HD)).then_inc(*given.dma())
                    sp.dma_start(pe_rows[:, j, v], I[f"a_cmp_pe_{kind}_2"][0]).then_inc(*given.dma())
                sp.dma_start(w2[:, j], I[f"a_cmp_w2_{kind}_2"][0]).then_inc(*given.dma())

        @block.tensor
        def _(pe):
            pe.wait_ge(*given.at(160))
            for j in range(2):
                mm = nc.tensor.transpose(K.ps[:, 0, j * CMP_BLOCK:(j + 1) * CMP_BLOCK], pe_rows[:, j].rearrange("l v d -> l (v d)"),
                                         K.cst[0:CMP_BLOCK, C_ID:C_ID + CMP_BLOCK])
            mm.then_inc(*turned.one())
            pe.wait_ge(*ready.at(1))
            for j in range(2):
                for v in range(2):
                    rows = slice(64 * v, 64 * v + 64)
                    for l in range(CMP_BLOCK):
                        x = xs[rows, j, l // half].rearrange("p (b r) -> p b r", r=half)[:, l // half:l // half + N_CMP, l % half]
                        mm = nc.tensor.matmul(K.ps[0:HD, 1 + 2 * j + v, 0:N_CMP], w1[rows, j, l], x,
                                              start=l == 0, stop=l == CMP_BLOCK - 1)
            mm.then_inc(*made.one())
            pe.wait_ge(*silu.at(1))
            for v in range(2):
                nc.tensor.matmul(K.ps[64 * v:64 * v + 64, 5, 0:N_CMP], w2[:, 0], hidden[:, 0, v], start=True, stop=True)
                mm = nc.tensor.matmul(K.ps[0:N_CMP, 6, v * HD:(v + 1) * HD], hidden[:, 1, v], w2[:, 1], start=True, stop=True)
            mm.then_inc(*out.one())

        @block.vector
        def _(dve):
            dve.wait_ge(*turned.at(1))
            link(dve, K.dve_step, nc.vector.tensor_copy(peT[:], K.ps[:, 0, 0:2 * CMP_BLOCK].rearrange("p (j l) -> p j l", j=2)))
            for j, x in enumerate((kc, vc)):
                for a in range(2):
                    last = nc.vector.tensor_tensor(xs[:, j, a].rearrange("p (b r) -> p b r", r=half), x.rearrange("p (b r) -> p b r", r=half),
                                                   peT[:, j:j + 1, a * half:(a + 1) * half].to_broadcast([P, SEQ // half, half]), ALU.add)
            last.then_inc(*ready.one())
            dve.wait_ge(*out.at(1))
            nc.vector.tensor_copy(kC[:], K.ps[:, 5, 0:N_CMP])
            nc.vector.tensor_copy(vC[:], K.ps[0:N_CMP, 6, 0:2 * HD].rearrange("n (v d) -> n v d", v=2))

        @block.scalar
        def _(act):
            act.wait_ge(*made.at(1))
            for j in range(2):
                last = nc.scalar.activation(hidden[:, j], K.ps[0:HD, 1 + 2 * j:3 + 2 * j, 0:N_CMP], ACT.Silu)
            last.then_inc(*silu.one())


def dense_branches(K, roped, vs, vg, gates, joined):
    nc = K.nc
    scale = HD ** -0.5
    units = [(b, v, g) for b in range(2) for v in range(NSA_KV) for g in range(NSA_GROUP)]
    n = len(units)
    W = 3 * P
    parts = [(0, 0, P), (1, P, W)]
    blocks = [(0, 0), (1, 0), (1, 1)]
    with ExitStack() as ctx:
        def sb(name, shape):
            return ctx.enter_context(nc.sbuf_tensor(name, shape, F32))
        S, Pr, PT = sb("nsa_s", [P, 3, W]), sb("nsa_p", [P, 3, W]), sb("nsa_pt", [P, 2, W])
        st = sb("nsa_stat", [P, 4, 2, 4])
        s_made, s_ready, e_made = K.sig("s_made"), K.sig("s_ready"), K.sig("e_made")
        t_made, t_taken, pv_made, o_taken = K.sig("t_made"), K.sig("t_taken"), K.sig("pv_made"), K.sig("o_taken")
        block = ctx.enter_context(nc.Block())

        @block.tensor
        def _(pe):
            for u in range(n + 2):
                if u < n:
                    b, v, g = units[u]
                    rows = slice(64 * v, 64 * v + 64)
                    if u >= 3:
                        pe.wait_ge(*s_ready.at(u - 2))
                    for t, lo, hi in parts:
                        mm = nc.tensor.matmul(K.ps[:, u % 3, lo:hi], roped[rows, g, t * P:(t + 1) * P], roped[rows, 5 + b, 0:hi - lo],
                                              start=True, stop=True)
                    mm.then_inc(*s_made.one())
                if 1 <= u <= n:
                    w = u - 1
                    pe.wait_ge(*e_made.at(w + 1))
                    if w >= 2:
                        pe.wait_ge(*t_taken.at(w - 1))
                    for j in range(3):
                        mm = nc.tensor.transpose(K.ps[:, 3 + w % 2, j * P:(j + 1) * P], Pr[:, w % 3, j * P:(j + 1) * P], K.con(C_ID))
                    mm.then_inc(*t_made.one())
                if u >= 2:
                    w = u - 2
                    b, v, g = units[w]
                    pe.wait_ge(*t_taken.at(w + 1))
                    if w >= 2:
                        pe.wait_ge(*o_taken.at(w - 1))
                    for j, (t, kt) in enumerate(blocks):
                        mm = nc.tensor.matmul(K.ps[:, 5 + w % 2, t * HD:(t + 1) * HD], PT[:, w % 2, j * P:(j + 1) * P],
                                              (vs, vg)[b][:, kt, v * HD:(v + 1) * HD], start=kt == 0, stop=kt == t)
                    mm.then_inc(*pv_made.one())

        @block.vector
        def _(dve):
            causal = K.cst[:, C_CAUSAL:C_CAUSAL + P]
            for u in range(n + 3):
                if u < n:
                    dve.wait_ge(*s_made.at(u + 1))
                    if u >= 3:
                        dve.wait_ge(*e_made.at(u - 2))
                    nc.vector.tensor_scalar(S[:, u % 3, P:2 * P], K.ps[:, u % 3, P:2 * P], scale, None, ALU.mult)
                    nc.vector.scalar_tensor_tensor(out=S[:, u % 3, 0:P], in0=K.ps[:, u % 3, 0:P], scalar=scale, in1=causal,
                                                   op0=ALU.mult, op1=ALU.add)
                    link(dve, K.dve_step, nc.vector.scalar_tensor_tensor(
                        out=S[:, u % 3, 2 * P:W], in0=K.ps[:, u % 3, 2 * P:W], scalar=scale, in1=causal, op0=ALU.mult, op1=ALU.add))
                    for t, lo, hi in parts:
                        last = nc.vector.reduce_max(st[:, u % 4, t, 3:4], S[:, u % 3, lo:hi], AX)
                    link(dve, K.dve_step, last)
                    nc.vector.tensor_scalar(st[:, u % 4, :, 0:1], st[:, u % 4, :, 3:4], -1.0, None, ALU.mult).then_inc(*s_ready.one())
                if u >= 3:
                    w = u - 3
                    b, v, g = units[w]
                    h = 4 * v + g
                    dve.wait_ge(*pv_made.at(w + 1))
                    link(dve, K.dve_step, nc.vector.reciprocal(st[:, w % 4, :, 2:3], st[:, w % 4, :, 1:2]))
                    link(dve, K.dve_step, nc.vector.tensor_tensor(st[:, w % 4, :, 2:3], st[:, w % 4, :, 2:3],
                                                                  gates[:, :, 3 * h + 1 + b:3 * h + 2 + b], ALU.mult))
                    for t in range(2):
                        o = joined[:, t, h * HD:(h + 1) * HD]
                        last = nc.vector.scalar_tensor_tensor(out=o, in0=K.ps[:, 5 + w % 2, t * HD:(t + 1) * HD], scalar=st[:, w % 4, t, 2:3],
                                                              in1=o, op0=ALU.mult, op1=ALU.add)
                    last.then_inc(*o_taken.one())

        @block.scalar
        def _(act):
            for u in range(n + 1):
                if u < n:
                    act.wait_ge(*s_ready.at(u + 1))
                    if u >= 3:
                        act.wait_ge(*t_made.at(u - 2))
                    for t, lo, hi in parts:
                        last = nc.scalar.activation(Pr[:, u % 3, lo:hi], S[:, u % 3, lo:hi], ACT.Exp, bias=st[:, u % 4, t, 0:1],
                                                    accum_out=st[:, u % 4, t, 1:2])
                    last.then_inc(*e_made.one())
                if u >= 1:
                    w = u - 1
                    act.wait_ge(*t_made.at(w + 1))
                    if w >= 2:
                        act.wait_ge(*pv_made.at(w - 1))
                    nc.scalar.copy(PT[:, w % 2], K.ps[:, 3 + w % 2, 0:W]).then_inc(*t_taken.one())


def ssd(K, xbc, z, dt, joined):
    nc, I = K.nc, K.ins
    NT = XBC // P
    with ExitStack() as ctx:
        def sb(name, shape):
            return ctx.enter_context(nc.sbuf_tensor(name, shape, F32))
        cv = sb("conv", [P, NT, SEQ])
        row = sb("ssd_rows", [P, 3, SSD_HEADS])
        normw = sb("ssd_normw", [P, SSD_INNER])
        sp_ = sb("softplus", [P, 2, 3, SSD_HEADS])
        dta, acs = sb("dta", [P, 2, SSD_HEADS]), sb("acs", [P, 2, 4, SSD_HEADS])
        given, conv_done = K.sig("rows_given"), K.sig("pooled")
        a_in, a_done = K.sig("exp_asked"), K.sig("exp_done")
        acs_made = K.sig("s_made")
        with nc.Block() as block:
            @block.sync
            def _(s):
                for j, name in enumerate(("b_dt_bias_2", "b_a_log_2", "b_d_skip_2")):
                    s.dma_start(row[:, j], I[name].to_broadcast([P, SSD_HEADS])).then_inc(*given.dma())
                s.dma_start(normw[:], I["b_norm_w_2"].to_broadcast([P, SSD_INNER])).then_inc(*given.dma())

            @block.vector
            def _(dve):
                v = nc.vector
                do = lambda ins: link(dve, K.dve_step, ins)
                dve.wait_ge(*given.at(64))
                for t in range(2):
                    do(v.tensor_tensor(sp_[:, t, 0], dt[:, t], row[:, 0], ALU.add))
                    do(v.tensor_scalar(sp_[:, t, 1], sp_[:, t, 0], -1.0, None, ALU.mult))
                    do(v.tensor_tensor(sp_[:, t, 1], sp_[:, t, 1], sp_[:, t, 0], ALU.min))
                    last = v.tensor_scalar(sp_[:, t, 0], sp_[:, t, 0], 0.0, None, ALU.max)
                last.then_inc(*a_in.one())
                cw = lambda tap, c: K.col("b_conv_w_2", tap * NT + c)
                for c in range(NT):
                    v.tensor_scalar(cv[:, c], xbc[:, c], cw(SSD_CONV - 1, c), K.col("b_conv_b_2", c), ALU.mult, ALU.add).then_inc(*K.dve_step.one())
                for s in range(1, SSD_CONV):
                    dve.wait_ge(*K.dve_step.now())
                    for c in range(NT):
                        last = v.scalar_tensor_tensor(out=cv[:, c, s:], in0=xbc[:, c, 0:SEQ - s], scalar=cw(SSD_CONV - 1 - s, c),
                                                      in1=cv[:, c, s:], op0=ALU.mult, op1=ALU.add)
                    last.then_inc(*K.dve_step.one())
                last2 = v.memset(acs[:], 0.0)
                last2.then_inc(*conv_done.one())
                dve.wait_ge(*a_done.at(1))
                for t in range(2):
                    do(v.tensor_tensor(dt[:, t], sp_[:, t, 0], sp_[:, t, 2], ALU.add))
                    last = v.scalar_tensor_tensor(out=dta[:, t], in0=dt[:, t], scalar=-1.0, in1=row[:, 1], op0=ALU.mult, op1=ALU.mult)
                last.then_inc(*a_in.one())
                dve.wait_ge(*acs_made.at(1))
                for t in range(2):
                    do(v.tensor_copy(acs[:, t, 0], K.ps[:, 0, t * 16:t * 16 + 16]))
                do(v.tensor_tensor(acs[:, 0, 1], K.ps[:, 0, 32:48], acs[:, 0, 0], ALU.subtract))

            @block.tensor
            def _(pe):
                pe.wait_ge(*a_in.at(2))
                for t in range(2):
                    nc.tensor.matmul(K.ps[:, 0, t * 16:t * 16 + 16], K.con(C_TRI), dta[:, t], start=True, stop=True)
                nc.tensor.matmul(K.ps[:, 0, 32:48], K.con(C_ONE), dta[:, 0], start=True, stop=True).then_inc(*acs_made.one())

            @block.scalar
            def _(act):
                act.wait_ge(*a_in.at(1))
                link(act, K.act_step, nc.scalar.activation(sp_[:, :, 1], sp_[:, :, 1], ACT.Exp))
                nc.scalar.activation(row[:, 1], row[:, 1], ACT.Exp)
                nc.scalar.activation(sp_[:, :, 2], sp_[:, :, 1], ACT.Ln, bias=1.0).then_inc(*a_done.one())
                act.wait_ge(*conv_done.at(1))
                nc.scalar.activation(cv[:], cv[:], ACT.Silu)
        ssd_chunks(K, cv, z, dt, dta, acs, row, normw, joined)


def ssd_chunks(K, cv, z, dt, dta, acs, row, normw, joined):
    nc = K.nc
    HG = SSD_HEADS // SSD_GROUPS
    hp = lambda ap: ap.rearrange("p (h d) -> p h d", d=HD)
    with ExitStack() as ctx:
        def sb(name, shape):
            return ctx.enter_context(nc.sbuf_tensor(name, shape, F32))
        xs, xd = sb("ssd_xs", [P, 2, SSD_INNER]), sb("ssd_xd", [P, 2, SSD_INNER])
        xdd = sb("ssd_xdd", [P, SSD_INNER])
        bt = sb("ssd_bt", [P, SSD_GROUPS, SSD_STATE])
        cb = sb("ssd_cb", [P, 2, SSD_GROUPS, P])
        state = sb("ssd_state", [P, SSD_GROUPS, HG * HD])
        ms = sb("ssd_ms", [P, 2, SSD_GROUPS, 2])
        made, taken = K.sig("tile_made"), K.sig("tile_stored")
        e_in, e_done = K.sig("exp_asked"), K.sig("exp_done")
        st_in, st_made, st_taken = K.sig("p_ready"), K.sig("pv_made"), K.sig("o_taken")
        with nc.Block() as block:
            @block.tensor
            def _(pe):
                for n in range(4):
                    for k in range(4):
                        mm = nc.tensor.transpose(K.ps[:, n, k * P:(k + 1) * P], cv[:, 4 * (n % 2) + k, (n // 2) * P:(n // 2 + 1) * P], K.con(C_ID))
                    mm.then_inc(*made.one())
                for g in range(SSD_GROUPS):
                    mm = nc.tensor.transpose(K.ps[:, 4, g * P:(g + 1) * P], cv[:, 8 + g, 0:P], K.con(C_ID))
                mm.then_inc(*made.one())
                for c in range(2):
                    for g in range(SSD_GROUPS):
                        t = slice(c * P, (c + 1) * P)
                        mm = nc.tensor.matmul(K.ps[:, 5, (2 * c + g) * P:(2 * c + g + 1) * P], cv[:, 8 + g, t], cv[:, 10 + g, t], start=True, stop=True)
                mm.then_inc(*made.one())
                pe.wait_ge(*st_in.at(1))
                for g in range(SSD_GROUPS):
                    mm = nc.tensor.matmul(K.ps[:, 6 + g], bt[:, g], xdd[:, g * 512:(g + 1) * 512], start=True, stop=True)
                mm.then_inc(*st_made.one())

            @block.scalar
            def _(act):
                nc.scalar.activation(acs[:, 0, 1], acs[:, 0, 1], ACT.Exp)
                nc.scalar.activation(acs[:, 1, 2], acs[:, 1, 0], ACT.Exp).then_inc(*e_done.one())
                nc.scalar.activation(z[:], z[:], ACT.Silu)

            @block.vector
            def _(dve):
                v = nc.vector
                do = lambda ins: link(dve, K.dve_step, ins)
                for n in range(4):
                    dve.wait_ge(*made.at(n + 1))
                    last = v.tensor_copy(xs[:, n // 2, 512 * (n % 2):512 * (n % 2) + 512], K.ps[:, n])
                do(last)
                for t in range(2):
                    do(v.tensor_tensor(hp(xd[:, t]), hp(xs[:, t]), dt[:, t].rearrange("p (h a) -> p h a", a=1).to_broadcast([P, 16, HD]), ALU.mult))
                dve.wait_ge(*e_done.at(1))
                do(v.tensor_tensor(hp(xdd[:]), hp(xd[:, 0]), acs[:, 0, 1].rearrange("p (h a) -> p h a", a=1).to_broadcast([P, 16, HD]), ALU.mult))
                dve.wait_ge(*made.at(5))
                v.tensor_copy(bt[:], K.ps[:, 4, 0:256].rearrange("p (g n) -> p g n", g=2)).then_inc(*st_in.one())
                dve.wait_ge(*made.at(6))
                v.tensor_tensor(cb[:].rearrange("p c g n -> p (c g) n"), K.ps[:, 5].rearrange("p (x n) -> p x n", x=4),
                                K.con(C_TRI).rearrange("p (a n) -> p a n", a=1).to_broadcast([P, 4, P]), ALU.mult)
                dve.wait_ge(*st_made.at(1))
                v.tensor_copy(state[:], K.ps[:, 6:8])
        units = [(c, g, q) for c in range(2) for g in range(SSD_GROUPS) for q in range(2)]
        n = len(units)
        seg = sb("ssd_seg", [P, 2, 4, P])
        made, s_ready, e_made, ready = K.sig("s_made"), K.sig("s_ready"), K.sig("e_made"), K.sig("p_ready")
        used, y_made, y_off = K.sig("t_made"), K.sig("pv_made"), K.sig("o_taken")
        with nc.Block() as block:
            @block.tensor
            def _(pe):
                for g in range(SSD_GROUPS):
                    mm = nc.tensor.matmul(K.ps[:, 6 + g], cv[:, 10 + g, P:2 * P], state[:, g], start=True, stop=True)
                mm.then_inc(*y_off.one())
                for u in range(n + 1):
                    if u < n:
                        c, g, q = units[u]
                        if u >= 2:
                            pe.wait_ge(*s_ready.at(u - 1))
                        for j in range(4):
                            h = g * HG + q * 4 + j
                            mm = nc.tensor.matmul(K.ps[:, u % 2, j * P:(j + 1) * P], dta[:, c, h:h + 1].to_broadcast([P, P]), K.con(C_TRI),
                                                  start=True, stop=True)
                        mm.then_inc(*made.one())
                    if u >= 1:
                        c, g, q = units[u - 1]
                        pe.wait_ge(*ready.at(u))
                        for j in range(4):
                            h = g * HG + q * 4 + j
                            at = (q * 4 + j) * HD
                            mm = nc.tensor.matmul(K.ps[:, 2 + 2 * c + g, at:at + HD], seg[:, (u - 1) % 2, j], xd[:, c, h * HD:(h + 1) * HD],
                                                  start=True, stop=True)
                        mm.then_inc(*y_made.one())

            @block.scalar
            def _(act):
                for u in range(n):
                    act.wait_ge(*s_ready.at(u + 1))
                    nc.scalar.activation(seg[:, u % 2], seg[:, u % 2], ACT.Exp).then_inc(*e_made.one())
                act.wait_ge(*used.at(1))
                for c in range(2):
                    for g in range(SSD_GROUPS):
                        last = nc.scalar.activation(xd[:, c, g * 512:(g + 1) * 512], xs[:, c, g * 512:(g + 1) * 512], ACT.Square,
                                                    accum_out=ms[:, c, g, 0:1])
                link(act, K.act_step, last)
                nc.scalar.activation(ms[:, :, :, 1:2], ms[:, :, :, 0:1], ACT.Sqrt, bias=K.eps[:, 1:2], scale=1.0 / (HG * HD)).then_inc(*used.one())

            @block.vector
            def _(dve):
                v = nc.vector
                do = lambda ins: link(dve, K.dve_step, ins)
                wide = lambda ap: ap.rearrange("p (h a) -> p h a", a=1)
                for u in range(n + 1):
                    if u < n:
                        c, g, q = units[u]
                        dve.wait_ge(*made.at(u + 1))
                        if u >= 2:
                            dve.wait_ge(*y_made.at(u - 1))
                        h = g * HG + q * 4
                        do(v.tensor_tensor(seg[:, u % 2], K.ps[:, u % 2].rearrange("p (j l) -> p j l", j=4),
                                           wide(acs[:, c, 0, h:h + 4]).to_broadcast([P, 4, P]), ALU.subtract))
                        v.tensor_scalar(seg[:, u % 2], seg[:, u % 2], 0.0, None, ALU.min).then_inc(*s_ready.one())
                    if u >= 1:
                        c, g, q = units[u - 1]
                        dve.wait_ge(*e_made.at(u))
                        v.tensor_tensor(seg[:, (u - 1) % 2], seg[:, (u - 1) % 2], cb[:, c, g:g + 1].to_broadcast([P, 4, P]), ALU.mult).then_inc(*ready.one())
                dve.wait_ge(*y_made.at(n))
                dve.wait_ge(*y_off.at(1))
                for c in range(2):
                    do(v.tensor_tensor(hp(xs[:, c]), hp(xs[:, c]), wide(row[:, 2]).to_broadcast([P, 16, HD]), ALU.mult))
                    for g in range(SSD_GROUPS):
                        part = xs[:, c, g * 512:(g + 1) * 512]
                        do(v.tensor_tensor(part, part, K.ps[:, 2 + 2 * c + g], ALU.add))
                        if c == 1:
                            tmp = xdd[:, g * 512:(g + 1) * 512]
                            do(v.tensor_tensor(hp(tmp), hp(K.ps[:, 6 + g]), wide(acs[:, 1, 2, g * HG:(g + 1) * HG]).to_broadcast([P, HG, HD]), ALU.mult))
                            do(v.tensor_tensor(part, part, tmp, ALU.add))
                last = v.tensor_tensor(xs[:], xs[:], z[:], ALU.mult)
                last.then_inc(*used.one())
                dve.wait_ge(*used.at(2))
                do(v.reciprocal(ms[:, :, :, 0:1], ms[:, :, :, 1:2]))
                for c in range(2):
                    for g in range(SSD_GROUPS):
                        at = g * 512
                        v.scalar_tensor_tensor(out=joined[:, c, 512 + at:1024 + at], in0=xs[:, c, at:at + 512], scalar=ms[:, c, g, 0:1],
                                               in1=normw[:, at:at + 512], op0=ALU.mult, op1=ALU.mult)


def rwkv(K, scratch):
    nc, I = K.nc, K.ins
    X = K.xn[:, :, 0:SEQ]
    with ExitStack() as ctx:
        def sb(name, shape):
            return ctx.enter_context(nc.sbuf_tensor(name, shape, F32))
        v, g = sb("rw_v", [P, 2, D]), sb("rw_g", [P, 2, D])
        y = sb("rw_y", [P, 2, D])
        with ExitStack() as inner:
            def sbi(name, shape):
                return inner.enter_context(nc.sbuf_tensor(name, shape, F32))
            r, k, sg, a = (sbi(f"rw_{n}", [P, KT, SEQ]) for n in ("r", "k", "sg", "a"))
            rwkv_projections(K, X, r, k, sg, a, v, g)
            ar = sbi("rw_ar", [P, KT, 2, SEQ])
            kk = sbi("rw_kk", [P, KT, SEQ])
            cl = sbi("rw_cl", [P, KT, N_RC])
            bon = sbi("rw_bonus", [P, 2, RW_HEADS])
            rwkv_factors(K, r, k, sg, a, kk, ar, cl)
            bp, kp = sbi("rw_bp", [P, 2, D]), sbi("rw_kp", [P, 2, D])
            sc = sbi("rw_sc", [P, 32, 4, RC])
            rwkv_scores(K, a, k, r, kk, ar, bp, kp, sc, bon)
            tm = sbi("rw_tm", [P, 32, RC])
            nv = sbi("rw_nv", [P, 2, 2, D])
            flat = lambda buf: buf[:].rearrange("p f t -> p (f t)")
            rwkv_inverse(K, sc, v, tm, nv, scratch, flat(sg), flat(kk))
            rwkv_chunks(K, ar, cl, bp, kp, sc, tm, nv, v, y, flat(a), flat(sg))
            rwkv_output(K, y, v, g, bon, flat(k).rearrange("p (j n) -> p j n", j=2), flat(r))
        project_joined(K, y, KT, I["c_w_o_2"][0])


def rwkv_projections(K, X, r, k, sg, a, v, g):
    nc, I = K.nc, K.ins
    with ExitStack() as ctx:
        def sb(name, shape):
            return ctx.enter_context(nc.sbuf_tensor(name, shape, F32))
        mix = sb("rw_mix", [P, 6, KT, SEQ])
        low = sb("rw_low", [P, 2, SEQ])
        xx = K.sq[:, :, 0:SEQ]
        with nc.Block() as block:
            @block.vector
            def _(dve):
                nc.vector.tensor_tensor(xx[:, :, 1:], X[:, :, 0:SEQ - 1], X[:, :, 1:], ALU.subtract)
                link(dve, K.dve_step, nc.vector.tensor_scalar(xx[:, :, 0:1], X[:, :, 0:1], -1.0, None, ALU.mult))
                for i in range(6):
                    for kt in range(KT):
                        nc.vector.scalar_tensor_tensor(out=mix[:, i, kt], in0=xx[:, kt], scalar=K.col("c_mu_2", 8 * i + kt),
                                                       in1=X[:, kt], op0=ALU.mult, op1=ALU.add)
        feat = lambda i: (lambda kt: mix[:, i, kt])
        tok = lambda i: (lambda kt, t0, tn: mix[:, i, kt, t0:t0 + tn])
        feature_linear(K, I["c_w_r_2"][0], feat(0), SEQ, lambda m, ps: nc.vector.tensor_copy(r[:, m], ps))
        feature_linear(K, I["c_w_k_2"][0], feat(2), SEQ, lambda m, ps: nc.vector.tensor_copy(k[:, m], ps))
        token_linear(K, I["c_w_v_2"][0], tok(3), KT, TT, lambda i, at, n, ps: nc.vector.tensor_copy(v[:, i, at:at + n], ps))
        feature_linear(K, I["c_w1_2"][0], feat(1), SEQ, lambda m, ps: nc.scalar.activation(low[0:64, 0], ps, ACT.Tanh), by="scalar")
        feature_linear(K, I["c_w2_2"][0], lambda kt: low[0:64, 0], SEQ,
                       lambda m, ps: nc.scalar.activation(sg[:, m], ps, ACT.Sigmoid, bias=K.col("c_w0_2", m)), by="scalar")
        feature_linear(K, I["c_a1_2"][0], feat(4), SEQ, lambda m, ps: nc.vector.tensor_copy(low[0:64, 1], ps))
        feature_linear(K, I["c_a2_2"][0], lambda kt: low[0:64, 1], SEQ,
                       lambda m, ps: nc.scalar.activation(a[:, m], ps, ACT.Sigmoid, bias=K.col("c_a0_2", m)), by="scalar")
        feature_linear(K, I["c_g1_2"][0], feat(5), SEQ,
                       lambda m, ps: nc.scalar.activation(low[0:ps.shape[0], m], ps, ACT.Sigmoid), by="scalar")
        token_linear(K, I["c_g2_2"][0, 0:P], lambda kt, t0, tn: low[:, 0, t0:t0 + tn], 1, TT,
                     lambda i, at, n, ps: nc.vector.tensor_copy(g[:, i, at:at + n], ps))
        token_linear(K, I["c_g2_2"][0, P:GATE_LORA], lambda kt, t0, tn: low[0:GATE_LORA - P, 1, t0:t0 + tn], 1, TT,
                     lambda i, at, n, ps: nc.vector.tensor_tensor(g[:, i, at:at + n], g[:, i, at:at + n], ps, ALU.add))


def rwkv_factors(K, r, k, sg, a, kk, ar, cl):
    nc = K.nc
    c1, c2 = K.sq[:, :, 0:SEQ], K.xn[:, :, 0:SEQ]
    ch = lambda ap: ap.rearrange("p f (c t) -> p f c t", t=RC)
    squared, made, rooted = K.sig("squared"), K.sig("tile_made"), K.sig("rooted")
    kk_in, cum, cum2, cexp = K.sig("s_ready"), K.sig("exp_asked"), K.sig("pooled"), K.sig("exp_done")
    with nc.Block() as block:
        @block.tensor
        def _(pe):
            pe.wait_ge(*squared.at(1))
            for f in range(KT):
                mm = nc.tensor.matmul(K.ps[:, f // 2, (f % 2) * SEQ:(f % 2 + 1) * SEQ], K.con(C_HEAD), ar[:, f, 0], start=True, stop=True)
            mm.then_inc(*made.one())

        @block.scalar
        def _(act):
            act.wait_ge(*kk_in.at(1))
            nc.scalar.activation(ar[:, :, 0], kk[:], ACT.Square).then_inc(*squared.one())
            act.wait_ge(*made.at(1))
            nc.scalar.activation(ar[:, :, 1], K.ps[:, 0:4].rearrange("p b (f t) -> p (b f) t", f=2), ACT.Sqrt).then_inc(*rooted.one())
            act.wait_ge(*cum.at(1))
            nc.scalar.activation(c2, c1, ACT.Exp).then_inc(*cexp.one())
            nc.scalar.activation(sg[:], sg[:], ACT.Exp).then_inc(*cexp.one())
            link(act, K.act_step, nc.scalar.activation(c1, c1, ACT.Exp, scale=-1.0))
            nc.scalar.copy(cl[:], ch(c2)[:, :, :, RC - 1]).then_inc(*cexp.one())

        @block.vector
        def _(dve):
            v = nc.vector
            do = lambda ins: link(dve, K.dve_step, ins)
            for f in range(KT):
                last = v.tensor_scalar(kk[:, f], k[:, f], K.col("c_k_k_2", f), None, ALU.mult)
            last.then_inc(*kk_in.one())
            for f in range(KT):
                last = v.tensor_scalar(c2[:, f], a[:, f], 1.0, K.col("c_k_a_2", f), ALU.subtract, ALU.mult)
            do(last)
            do(v.scalar_tensor_tensor(out=k[:], in0=c2, scalar=1.0, in1=k[:], op0=ALU.add, op1=ALU.mult))
            do(v.tensor_scalar(sg[:], sg[:], -math.exp(-0.5), None, ALU.mult))
            src, dst = sg[:], c1
            s = 1
            while s < RC:
                v.tensor_copy(ch(dst)[:, :, :, 0:s], ch(src)[:, :, :, 0:s])
                for f in range(KT):
                    last = v.tensor_tensor(ch(dst)[:, f, :, s:], ch(src)[:, f, :, s:], ch(src)[:, f, :, 0:RC - s], ALU.add)
                do(last)
                src, dst = dst, (c2 if dst is c1 else c1)
                s *= 2
            assert src is c1
            v.tensor_tensor(sg[:], c1, sg[:], ALU.subtract).then_inc(*cum.one())
            dve.wait_ge(*rooted.at(1))
            do(v.tensor_scalar(ar[:, :, 1], ar[:, :, 1], 1e-12, None, ALU.max))
            do(v.reciprocal(ar[:, :, 1], ar[:, :, 1]))
            do(v.tensor_tensor(kk[:], kk[:], ar[:, :, 1], ALU.mult))
            do(v.tensor_tensor(a[:], a[:], kk[:], ALU.mult))
            dve.wait_ge(*cexp.at(1))
            do(v.tensor_tensor(ar[:, :, 1], c2, r[:], ALU.mult))
            for f in range(KT):
                last = v.scalar_tensor_tensor(out=r[:, f], in0=r[:, f], scalar=K.col("c_r_k_2", f), in1=k[:, f], op0=ALU.mult, op1=ALU.mult)
            do(last)
            dve.wait_ge(*cexp.at(2))
            v.scalar_tensor_tensor(out=ar[:, :, 0], in0=sg[:], scalar=-1.0, in1=kk[:], op0=ALU.mult, op1=ALU.mult).then_inc(*K.dve_step.one())
            dve.wait_ge(*cexp.at(3))
            v.tensor_tensor(a[:], a[:], c1, ALU.mult).then_inc(*K.dve_step.one())
            do(v.tensor_tensor(k[:], k[:], c1, ALU.mult))
            for f in range(KT):
                end = cl[:, f].rearrange("p (c a) -> p c a", a=1).to_broadcast([P, N_RC, RC])
                v.tensor_tensor(ch(c2)[:, f], ch(a[:])[:, f], end, ALU.mult)
                v.tensor_tensor(ch(kk[:])[:, f], ch(k[:])[:, f], end, ALU.mult)


def rwkv_scores(K, bt, kt, rk, kend, ar, bp, kp, sc, bon):
    nc = K.nc
    bend = K.xn[:, :, 0:SEQ]
    made, taken = K.sig("tile_made"), K.sig("tile_stored")
    with nc.Block() as block:
        @block.tensor
        def _(pe):
            for n in range(8):
                src = (bend, kend)[n // 4]
                t, half = n // 2 % 2, n % 2
                for j in range(4):
                    mm = nc.tensor.transpose(K.ps[:, n, j * P:(j + 1) * P], src[:, 4 * half + j, t * P:(t + 1) * P], K.con(C_ID))
                mm.then_inc(*made.one())
            for u in range(32):
                par, t, f = u // 16, u // 8 % 2, u % 8
                rows = slice(64 * par, 64 * par + 64)
                if u % 4 == 0:
                    pe.wait_ge(*taken.at(u // 4 + 1))
                for c in range(4):
                    tok = slice(t * P + c * RC, t * P + (c + 1) * RC)
                    for j, src in enumerate((bt, kt)):
                        at = (u % 4) * P + j * 2 * RC
                        mm = nc.tensor.matmul(K.ps[RC * c:RC * c + RC, u // 4, at:at + 2 * RC], src[rows, f, tok], ar[rows, f, :, tok],
                                              start=True, stop=True)
                if u % 4 == 3:
                    mm.then_inc(*made.one())
            pe.wait_ge(*taken.at(9))
            for t in range(2):
                for f in range(KT):
                    at = t * RW_HEADS + 2 * f
                    mm = nc.tensor.matmul(K.ps[:, 0, at:at + 2], rk[:, f, t * P:(t + 1) * P], K.con(C_HSEL, 2), start=True, stop=True)
            mm.then_inc(*made.one())

        @block.vector
        def _(dve):
            v = nc.vector
            for n in range(8):
                dve.wait_ge(*made.at(n + 1))
                v.tensor_copy((bp, kp)[n // 4][:, n // 2 % 2, 512 * (n % 2):512 * (n % 2) + 512], K.ps[:, n]).then_inc(*taken.one())
            for b in range(8):
                dve.wait_ge(*made.at(9 + b))
                for j in range(2):
                    mask = sc_mask(K, j)
                    for w in range(2):
                        last = v.tensor_tensor(sc[:, 4 * b:4 * b + 4, 2 * w + j], K.ps[:, b].rearrange("p (u m t) -> p u m t", u=4, m=4)[:, :, 2 * w + j],
                                               mask, ALU.mult)
                last.then_inc(*taken.one())
            dve.wait_ge(*made.at(17))
            v.tensor_copy(bon[:], K.ps[:, 0, 0:2 * RW_HEADS].rearrange("p (t h) -> p t h", t=2))


def sc_mask(K, j):
    return K.con(C_RWK + j * RC, RC).rearrange("p (a t) -> p a t", a=1).to_broadcast([P, 4, RC])


def rwkv_inverse(K, sc, v, tm, nv, scratch, room, room2):
    nc = K.nc
    with ExitStack() as ctx:
        square = lambda ap: ap.rearrange("p (s t) -> p s t", s=RC)
        N, T = square(room[:, 0:RC * RC]), square(room[:, RC * RC:2 * RC * RC])
        prod = square(room2[:, 0:RC * RC])
        out, back = K.sig("inv_out"), K.sig("inv_back")
        solved, made = K.sig("p_ready"), K.sig("tile_made")
        block = ctx.enter_context(nc.Block())

        @block.sync
        def _(sp):
            for c in range(4):
                dst = scratch[0, c * 32:(c + 1) * 32].rearrange("u (s t) -> s u t", s=RC)
                sp.dma_start(dst, sc[c * RC:(c + 1) * RC, :, 0]).then_inc(*out.dma())
            sp.wait_ge(*out.now())
            sp.dma_start(N[:].rearrange("p s t -> p (s t)"), scratch[0]).then_inc(*back.dma())
            sp.wait_ge(*solved.at(1))
            sp.dma_start(scratch[1], prod[:].rearrange("p s t -> p (s t)")).then_inc(*out.dma())
            sp.wait_ge(*out.now())
            for c in range(4):
                src = scratch[1, c * 32:(c + 1) * 32].rearrange("u (s t) -> s u t", s=RC)
                sp.dma_start(tm[c * RC:(c + 1) * RC], src).then_inc(*back.dma())
            sp.wait_ge(*back.now())

        @block.tensor
        def _(pe):
            for t in range(2):
                for par in range(2):
                    for j in range(2):
                        for c in range(4):
                            R = slice(c * RC, (c + 1) * RC)
                            for f in range(KT):
                                h, u = 2 * f + par, par * 16 + t * 8 + f
                                mm = nc.tensor.matmul(K.ps[R, 4 * t + 2 * j + par, f * HD:(f + 1) * HD], sc[R, u, 2 + j],
                                                      v[R, t, h * HD:(h + 1) * HD], start=True, stop=True)
                        mm.then_inc(*made.one())

        @block.scalar
        def _(act):
            n = 0
            for t in range(2):
                for par in range(2):
                    for j in range(2):
                        act.wait_ge(*made.at(n + 1))
                        dst = nv[:, j, t].rearrange("p (f q i) -> p q f i", q=2, i=HD)[:, par]
                        nc.scalar.copy(dst, K.ps[:, 4 * t + 2 * j + par].rearrange("p (f i) -> p f i", i=HD))
                        n += 1

        @block.vector
        def _(dve):
            vv = nc.vector
            do = lambda ins: link(dve, K.dve_step, ins)
            do(vv.memset(T[:], 0.0))
            do(vv.memset(T[:].rearrange("p s t -> p (s t)")[:, 0:RC * RC:RC + 1], 1.0))
            dve.wait_ge(*back.at(16))
            for t in range(1, RC):
                coef = N[:, 0:t, t:t + 1].rearrange("p s a -> p a s").to_broadcast([P, t, t])
                pr = prod[:].rearrange("p s t -> p (s t)")[:, 0:t * t].rearrange("p (c s) -> p c s", s=t)
                do(vv.tensor_tensor(pr, T[:, 0:t, 0:t].rearrange("p s c -> p c s"), coef, ALU.mult))
                do(vv.reduce_sum(T[:, t, 0:t].rearrange("p (c a) -> p c a", a=1), pr, AX))
            vv.tensor_copy(prod[:], T[:].rearrange("p t s -> p s t")).then_inc(*solved.one())


def rwkv_chunks(K, ar, cl, bp, kp, sc, tm, nv, v, y, room, room2):
    nc = K.nc
    with ExitStack() as ctx:
        S, Sd = (room2[:, j * KT * HD:(j + 1) * KT * HD].rearrange("p (f i) -> p f i", i=HD) for j in range(2))
        W, SA = room[:, 0:D], room[:, D:2 * D]
        as_made, w_ready, sa_made, sa_ready = K.sig("s_made"), K.sig("s_ready"), K.sig("e_made"), K.sig("p_ready")
        st_made, st_ready, y_made, y_taken = K.sig("t_made"), K.sig("t_taken"), K.sig("pv_made"), K.sig("o_taken")
        by_par = lambda ap, par: ap.rearrange("p (f q i) -> p q f i", q=2, i=HD)[:, par]
        bank = lambda R, b: K.ps[R, b].rearrange("p (f i) -> p f i", i=HD)
        block = ctx.enter_context(nc.Block())

        @block.tensor
        def _(pe):
            for c in range(N_RC):
                t, R = c // 4, slice((c % 4) * RC, (c % 4 + 1) * RC)
                tok = slice(c * RC, (c + 1) * RC)
                if c:
                    pe.wait_ge(*st_ready.at(c))
                    pe.wait_ge(*y_taken.at(c))
                    for j in range(2):
                        for par in range(2):
                            rows = slice(64 * par, 64 * par + 64)
                            for f in range(KT):
                                mm = nc.tensor.matmul(K.ps[R, 5 * j + par, f * HD:(f + 1) * HD], ar[rows, f, j, tok], S[rows, f],
                                                      start=True, stop=True)
                        if j == 0:
                            mm.then_inc(*as_made.one())
                pe.wait_ge(*w_ready.at(c + 1))
                for par in range(2):
                    for f in range(KT):
                        h, u = 2 * f + par, par * 16 + t * 8 + f
                        mm = nc.tensor.matmul(K.ps[R, 2 + par, f * HD:(f + 1) * HD], tm[R, u], W[R, h * HD:(h + 1) * HD], start=True, stop=True)
                mm.then_inc(*sa_made.one())
                pe.wait_ge(*sa_ready.at(c + 1))
                if c < N_RC - 1:
                    for h in range(RW_HEADS):
                        o = K.ps[64 * (h % 2):64 * (h % 2) + 64, 4, (h // 2) * HD:(h // 2 + 1) * HD]
                        nc.tensor.matmul(o, bp[R, t, h * HD:(h + 1) * HD], SA[R, h * HD:(h + 1) * HD], start=True, stop=False)
                        mm = nc.tensor.matmul(o, kp[R, t, h * HD:(h + 1) * HD], v[R, t, h * HD:(h + 1) * HD], start=False, stop=True)
                    mm.then_inc(*st_made.one())
                for par in range(2):
                    for f in range(KT):
                        h, u = 2 * f + par, par * 16 + t * 8 + f
                        mm = nc.tensor.matmul(K.ps[R, par, f * HD:(f + 1) * HD], sc[R, u, 1], SA[R, h * HD:(h + 1) * HD], start=True, stop=True)
                mm.then_inc(*y_made.one())

        @block.vector
        def _(dve):
            vv = nc.vector
            do = lambda ins: link(dve, K.dve_step, ins)
            for c in range(N_RC):
                t, R = c // 4, slice((c % 4) * RC, (c % 4 + 1) * RC)
                if c:
                    dve.wait_ge(*as_made.at(c))
                    for par in range(2):
                        last = vv.tensor_tensor(by_par(W[R], par), bank(R, par), by_par(nv[R, 0, t], par), ALU.add)
                else:
                    last = vv.tensor_copy(W[R], nv[R, 0, t])
                last.then_inc(*w_ready.one())
                if c:
                    end = cl[:, :, c:c + 1].to_broadcast([P, KT, HD])
                    vv.tensor_tensor(Sd[:], S[:], end, ALU.mult).then_inc(*K.dve_step.one())
                dve.wait_ge(*sa_made.at(c + 1))
                for par in range(2):
                    last = vv.tensor_copy(by_par(SA[R], par), bank(R, 2 + par))
                last.then_inc(*sa_ready.one())
                if c < N_RC - 1:
                    dve.wait_ge(*st_made.at(c + 1))
                    if c:
                        dve.wait_ge(*K.dve_step.now())
                        vv.tensor_tensor(S[:], Sd[:], bank(slice(0, P), 4), ALU.add).then_inc(*st_ready.one())
                    else:
                        vv.tensor_copy(S[:], bank(slice(0, P), 4)).then_inc(*st_ready.one())
                dve.wait_ge(*y_made.at(c + 1))
                for par in range(2):
                    last = vv.tensor_tensor(by_par(y[R, t], par), bank(R, par), by_par(nv[R, 1, t], par), ALU.add)
                if c:
                    do(last)
                    for par in range(2):
                        last = vv.tensor_tensor(by_par(y[R, t], par), bank(R, 5 + par), by_par(y[R, t], par), ALU.add)
                last.then_inc(*y_taken.one())


def rwkv_output(K, y, v, g, bon, ln, tmp):
    nc, I = K.nc, K.ins
    n = 2 * RW_HEADS
    with ExitStack() as ctx:
        def sb(name, shape):
            return ctx.enter_context(nc.sbuf_tensor(name, shape, F32))
        st = sb("rw_st", [P, 4, n, 1])
        given, sq_in, sq_done = K.sig("rows_given"), K.sig("exp_asked"), K.sig("exp_done")
        block = ctx.enter_context(nc.Block())
        heads = lambda ap: ap.rearrange("p (h d) -> p h d", d=HD)
        Y = heads(y[:].rearrange("p t f -> p (t f)"))
        V = heads(v[:].rearrange("p t f -> p (t f)"))
        TMP = heads(tmp[:])
        wide = lambda i: st[:, i].to_broadcast([P, n, HD])

        @block.sync
        def _(sp):
            sp.dma_start(ln[:, 0], I["c_ln_g_2"].to_broadcast([P, D])).then_inc(*given.dma())
            sp.dma_start(ln[:, 1], I["c_ln_b_2"].to_broadcast([P, D])).then_inc(*given.dma())

        @block.scalar
        def _(act):
            act.wait_ge(*sq_in.at(1))
            nc.scalar.activation(TMP, Y, ACT.Square).then_inc(*sq_done.one())
            act.wait_ge(*sq_in.at(2))
            nc.scalar.activation(st[:, 2], st[:, 1], ACT.Sqrt, bias=K.eps[:, 2:3], scale=1.0 / HD).then_inc(*sq_done.one())

        @block.vector
        def _(dve):
            vv = nc.vector
            do = lambda ins: link(dve, K.dve_step, ins)
            do(vv.reduce_sum(st[:, 0], Y, AX))
            do(vv.tensor_scalar(st[:, 0], st[:, 0], 1.0 / HD, None, ALU.mult))
            vv.tensor_tensor(Y, Y, wide(0), ALU.subtract).then_inc(*sq_in.one())
            dve.wait_ge(*sq_done.at(1))
            vv.reduce_sum(st[:, 1], TMP, AX).then_inc(*sq_in.one())
            dve.wait_ge(*sq_done.at(2))
            do(vv.reciprocal(st[:, 3], st[:, 2]))
            do(vv.tensor_tensor(Y, Y, wide(3), ALU.mult))
            dve.wait_ge(*given.at(32))
            for j, op in ((0, ALU.mult), (1, ALU.add)):
                row = ln[:, j:j + 1].to_broadcast([P, 2, D])
                do(vv.tensor_tensor(y[:], y[:], row, op))
            do(vv.tensor_tensor(TMP, V, bon[:].rearrange("p t (h a) -> p (t h) a", a=1).to_broadcast([P, n, HD]), ALU.mult))
            do(vv.tensor_tensor(Y, Y, TMP, ALU.add))
            do(vv.tensor_tensor(y[:], y[:], g[:], ALU.mult))


def second_block(K, scratch):
    H, X = K.h[:, :, 0:SEQ], K.xn[:, :, 0:SEQ]
    for layer in range(2):
        gain = lambda j: K.col("norm_gains_2", (6 * layer + j) * KT, KT)
        ffn(K, *[K.ins[f"ffn1_w_{w}_2"][layer] for w in ("gate", "up", "down")], gain(0), gain(1))
        rms_norm(K, H, X, gain(2))
        if layer == 0:
            nsa_ssd(K)
        else:
            rwkv(K, scratch)
        rms_norm(K, X, X, gain(3), add_to=H)
        ffn(K, *[K.ins[f"ffn2_w_{w}_2"][layer] for w in ("gate", "up", "down")], gain(4), gain(5))


def token_model_kernel(nc, ins, out, gates_dram, scratch):
    K = Core(nc, ins)
    load_all(K)
    first_block(K, gates_dram)
    second_block(K, scratch)
    store_tokens(K, out)


def first_block(K, gates_dram):
    rms_norm(K, K.h[:], K.xn, K.col("a_norm", 0, KT))
    pool_mixer(K)
    rms_norm(K, K.h[:], K.xn, K.col("ffn_norm", 0, KT))
    moe(K, 0, gates_dram)
    with ExitStack() as ctx:
        kv = latent_kv(K, ctx)
        mla(K, kv)
    rms_norm(K, K.h[:], K.xn, K.col("ffn_norm", KT, KT))
    moe(K, 1, gates_dram)
    final_norm(K)


INS = ["x", "meta_tokens", "a_norm", "a_w", "a_scale", "b_norm", "b_w_dq", "b_q_norm", "b_w_uq", "b_w_o", "kv_norm",
       "w_dkv", "kv_lat_norm", "w_uk", "w_uv", "ffn_norm", "router_g", "router_g_bias", "router_e", "router_e_bias",
       "w_gate", "w_up", "w_down", "final_norm", "norm_gains_2", "ffn1_w_gate_2", "ffn1_w_up_2", "ffn1_w_down_2",
       "ffn2_w_gate_2", "ffn2_w_up_2", "ffn2_w_down_2", "ab_w_in_2", "a_cmp_pe_k_2", "a_cmp_w1_k_2", "a_cmp_w2_k_2",
       "a_cmp_pe_v_2", "a_cmp_w1_v_2", "a_cmp_w2_v_2", "b_conv_w_2", "b_conv_b_2", "b_dt_bias_2", "b_a_log_2",
       "b_d_skip_2", "b_norm_w_2", "ab_w_out_2", "c_mu_2", "c_w_r_2", "c_w_k_2", "c_w_v_2", "c_w_o_2", "c_w0_2",
       "c_w1_2", "c_w2_2", "c_a0_2", "c_a1_2", "c_a2_2", "c_g1_2", "c_g2_2", "c_k_k_2", "c_k_a_2", "c_r_k_2",
       "c_ln_g_2", "c_ln_b_2"]


def kernel(**inputs):
    import concourse.bacc as bacc
    from concourse.bass_utils import run_bass_kernel_spmd

    nc = bacc.Bacc("TRN2", target_bir_lowering=False, num_devices=1)
    arrays = {f"in_{n}": np.ascontiguousarray(inputs[n]) for n in INS}
    arrays["in_constants"] = constants()
    ins = {n[3:]: nc.dram_tensor(n, a.shape, F32, kind="ExternalInput").ap() for n, a in arrays.items()}
    out = nc.dram_tensor("out", (1, SEQ, D), F32, kind="ExternalOutput").ap()
    gates = nc.dram_tensor("gates", (N_EXP, L1), F32, kind="Internal").ap()
    scratch = nc.dram_tensor("scratch", (2, P, RC * RC), F32, kind="Internal").ap()
    token_model_kernel(nc, ins, out, gates, scratch)
    result = run_bass_kernel_spmd(nc, [arrays], core_ids=[0])
    return result.results[0]["out"]
```

```python
import math
from contextlib import ExitStack

import numpy as np
import concourse.bass as bass
from concourse import mybir

F32 = mybir.dt.float32
ALU = mybir.AluOpType
ACT = mybir.ActivationFunctionType
AX = mybir.AxisListType.X

P = 128
D = 1024
KT = D // P
SEQ = 256
N_META = 16
L1 = SEQ + N_META
Q_TILES_1 = [(0, 128), (128, 128), (256, 16)]
NEG = -1e30
EPS = [1e-6, 1e-5, 64e-5, 4e-6]

POOL_G = 4
POOL_WINDOWS = (2, 4, 8, 16)
HEADS = 8
NOPE = 128
ROPE = 64
V_DIM = 128
Q_LORA = 384
KV_LORA = 256
MLA_SCALE = (NOPE + ROPE) ** -0.5
N_GROUPS = 4
PER_GROUP = 8
N_EXP = N_GROUPS * PER_GROUP
D_EXP = 256
CAP = 32

D_FF = 2816
FF_T = D_FF // P
GU_COLS = 256
NSA_KV = 2
NSA_GROUP = 4
HD = 64
CMP_BLOCK = 32
CMP_STRIDE = 16
N_CMP = (SEQ - CMP_BLOCK) // CMP_STRIDE + 1
SSD_HEADS = 16
SSD_GROUPS = 2
SSD_STATE = 128
SSD_CONV = 4
SSD_INNER = 1024
XBC = SSD_INNER + 2 * SSD_GROUPS * SSD_STATE
SPLITS = (512, 128, 128, 128, 128, 128, 128, 24, SSD_INNER, XBC, SSD_HEADS)
OFF = [sum(SPLITS[:i]) for i in range(len(SPLITS) + 1)]
RW_HEADS = 16
RC = 32
N_RC = SEQ // RC
GATE_LORA = 160

C_ID, C_ONE, C_CAUSAL, C_TRI, C_ROT, C_HEAD = 0, 128, 256, 384, 512, 640
C_COS, C_SIN = 768, 768 + L1
C_CNT = C_SIN + L1
C_CMPM = C_CNT + 4 * L1
C_RWK = C_CMPM + 2 * (N_CMP + 1)
C_IOTA = C_RWK + 2 * RC
C_HSEL = C_IOTA + 8
C_TRI1 = C_HSEL + 2
C_SLOT = C_TRI1 + P
C_END = C_SLOT + CAP


def constants():
    c = np.zeros((P, C_END), np.float32)
    p = np.arange(P)
    c[:, C_ID:C_ID + P] = np.eye(P)
    c[:, C_ONE:C_ONE + P] = 1.0
    c[:, C_CAUSAL:C_CAUSAL + P] = np.where(p[None, :] <= p[:, None], 0.0, NEG)
    c[:, C_TRI:C_TRI + P] = p[:, None] <= p[None, :]
    for m in range(P):
        if m % 64 < 32:
            c[m + 32, C_ROT + m] = -1.0
        else:
            c[m - 32, C_ROT + m] = 1.0
    c[:, C_HEAD:C_HEAD + P] = (p[:, None] // 64) == (p[None, :] // 64)
    inv = (np.float32(10000.0) ** (-np.arange(0, ROPE, 2, dtype=np.float32) / np.float32(ROPE))).astype(np.float32)
    ang = (np.arange(L1, dtype=np.float32)[None, :] * inv[p % 32][:, None]).astype(np.float32)
    c[:, C_COS:C_COS + L1] = np.cos(ang)
    c[:, C_SIN:C_SIN + L1] = np.sin(ang)
    t = np.arange(L1)
    for g, w in enumerate(POOL_WINDOWS):
        c[:, C_CNT + g * L1:C_CNT + (g + 1) * L1] = 1.0 / np.minimum(t + 1, w).astype(np.float32)
    for i in range(2):
        for n in range(N_CMP):
            c[:, C_CMPM + i * (N_CMP + 1) + n] = (n * CMP_STRIDE + CMP_BLOCK - 1) <= (p + i * P)
    tc = np.arange(RC)
    c[:, C_RWK:C_RWK + RC] = (p[:, None] % RC) < tc[None, :]
    c[:, C_RWK + RC:C_RWK + 2 * RC] = (p[:, None] % RC) <= tc[None, :]
    c[:, C_IOTA:C_IOTA + 8] = 8.0 - np.arange(8)
    c[:, C_HSEL:C_HSEL + 2] = (p[:, None] // 64) == np.arange(2)[None, :]
    c[:, C_TRI1:C_TRI1 + P] = p[:, None] < p[None, :]
    c[:, C_SLOT:C_SLOT + CAP] = np.arange(CAP)
    return c


VECTORS = [("a_norm", 8), ("a_scale", 8), ("b_norm", 8), ("kv_norm", 8), ("ffn_norm", 16), ("final_norm", 8),
           ("norm_gains_2", 96), ("c_mu_2", 48), ("c_w0_2", 8), ("c_a0_2", 8), ("c_k_k_2", 8), ("c_k_a_2", 8),
           ("c_r_k_2", 8), ("kv_lat_norm", 2), ("b_q_norm", 3), ("b_conv_w_2", 48), ("b_conv_b_2", 12)]
VEC_AT = {}
_n = 0
for _name, _rows in VECTORS:
    VEC_AT[_name] = _n
    _n += _rows
VEC_ROWS = _n
VEC_TILES = -(-VEC_ROWS // P)


class Signal:

    def __init__(self, nc, name):
        self.sem = nc.alloc_semaphore(name)
        self.given = self.base = 0

    def begin(self):
        self.base = self.given
        return self

    def at(self, n):
        return self.sem, self.base + n

    def one(self):
        self.given += 1
        return self.sem, 1

    def dma(self):
        self.given += 16
        return self.sem, 16

    def now(self):
        return self.sem, self.given


class Core:

    def __init__(self, nc, ins):
        self.nc, self.ins = nc, ins
        self.signals, self.stage = {}, 0
        self.coming = None
        self.ring = 0
        self.free = {}
        self.h = nc.alloc_sbuf_tensor("h", [P, KT, L1], F32)
        self.xn = nc.alloc_sbuf_tensor("xn", [P, KT, L1], F32)
        self.sq = nc.alloc_sbuf_tensor("sq", [P, KT, L1], F32)
        self.rs = nc.alloc_sbuf_tensor("rs", [P, 3, L1], F32)
        self.cst = nc.alloc_sbuf_tensor("cst", [P, C_END], F32)
        self.vec = nc.alloc_sbuf_tensor("vec", [P, VEC_TILES * P], F32)
        self.w = nc.alloc_sbuf_tensor("w", [P, 2, 4096], F32)
        self.ps = nc.alloc_psum_tensor("ps", [P, 8, 512], F32)
        self.eps = nc.alloc_sbuf_tensor("eps", [P, len(EPS)], F32)
        self.loaded = [Signal(nc, f"w_loaded_{s}") for s in range(2)]
        self.dve_step, self.act_step = Signal(nc, "dve_step"), Signal(nc, "act_step")

    def sig(self, name):
        if name not in self.signals:
            self.signals[name] = Signal(self.nc, name)
        return self.signals[name].begin()

    def next(self):
        self.stage += 1
        return self.stage

    def fullest(self, engine, count):
        return engine.value_load(count[0:1, 0:1], min_val=0, max_val=L1)

    def con(self, at, n=P):
        return self.cst[:, at:at + n]

    def col(self, name, i=0, n=1):
        at = VEC_AT[name] + i
        return self.vec[:, at:at + n]


def load_ahead(K, block):
    if K.coming is not None:
        @block.sync
        def _(sp):
            K.coming.ahead(sp)


def link(eng, signal, instruction):
    instruction.then_inc(*signal.one())
    eng.wait_ge(*signal.now())


def rms_norm(K, src, dst, gain, eps=1e-6, add_to=None, factor=1.0):
    nc = K.nc
    n, T = src.shape[1], src.shape[2]
    grow = factor ** -2
    squared_a, squared_v = K.sig("squared"), K.sig("squared_v")
    summed, rooted, scaled, inverse = K.sig("summed"), K.sig("rooted"), K.sig("scaled"), K.sig("inverse")
    with nc.Block() as block:
        load_ahead(K, block)

        @block.tensor
        def _(pe):
            for k in range(n):
                pe.wait_ge(*(squared_a, squared_v)[k % 2].at(k // 2 + 1))
                mm = nc.tensor.matmul(K.ps[:, 0, 0:T], K.con(C_ONE), K.sq[:, k, 0:T], start=k == 0, stop=k == n - 1)
            mm.then_inc(*summed.one())

        @block.scalar
        def _(act):
            for k in range(0, n, 2):
                nc.scalar.activation(K.sq[:, k, 0:T], src[:, k], ACT.Square).then_inc(*squared_a.one())
            act.wait_ge(*squared_v.at(n // 2))
            if dst is src:
                act.wait_ge(*squared_a.at((n + 1) // 2))
            for k in range(n):
                last = nc.scalar.activation(dst[:, k], src[:, k], ACT.Copy, scale=gain[:, k:k + 1])
            last.then_inc(*scaled.one())
            act.wait_ge(*summed.at(1))
            nc.scalar.activation(K.rs[:, 0, 0:T], K.ps[:, 0, 0:T], ACT.Sqrt, bias=K.eps[:, EPS.index(grow * eps):EPS.index(grow * eps) + 1],
                                 scale=grow / (n * P)).then_inc(*rooted.one())

        @block.vector
        def _(dve):
            for k in range(1, n, 2):
                nc.vector.tensor_tensor(K.sq[:, k, 0:T], src[:, k], src[:, k], ALU.mult).then_inc(*squared_v.one())
            dve.wait_ge(*rooted.at(1))
            link(dve, K.dve_step, nc.vector.reciprocal(K.rs[:, 1, 0:T], K.rs[:, 0, 0:T]))
            dve.wait_ge(*scaled.at(1))
            last = nc.vector.tensor_tensor(dst, dst, K.rs[:, 1:2, 0:T].to_broadcast([P, n, T]), ALU.mult)
            if add_to is not None:
                link(dve, K.dve_step, last)
                nc.vector.tensor_tensor(add_to, add_to, dst, ALU.add)


class Linear:

    def __init__(self, w, x, store, T=None, tiles=None, by="vector", pieces=None, after=None, onto=None):
        self.w, self.x, self.store, self.T, self.token_tiles, self.by, self.after, self.onto = w, x, store, T, tiles, by, after, onto
        rows, N = w.shape
        self.kr = min(rows, P)
        self.nk = rows // self.kr
        self.view = w.rearrange("(k p) n -> p k n", p=self.kr)
        wide = 512 if tiles else min(4096 // self.nk // P * P, 512)
        self.loads = [(c, min(wide, N - c)) for c in range(0, N, wide)]
        self.pieces = pieces

    def outputs(self, b):
        cw = self.loads[b][1]
        if self.token_tiles:
            return [(0, cw, i) for i in range(len(self.token_tiles))]
        return [(at, min(P, cw - at), None) for at in range(0, cw, P)]


class Linears:

    def __init__(self, K, group):
        self.K, self.group, self.issued, self.ready = K, group, 0, []
        self.loads = [(g, b) for g in group for b in range(len(g.loads))]
        self.first = K.ring
        K.ring += len(self.loads)
        self.loaded = K.loaded

    def load(self, sp, i):
        g, b = self.loads[i]
        slot = (self.first + i) % 2
        c, cw = g.loads[b]
        room = self.K.w[0:g.kr, slot, 0:g.nk * cw].rearrange("p (k n) -> p k n", k=g.nk)
        with self.K.nc.allow_non_contiguous_dma(reason="some matrices have few columns"):
            for to, at, n in g.pieces or [(0, c, cw)]:
                sp.dma_start(room[:, :, to:to + n], g.view[:, :, at:at + n]).then_inc(*self.loaded[slot].dma())
        self.ready.append(self.loaded[slot].now())
        self.issued += 1

    def ahead(self, sp):
        for i in range(self.issued, min(2, len(self.loads))):
            free = self.K.free.pop((self.first + i) % 2, None)
            if free is not None:
                sp.wait_ge(*free)
            self.load(sp, i)

    def run(self, before={}):
        K, nc = self.K, self.K.nc
        made = K.sig("lin_made")
        stored = {"vector": K.sig("lin_stored_v"), "scalar": K.sig("lin_stored_s")}
        tiles, upto = [], []
        for i, (g, b) in enumerate(self.loads):
            tiles += [(i, o) for o in g.outputs(b)]
            upto.append(len(tiles))
        given = {"vector": 0, "scalar": 0}
        store_at, done = [], {}
        for i, o in tiles:
            g = self.loads[i][0]
            given[g.by] += 1
            store_at.append(stored[g.by].at(given[g.by]))
            done[id(g)] = store_at[-1]
        if K.coming is self:
            K.coming = None

        with nc.Block() as block:
            @block.sync
            def _(sp):
                self.ahead(sp)
                for i in range(self.issued, len(self.loads)):
                    sp.wait_ge(*made.at(upto[i - 2]))
                    self.load(sp, i)
                for i in range(max(0, len(self.loads) - 2), len(self.loads)):
                    K.free[(self.first + i) % 2] = made.at(upto[i])
                if K.coming is not None:
                    K.coming.ahead(sp)

            @block.tensor
            def _(pe):
                before.get("tensor", lambda pe: None)(pe)
                seen = set()
                for n, (i, (at, cw, tile)) in enumerate(tiles):
                    g, b = self.loads[i]
                    wide = g.loads[b][1]
                    if i not in seen:
                        seen.add(i)
                        pe.wait_ge(*self.ready[i])
                        if g.after is not None:
                            pe.wait_ge(*done[id(g.after)])
                    if n >= 8:
                        pe.wait_ge(*store_at[n - 8])
                    for k in range(g.nk):
                        wk = K.w[0:g.kr, (self.first + i) % 2, k * wide + at:k * wide + at + cw]
                        if g.token_tiles:
                            t0, tn = g.token_tiles[tile]
                            mm = nc.tensor.matmul(K.ps[0:tn, n % 8, 0:cw], g.x(k, t0, tn), wk, start=k == 0, stop=k == g.nk - 1)
                        else:
                            mm = nc.tensor.matmul(K.ps[0:cw, n % 8, 0:g.T], wk, g.x(k), start=k == 0, stop=k == g.nk - 1)
                    mm.then_inc(*made.one())

            def take(eng, by):
                for n, (i, (at, cw, tile)) in enumerate(tiles):
                    g, b = self.loads[i]
                    if g.by != by:
                        continue
                    if g.onto is not None:
                        eng.wait_ge(*done[id(g.onto)])
                    eng.wait_ge(*made.at(n + 1))
                    c = g.loads[b][0]
                    if g.token_tiles:
                        last = g.store(tile, c, cw, K.ps[0:g.token_tiles[tile][1], n % 8, 0:cw])
                    else:
                        last = g.store((c + at) // P, K.ps[0:cw, n % 8, 0:g.T])
                    last.then_inc(*stored[by].one())

            @block.vector
            def _(dve):
                before.get("vector", lambda dve: None)(dve)
                take(dve, "vector")

            @block.scalar
            def _(act):
                before.get("scalar", lambda act: None)(act)
                take(act, "scalar")


def load_all(K):
    nc, I = K.nc, K.ins
    with ExitStack() as ctx:
        rows = ctx.enter_context(nc.sbuf_tensor("vec_rows", [P, VEC_TILES, P], F32))
        tok = ctx.enter_context(nc.sbuf_tensor("tok_rows", [P, 3, D], F32))
        given, blank = K.sig("rows_given"), K.sig("rows_blank")
        made, stored = K.sig("tile_made"), K.sig("tile_stored")
        n_dma = 16 * (1 + 2 + len(VECTORS) + 2)
        pieces = []
        for name, n in VECTORS:
            flat = I[name]
            dims = " ".join(f"a{i}" for i in range(len(flat.shape)))
            flat = flat.rearrange(f"{dims} -> ({dims})").rearrange("(r c) -> r c", c=P)
            at, done = VEC_AT[name], 0
            while done < n:
                take = min(n - done, P - (at + done) % P)
                pieces.append(((at + done) // P, (at + done) % P, take, flat[done:done + take]))
                done += take
        block = ctx.enter_context(nc.Block())

        @block.sync
        def _(sp):
            sp.dma_start(K.cst[:], I["constants"]).then_inc(*given.dma())
            sp.dma_start(tok[0:N_META, 0], I["meta_tokens"]).then_inc(*given.dma())
            sp.dma_start(tok[N_META:P, 0], I["x"][0, 0:P - N_META]).then_inc(*given.dma())
            sp.dma_start(tok[:, 1], I["x"][0, P - N_META:2 * P - N_META]).then_inc(*given.dma())
            sp.dma_start(tok[0:N_META, 2], I["x"][0, 2 * P - N_META:SEQ]).then_inc(*given.dma())
            sp.wait_ge(*blank.at(1))
            for tile, row, n, src in pieces:
                sp.dma_start(rows[row:row + n, tile], src).then_inc(*given.dma())

        @block.vector
        def _(dve):
            for i, e in enumerate(EPS):
                nc.vector.memset(K.eps[:, i:i + 1], e)
            nc.vector.memset(rows[:], 0.0).then_inc(*blank.one())
            for n in range(VEC_TILES + 2 * 3):
                dve.wait_ge(*made.at(n + 1))
                if n < VEC_TILES:
                    last = nc.vector.tensor_copy(K.vec[:, n * P:(n + 1) * P], K.ps[:, n % 8, 0:P])
                else:
                    i, half = divmod(n - VEC_TILES, 2)
                    t0, tn = Q_TILES_1[i]
                    last = nc.vector.tensor_copy(K.h[:, 4 * half:4 * half + 4, t0:t0 + tn],
                                                 K.ps[:, n % 8, :].rearrange("p (k t) -> p k t", k=4)[:, :, 0:tn])
                last.then_inc(*stored.one())

        @block.tensor
        def _(pe):
            pe.wait_ge(*given.now())
            n = 0
            for i in range(VEC_TILES):
                nc.tensor.transpose(K.ps[:, n % 8, 0:P], rows[:, i], K.con(C_ID)).then_inc(*made.one())
                n += 1
            for i, (t0, tn) in enumerate(Q_TILES_1):
                for half in range(2):
                    if n >= 8:
                        pe.wait_ge(*stored.at(n - 7))
                    for k in range(4):
                        mm = nc.tensor.transpose(K.ps[:, n % 8, k * P:k * P + tn],
                                                 tok[0:tn, i, (4 * half + k) * P:(4 * half + k + 1) * P],
                                                 K.cst[0:tn, C_ID:C_ID + tn])
                    mm.then_inc(*made.one())
                    n += 1


def pool_mixer(K):
    nc, I = K.nc, K.ins
    gt = KT // POOL_G
    with ExitStack() as ctx:
        pad = max(POOL_WINDOWS)
        run = ctx.enter_context(nc.sbuf_tensor("run", [P, 2, KT, pad + L1], F32))
        wg = ctx.enter_context(nc.sbuf_tensor("pool_w", [P, POOL_G * gt, gt * P], F32))
        given, pooled = K.sig("rows_given"), K.sig("pooled")
        made, stored = K.sig("tile_made"), K.sig("tile_stored")
        block = ctx.enter_context(nc.Block())

        @block.sync
        def _(sp):
            sp.dma_start(wg[:], I["a_w"][0].rearrange("g (k p) n -> p (g k) n", p=P)).then_inc(*given.dma())

        @block.vector
        def _(dve):
            nc.vector.memset(run[:, :, :, 0:pad], 0.0)
            link(dve, K.dve_step, nc.vector.tensor_copy(run[:, 0, :, pad:], K.xn[:]))
            at = [0, 0, 0, 0]
            src, width = 0, 1
            for g, w in enumerate(POOL_WINDOWS):
                lo = g * gt
                link(dve, K.dve_step, nc.vector.tensor_tensor(
                    run[:, 1 - src, lo:, pad:], run[:, src, lo:, pad:], run[:, src, lo:, pad - width:pad - width + L1], ALU.add))
                src, width = 1 - src, w
                at[g] = src
                for k in range(lo, lo + gt):
                    link(dve, K.dve_step, nc.vector.tensor_tensor(K.sq[:, k], run[:, src, k, pad:],
                                                                  K.con(C_CNT + g * L1, L1), ALU.mult))
                last = nc.vector.tensor_tensor(K.sq[:, lo:lo + gt], K.sq[:, lo:lo + gt], K.xn[:, lo:lo + gt], ALU.subtract)
                last.then_inc(*pooled.one())
            for m in range(KT):
                dve.wait_ge(*made.at(m + 1))
                nc.vector.scalar_tensor_tensor(out=K.h[:, m], in0=K.ps[:, m, 0:L1], scalar=K.col("a_scale", m),
                                               in1=K.h[:, m], op0=ALU.mult, op1=ALU.add)

        @block.tensor
        def _(pe):
            pe.wait_ge(*given.at(16))
            for g in range(POOL_G):
                pe.wait_ge(*pooled.at(g + 1))
                for m in range(gt):
                    for k in range(gt):
                        mm = nc.tensor.matmul(K.ps[:, g * gt + m, 0:L1], wg[:, g * gt + k, m * P:(m + 1) * P], K.sq[:, g * gt + k],
                                              start=k == 0, stop=k == gt - 1)
                    mm.then_inc(*made.one())


def first_of(dve, K, mask, score, top):
    nc, n = K.nc, mask.shape[2]
    iota = K.con(C_IOTA + 8 - n, n).rearrange("p (a n) -> p a n", a=1).to_broadcast([P, 3, n])
    link(dve, K.dve_step, nc.vector.tensor_tensor(score, mask, iota, ALU.mult))
    link(dve, K.dve_step, nc.vector.reduce_max(top, score, AX))
    link(dve, K.dve_step, nc.vector.tensor_tensor(mask, score, top.to_broadcast([P, 3, n]), ALU.is_equal))


def moe(K, layer, gates_dram):
    nc, I = K.nc, K.ins
    nr = N_GROUPS + N_EXP
    ET = D_EXP // P
    with ExitStack() as ctx:
        def sb(name, shape, dt=F32):
            return ctx.enter_context(nc.sbuf_tensor(f"{name}_{layer}", shape, dt))
        gate = sb("gate", [P, 3, N_EXP])
        count = sb("count", [1, 1], mybir.dt.int32)
        xg = sb("xg", [P, KT, N_EXP * CAP])
        spread = sb("spread", [P, N_EXP * CAP // P, L1])
        wd = sb("wd", [P, 4, ET, D])
        wgu = [K.w[:, j].rearrange("p (a k n) -> p a k n", a=2, k=KT) for j in range(2)]
        more = sb("wgu", [P, 2, 2, KT, D_EXP])
        wgu += [more[:, j] for j in range(2)]
        w_in = [K.sig(f"expert_w_{j}_{layer}") for j in range(4)]
        views = [I[n][layer].rearrange("e (k p) n -> p e k n", p=P) for n in ("w_gate", "w_up", "w_down")]

        def load_expert(sp, e, j):
            one = bass.ds(e, 1)
            sp.dma_start(wgu[j][:, 0], views[0][:, one]).then_inc(w_in[j].sem, 16)
            sp.dma_start(wgu[j][:, 1], views[1][:, one]).then_inc(w_in[j].sem, 16)
            sp.dma_start(wd[:, j], views[2][:, one]).then_inc(w_in[j].sem, 16)
        with ExitStack() as inner:
            route(K, layer, inner, gate, count, xg, spread, load_expert)
        with ExitStack() as inner:
            over_all = experts_over_all(K, layer, inner, gates_dram, gate, wgu, wd, w_in)
            in_slots = experts_in_slots(K, layer, inner, xg, spread, wgu, wd, w_in, load_expert)
            block = inner.enter_context(nc.Block())

            @block.sync
            def _(sp):
                with sp.If(K.fullest(sp, count) > CAP):
                    over_all["sync"](sp)
                with sp.Else():
                    in_slots["sync"](sp)

            @block.tensor
            def _(pe):
                with pe.If(K.fullest(pe, count) > CAP):
                    over_all["tensor"](pe)
                with pe.Else():
                    in_slots["tensor"](pe)

            @block.scalar
            def _(act):
                with act.If(K.fullest(act, count) > CAP):
                    over_all["scalar"](act)
                with act.Else():
                    in_slots["scalar"](act)

            @block.vector
            def _(dve):
                with dve.If(K.fullest(dve, count) > CAP):
                    over_all["vector"](dve)
                with dve.Else():
                    in_slots["vector"](dve)

            @block.gpsimd
            def _(pool):
                with pool.If(K.fullest(pool, count) <= CAP):
                    in_slots["gpsimd"](pool)


def route(K, layer, ctx, gate, count, xg, spread, load_expert):
    nc, I = K.nc, K.ins
    nr = N_GROUPS + N_EXP
    SG = N_EXP * CAP // P
    def sb(name, shape):
        return ctx.enter_context(nc.sbuf_tensor(f"{name}_{layer}", shape, F32))
    wr = sb("wr", [P, KT, nr])
    bias = sb("rbias", [P, nr])
    lg = sb("lg", [P, 3, nr])
    small = sb("small", [P, 3, 64])
    mask, pos = sb("mask", [P, 3, N_EXP]), sb("pos", [P, 3, N_EXP])
    xt = sb("xt", [P, 3, D])
    sel = sb("sel", [P, 3, N_EXP * CAP])
    given, logits, routed = K.sig("rows_given"), K.sig("logits"), K.sig("routed")
    ex, exd = K.sig("exp_asked"), K.sig("exp_done")
    x_turned, x_taken, placed = K.sig("t_made"), K.sig("t_taken"), K.sig("placed")
    chosen, sel_made, made, taken_v, taken_s = (K.sig(n) for n in ("chosen", "sel_made", "tile_made", "taken_v", "taken_s"))
    s_turned, gated = K.sig("s_turned"), K.sig("gated")
    with nc.Block() as block:
        @block.sync
        def _(sp):
            with nc.allow_non_contiguous_dma(reason="router columns are narrow"):
                sp.dma_start(wr[:, :, 0:N_GROUPS], I["router_g"][layer].rearrange("(k p) n -> p k n", p=P)).then_inc(*given.dma())
                sp.dma_start(wr[:, :, N_GROUPS:], I["router_e"][layer].rearrange("(k p) n -> p k n", p=P)).then_inc(*given.dma())
                sp.dma_start(bias[:, 0:N_GROUPS], I["router_g_bias"][layer:layer + 1].to_broadcast([P, N_GROUPS])).then_inc(*given.dma())
                sp.dma_start(bias[:, N_GROUPS:], I["router_e_bias"][layer:layer + 1].to_broadcast([P, N_EXP])).then_inc(*given.dma())
            for j in range(4):
                load_expert(sp, j, j)

        @block.tensor
        def _(pe):
            for n in range(6):
                i, half = divmod(n, 2)
                t0, tn = Q_TILES_1[i]
                for k in range(4):
                    mm = nc.tensor.transpose(K.ps[0:tn, n, k * P:(k + 1) * P], K.xn[:, 4 * half + k, t0:t0 + tn], K.con(C_ID))
                mm.then_inc(*x_turned.one())
            pe.wait_ge(*given.at(64))
            for i, (t0, tn) in enumerate(Q_TILES_1):
                for k in range(KT):
                    mm = nc.tensor.matmul(K.ps[0:tn, 6, i * nr:(i + 1) * nr], K.xn[:, k, t0:t0 + tn], wr[:, k], start=k == 0, stop=k == KT - 1)
            mm.then_inc(*logits.one())
            pe.wait_ge(*chosen.at(1))
            for i, (t0, tn) in enumerate(Q_TILES_1):
                for j in range(i + 1):
                    kn_ = Q_TILES_1[j][1]
                    before = K.cst[0:kn_, C_TRI1:C_TRI1 + tn] if j == i else K.cst[0:kn_, C_ONE:C_ONE + tn]
                    nc.tensor.matmul(K.ps[0:tn, 7, i * N_EXP:(i + 1) * N_EXP], before, mask[0:kn_, j], start=j == 0, stop=j == i)
            for j, (t0, kn_) in enumerate(Q_TILES_1):
                mm = nc.tensor.matmul(K.ps[0:1, 7, 3 * N_EXP:4 * N_EXP], K.cst[0:kn_, C_ONE:C_ONE + 1], mask[0:kn_, j], start=j == 0, stop=j == 2)
            mm.then_inc(*placed.one())
            pe.wait_ge(*x_taken.at(2))
            pe.wait_ge(*sel_made.at(1))
            for n in range(2 * KT):
                k, half = divmod(n, 2)
                if n >= 8:
                    pe.wait_ge(*(taken_v, taken_s)[n % 2].at((n - 8) // 2 + 1))
                for i, (t0, tn) in enumerate(Q_TILES_1):
                    mm = nc.tensor.matmul(K.ps[:, n % 8, :], xt[0:tn, i, k * P:(k + 1) * P], sel[0:tn, i, half * 512:(half + 1) * 512],
                                          start=i == 0, stop=i == 2)
                mm.then_inc(*made.one())
            pe.wait_ge(*gated.at(1))
            for s in range(SG):
                if s % 2 == 0:
                    pe.wait_ge(*taken_v.at(4 + s // 2 + 1))
                else:
                    pe.wait_ge(*taken_s.at(4 + s // 2 + 1))
                for i, (t0, tn) in enumerate(Q_TILES_1):
                    mm = nc.tensor.transpose(K.ps[:, s, t0:t0 + tn], sel[0:tn, i, s * P:(s + 1) * P], K.cst[0:tn, C_ID:C_ID + tn])
                mm.then_inc(*s_turned.one())

        @block.scalar
        def _(act):
            for i in range(3):
                act.wait_ge(*x_turned.at(2 * i + 2))
                tn = Q_TILES_1[i][1]
                last = nc.scalar.copy(xt[0:tn, i, 512:], K.ps[0:tn, 2 * i + 1])
            last.then_inc(*x_taken.one())
            act.wait_ge(*ex.at(1))
            nc.scalar.activation(small[:, :, 4:8], small[:, :, 0:4], ACT.Exp).then_inc(*exd.one())
            act.wait_ge(*ex.at(2))
            nc.scalar.activation(small[:, :, 57:58], small[:, :, 56:57], ACT.Exp).then_inc(*exd.one())
            for k in range(KT):
                act.wait_ge(*made.at(2 * k + 2))
                nc.scalar.copy(xg[:, k, 512:], K.ps[:, (2 * k + 1) % 8]).then_inc(*taken_s.one())
            for s in range(1, SG, 2):
                act.wait_ge(*s_turned.at(s + 1))
                nc.scalar.copy(spread[:, s], K.ps[:, s, 0:L1])

        @block.vector
        def _(dve):
            def do(ins):
                link(dve, K.dve_step, ins)
            v = nc.vector
            S = lambda a, b: small[:, :, a:b]
            v.memset(mask[:], 0.0)
            do(v.memset(lg[:], 0.0))
            for i in range(3):
                dve.wait_ge(*x_turned.at(2 * i + 1))
                tn = Q_TILES_1[i][1]
                last = v.tensor_copy(xt[0:tn, i, 0:512], K.ps[0:tn, 2 * i])
            last.then_inc(*x_taken.one())
            dve.wait_ge(*given.at(64))
            dve.wait_ge(*logits.at(1))
            for i, (t0, tn) in enumerate(Q_TILES_1):
                last = v.tensor_tensor(lg[0:tn, i], K.ps[0:tn, 6, i * nr:(i + 1) * nr], bias[0:tn], ALU.add)
            do(last)
            G = lg[:, :, 0:N_GROUPS]
            do(v.reduce_max(S(8, 9), G, AX))
            v.tensor_tensor(S(0, 4), G, S(8, 9).to_broadcast([P, 3, 4]), ALU.subtract).then_inc(*ex.one())
            do(v.tensor_tensor(S(12, 16), G, S(8, 9).to_broadcast([P, 3, 4]), ALU.is_equal))
            first_of(dve, K, S(12, 16), S(16, 20), S(9, 10))
            for g in range(N_GROUPS):
                E = lg[:, :, N_GROUPS + g * PER_GROUP:N_GROUPS + (g + 1) * PER_GROUP]
                m = S(12 + g, 13 + g).to_broadcast([P, 3, PER_GROUP])
                if g == 0:
                    do(v.tensor_tensor(S(24, 32), E, m, ALU.mult))
                else:
                    do(v.tensor_tensor(S(32, 40), E, m, ALU.mult))
                    do(v.tensor_tensor(S(24, 32), S(24, 32), S(32, 40), ALU.add))
            do(v.reduce_max(S(10, 11), S(24, 32), AX))
            do(v.tensor_tensor(S(40, 48), S(24, 32), S(10, 11).to_broadcast([P, 3, 8]), ALU.is_equal))
            first_of(dve, K, S(40, 48), S(32, 40), S(9, 10))
            do(v.scalar_tensor_tensor(out=S(24, 32), in0=S(40, 48), scalar=NEG, in1=S(24, 32), op0=ALU.mult, op1=ALU.add))
            do(v.reduce_max(S(11, 12), S(24, 32), AX))
            v.tensor_tensor(S(56, 57), S(11, 12), S(10, 11), ALU.subtract).then_inc(*ex.one())
            do(v.tensor_tensor(S(48, 56), S(24, 32), S(11, 12).to_broadcast([P, 3, 8]), ALU.is_equal))
            first_of(dve, K, S(48, 56), S(32, 40), S(9, 10))
            do(v.tensor_tensor(S(24, 32), S(40, 48), S(48, 56), ALU.add))
            for g in range(N_GROUPS):
                for i, (t0, tn) in enumerate(Q_TILES_1):
                    last = v.tensor_tensor(mask[0:tn, i, g * PER_GROUP:(g + 1) * PER_GROUP], small[0:tn, i, 24:32],
                                           small[0:tn, i, 12 + g:13 + g].to_broadcast([tn, PER_GROUP]), ALU.mult)
            last.then_inc(*chosen.one())
            dve.wait_ge(*exd.at(2))
            do(v.reduce_sum(S(58, 59), S(4, 8), AX))
            do(v.tensor_scalar(S(59, 60), S(57, 58), 1.0, None, ALU.add))
            do(v.tensor_tensor(S(60, 61), S(58, 59), S(59, 60), ALU.mult))
            do(v.reciprocal(S(61, 62), S(60, 61)))
            do(v.tensor_tensor(S(62, 63), S(61, 62), S(57, 58), ALU.mult))
            do(v.tensor_tensor(S(32, 40), S(40, 48), S(61, 62).to_broadcast([P, 3, 8]), ALU.mult))
            do(v.tensor_tensor(S(24, 32), S(48, 56), S(62, 63).to_broadcast([P, 3, 8]), ALU.mult))
            do(v.tensor_tensor(S(32, 40), S(32, 40), S(24, 32), ALU.add))
            for g in range(N_GROUPS):
                last = v.tensor_tensor(gate[:, :, g * PER_GROUP:(g + 1) * PER_GROUP], S(32, 40),
                                       S(12 + g, 13 + g).to_broadcast([P, 3, PER_GROUP]), ALU.mult)
            do(last)
            dve.wait_ge(*placed.at(1))
            do(v.reduce_max(small[0:1, 0, 63:64], K.ps[0:1, 7, 3 * N_EXP:4 * N_EXP], AX))
            v.tensor_copy(count[:], small[0:1, 0, 63:64])
            for i, (t0, tn) in enumerate(Q_TILES_1):
                do(v.scalar_tensor_tensor(out=pos[0:tn, i], in0=K.ps[0:tn, 7, i * N_EXP:(i + 1) * N_EXP], scalar=1.0, in1=mask[0:tn, i],
                                          op0=ALU.add, op1=ALU.mult))
                do(v.tensor_scalar(pos[0:tn, i], pos[0:tn, i], -1.0, None, ALU.add))
            slots = lambda ap: ap.rearrange("p (e c) -> p e c", c=CAP)
            for i, (t0, tn) in enumerate(Q_TILES_1):
                iota = K.cst[0:tn, C_SLOT:C_SLOT + CAP].rearrange("p (a c) -> p a c", a=1).to_broadcast([tn, N_EXP, CAP])
                last = v.tensor_tensor(slots(sel[0:tn, i]), iota, pos[0:tn, i].rearrange("p (e a) -> p e a", a=1).to_broadcast([tn, N_EXP, CAP]),
                                       ALU.is_equal)
            last.then_inc(*sel_made.one())
            for k in range(KT):
                dve.wait_ge(*made.at(2 * k + 1))
                v.tensor_copy(xg[:, k, 0:512], K.ps[:, (2 * k) % 8]).then_inc(*taken_v.one())
            dve.wait_ge(*made.at(2 * KT))
            for i, (t0, tn) in enumerate(Q_TILES_1):
                last = v.tensor_tensor(slots(sel[0:tn, i]), slots(sel[0:tn, i]),
                                       gate[0:tn, i].rearrange("p (e a) -> p e a", a=1).to_broadcast([tn, N_EXP, CAP]), ALU.mult)
            last.then_inc(*gated.one())
            for s in range(0, SG, 2):
                dve.wait_ge(*s_turned.at(s + 1))
                v.tensor_copy(spread[:, s], K.ps[:, s, 0:L1])


def experts_in_slots(K, layer, ctx, xg, spread, wgu, wd, w_in, load_expert):
    nc = K.nc
    ET = D_EXP // P
    turns = N_EXP // 4
    def sb(name, shape):
        return ctx.enter_context(nc.sbuf_tensor(f"{name}_{layer}", shape, F32))
    xe = sb("slot_x", [P, 2, KT, CAP])
    sil, hid = sb("slot_sil", [CAP, 2, D_EXP]), sb("slot_hid", [CAP, 2, D_EXP])
    hidT = sb("slot_hidT", [P, 2, ET, CAP])
    yt = sb("slot_y", [P, D])
    s = lambda name: K.sig(f"slot_{name}_{layer}")
    x_ready, gu_made, silu_made, hid_made, hid_turned, hidT_made = s("x_ready"), s("gu"), s("silu"), s("hid"), s("turn"), s("hidT")
    y_made, y_taken, back, added = s("y"), s("y_out"), s("back"), s("added")
    def sync(sp):
        with sp.Fori(1, turns) as i:
            for j in range(4):
                sp.wait_ge(y_made.sem, 4 * i + j - 3)
                load_expert(sp, 4 * i + j, j)

    def tensor(pe):
        def gate_up(j, k):
            return nc.tensor.matmul(K.ps[0:CAP, j % 2, :].rearrange("p (a n) -> p a n", a=2), xe[:, j % 2, k], wgu[j % 4][:, :, k],
                                    start=k == 0, stop=k == KT - 1)

        def expert(i, j, first=False, last=False):
            nj = (j + 1) % 4
            if not last:
                pe.wait_ge(w_in[nj].sem, 48 * (i + (j + 1) // 4) + 48)
                pe.wait_ge(x_ready.sem, 4 * i + j + 2)
                for k in range(KT // 2):
                    gate_up(nj, k)
            pe.wait_ge(hid_made.sem, 4 * i + j + 1)
            for m in range(ET):
                mm = nc.tensor.matmul(K.ps[:, 2 + j % 2, m * CAP:(m + 1) * CAP], hid[:, j % 2, m * P:(m + 1) * P],
                                      K.cst[0:CAP, C_ID:C_ID + CAP], start=True, stop=True)
            mm.then_inc(hid_turned.sem, 1)
            if not last:
                for k in range(KT // 2, KT):
                    mm = gate_up(nj, k)
                mm.then_inc(gu_made.sem, 1)
            pe.wait_ge(hidT_made.sem, 4 * i + j + 1)
            if not first:
                pe.wait_ge(y_taken.sem, 4 * i + j - 3)
            for half in range(2):
                for k in range(ET):
                    mm = nc.tensor.matmul(K.ps[j * CAP:(j + 1) * CAP, 4 + half, :], hidT[:, j % 2, k], wd[:, j, k, half * 512:(half + 1) * 512],
                                          start=k == 0, stop=k == ET - 1, tile_position=(0, j * CAP))
            mm.then_inc(y_made.sem, 1)

        def by_token(i, first=False):
            pe.wait_ge(y_taken.sem, 4 * i + 4)
            for m in range(KT):
                if not (first and m < 2):
                    pe.wait_ge(added.sem, KT * i + m - 1)
                nc.tensor.matmul(K.ps[:, 6 + m % 2, 0:L1], yt[:, m * P:(m + 1) * P], spread[:, bass.ds(i, 1)],
                                 start=True, stop=True).then_inc(back.sem, 1)
        pe.wait_ge(w_in[0].sem, 48)
        pe.wait_ge(x_ready.sem, 1)
        for k in range(KT):
            mm = gate_up(0, k)
        mm.then_inc(gu_made.sem, 1)
        for j in range(4):
            expert(0, j, first=True)
        expert(1, 0)
        by_token(0, first=True)
        for j in range(1, 4):
            expert(1, j)
        with pe.Fori(2, turns - 1) as i:
            expert(i, 0)
            by_token(i - 1)
            for j in range(1, 4):
                expert(i, j)
        expert(turns - 1, 0)
        by_token(turns - 2)
        for j in range(1, 4):
            expert(turns - 1, j, last=j == 3)
        by_token(turns - 1)

    def scalar(act):
        def silu(i, j):
            act.wait_ge(gu_made.sem, 4 * i + j + 1)
            nc.scalar.activation(sil[:, j % 2], K.ps[0:CAP, j % 2, 0:D_EXP], ACT.Silu).then_inc(silu_made.sem, 1)

        def output(i, j):
            act.wait_ge(y_made.sem, 4 * i + j + 1)
            nc.scalar.copy(yt[j * CAP:(j + 1) * CAP].rearrange("p (a n) -> p a n", a=2), K.ps[j * CAP:(j + 1) * CAP, 4:6, :]).then_inc(y_taken.sem, 1)

        def turn(i, last=False):
            for j in range(4):
                if not (last and j == 3):
                    silu(i, j + 1)
                if j == 0 and not (isinstance(i, int) and i == 0):
                    act.wait_ge(back.sem, KT * i)
                output(i, j)
        silu(0, 0)
        turn(0)
        with act.Fori(1, turns - 1) as i:
            turn(i)
        turn(turns - 1, True)

    def vector(dve):
        def hidden(i, j):
            dve.wait_ge(silu_made.sem, 4 * i + j + 1)
            nc.vector.tensor_tensor(hid[:, j % 2], sil[:, j % 2], K.ps[0:CAP, j % 2, D_EXP:2 * D_EXP], ALU.mult).then_inc(hid_made.sem, 1)

        def turned(i, j):
            dve.wait_ge(hid_turned.sem, 4 * i + j + 1)
            nc.vector.tensor_copy(hidT[:, j % 2], K.ps[:, 2 + j % 2, 0:ET * CAP].rearrange("p (m c) -> p m c", m=ET)).then_inc(hidT_made.sem, 1)

        def add(i):
            for m in range(KT):
                dve.wait_ge(back.sem, KT * i + m + 1)
                nc.vector.tensor_tensor(K.h[:, m], K.h[:, m], K.ps[:, 6 + m % 2, 0:L1], ALU.add).then_inc(added.sem, 1)

        def turn(i, first=False, last=False):
            for j in range(4):
                turned(i, j)
                if not (last and j == 3):
                    hidden(i, j + 1)
                if j == 0 and not first:
                    add(i - 1)
        hidden(0, 0)
        turn(0, first=True)
        with dve.Fori(1, turns - 1) as i:
            turn(i)
        turn(turns - 1, last=True)
        add(turns - 1)

    def gpsimd(pool):
        def tokens(e, j):
            nc.gpsimd.tensor_copy(xe[:, j % 2], xg[:, :, bass.ds(e * CAP, CAP)]).then_inc(x_ready.sem, 1)
        tokens(0, 0)
        tokens(1, 1)
        pool.wait_ge(gu_made.sem, 1)
        tokens(2, 0)
        pool.wait_ge(gu_made.sem, 2)
        tokens(3, 1)
        with pool.Fori(1, turns) as i:
            for j in range(4):
                pool.wait_ge(gu_made.sem, 4 * i + j - 1)
                tokens(4 * i + j, j)
    return {"sync": sync, "tensor": tensor, "scalar": scalar, "vector": vector, "gpsimd": gpsimd}


def experts_over_all(K, layer, ctx, gates_dram, gate, wgu, wd, w_in):
    nc, I = K.nc, K.ins
    ET = D_EXP // P
    def sb(name, shape):
        return ctx.enter_context(nc.sbuf_tensor(f"{name}_{layer}", shape, F32))
    gT = sb("gT", [N_EXP, L1])
    gb = sb("gb", [P, 2, L1])
    sil = sb("sil", [P, 2, ET, L1])
    hid = sb("hid", [P, 2, ET, L1])
    sg = lambda name: K.sig(f"all_{name}_{layer}")
    turned, copied, saved = sg("turned"), sg("copied"), sg("saved")
    gu_in, d_in = [sg("gu_in_0"), sg("gu_in_1")], [sg("d_in_0"), sg("d_in_1")]
    gu_made, hid_made, d_made, d_taken = sg("gu_made"), sg("hid_made"), sg("d_made"), sg("d_taken")
    silu_made, gated = sg("silu_made"), sg("gated")
    wg_v = I["w_gate"][layer].rearrange("e (k p) n -> p e k n", p=P)
    wu_v = I["w_up"][layer].rearrange("e (k p) n -> p e k n", p=P)
    wd_v = I["w_down"][layer].rearrange("e (k p) n -> p e k n", p=P)

    def sync(sp):
        def load(e, s, first=False):
            if not first:
                sp.wait_ge(gu_made.sem, ET * (e - 1))
                sp.wait_ge(hid_made.sem, ET * (e - 1))
            one = bass.ds(e, 1)
            sp.dma_start(wgu[s][:, 0], wg_v[:, one]).then_inc(gu_in[s].sem, 16)
            sp.dma_start(wgu[s][:, 1], wu_v[:, one]).then_inc(gu_in[s].sem, 16)
            sp.dma_start(gb[:, s], gates_dram[one].to_broadcast([P, L1])).then_inc(gu_in[s].sem, 16)
            if not first:
                sp.wait_ge(d_made.sem, KT * (e - 1))
            sp.dma_start(wd[:, s], wd_v[:, one]).then_inc(d_in[s].sem, 16)
        for j in range(4):
            sp.wait_ge(w_in[j].sem, 48)
        sp.wait_ge(copied.sem, 1)
        sp.dma_start(gates_dram, gT[:]).then_inc(saved.sem, 16)
        sp.wait_ge(saved.sem, 16)
        load(0, 0, True)
        load(1, 1, True)
        with sp.Fori(1, N_EXP // 2) as i:
            load(2 * i, 0)
            load(2 * i + 1, 1)

    def tensor(pe):
        for i, (t0, tn) in enumerate(Q_TILES_1):
            mm = nc.tensor.transpose(K.ps[0:N_EXP, 7, t0:t0 + tn], gate[0:tn, i], K.cst[0:tn, C_ID:C_ID + tn])
        mm.then_inc(turned.sem, 1)
        pe.wait_ge(copied.sem, 1)

        def expert(e, s, i, first=False):
            pe.wait_ge(gu_in[s].sem, 48 * i + 48)
            for m in range(ET):
                if not first:
                    pe.wait_ge(hid_made.sem, ET * (e - 1) + m + 1)
                for j in range(2):
                    for k in range(KT):
                        mm = nc.tensor.matmul(K.ps[:, 2 * j + m, 0:L1], wgu[s][:, j, k, m * P:(m + 1) * P], K.xn[:, k],
                                              start=k == 0, stop=k == KT - 1)
                mm.then_inc(gu_made.sem, 1)
            pe.wait_ge(d_in[s].sem, 16 * i + 16)
            pe.wait_ge(hid_made.sem, ET * e + ET)
            for m in range(KT):
                if not (first and m < 4):
                    pe.wait_ge(d_taken.sem, KT * e + m - 3)
                for k in range(ET):
                    mm = nc.tensor.matmul(K.ps[:, 4 + m % 4, 0:L1], wd[:, s, k, m * P:(m + 1) * P], hid[:, s, k],
                                          start=k == 0, stop=k == ET - 1)
                mm.then_inc(d_made.sem, 1)
        expert(0, 0, 0, True)
        expert(1, 1, 0)
        with pe.Fori(1, N_EXP // 2) as i:
            expert(2 * i, 0, i)
            expert(2 * i + 1, 1, i)

    def scalar(act):
        with act.Fori(0, N_EXP // 2) as i:
            for s in range(2):
                for m in range(ET):
                    act.wait_ge(gu_made.sem, ET * (2 * i + s) + m + 1)
                    nc.scalar.activation(sil[:, s, m], K.ps[:, m, 0:L1], ACT.Silu).then_inc(silu_made.sem, 1)

    def vector(dve):
        dve.wait_ge(turned.sem, 1)
        nc.vector.tensor_copy(gT[:], K.ps[0:N_EXP, 7, 0:L1]).then_inc(copied.sem, 1)
        with dve.Fori(0, N_EXP // 2) as i:
            for s in range(2):
                e = 2 * i + s
                dve.wait_ge(gu_in[s].sem, 48 * i + 48)
                for m in range(ET):
                    dve.wait_ge(silu_made.sem, ET * e + m + 1)
                    nc.vector.tensor_tensor(sil[:, s, m], sil[:, s, m], gb[:, s], ALU.mult).then_inc(gated.sem, 1)
                    dve.wait_ge(gated.sem, ET * e + m + 1)
                    nc.vector.tensor_tensor(hid[:, s, m], sil[:, s, m], K.ps[:, 2 + m, 0:L1], ALU.mult).then_inc(hid_made.sem, 1)
                for m in range(KT):
                    dve.wait_ge(d_made.sem, KT * e + m + 1)
                    nc.vector.tensor_tensor(K.h[:, m], K.h[:, m], K.ps[:, 4 + m % 4, 0:L1], ALU.add).then_inc(d_taken.sem, 1)
    return {"sync": sync, "tensor": tensor, "scalar": scalar, "vector": vector}


def store_tokens(K, out):
    nc = K.nc
    with ExitStack() as ctx:
        tok = ctx.enter_context(nc.sbuf_tensor("tok_out", [P, 2, D], F32))
        made, stored, saved = K.sig("tile_made"), K.sig("tile_stored"), K.sig("out_saved")
        block = ctx.enter_context(nc.Block())

        @block.tensor
        def _(pe):
            for n in range(4):
                for k in range(4):
                    mm = nc.tensor.transpose(K.ps[:, n, k * P:(k + 1) * P], K.h[:, 4 * (n % 2) + k, (n // 2) * P:(n // 2 + 1) * P],
                                             K.con(C_ID))
                mm.then_inc(*made.one())

        @block.vector
        def _(dve):
            for n in range(4):
                dve.wait_ge(*made.at(n + 1))
                nc.vector.tensor_copy(tok[:, n // 2, 512 * (n % 2):512 * (n % 2) + 512], K.ps[:, n]).then_inc(*stored.one())

        @block.sync
        def _(sp):
            for i in range(2):
                sp.wait_ge(*stored.at(2 * i + 2))
                sp.dma_start(out[0, i * P:(i + 1) * P], tok[:, i]).then_inc(*saved.dma())
            sp.wait_ge(*saved.now())


def rope(K, x, out, rows, T):
    nc = K.nc
    n = len(x)
    with ExitStack() as ctx:
        made, taken = K.sig("tile_made"), K.sig("tile_stored")
        block = ctx.enter_context(nc.Block())
        load_ahead(K, block)

        @block.tensor
        def _(pe):
            for i in range(n):
                if i >= 8:
                    pe.wait_ge(*taken.at(i - 7))
                nc.tensor.matmul(K.ps[0:rows, i % 8, 0:T], K.cst[0:rows, C_ROT:C_ROT + rows], x[i], start=True, stop=True).then_inc(*made.one())

        @block.vector
        def _(dve):
            for i in range(n):
                dve.wait_ge(*made.at(i + 1))
                rot = K.rs[0:rows, i % 2, 0:T]
                nc.vector.tensor_tensor(rot, K.ps[0:rows, i % 8, 0:T], K.cst[0:rows, C_SIN:C_SIN + T], ALU.mult).then_inc(*taken.one())
                link(dve, K.dve_step, nc.vector.tensor_tensor(out[i], x[i], K.cst[0:rows, C_COS:C_COS + T], ALU.mult))
                link(dve, K.dve_step, nc.vector.tensor_tensor(out[i], out[i], rot, ALU.add))


def latent_kv(K, ctx):
    nc, I = K.nc, K.ins
    kn = ctx.enter_context(nc.sbuf_tensor("mla_kn", [P, HEADS, L1], F32))
    kr = ctx.enter_context(nc.sbuf_tensor("mla_kr", [ROPE, L1], F32))
    v = ctx.enter_context(nc.sbuf_tensor("mla_v", [P, 3, HEADS * V_DIM], F32))
    with ExitStack() as inner:
        c = inner.enter_context(nc.sbuf_tensor("lat_c", [P, 3, L1], F32))
        cn = inner.enter_context(nc.sbuf_tensor("lat_cn", [P, 2, L1], F32))
        down = Linears(K, [Linear(I["w_dkv"], lambda k: K.xn[:, k], lambda m, ps: nc.vector.tensor_copy(c[0:ps.shape[0], m], ps), T=L1)])
        up = Linears(K, [
            Linear(I["w_uk"].rearrange("r h d -> r (h d)"), lambda k: cn[:, k], lambda m, ps: nc.vector.tensor_copy(kn[:, m], ps), T=L1),
            Linear(I["w_uv"].rearrange("r h d -> r (h d)"), lambda k, t0, tn: cn[:, k, t0:t0 + tn],
                   lambda i, at, n, ps: nc.scalar.copy(v[0:ps.shape[0], i, at:at + n], ps), tiles=Q_TILES_1, by="scalar")])
        K.coming = down
        rms_norm(K, K.h[:], K.xn[:], K.col("kv_norm", 0, KT))
        K.coming = up
        down.run()
        rms_norm(K, c[:, 0:2], cn[:], K.col("kv_lat_norm", 0, 2))
        rope(K, [c[0:ROPE, 2]], [kr[:]], ROPE, L1)
        up.run()
    return kn, kr, v


def mla(K, kv):
    nc, I = K.nc, K.ins
    kn, kr, v = kv
    with ExitStack() as ctx:
        def sb(name, shape):
            return ctx.enter_context(nc.sbuf_tensor(name, shape, F32))
        qn, qr = sb("mla_qn", [P, HEADS, L1]), sb("mla_qr", [ROPE, HEADS, L1])
        with ExitStack() as inner:
            cq = inner.enter_context(nc.sbuf_tensor("cq", [P, 3, L1], F32))
            cqn = inner.enter_context(nc.sbuf_tensor("cqn", [P, 3, L1], F32))
            wq = inner.enter_context(nc.sbuf_tensor("wq", [P, Q_LORA // P, HEADS * (NOPE + ROPE)], F32))
            wq_in = K.sig("rows_given")
            with nc.Block() as block:
                @block.sync
                def _(sp):
                    sp.dma_start(wq[:], I["b_w_uq"][0].rearrange("(k p) h d -> p k (h d)", p=P)).then_inc(*wq_in.dma())
            down = Linears(K, [Linear(I["b_w_dq"][0], lambda k: K.xn[:, k], lambda m, ps: nc.vector.tensor_copy(cq[:, m], ps), T=L1)])
            K.coming = down
            rms_norm(K, K.h[:], K.xn[:], K.col("b_norm", 0, KT))
            down.run()
            rms_norm(K, cq[:], cqn[:], K.col("b_q_norm", 0, 3))
            latent_queries(K, wq, wq_in, cqn, qn, qr)
        oT = sb("mla_oT", [P, HEADS, L1])
        out = Linears(K, [Linear(I["b_w_o"][0], lambda k: oT[:, k], lambda m, ps: nc.vector.tensor_tensor(K.h[:, m], K.h[:, m], ps, ALU.add), T=L1)])
        K.coming = out
        rope(K, [qr[:, h] for h in range(HEADS)], [K.xn[0:ROPE, h] for h in range(HEADS)], ROPE, L1)
        mla_attention(K, qn, K.xn, kn, kr, v, oT)
        out.run()


def latent_queries(K, wq, wq_in, cqn, qn, qr):
    nc, I = K.nc, K.ins
    kq = Q_LORA // P
    w = NOPE + ROPE
    with ExitStack() as ctx:
        made, taken = K.sig("tile_made"), K.sig("tile_stored")
        block = ctx.enter_context(nc.Block())

        @block.tensor
        def _(pe):
            pe.wait_ge(*wq_in.at(16))
            for n in range(2 * HEADS):
                h, r = divmod(n, 2)
                if n >= 8:
                    pe.wait_ge(*taken.at(n - 7))
                at, mw = h * w + NOPE * r, (NOPE, ROPE)[r]
                for k in range(kq):
                    mm = nc.tensor.matmul(K.ps[0:mw, n % 8, 0:L1], wq[:, k, at:at + mw], cqn[:, k], start=k == 0, stop=k == kq - 1)
                mm.then_inc(*made.one())

        @block.vector
        def _(dve):
            for n in range(2 * HEADS):
                h, r = divmod(n, 2)
                dve.wait_ge(*made.at(n + 1))
                nc.vector.tensor_copy((qn, qr)[r][:, h], K.ps[0:(NOPE, ROPE)[r], n % 8, 0:L1]).then_inc(*taken.one())


def mla_attention(K, qn, qr, kn, kr, v, oT):
    nc = K.nc
    units = [(h, i) for h in range(HEADS) for i in range(3)]
    n = len(units)
    keys = [t0 + tn for t0, tn in Q_TILES_1]
    with ExitStack() as ctx:
        def sb(name, shape):
            return ctx.enter_context(nc.sbuf_tensor(name, shape, F32))
        S, Pr, PT = sb("att_s", [P, 3, L1]), sb("att_p", [P, 3, L1]), sb("att_pt", [P, 2, 3, P])
        st = sb("att_stat", [P, 3, 4])
        s_made, s_ready, e_made, p_ready = K.sig("s_made"), K.sig("s_ready"), K.sig("e_made"), K.sig("p_ready")
        t_made, t_taken, pv_made, o_taken = K.sig("t_made"), K.sig("t_taken"), K.sig("pv_made"), K.sig("o_taken")
        block = ctx.enter_context(nc.Block())

        @block.tensor
        def _(pe):
            for u in range(n + 2):
                if u < n:
                    h, i = units[u]
                    t0, tn = Q_TILES_1[i]
                    if u >= 3:
                        pe.wait_ge(*s_ready.at(u - 2))
                    nc.tensor.matmul(K.ps[0:tn, u % 3, 0:keys[i]], qn[:, h, t0:t0 + tn], kn[:, h, 0:keys[i]], start=True, stop=False)
                    nc.tensor.matmul(K.ps[0:tn, u % 3, 0:keys[i]], qr[0:ROPE, h, t0:t0 + tn], kr[0:ROPE, 0:keys[i]],
                                     start=False, stop=True).then_inc(*s_made.one())
                if 1 <= u <= n:
                    w = u - 1
                    i = units[w][1]
                    tn = Q_TILES_1[i][1]
                    pe.wait_ge(*p_ready.at(w + 1))
                    if w >= 2:
                        pe.wait_ge(*t_taken.at(w - 1))
                    for j in range(i + 1):
                        k0, kn_ = Q_TILES_1[j]
                        mm = nc.tensor.transpose(K.ps[0:kn_, 3 + w % 2, j * P:j * P + tn], Pr[0:tn, w % 3, k0:k0 + kn_],
                                                 K.cst[0:tn, C_ID:C_ID + tn])
                    mm.then_inc(*t_made.one())
                if u >= 2:
                    w = u - 2
                    h, i = units[w]
                    t0, tn = Q_TILES_1[i]
                    pe.wait_ge(*t_taken.at(w + 1))
                    if i == 0 and h >= 2:
                        pe.wait_ge(*o_taken.at(h - 1))
                    for j in range(i + 1):
                        kn_ = Q_TILES_1[j][1]
                        mm = nc.tensor.matmul(K.ps[:, 5 + h % 2, t0:t0 + tn], v[0:kn_, j, h * V_DIM:(h + 1) * V_DIM],
                                              PT[0:kn_, w % 2, j, 0:tn], start=j == 0, stop=j == i)
                    mm.then_inc(*pv_made.one())

        @block.vector
        def _(dve):
            for u in range(n + 4):
                if u < n:
                    h, i = units[u]
                    t0, tn = Q_TILES_1[i]
                    dve.wait_ge(*s_made.at(u + 1))
                    if u >= 3:
                        dve.wait_ge(*e_made.at(u - 2))
                    if i:
                        nc.vector.tensor_scalar(S[0:tn, u % 3, 0:t0], K.ps[0:tn, u % 3, 0:t0], MLA_SCALE, None, ALU.mult)
                    link(dve, K.dve_step, nc.vector.scalar_tensor_tensor(
                        out=S[0:tn, u % 3, t0:t0 + tn], in0=K.ps[0:tn, u % 3, t0:t0 + tn], scalar=MLA_SCALE,
                        in1=K.cst[0:tn, C_CAUSAL:C_CAUSAL + tn], op0=ALU.mult, op1=ALU.add))
                    link(dve, K.dve_step, nc.vector.reduce_max(st[0:tn, u % 3, 3:4], S[0:tn, u % 3, 0:keys[i]], AX))
                    nc.vector.tensor_scalar(st[0:tn, u % 3, 0:1], st[0:tn, u % 3, 3:4], -1.0, None, ALU.mult).then_inc(*s_ready.one())
                if 1 <= u <= n:
                    w = u - 1
                    i = units[w][1]
                    tn = Q_TILES_1[i][1]
                    dve.wait_ge(*e_made.at(w + 1))
                    link(dve, K.dve_step, nc.vector.reciprocal(st[0:tn, w % 3, 2:3], st[0:tn, w % 3, 1:2]))
                    nc.vector.tensor_scalar(Pr[0:tn, w % 3, 0:keys[i]], Pr[0:tn, w % 3, 0:keys[i]], st[0:tn, w % 3, 2:3],
                                            None, ALU.mult).then_inc(*p_ready.one())
                if u >= 4 and units[u - 4][1] == 2:
                    h = units[u - 4][0]
                    dve.wait_ge(*pv_made.at(u - 3))
                    nc.vector.tensor_copy(oT[:, h], K.ps[:, 5 + h % 2, 0:L1]).then_inc(*o_taken.one())

        @block.scalar
        def _(act):
            for u in range(n + 1):
                if u < n:
                    i = units[u][1]
                    tn = Q_TILES_1[i][1]
                    act.wait_ge(*s_ready.at(u + 1))
                    if u >= 3:
                        act.wait_ge(*t_made.at(u - 2))
                    nc.scalar.activation(Pr[0:tn, u % 3, 0:keys[i]], S[0:tn, u % 3, 0:keys[i]], ACT.Exp, bias=st[0:tn, u % 3, 0:1],
                                         accum_out=st[0:tn, u % 3, 1:2]).then_inc(*e_made.one())
                if u >= 1:
                    w = u - 1
                    i = units[w][1]
                    tn = Q_TILES_1[i][1]
                    act.wait_ge(*t_made.at(w + 1))
                    if w >= 2:
                        act.wait_ge(*pv_made.at(w - 1))
                    full = min(i + 1, 2)
                    view = K.ps[:, 3 + w % 2, :].rearrange("p (j t) -> p j t", j=4)
                    last = nc.scalar.copy(PT[:, w % 2, 0:full, 0:tn], view[:, 0:full, 0:tn])
                    if i == 2:
                        kn_ = Q_TILES_1[2][1]
                        last = nc.scalar.copy(PT[0:kn_, w % 2, 2, 0:tn], K.ps[0:kn_, 3 + w % 2, 2 * P:2 * P + tn])
                    last.then_inc(*t_taken.one())


def final_norm(K):
    nc = K.nc
    rms_norm(K, K.h[:], K.xn[:], K.col("final_norm", 0, KT))
    with nc.Block() as block:
        @block.vector
        def _(dve):
            nc.vector.tensor_copy(K.h[:, :, 0:SEQ], K.xn[:, :, N_META:])


F32R = mybir.dt.float32r


def split_high(nc, x, high):
    return nc.vector.tensor_copy(high, x)


def split_low(nc, x, high, low):
    return nc.vector.tensor_tensor(low, x, high, ALU.subtract)


def split_matmul(nc, out, wh, wl, xh, xl, start, stop):
    nc.tensor.matmul(out, wh, xh, start=start, stop=False)
    nc.tensor.matmul(out, wh, xl, start=False, stop=False)
    return nc.tensor.matmul(out, wl, xh, start=False, stop=stop)


def ffn(K, w_gate, w_up, w_down, g_in, g_out):
    nc = K.nc
    H, X = K.h[:, :, 0:SEQ], K.xn[:, :, 0:SEQ]
    gu_len = KT * P
    half = FF_T // 2
    n_down = 2 * KT
    turns, dturns = FF_T // 4, n_down // 4
    assert FF_T % 4 == 2 and half * P <= 2 * gu_len
    ring = K.w[:].rearrange("p a (b n) -> p (a b) n", b=2)
    wg, wu = (w.rearrange("(k p) n -> p k n", p=P) for w in (w_gate, w_up))
    wd = w_down.rearrange("(k p) n -> p k n", p=P)
    gu_in = [K.sig(f"gu_in_{s}") for s in range(4)]

    def load_gate_up(sp, b, s):
        for a, w in enumerate((wg, wu)):
            sp.dma_start(ring[:, s, a * gu_len:(a + 1) * gu_len].rearrange("p (k n) -> p k n", k=KT),
                         w[:, :, bass.ds(b * P, P)]).then_inc(gu_in[s].sem, 16)

    class FirstLoads:
        @staticmethod
        def ahead(sp):
            for slot in range(2):
                free = K.free.pop(slot, None)
                if free is not None:
                    sp.wait_ge(*free)
            for s in range(4):
                load_gate_up(sp, s, s)
    K.coming = FirstLoads
    rms_norm(K, H, X, g_in)
    K.coming = None
    with ExitStack() as ctx:
        def sb(name, shape, dt=F32R):
            return ctx.enter_context(nc.sbuf_tensor(f"{name}_{K.next()}", shape, dt))
        high, low = sb("ffn_wh", [P, 4, 2 * gu_len]), sb("ffn_wl", [P, 4, 2 * gu_len])
        XH, XL = sb("ffn_xh", [P, KT, SEQ]), sb("ffn_xl", [P, KT, SEQ])
        hidh, hidl = sb("ffn_hidh", [P, FF_T, SEQ]), sb("ffn_hidl", [P, FF_T, SEQ])
        sil, hid = sb("ffn_sil", [P, 4, SEQ], F32), sb("ffn_hid", [P, 2, SEQ], F32)
        dn_in = [K.sig(f"d_in_{s}") for s in range(4)]
        x_high, x_split = K.sig("x_high"), K.sig("x_split")
        w_high, w_split, wd_high, wd_split = K.sig("w_high"), K.sig("w_split"), K.sig("wd_high"), K.sig("wd_split")
        gu_made, silu_made, product, hid_high, hid_made = (K.sig(n) for n in ("gu_made", "silu_made", "product", "hid_high", "hid_made"))
        dn_made, taken = K.sig("d_made"), K.sig("d_taken")
        block = ctx.enter_context(nc.Block())
        def wait(eng, sig, n):
            eng.wait_ge(sig.sem, sig.base + n)

        @block.sync
        def _(sp):
            def down(d, s, i):
                t = (s + 2) % 4
                sp.dma_start(ring[:, t, 0:half * P].rearrange("p (k n) -> p k n", k=half),
                             wd[:, (s % 2) * half:(s % 2 + 1) * half, bass.ds((2 * i + s // 2) * P, P)]).then_inc(dn_in[t].sem, 16)
            with sp.Fori(1, turns) as i:
                for s in range(4):
                    wait(sp, w_split, 4 * i + s - 3)
                    load_gate_up(sp, 4 * i + s, s)
            for s in range(2):
                wait(sp, w_split, 4 * turns + s - 3)
                load_gate_up(sp, 4 * turns + s, s)
            for s in range(4):
                wait(sp, w_split, FF_T - 3 + s)
                down(s, s, 0)
            with sp.Fori(1, dturns) as i:
                for s in range(4):
                    wait(sp, wd_split, 4 * i + s - 3)
                    down(4 * i + s, s, i)

        @block.tensor
        def _(pe):
            def gate_up(b, s, first=False):
                wait(pe, w_split, b + 1)
                if not first:
                    wait(pe, product, b - 3)
                for a in range(2):
                    for k in range(KT):
                        w = slice(a * gu_len + k * P, a * gu_len + (k + 1) * P)
                        mm = split_matmul(nc, K.ps[:, s, a * SEQ:(a + 1) * SEQ], high[:, s, w], low[:, s, w], XH[:, k], XL[:, k],
                                          k == 0, k == KT - 1)
                mm.then_inc(gu_made.sem, 1)

            def down(d, s, j, first=False):
                t = (s + 2) % 4
                wait(pe, wd_split, d + 1)
                if s % 2 == 0 and not first:
                    wait(pe, taken, j - 1)
                for k in range(half):
                    f = (s % 2) * half + k
                    mm = split_matmul(nc, K.ps[:, 4 + s // 2, 0:SEQ], high[:, t, k * P:(k + 1) * P], low[:, t, k * P:(k + 1) * P],
                                      hidh[:, f], hidl[:, f], f == 0, f == FF_T - 1)
                mm.then_inc(dn_made.sem, 1)
            wait(pe, x_split, 1)
            for s in range(4):
                gate_up(s, s, True)
            with pe.Fori(1, turns) as i:
                for s in range(4):
                    gate_up(4 * i + s, s)
            for s in range(2):
                gate_up(4 * turns + s, s)
            wait(pe, hid_made, FF_T)
            for s in range(4):
                down(s, s, s // 2, True)
            with pe.Fori(1, dturns) as i:
                for s in range(4):
                    down(4 * i + s, s, 2 * i + s // 2)

        @block.scalar
        def _(act):
            def silu(b, s):
                wait(act, gu_made, b + 1)
                nc.scalar.activation(sil[:, s], K.ps[:, s, 0:SEQ], ACT.Silu).then_inc(silu_made.sem, 1)
            with act.Fori(0, turns) as i:
                for s in range(4):
                    silu(4 * i + s, s)
            for s in range(2):
                silu(4 * turns + s, s)

        @block.vector
        def _(dve):
            def split(slot, n, high_made, made, count):
                split_high(nc, ring[:, slot, 0:n], high[:, slot, 0:n]).then_inc(high_made.sem, 1)
                wait(dve, high_made, count)
                split_low(nc, ring[:, slot, 0:n], high[:, slot, 0:n], low[:, slot, 0:n]).then_inc(made.sem, 1)

            def split_gate_up(b, s, turn, first=False):
                wait(dve, gu_in[s], 32 * turn + 32)
                if not first:
                    wait(dve, gu_made, b - 3)
                split(s, 2 * gu_len, w_high, w_split, b + 1)

            def split_down(d, s, turn, first=False):
                t = (s + 2) % 4
                wait(dve, dn_in[t], 16 * turn + 16)
                if first:
                    wait(dve, gu_made, FF_T - 3 + d)
                else:
                    wait(dve, dn_made, d - 3)
                split(t, half * P, wd_high, wd_split, d + 1)

            def times(b, s):
                wait(dve, silu_made, b + 1)
                at = bass.ds(b, 1)
                nc.vector.tensor_tensor(hid[:, s % 2:s % 2 + 1], sil[:, s:s + 1], K.ps[:, s:s + 1, SEQ:2 * SEQ], ALU.mult).then_inc(product.sem, 1)
                wait(dve, product, b + 1)
                split_high(nc, hid[:, s % 2:s % 2 + 1], hidh[:, at]).then_inc(hid_high.sem, 1)
                wait(dve, hid_high, b + 1)
                split_low(nc, hid[:, s % 2:s % 2 + 1], hidh[:, at], hidl[:, at]).then_inc(hid_made.sem, 1)
                wait(dve, hid_made, b + 1)

            def output(j, t):
                wait(dve, dn_made, 2 * j + 2)
                nc.vector.tensor_copy(X[:, bass.ds(j, 1)], K.ps[:, 4 + t:5 + t, 0:SEQ]).then_inc(taken.sem, 1)
            split_high(nc, X, XH[:]).then_inc(x_high.sem, 1)
            wait(dve, x_high, 1)
            split_low(nc, X, XH[:], XL[:]).then_inc(x_split.sem, 1)
            split_gate_up(0, 0, 0, True)
            split_gate_up(1, 1, 0, True)
            for s in range(4):
                split_gate_up(s + 2, (s + 2) % 4, (s + 2) // 4, s < 2)
                times(s, s)
            with dve.Fori(1, turns) as i:
                for s in range(4):
                    split_gate_up(4 * i + s + 2, (s + 2) % 4, i + (s + 2) // 4)
                    times(4 * i + s, s)
            for s in range(2):
                split_down(s, s, 0, True)
                times(4 * turns + s, s)
            for s in range(4):
                split_down(s + 2, (s + 2) % 4, (s + 2) // 4, s < 2)
                if s % 2:
                    output(s // 2, s // 2)
            with dve.Fori(1, dturns - 1) as i:
                for s in range(4):
                    split_down(4 * i + s + 2, (s + 2) % 4, i + (s + 2) // 4)
                    if s % 2:
                        output(2 * i + s // 2, s // 2)
            for s in range(2):
                split_down(n_down - 2 + s, s + 2, dturns - 1)
            for t in range(2):
                output(KT - 2 + t, t)
        for s in range(4):
            gu_in[s].given += 32 * (turns + (s < 2))
            dn_in[s].given += 16 * dturns
        for sig, n in ((x_high, 1), (x_split, 1), (w_high, FF_T), (w_split, FF_T), (wd_high, n_down), (wd_split, n_down),
                       (gu_made, FF_T), (silu_made, FF_T), (product, FF_T), (hid_high, FF_T), (hid_made, FF_T),
                       (dn_made, n_down), (taken, KT)):
            sig.given += n
    rms_norm(K, X, X, g_out, add_to=H, factor=0.5)


TT = [(0, P), (P, P)]


def nsa_ssd(K, gain):
    nc, I = K.nc, K.ins
    X = K.xn[:, :, 0:SEQ]
    W = I["ab_w_in_2"][0]
    xk = lambda k: X[:, k]
    xt = lambda k, t0, tn: X[:, k, t0:t0 + tn]
    with ExitStack() as outer:
        joined = outer.enter_context(nc.sbuf_tensor("joined", [P, 2, 512 + SSD_INNER], F32))
        with ExitStack() as ctx:
            def sb(name, shape):
                return ctx.enter_context(nc.sbuf_tensor(name, shape, F32))
            q, kcv, kw = sb("q", [P, 4, SEQ]), sb("kcv", [P, 3, SEQ]), sb("kw", [P, 1, SEQ])
            vs, vg = sb("vs", [P, 2, 128]), sb("vg", [P, 2, 152])
            xbc, z, dt = sb("xbc", [P, 12, SEQ]), sb("z", [P, 2, SSD_INNER]), sb("dt", [P, 2, SSD_HEADS])
            copy = lambda dst: (lambda m, ps: nc.vector.tensor_copy(dst[:, m], ps))
            tcopy = lambda dst: (lambda i, at, n, ps: nc.scalar.copy(dst[:, i, at:at + n], ps))
            feat = lambda a, b, dst, **more: Linear(W[:, OFF[a]:OFF[b]], xk, copy(dst), T=SEQ, **more)
            tok = lambda a, b, dst: Linear(W[:, OFF[a]:OFF[b]], xt, tcopy(dst), tiles=TT, by="scalar")
            pieces = [((2 * g + v) * HD, (NSA_GROUP * v + g) * HD, HD) for g in range(NSA_GROUP) for v in range(NSA_KV)]
            project = Linears(K, [feat(0, 1, q, pieces=pieces), feat(1, 4, kcv), feat(5, 6, kw), feat(9, 10, xbc),
                                  tok(4, 5, vs), tok(6, 8, vg), tok(8, 9, z), tok(10, 11, dt)])
            weights = compress_weights(K, ctx)
            K.coming = project
            rms_norm(K, K.h[:, :, 0:SEQ], X, gain)
            project.run()
            rot = [q[:, g] for g in range(4)] + [kcv[:, 0], kcv[:, 2], kw[:, 0]]
            turned = K.sq[:, 0:7, 0:SEQ]
            rope(K, rot, [turned[:, i] for i in range(7)], P, SEQ)
            nsa(K, weights, turned, kcv[:, 1], vs, vg, joined)
            ssd(K, xbc, z, dt, joined)
        project_joined(K, joined, (512 + SSD_INNER) // P, I["ab_w_out_2"][0])


def project_joined(K, tok, n, w):
    nc = K.nc
    with ExitStack() as ctx:
        feat = ctx.enter_context(nc.sbuf_tensor(f"feat_{K.next()}", [P, n, SEQ], F32))
        made, taken = K.sig("tile_made"), K.sig("tile_stored")
        out = Linears(K, [Linear(w, lambda k: feat[:, k], lambda m, ps: nc.vector.tensor_copy(K.xn[:, m, 0:SEQ], ps), T=SEQ)])
        K.coming = out
        with nc.Block() as block:
            load_ahead(K, block)

            @block.tensor
            def _(pe):
                for m in range(n // 2):
                    if m >= 8:
                        pe.wait_ge(*taken.at(m - 7))
                    for j in range(2):
                        for t in range(2):
                            at = (2 * m + j) * P
                            mm = nc.tensor.transpose(K.ps[:, m % 8, (2 * j + t) * P:(2 * j + t + 1) * P], tok[:, t, at:at + P], K.con(C_ID))
                    mm.then_inc(*made.one())

            @block.vector
            def _(dve):
                for m in range(n // 2):
                    dve.wait_ge(*made.at(m + 1))
                    nc.vector.tensor_copy(feat[:, 2 * m:2 * m + 2], K.ps[:, m % 8, :].rearrange("p (j t) -> p j t", j=2)).then_inc(*taken.one())
        out.run()


def nsa(K, weights, roped, vc, vs, vg, joined):
    nc, I = K.nc, K.ins
    scale = HD ** -0.5
    with ExitStack() as ctx:
        def sb(name, shape):
            return ctx.enter_context(nc.sbuf_tensor(name, shape, F32))
        kC, vC = sb("kC", [P, N_CMP]), sb("vC", [N_CMP, 2, HD])
        gates = sb("nsa_gates", [P, 2, 24])
        compress(K, weights, roped[:, 4], vc, kC, vC)
        pc = sb("pc", [P, 2, 8, N_CMP])
        stat = sb("pc_stat", [P, 2, 8, 2])
        madd = sb("pc_mask", [P, 2, N_CMP])
        pcT = sb("pcT", [N_CMP, 2, 8, P])
        made, e_in, e_done, ready = K.sig("tile_made"), K.sig("s_ready"), K.sig("e_made"), K.sig("p_ready")
        turned, copied, pv, gated = K.sig("t_made"), K.sig("t_taken"), K.sig("pv_made"), K.sig("gated")
        M = K.con(C_CMPM, 2 * (N_CMP + 1)).rearrange("p (t n) -> p t n", t=2)[:, :, 0:N_CMP]
        with nc.Block() as block:
            @block.tensor
            def _(pe):
                for t in range(2):
                    for v in range(NSA_KV):
                        for g in range(NSA_GROUP):
                            at = (t * NSA_GROUP + g) * 16
                            mm = nc.tensor.matmul(K.ps[:, v, at:at + N_CMP], roped[64 * v:64 * v + 64, g, t * P:(t + 1) * P],
                                                  kC[64 * v:64 * v + 64, :], start=True, stop=True)
                mm.then_inc(*made.one())
                pe.wait_ge(*ready.at(1))
                for t in range(2):
                    for h in range(8):
                        mm = nc.tensor.transpose(K.ps[0:N_CMP, 2 + 2 * t + h // 4, (h % 4) * P:(h % 4 + 1) * P], pc[:, t, h], K.con(C_ID))
                mm.then_inc(*turned.one())
                pe.wait_ge(*copied.at(1))
                for t in range(2):
                    for h in range(8):
                        mm = nc.tensor.matmul(K.ps[:, 6 + t, h * HD:(h + 1) * HD], pcT[:, t, h], vC[:, h // 4], start=True, stop=True)
                mm.then_inc(*pv.one())

            @block.scalar
            def _(act):
                nc.scalar.activation(gates[:], vg[:, :, 128:152], ACT.Sigmoid).then_inc(*gated.one())
                act.wait_ge(*e_in.at(1))
                nc.scalar.activation(pc[:], pc[:], ACT.Exp).then_inc(*e_done.one())

            @block.vector
            def _(dve):
                v = nc.vector
                do = lambda ins: link(dve, K.dve_step, ins)
                bc = lambda ap: ap.to_broadcast([P, 8, N_CMP])
                do(v.tensor_scalar(madd[:], M, 1.0, -NEG, ALU.subtract, ALU.mult))
                dve.wait_ge(*made.at(1))
                S = K.ps[:, 0:2, 0:128].rearrange("p v (t g n) -> p t v g n", t=2, g=NSA_GROUP)
                for t in range(2):
                    for kv in range(NSA_KV):
                        last = v.scalar_tensor_tensor(out=pc[:, t, 4 * kv:4 * kv + 4], in0=S[:, t, kv, :, 0:N_CMP], scalar=scale,
                                                      in1=madd[:, t:t + 1].to_broadcast([P, 4, N_CMP]), op0=ALU.mult, op1=ALU.add)
                    do(last)
                    do(v.reduce_max(stat[:, t, :, 0:1], pc[:, t], AX))
                    last = v.tensor_tensor(pc[:, t], pc[:, t], bc(stat[:, t, :, 0:1]), ALU.subtract)
                last.then_inc(*e_in.one())
                dve.wait_ge(*e_done.at(1))
                dve.wait_ge(*gated.at(1))
                for t in range(2):
                    do(v.tensor_tensor(pc[:, t], pc[:, t], bc(M[:, t:t + 1]), ALU.mult))
                    do(v.reduce_sum(stat[:, t, :, 0:1], pc[:, t], AX))
                    do(v.tensor_scalar(stat[:, t, :, 0:1], stat[:, t, :, 0:1], 1e-30, None, ALU.max))
                    do(v.reciprocal(stat[:, t, :, 1:2], stat[:, t, :, 0:1]))
                    gt = gates[:, t].rearrange("p (h c) -> p h c", c=3)
                    do(v.tensor_tensor(stat[:, t, :, 1:2], stat[:, t, :, 1:2], gt[:, :, 0:1], ALU.mult))
                    last = v.tensor_tensor(pc[:, t], pc[:, t], bc(stat[:, t, :, 1:2]), ALU.mult)
                last.then_inc(*ready.one())
                dve.wait_ge(*turned.at(1))
                for t in range(2):
                    last = v.tensor_copy(pcT[:, t].rearrange("c (a h) q -> c a (h q)", a=2), K.ps[0:N_CMP, 2 + 2 * t:4 + 2 * t, :])
                last.then_inc(*copied.one())
                dve.wait_ge(*pv.at(1))
                for t in range(2):
                    v.tensor_copy(joined[:, t, 0:512], K.ps[:, 6 + t])
        dense_branches(K, roped, vs, vg, gates, joined)


def compress_weights(K, ctx):
    nc, I = K.nc, K.ins
    def sb(name, shape):
        return ctx.enter_context(nc.sbuf_tensor(name, shape, F32))
    w1, w2, pe_rows = sb("cw1", [P, 2, CMP_BLOCK, HD]), sb("cw2", [HD, 2, HD]), sb("pe_rows", [CMP_BLOCK, 2, 2, HD])
    given = K.sig("compress_given")
    with nc.Block() as block:
        @block.sync
        def _(sp):
            for j, kind in enumerate("kv"):
                for v in range(2):
                    sp.dma_start(w1[64 * v:64 * v + 64, j], I[f"a_cmp_w1_{kind}_2"][0].rearrange("(l d) m -> d l m", d=HD)).then_inc(*given.dma())
                    sp.dma_start(pe_rows[:, j, v], I[f"a_cmp_pe_{kind}_2"][0]).then_inc(*given.dma())
                sp.dma_start(w2[:, j], I[f"a_cmp_w2_{kind}_2"][0]).then_inc(*given.dma())
    return w1, w2, pe_rows, given


def compress(K, weights, kc, vc, kC, vC):
    nc, I = K.nc, K.ins
    half = CMP_STRIDE
    w1, w2, pe_rows, given = weights
    with ExitStack() as ctx:
        def sb(name, shape):
            return ctx.enter_context(nc.sbuf_tensor(name, shape, F32))
        peT = sb("peT", [P, 2, CMP_BLOCK])
        xs = sb("cmp_x", [P, 2, 2, SEQ])
        hidden = sb("cmp_h", [HD, 2, 2, N_CMP])
        turned, ready = K.sig("t_made"), K.sig("p_ready")
        made, silu, out = K.sig("tile_made"), K.sig("silu_made"), K.sig("pv_made")
        block = ctx.enter_context(nc.Block())

        @block.tensor
        def _(pe):
            pe.wait_ge(*given.at(160))
            for j in range(2):
                mm = nc.tensor.transpose(K.ps[:, 0, j * CMP_BLOCK:(j + 1) * CMP_BLOCK], pe_rows[:, j].rearrange("l v d -> l (v d)"),
                                         K.cst[0:CMP_BLOCK, C_ID:C_ID + CMP_BLOCK])
            mm.then_inc(*turned.one())
            pe.wait_ge(*ready.at(1))
            for j in range(2):
                for v in range(2):
                    rows = slice(64 * v, 64 * v + 64)
                    for l in range(CMP_BLOCK):
                        x = xs[rows, j, l // half].rearrange("p (b r) -> p b r", r=half)[:, l // half:l // half + N_CMP, l % half]
                        mm = nc.tensor.matmul(K.ps[0:HD, 1 + 2 * j + v, 0:N_CMP], w1[rows, j, l], x,
                                              start=l == 0, stop=l == CMP_BLOCK - 1)
            mm.then_inc(*made.one())
            pe.wait_ge(*silu.at(1))
            for v in range(2):
                nc.tensor.matmul(K.ps[64 * v:64 * v + 64, 5, 0:N_CMP], w2[:, 0], hidden[:, 0, v], start=True, stop=True)
                mm = nc.tensor.matmul(K.ps[0:N_CMP, 6, v * HD:(v + 1) * HD], hidden[:, 1, v], w2[:, 1], start=True, stop=True)
            mm.then_inc(*out.one())

        @block.vector
        def _(dve):
            dve.wait_ge(*turned.at(1))
            link(dve, K.dve_step, nc.vector.tensor_copy(peT[:], K.ps[:, 0, 0:2 * CMP_BLOCK].rearrange("p (j l) -> p j l", j=2)))
            for j, x in enumerate((kc, vc)):
                for a in range(2):
                    last = nc.vector.tensor_tensor(xs[:, j, a].rearrange("p (b r) -> p b r", r=half), x.rearrange("p (b r) -> p b r", r=half),
                                                   peT[:, j:j + 1, a * half:(a + 1) * half].to_broadcast([P, SEQ // half, half]), ALU.add)
            last.then_inc(*ready.one())
            dve.wait_ge(*out.at(1))
            nc.vector.tensor_copy(kC[:], K.ps[:, 5, 0:N_CMP])
            nc.vector.tensor_copy(vC[:], K.ps[0:N_CMP, 6, 0:2 * HD].rearrange("n (v d) -> n v d", v=2))

        @block.scalar
        def _(act):
            act.wait_ge(*made.at(1))
            for j in range(2):
                last = nc.scalar.activation(hidden[:, j], K.ps[0:HD, 1 + 2 * j:3 + 2 * j, 0:N_CMP], ACT.Silu)
            last.then_inc(*silu.one())


def dense_branches(K, roped, vs, vg, gates, joined):
    nc = K.nc
    scale = HD ** -0.5
    units = [(b, v, g) for b in range(2) for v in range(NSA_KV) for g in range(NSA_GROUP)]
    n = len(units)
    W = 3 * P
    parts = [(0, 0, P), (1, P, W)]
    blocks = [(0, 0), (1, 0), (1, 1)]
    with ExitStack() as ctx:
        def sb(name, shape):
            return ctx.enter_context(nc.sbuf_tensor(name, shape, F32))
        S, Pr, PT = sb("nsa_s", [P, 3, W]), sb("nsa_p", [P, 3, W]), sb("nsa_pt", [P, 2, W])
        st = sb("nsa_stat", [P, 4, 2, 4])
        s_made, s_ready, e_made = K.sig("s_made"), K.sig("s_ready"), K.sig("e_made")
        t_made, t_taken, pv_made, o_taken = K.sig("t_made"), K.sig("t_taken"), K.sig("pv_made"), K.sig("o_taken")
        block = ctx.enter_context(nc.Block())

        @block.tensor
        def _(pe):
            for u in range(n + 2):
                if u < n:
                    b, v, g = units[u]
                    rows = slice(64 * v, 64 * v + 64)
                    if u >= 3:
                        pe.wait_ge(*s_ready.at(u - 2))
                    for t, lo, hi in parts:
                        mm = nc.tensor.matmul(K.ps[:, u % 3, lo:hi], roped[rows, g, t * P:(t + 1) * P], roped[rows, 5 + b, 0:hi - lo],
                                              start=True, stop=True)
                    mm.then_inc(*s_made.one())
                if 1 <= u <= n:
                    w = u - 1
                    pe.wait_ge(*e_made.at(w + 1))
                    if w >= 2:
                        pe.wait_ge(*t_taken.at(w - 1))
                    for j in range(3):
                        mm = nc.tensor.transpose(K.ps[:, 3 + w % 2, j * P:(j + 1) * P], Pr[:, w % 3, j * P:(j + 1) * P], K.con(C_ID))
                    mm.then_inc(*t_made.one())
                if u >= 2:
                    w = u - 2
                    b, v, g = units[w]
                    pe.wait_ge(*t_taken.at(w + 1))
                    if w >= 2:
                        pe.wait_ge(*o_taken.at(w - 1))
                    for j, (t, kt) in enumerate(blocks):
                        mm = nc.tensor.matmul(K.ps[:, 5 + w % 2, t * HD:(t + 1) * HD], PT[:, w % 2, j * P:(j + 1) * P],
                                              (vs, vg)[b][:, kt, v * HD:(v + 1) * HD], start=kt == 0, stop=kt == t)
                    mm.then_inc(*pv_made.one())

        @block.vector
        def _(dve):
            causal = K.cst[:, C_CAUSAL:C_CAUSAL + P]
            for u in range(n + 3):
                if u < n:
                    dve.wait_ge(*s_made.at(u + 1))
                    if u >= 3:
                        dve.wait_ge(*e_made.at(u - 2))
                    nc.vector.tensor_scalar(S[:, u % 3, P:2 * P], K.ps[:, u % 3, P:2 * P], scale, None, ALU.mult)
                    nc.vector.scalar_tensor_tensor(out=S[:, u % 3, 0:P], in0=K.ps[:, u % 3, 0:P], scalar=scale, in1=causal,
                                                   op0=ALU.mult, op1=ALU.add)
                    link(dve, K.dve_step, nc.vector.scalar_tensor_tensor(
                        out=S[:, u % 3, 2 * P:W], in0=K.ps[:, u % 3, 2 * P:W], scalar=scale, in1=causal, op0=ALU.mult, op1=ALU.add))
                    for t, lo, hi in parts:
                        last = nc.vector.reduce_max(st[:, u % 4, t, 3:4], S[:, u % 3, lo:hi], AX)
                    link(dve, K.dve_step, last)
                    nc.vector.tensor_scalar(st[:, u % 4, :, 0:1], st[:, u % 4, :, 3:4], -1.0, None, ALU.mult).then_inc(*s_ready.one())
                if u >= 3:
                    w = u - 3
                    b, v, g = units[w]
                    h = 4 * v + g
                    dve.wait_ge(*pv_made.at(w + 1))
                    link(dve, K.dve_step, nc.vector.reciprocal(st[:, w % 4, :, 2:3], st[:, w % 4, :, 1:2]))
                    link(dve, K.dve_step, nc.vector.tensor_tensor(st[:, w % 4, :, 2:3], st[:, w % 4, :, 2:3],
                                                                  gates[:, :, 3 * h + 1 + b:3 * h + 2 + b], ALU.mult))
                    for t in range(2):
                        o = joined[:, t, h * HD:(h + 1) * HD]
                        last = nc.vector.scalar_tensor_tensor(out=o, in0=K.ps[:, 5 + w % 2, t * HD:(t + 1) * HD], scalar=st[:, w % 4, t, 2:3],
                                                              in1=o, op0=ALU.mult, op1=ALU.add)
                    last.then_inc(*o_taken.one())

        @block.scalar
        def _(act):
            for u in range(n + 1):
                if u < n:
                    act.wait_ge(*s_ready.at(u + 1))
                    if u >= 3:
                        act.wait_ge(*t_made.at(u - 2))
                    for t, lo, hi in parts:
                        last = nc.scalar.activation(Pr[:, u % 3, lo:hi], S[:, u % 3, lo:hi], ACT.Exp, bias=st[:, u % 4, t, 0:1],
                                                    accum_out=st[:, u % 4, t, 1:2])
                    last.then_inc(*e_made.one())
                if u >= 1:
                    w = u - 1
                    act.wait_ge(*t_made.at(w + 1))
                    if w >= 2:
                        act.wait_ge(*pv_made.at(w - 1))
                    nc.scalar.copy(PT[:, w % 2], K.ps[:, 3 + w % 2, 0:W]).then_inc(*t_taken.one())


def ssd(K, xbc, z, dt, joined):
    nc, I = K.nc, K.ins
    NT = XBC // P
    with ExitStack() as ctx:
        def sb(name, shape):
            return ctx.enter_context(nc.sbuf_tensor(name, shape, F32))
        cv = sb("conv", [P, NT, SEQ])
        row = sb("ssd_rows", [P, 3, SSD_HEADS])
        normw = sb("ssd_normw", [P, SSD_INNER])
        sp_ = sb("softplus", [P, 2, 3, SSD_HEADS])
        dta, acs = sb("dta", [P, 2, SSD_HEADS]), sb("acs", [P, 2, 4, SSD_HEADS])
        given, conv_done = K.sig("rows_given"), K.sig("pooled")
        a_in, a_done = K.sig("exp_asked"), K.sig("exp_done")
        acs_made = K.sig("s_made")
        with nc.Block() as block:
            @block.sync
            def _(s):
                for j, name in enumerate(("b_dt_bias_2", "b_a_log_2", "b_d_skip_2")):
                    s.dma_start(row[:, j], I[name].to_broadcast([P, SSD_HEADS])).then_inc(*given.dma())
                s.dma_start(normw[:], I["b_norm_w_2"].to_broadcast([P, SSD_INNER])).then_inc(*given.dma())

            @block.vector
            def _(dve):
                v = nc.vector
                do = lambda ins: link(dve, K.dve_step, ins)
                dve.wait_ge(*given.at(64))
                for t in range(2):
                    do(v.tensor_tensor(sp_[:, t, 0], dt[:, t], row[:, 0], ALU.add))
                    do(v.tensor_scalar(sp_[:, t, 1], sp_[:, t, 0], -1.0, None, ALU.mult))
                    do(v.tensor_tensor(sp_[:, t, 1], sp_[:, t, 1], sp_[:, t, 0], ALU.min))
                    last = v.tensor_scalar(sp_[:, t, 0], sp_[:, t, 0], 0.0, None, ALU.max)
                last.then_inc(*a_in.one())
                cw = lambda tap, c: K.col("b_conv_w_2", tap * NT + c)
                for c in range(NT):
                    v.tensor_scalar(cv[:, c], xbc[:, c], cw(SSD_CONV - 1, c), K.col("b_conv_b_2", c), ALU.mult, ALU.add).then_inc(*K.dve_step.one())
                for s in range(1, SSD_CONV):
                    dve.wait_ge(*K.dve_step.now())
                    for c in range(NT):
                        last = v.scalar_tensor_tensor(out=cv[:, c, s:], in0=xbc[:, c, 0:SEQ - s], scalar=cw(SSD_CONV - 1 - s, c),
                                                      in1=cv[:, c, s:], op0=ALU.mult, op1=ALU.add)
                    last.then_inc(*K.dve_step.one())
                last2 = v.memset(acs[:], 0.0)
                last2.then_inc(*conv_done.one())
                dve.wait_ge(*a_done.at(1))
                for t in range(2):
                    do(v.tensor_tensor(dt[:, t], sp_[:, t, 0], sp_[:, t, 2], ALU.add))
                    last = v.scalar_tensor_tensor(out=dta[:, t], in0=dt[:, t], scalar=-1.0, in1=row[:, 1], op0=ALU.mult, op1=ALU.mult)
                last.then_inc(*a_in.one())
                dve.wait_ge(*acs_made.at(1))
                for t in range(2):
                    do(v.tensor_copy(acs[:, t, 0], K.ps[:, 0, t * 16:t * 16 + 16]))
                do(v.tensor_tensor(acs[:, 0, 1], K.ps[:, 0, 32:48], acs[:, 0, 0], ALU.subtract))

            @block.tensor
            def _(pe):
                pe.wait_ge(*a_in.at(2))
                for t in range(2):
                    nc.tensor.matmul(K.ps[:, 0, t * 16:t * 16 + 16], K.con(C_TRI), dta[:, t], start=True, stop=True)
                nc.tensor.matmul(K.ps[:, 0, 32:48], K.con(C_ONE), dta[:, 0], start=True, stop=True).then_inc(*acs_made.one())

            @block.scalar
            def _(act):
                act.wait_ge(*a_in.at(1))
                link(act, K.act_step, nc.scalar.activation(sp_[:, :, 1], sp_[:, :, 1], ACT.Exp))
                nc.scalar.activation(row[:, 1], row[:, 1], ACT.Exp)
                nc.scalar.activation(sp_[:, :, 2], sp_[:, :, 1], ACT.Ln, bias=1.0).then_inc(*a_done.one())
                act.wait_ge(*conv_done.at(1))
                nc.scalar.activation(cv[:], cv[:], ACT.Silu)
        ssd_chunks(K, cv, z, dt, dta, acs, row, normw, joined)


def ssd_chunks(K, cv, z, dt, dta, acs, row, normw, joined):
    nc = K.nc
    HG = SSD_HEADS // SSD_GROUPS
    hp = lambda ap: ap.rearrange("p (h d) -> p h d", d=HD)
    with ExitStack() as ctx:
        def sb(name, shape):
            return ctx.enter_context(nc.sbuf_tensor(name, shape, F32))
        xs, xd = sb("ssd_xs", [P, 2, SSD_INNER]), sb("ssd_xd", [P, 2, SSD_INNER])
        xdd = sb("ssd_xdd", [P, SSD_INNER])
        bt = sb("ssd_bt", [P, SSD_GROUPS, SSD_STATE])
        cb = sb("ssd_cb", [P, 2, SSD_GROUPS, P])
        state = sb("ssd_state", [P, SSD_GROUPS, HG * HD])
        ms = sb("ssd_ms", [P, 2, SSD_GROUPS, 2])
        made, taken = K.sig("tile_made"), K.sig("tile_stored")
        e_in, e_done = K.sig("exp_asked"), K.sig("exp_done")
        st_in, st_made, st_taken = K.sig("p_ready"), K.sig("pv_made"), K.sig("o_taken")
        with nc.Block() as block:
            @block.tensor
            def _(pe):
                for n in range(4):
                    for k in range(4):
                        mm = nc.tensor.transpose(K.ps[:, n, k * P:(k + 1) * P], cv[:, 4 * (n % 2) + k, (n // 2) * P:(n // 2 + 1) * P], K.con(C_ID))
                    mm.then_inc(*made.one())
                for g in range(SSD_GROUPS):
                    mm = nc.tensor.transpose(K.ps[:, 4, g * P:(g + 1) * P], cv[:, 8 + g, 0:P], K.con(C_ID))
                mm.then_inc(*made.one())
                for c in range(2):
                    for g in range(SSD_GROUPS):
                        t = slice(c * P, (c + 1) * P)
                        mm = nc.tensor.matmul(K.ps[:, 5, (2 * c + g) * P:(2 * c + g + 1) * P], cv[:, 8 + g, t], cv[:, 10 + g, t], start=True, stop=True)
                mm.then_inc(*made.one())
                pe.wait_ge(*st_in.at(1))
                for g in range(SSD_GROUPS):
                    mm = nc.tensor.matmul(K.ps[:, 6 + g], bt[:, g], xdd[:, g * 512:(g + 1) * 512], start=True, stop=True)
                mm.then_inc(*st_made.one())

            @block.scalar
            def _(act):
                nc.scalar.activation(acs[:, 0, 1], acs[:, 0, 1], ACT.Exp)
                nc.scalar.activation(acs[:, 1, 2], acs[:, 1, 0], ACT.Exp).then_inc(*e_done.one())
                nc.scalar.activation(z[:], z[:], ACT.Silu)

            @block.vector
            def _(dve):
                v = nc.vector
                do = lambda ins: link(dve, K.dve_step, ins)
                for n in range(4):
                    dve.wait_ge(*made.at(n + 1))
                    last = v.tensor_copy(xs[:, n // 2, 512 * (n % 2):512 * (n % 2) + 512], K.ps[:, n])
                do(last)
                for t in range(2):
                    do(v.tensor_tensor(hp(xd[:, t]), hp(xs[:, t]), dt[:, t].rearrange("p (h a) -> p h a", a=1).to_broadcast([P, 16, HD]), ALU.mult))
                dve.wait_ge(*e_done.at(1))
                do(v.tensor_tensor(hp(xdd[:]), hp(xd[:, 0]), acs[:, 0, 1].rearrange("p (h a) -> p h a", a=1).to_broadcast([P, 16, HD]), ALU.mult))
                dve.wait_ge(*made.at(5))
                v.tensor_copy(bt[:], K.ps[:, 4, 0:256].rearrange("p (g n) -> p g n", g=2)).then_inc(*st_in.one())
                dve.wait_ge(*made.at(6))
                v.tensor_tensor(cb[:].rearrange("p c g n -> p (c g) n"), K.ps[:, 5].rearrange("p (x n) -> p x n", x=4),
                                K.con(C_TRI).rearrange("p (a n) -> p a n", a=1).to_broadcast([P, 4, P]), ALU.mult)
                dve.wait_ge(*st_made.at(1))
                v.tensor_copy(state[:], K.ps[:, 6:8])
        units = [(c, g, q) for c in range(2) for g in range(SSD_GROUPS) for q in range(2)]
        n = len(units)
        seg = sb("ssd_seg", [P, 2, 4, P])
        made, s_ready, e_made, ready = K.sig("s_made"), K.sig("s_ready"), K.sig("e_made"), K.sig("p_ready")
        used, y_made, y_off = K.sig("t_made"), K.sig("pv_made"), K.sig("o_taken")
        with nc.Block() as block:
            @block.tensor
            def _(pe):
                for g in range(SSD_GROUPS):
                    mm = nc.tensor.matmul(K.ps[:, 6 + g], cv[:, 10 + g, P:2 * P], state[:, g], start=True, stop=True)
                mm.then_inc(*y_off.one())
                for u in range(n + 1):
                    if u < n:
                        c, g, q = units[u]
                        if u >= 2:
                            pe.wait_ge(*s_ready.at(u - 1))
                        for j in range(4):
                            h = g * HG + q * 4 + j
                            mm = nc.tensor.matmul(K.ps[:, u % 2, j * P:(j + 1) * P], dta[:, c, h:h + 1].to_broadcast([P, P]), K.con(C_TRI),
                                                  start=True, stop=True)
                        mm.then_inc(*made.one())
                    if u >= 1:
                        c, g, q = units[u - 1]
                        pe.wait_ge(*ready.at(u))
                        for j in range(4):
                            h = g * HG + q * 4 + j
                            at = (q * 4 + j) * HD
                            mm = nc.tensor.matmul(K.ps[:, 2 + 2 * c + g, at:at + HD], seg[:, (u - 1) % 2, j], xd[:, c, h * HD:(h + 1) * HD],
                                                  start=True, stop=True)
                        mm.then_inc(*y_made.one())

            @block.scalar
            def _(act):
                for u in range(n):
                    act.wait_ge(*s_ready.at(u + 1))
                    nc.scalar.activation(seg[:, u % 2], seg[:, u % 2], ACT.Exp).then_inc(*e_made.one())
                act.wait_ge(*used.at(1))
                for c in range(2):
                    for g in range(SSD_GROUPS):
                        last = nc.scalar.activation(xd[:, c, g * 512:(g + 1) * 512], xs[:, c, g * 512:(g + 1) * 512], ACT.Square,
                                                    accum_out=ms[:, c, g, 0:1])
                link(act, K.act_step, last)
                nc.scalar.activation(ms[:, :, :, 1:2], ms[:, :, :, 0:1], ACT.Sqrt, bias=K.eps[:, 1:2], scale=1.0 / (HG * HD)).then_inc(*used.one())

            @block.vector
            def _(dve):
                v = nc.vector
                do = lambda ins: link(dve, K.dve_step, ins)
                wide = lambda ap: ap.rearrange("p (h a) -> p h a", a=1)
                for u in range(n + 1):
                    if u < n:
                        c, g, q = units[u]
                        dve.wait_ge(*made.at(u + 1))
                        if u >= 2:
                            dve.wait_ge(*y_made.at(u - 1))
                        h = g * HG + q * 4
                        do(v.tensor_tensor(seg[:, u % 2], K.ps[:, u % 2].rearrange("p (j l) -> p j l", j=4),
                                           wide(acs[:, c, 0, h:h + 4]).to_broadcast([P, 4, P]), ALU.subtract))
                        v.tensor_scalar(seg[:, u % 2], seg[:, u % 2], 0.0, None, ALU.min).then_inc(*s_ready.one())
                    if u >= 1:
                        c, g, q = units[u - 1]
                        dve.wait_ge(*e_made.at(u))
                        v.tensor_tensor(seg[:, (u - 1) % 2], seg[:, (u - 1) % 2], cb[:, c, g:g + 1].to_broadcast([P, 4, P]), ALU.mult).then_inc(*ready.one())
                dve.wait_ge(*y_made.at(n))
                dve.wait_ge(*y_off.at(1))
                for c in range(2):
                    do(v.tensor_tensor(hp(xs[:, c]), hp(xs[:, c]), wide(row[:, 2]).to_broadcast([P, 16, HD]), ALU.mult))
                    for g in range(SSD_GROUPS):
                        part = xs[:, c, g * 512:(g + 1) * 512]
                        do(v.tensor_tensor(part, part, K.ps[:, 2 + 2 * c + g], ALU.add))
                        if c == 1:
                            tmp = xdd[:, g * 512:(g + 1) * 512]
                            do(v.tensor_tensor(hp(tmp), hp(K.ps[:, 6 + g]), wide(acs[:, 1, 2, g * HG:(g + 1) * HG]).to_broadcast([P, HG, HD]), ALU.mult))
                            do(v.tensor_tensor(part, part, tmp, ALU.add))
                last = v.tensor_tensor(xs[:], xs[:], z[:], ALU.mult)
                last.then_inc(*used.one())
                dve.wait_ge(*used.at(2))
                do(v.reciprocal(ms[:, :, :, 0:1], ms[:, :, :, 1:2]))
                for c in range(2):
                    for g in range(SSD_GROUPS):
                        at = g * 512
                        v.scalar_tensor_tensor(out=joined[:, c, 512 + at:1024 + at], in0=xs[:, c, at:at + 512], scalar=ms[:, c, g, 0:1],
                                               in1=normw[:, at:at + 512], op0=ALU.mult, op1=ALU.mult)


def rwkv(K, scratch, gain):
    nc, I = K.nc, K.ins
    X = K.xn[:, :, 0:SEQ]
    with ExitStack() as ctx:
        def sb(name, shape):
            return ctx.enter_context(nc.sbuf_tensor(name, shape, F32))
        v, g = sb("rw_v", [P, 2, D]), sb("rw_g", [P, 2, D])
        y = sb("rw_y", [P, 2, D])
        with ExitStack() as inner:
            def sbi(name, shape):
                return inner.enter_context(nc.sbuf_tensor(name, shape, F32))
            r, k, sg, a = (sbi(f"rw_{n}", [P, KT, SEQ]) for n in ("r", "k", "sg", "a"))
            mix_v = y[:].rearrange("p a (k t) -> p (a k) t", t=SEQ)
            values = Linears(K, [Linear(I["c_w_v_2"][0], lambda k, t0, tn: mix_v[:, k, t0:t0 + tn],
                                        lambda i, at, n, ps: nc.scalar.copy(v[:, i, at:at + n], ps), tiles=TT, by="scalar")])
            rwkv_projections(K, gain, values, X, r, k, sg, a, mix_v, g)
            ar = sbi("rw_ar", [P, KT, 2, SEQ])
            kk = sbi("rw_kk", [P, KT, SEQ])
            cl = sbi("rw_cl", [P, KT, N_RC])
            bon = sbi("rw_bonus", [P, 2, RW_HEADS])
            rwkv_factors(K, values, r, k, sg, a, kk, ar, cl)
            bp, kp = sbi("rw_bp", [P, 2, D]), sbi("rw_kp", [P, 2, D])
            sc = sbi("rw_sc", [P, 32, 4, RC])
            rwkv_scores(K, a, k, r, kk, ar, bp, kp, sc, bon)
            tm = sbi("rw_tm", [P, 32, RC])
            nv = sbi("rw_nv", [P, 2, 2, D])
            flat = lambda buf: buf[:].rearrange("p f t -> p (f t)")
            rwkv_inverse(K, sc, v, tm, nv, scratch, flat(sg), flat(kk))
            rwkv_chunks(K, ar, cl, bp, kp, sc, tm, nv, v, y, flat(a), flat(sg))
            rwkv_output(K, y, v, g, bon, flat(k).rearrange("p (j n) -> p j n", j=2), flat(r))
        project_joined(K, y, KT, I["c_w_o_2"][0])


def rwkv_projections(K, gain, values, X, r, k, sg, a, mix_v, g):
    nc, I = K.nc, K.ins
    with ExitStack() as ctx:
        def sb(name, shape):
            return ctx.enter_context(nc.sbuf_tensor(name, shape, F32))
        mixed = sb("rw_mix", [P, 5, KT, SEQ])
        mix = [mixed[:, i] for i in range(3)] + [mix_v] + [mixed[:, i] for i in (3, 4)]
        low = sb("rw_low", [P, 2, SEQ])
        xx = K.sq[:, :, 0:SEQ]
        feat = lambda i: (lambda kt: mix[i][:, kt])
        def matrix(name, x, store, **more):
            return Linear(I[f"c_{name}_2"][0], x, store, **more)
        def lora_in(name, i, row, func):
            return matrix(name, feat(i), lambda m, ps: nc.scalar.activation(K.rs[0:64, row, 0:SEQ], ps, func), T=SEQ, by="scalar")
        def lora_out(name, row, dst, bias, after):
            return matrix(name, lambda kt: K.rs[0:64, row, 0:SEQ],
                          lambda m, ps: nc.scalar.activation(dst[:, m], ps, ACT.Sigmoid, bias=K.col(bias, m)), T=SEQ, by="scalar", after=after)
        w1, a1 = lora_in("w1", 1, 0, ACT.Tanh), lora_in("a1", 4, 1, ACT.Copy)
        g1 = matrix("g1", feat(5), lambda m, ps: nc.scalar.activation(low[0:ps.shape[0], m], ps, ACT.Sigmoid), T=SEQ, by="scalar")
        ga = Linear(I["c_g2_2"][0, 0:P], lambda kt, t0, tn: low[:, 0, t0:t0 + tn],
                    lambda i, at, n, ps: nc.vector.tensor_copy(g[:, i, at:at + n], ps), tiles=TT, after=g1)
        gb = Linear(I["c_g2_2"][0, P:GATE_LORA], lambda kt, t0, tn: low[0:GATE_LORA - P, 1, t0:t0 + tn],
                    lambda i, at, n, ps: nc.vector.tensor_tensor(g[:, i, at:at + n], g[:, i, at:at + n], ps, ALU.add),
                    tiles=TT, after=g1, onto=ga)
        project = Linears(K, [
            w1, a1, g1, matrix("w_r", feat(0), lambda m, ps: nc.vector.tensor_copy(r[:, m], ps), T=SEQ),
            lora_out("w2", 0, sg, "c_w0_2", w1), lora_out("a2", 1, a, "c_a0_2", a1), ga, gb,
            matrix("w_k", feat(2), lambda m, ps: nc.vector.tensor_copy(k[:, m], ps), T=SEQ)])
        K.coming = project
        rms_norm(K, K.h[:, :, 0:SEQ], X, gain)
        with nc.Block() as block:
            load_ahead(K, block)

            @block.vector
            def _(dve):
                nc.vector.tensor_tensor(xx[:, :, 1:], X[:, :, 0:SEQ - 1], X[:, :, 1:], ALU.subtract)
                link(dve, K.dve_step, nc.vector.tensor_scalar(xx[:, :, 0:1], X[:, :, 0:1], -1.0, None, ALU.mult))
                for i in range(6):
                    for kt in range(KT):
                        nc.vector.scalar_tensor_tensor(out=mix[i][:, kt], in0=xx[:, kt], scalar=K.col("c_mu_2", 8 * i + kt),
                                                       in1=X[:, kt], op0=ALU.mult, op1=ALU.add)
        K.coming = values
        project.run()


def rwkv_factors(K, values, r, k, sg, a, kk, ar, cl):
    nc = K.nc
    c1, c2 = K.sq[:, :, 0:SEQ], K.xn[:, :, 0:SEQ]
    ch = lambda ap: ap.rearrange("p f (c t) -> p f c t", t=RC)
    squared, made, rooted = K.sig("squared"), K.sig("tile_made"), K.sig("rooted")
    kk_in, cum, cum2, cexp = K.sig("s_ready"), K.sig("exp_asked"), K.sig("pooled"), K.sig("exp_done")
    def tensor(pe):
        pe.wait_ge(*squared.at(1))
        for f in range(KT):
            mm = nc.tensor.matmul(K.ps[:, 4 + f // 2, (f % 2) * SEQ:(f % 2 + 1) * SEQ], K.con(C_HEAD), ar[:, f, 0], start=True, stop=True)
        mm.then_inc(*made.one())

    def scalar(act):
        act.wait_ge(*kk_in.at(1))
        nc.scalar.activation(ar[:, :, 0], kk[:], ACT.Square).then_inc(*squared.one())
        act.wait_ge(*made.at(1))
        nc.scalar.activation(ar[:, :, 1], K.ps[:, 4:8].rearrange("p b (f t) -> p (b f) t", f=2), ACT.Sqrt).then_inc(*rooted.one())
        act.wait_ge(*cum.at(1))
        nc.scalar.activation(c2, c1, ACT.Exp).then_inc(*cexp.one())
        nc.scalar.activation(sg[:], sg[:], ACT.Exp).then_inc(*cexp.one())
        link(act, K.act_step, nc.scalar.activation(c1, c1, ACT.Exp, scale=-1.0))
        nc.scalar.copy(cl[:], ch(c2)[:, :, :, RC - 1]).then_inc(*cexp.one())

    def vector(dve):
        v = nc.vector
        do = lambda ins: link(dve, K.dve_step, ins)
        for f in range(KT):
            last = v.tensor_scalar(kk[:, f], k[:, f], K.col("c_k_k_2", f), None, ALU.mult)
        last.then_inc(*kk_in.one())
        for f in range(KT):
            last = v.tensor_scalar(c2[:, f], a[:, f], 1.0, K.col("c_k_a_2", f), ALU.subtract, ALU.mult)
        do(last)
        do(v.scalar_tensor_tensor(out=k[:], in0=c2, scalar=1.0, in1=k[:], op0=ALU.add, op1=ALU.mult))
        do(v.tensor_scalar(sg[:], sg[:], -math.exp(-0.5), None, ALU.mult))
        src, dst = sg[:], c1
        s = 1
        while s < RC:
            v.tensor_copy(ch(dst)[:, :, :, 0:s], ch(src)[:, :, :, 0:s])
            for f in range(KT):
                last = v.tensor_tensor(ch(dst)[:, f, :, s:], ch(src)[:, f, :, s:], ch(src)[:, f, :, 0:RC - s], ALU.add)
            do(last)
            src, dst = dst, (c2 if dst is c1 else c1)
            s *= 2
        assert src is c1
        v.tensor_tensor(sg[:], c1, sg[:], ALU.subtract).then_inc(*cum.one())
        dve.wait_ge(*rooted.at(1))
        do(v.tensor_scalar(ar[:, :, 1], ar[:, :, 1], 1e-12, None, ALU.max))
        do(v.reciprocal(ar[:, :, 1], ar[:, :, 1]))
        do(v.tensor_tensor(kk[:], kk[:], ar[:, :, 1], ALU.mult))
        do(v.tensor_tensor(a[:], a[:], kk[:], ALU.mult))
        dve.wait_ge(*cexp.at(1))
        do(v.tensor_tensor(ar[:, :, 1], c2, r[:], ALU.mult))
        for f in range(KT):
            last = v.scalar_tensor_tensor(out=r[:, f], in0=r[:, f], scalar=K.col("c_r_k_2", f), in1=k[:, f], op0=ALU.mult, op1=ALU.mult)
        do(last)
        dve.wait_ge(*cexp.at(2))
        v.scalar_tensor_tensor(out=ar[:, :, 0], in0=sg[:], scalar=-1.0, in1=kk[:], op0=ALU.mult, op1=ALU.mult).then_inc(*K.dve_step.one())
        dve.wait_ge(*cexp.at(3))
        v.tensor_tensor(a[:], a[:], c1, ALU.mult).then_inc(*K.dve_step.one())
        do(v.tensor_tensor(k[:], k[:], c1, ALU.mult))
        for f in range(KT):
            end = cl[:, f].rearrange("p (c a) -> p c a", a=1).to_broadcast([P, N_RC, RC])
            v.tensor_tensor(ch(c2)[:, f], ch(a[:])[:, f], end, ALU.mult)
            v.tensor_tensor(ch(kk[:])[:, f], ch(k[:])[:, f], end, ALU.mult)
    values.run(before={"tensor": tensor, "scalar": scalar, "vector": vector})


def rwkv_scores(K, bt, kt, rk, kend, ar, bp, kp, sc, bon):
    nc = K.nc
    bend = K.xn[:, :, 0:SEQ]
    made, taken = K.sig("tile_made"), K.sig("tile_stored")
    with nc.Block() as block:
        @block.tensor
        def _(pe):
            for n in range(8):
                src = (bend, kend)[n // 4]
                t, half = n // 2 % 2, n % 2
                for j in range(4):
                    mm = nc.tensor.transpose(K.ps[:, n, j * P:(j + 1) * P], src[:, 4 * half + j, t * P:(t + 1) * P], K.con(C_ID))
                mm.then_inc(*made.one())
            for u in range(32):
                par, t, f = u // 16, u // 8 % 2, u % 8
                rows = slice(64 * par, 64 * par + 64)
                if u % 4 == 0:
                    pe.wait_ge(*taken.at(u // 4 + 1))
                for c in range(4):
                    tok = slice(t * P + c * RC, t * P + (c + 1) * RC)
                    for j, src in enumerate((bt, kt)):
                        at = (u % 4) * P + j * 2 * RC
                        mm = nc.tensor.matmul(K.ps[RC * c:RC * c + RC, u // 4, at:at + 2 * RC], src[rows, f, tok], ar[rows, f, :, tok],
                                              start=True, stop=True)
                if u % 4 == 3:
                    mm.then_inc(*made.one())
            pe.wait_ge(*taken.at(9))
            for t in range(2):
                for f in range(KT):
                    at = t * RW_HEADS + 2 * f
                    mm = nc.tensor.matmul(K.ps[:, 0, at:at + 2], rk[:, f, t * P:(t + 1) * P], K.con(C_HSEL, 2), start=True, stop=True)
            mm.then_inc(*made.one())

        @block.vector
        def _(dve):
            v = nc.vector
            for n in range(8):
                dve.wait_ge(*made.at(n + 1))
                v.tensor_copy((bp, kp)[n // 4][:, n // 2 % 2, 512 * (n % 2):512 * (n % 2) + 512], K.ps[:, n]).then_inc(*taken.one())
            for b in range(8):
                dve.wait_ge(*made.at(9 + b))
                for j in range(2):
                    mask = sc_mask(K, j)
                    for w in range(2):
                        last = v.tensor_tensor(sc[:, 4 * b:4 * b + 4, 2 * w + j], K.ps[:, b].rearrange("p (u m t) -> p u m t", u=4, m=4)[:, :, 2 * w + j],
                                               mask, ALU.mult)
                last.then_inc(*taken.one())
            dve.wait_ge(*made.at(17))
            v.tensor_copy(bon[:], K.ps[:, 0, 0:2 * RW_HEADS].rearrange("p (t h) -> p t h", t=2))


def sc_mask(K, j):
    return K.con(C_RWK + j * RC, RC).rearrange("p (a t) -> p a t", a=1).to_broadcast([P, 4, RC])


def rwkv_inverse(K, sc, v, tm, nv, scratch, room, room2):
    nc = K.nc
    with ExitStack() as ctx:
        square = lambda ap: ap.rearrange("p (s t) -> p s t", s=RC)
        N, T = square(room[:, 0:RC * RC]), square(room[:, RC * RC:2 * RC * RC])
        prod = square(room2[:, 0:RC * RC])
        out, back = K.sig("inv_out"), K.sig("inv_back")
        solved, made = K.sig("p_ready"), K.sig("tile_made")
        block = ctx.enter_context(nc.Block())

        @block.sync
        def _(sp):
            for c in range(4):
                dst = scratch[0, c * 32:(c + 1) * 32].rearrange("u (s t) -> s u t", s=RC)
                sp.dma_start(dst, sc[c * RC:(c + 1) * RC, :, 0]).then_inc(*out.dma())
            sp.wait_ge(*out.now())
            sp.dma_start(N[:].rearrange("p s t -> p (s t)"), scratch[0]).then_inc(*back.dma())
            sp.wait_ge(*solved.at(1))
            sp.dma_start(scratch[1], prod[:].rearrange("p s t -> p (s t)")).then_inc(*out.dma())
            sp.wait_ge(*out.now())
            for c in range(4):
                src = scratch[1, c * 32:(c + 1) * 32].rearrange("u (s t) -> s u t", s=RC)
                sp.dma_start(tm[c * RC:(c + 1) * RC], src).then_inc(*back.dma())
            sp.wait_ge(*back.now())

        @block.tensor
        def _(pe):
            for t in range(2):
                for par in range(2):
                    for j in range(2):
                        for c in range(4):
                            R = slice(c * RC, (c + 1) * RC)
                            for f in range(KT):
                                h, u = 2 * f + par, par * 16 + t * 8 + f
                                mm = nc.tensor.matmul(K.ps[R, 4 * t + 2 * j + par, f * HD:(f + 1) * HD], sc[R, u, 2 + j],
                                                      v[R, t, h * HD:(h + 1) * HD], start=True, stop=True)
                        mm.then_inc(*made.one())

        @block.scalar
        def _(act):
            n = 0
            for t in range(2):
                for par in range(2):
                    for j in range(2):
                        act.wait_ge(*made.at(n + 1))
                        dst = nv[:, j, t].rearrange("p (f q i) -> p q f i", q=2, i=HD)[:, par]
                        nc.scalar.copy(dst, K.ps[:, 4 * t + 2 * j + par].rearrange("p (f i) -> p f i", i=HD))
                        n += 1

        @block.vector
        def _(dve):
            vv = nc.vector
            do = lambda ins: link(dve, K.dve_step, ins)
            do(vv.memset(T[:], 0.0))
            do(vv.memset(T[:].rearrange("p s t -> p (s t)")[:, 0:RC * RC:RC + 1], 1.0))
            dve.wait_ge(*back.at(16))
            for t in range(1, RC):
                coef = N[:, 0:t, t:t + 1].rearrange("p s a -> p a s").to_broadcast([P, t, t])
                pr = prod[:].rearrange("p s t -> p (s t)")[:, 0:t * t].rearrange("p (c s) -> p c s", s=t)
                do(vv.tensor_tensor(pr, T[:, 0:t, 0:t].rearrange("p s c -> p c s"), coef, ALU.mult))
                do(vv.reduce_sum(T[:, t, 0:t].rearrange("p (c a) -> p c a", a=1), pr, AX))
            vv.tensor_copy(prod[:], T[:].rearrange("p t s -> p s t")).then_inc(*solved.one())

def rwkv_chunks(K, ar, cl, bp, kp, sc, tm, nv, v, y, room, room2):
    nc = K.nc
    with ExitStack() as ctx:
        S, Sd = (room2[:, j * KT * HD:(j + 1) * KT * HD].rearrange("p (f i) -> p f i", i=HD) for j in range(2))
        W, SA = room[:, 0:D], room[:, D:2 * D]
        as_made, w_ready, sa_made, sa_ready = K.sig("s_made"), K.sig("s_ready"), K.sig("e_made"), K.sig("p_ready")
        sa_ready_a, rs_made, kv_made = K.sig("sa_ready_a"), K.sig("rs_made"), K.sig("kv_made")
        st_made, st_ready, y_made, y_taken = K.sig("t_made"), K.sig("t_taken"), K.sig("pv_made"), K.sig("o_taken")
        by_par = lambda ap, par: ap.rearrange("p (f q i) -> p q f i", q=2, i=HD)[:, par]
        bank = lambda R, b: K.ps[R, b].rearrange("p (f i) -> p f i", i=HD)
        block = ctx.enter_context(nc.Block())

        @block.tensor
        def _(pe):
            for c in range(N_RC):
                t, R = c // 4, slice((c % 4) * RC, (c % 4 + 1) * RC)
                tok = slice(c * RC, (c + 1) * RC)
                state = lambda h, b: K.ps[64 * (h % 2):64 * (h % 2) + 64, b, (h // 2) * HD:(h // 2 + 1) * HD]
                if c:
                    pe.wait_ge(*st_ready.at(c))
                    if c >= 4:
                        pe.wait_ge(*y_taken.at(c - 3))
                    for j in range(2):
                        for par in range(2):
                            rows = slice(64 * par, 64 * par + 64)
                            for f in range(KT):
                                mm = nc.tensor.matmul(K.ps[R, 5 * j + par, f * HD:(f + 1) * HD], ar[rows, f, j, tok], S[rows, f],
                                                      start=True, stop=True)
                        mm.then_inc(*(as_made, rs_made)[j].one())
                pe.wait_ge(*w_ready.at(c + 1))
                for par in range(2):
                    for f in range(KT):
                        h, u = 2 * f + par, par * 16 + t * 8 + f
                        mm = nc.tensor.matmul(K.ps[R, 2 + par, f * HD:(f + 1) * HD], tm[R, u], W[R, h * HD:(h + 1) * HD], start=True, stop=True)
                mm.then_inc(*sa_made.one())
                if c < N_RC - 1:
                    for h in range(RW_HEADS):
                        mm = nc.tensor.matmul(state(h, 7), kp[R, t, h * HD:(h + 1) * HD], v[R, t, h * HD:(h + 1) * HD], start=True, stop=True)
                    mm.then_inc(*kv_made.one())
                pe.wait_ge(*sa_ready.at(c + 1))
                pe.wait_ge(*sa_ready_a.at(c + 1))
                if c < N_RC - 1:
                    for h in range(RW_HEADS):
                        mm = nc.tensor.matmul(state(h, 4), bp[R, t, h * HD:(h + 1) * HD], SA[R, h * HD:(h + 1) * HD], start=True, stop=True)
                    mm.then_inc(*st_made.one())
                for par in range(2):
                    for f in range(KT):
                        h, u = 2 * f + par, par * 16 + t * 8 + f
                        mm = nc.tensor.matmul(K.ps[R, par, f * HD:(f + 1) * HD], sc[R, u, 1], SA[R, h * HD:(h + 1) * HD], start=True, stop=True)
                mm.then_inc(*y_made.one())

        @block.scalar
        def _(act):
            for c in range(N_RC):
                R = slice((c % 4) * RC, (c % 4 + 1) * RC)
                act.wait_ge(*sa_made.at(c + 1))
                nc.scalar.copy(by_par(SA[R], 1), bank(R, 3)).then_inc(*sa_ready_a.one())

        @block.vector
        def _(dve):
            vv = nc.vector

            def output(c):
                t, R = c // 4, slice((c % 4) * RC, (c % 4 + 1) * RC)
                dve.wait_ge(*y_made.at(c + 1))
                if c:
                    dve.wait_ge(*carried)
                for par in range(2):
                    last = vv.tensor_tensor(by_par(y[R, t], par), bank(R, par), by_par(y[R, t] if c else nv[R, 1, t], par), ALU.add)
                last.then_inc(*y_taken.one())
            for c in range(N_RC):
                t, R = c // 4, slice((c % 4) * RC, (c % 4 + 1) * RC)
                if c:
                    dve.wait_ge(*as_made.at(c))
                    for par in range(2):
                        last = vv.tensor_tensor(by_par(W[R], par), bank(R, par), by_par(nv[R, 0, t], par), ALU.add)
                    last.then_inc(*w_ready.one())
                    end = cl[:, :, c:c + 1].to_broadcast([P, KT, HD])
                    if c < N_RC - 1:
                        vv.tensor_tensor(Sd[:], S[:], end, ALU.mult).then_inc(*K.dve_step.one())
                        decayed = K.dve_step.now()
                    output(c - 1)
                    dve.wait_ge(*rs_made.at(c))
                    for par in range(2):
                        last = vv.tensor_tensor(by_par(y[R, t], par), bank(R, 5 + par), by_par(nv[R, 1, t], par), ALU.add)
                    last.then_inc(*K.dve_step.one())
                    carried = K.dve_step.now()
                else:
                    vv.tensor_copy(W[R], nv[R, 0, t]).then_inc(*w_ready.one())
                dve.wait_ge(*sa_made.at(c + 1))
                vv.tensor_copy(by_par(SA[R], 0), bank(R, 2)).then_inc(*sa_ready.one())
                if c < N_RC - 1:
                    dve.wait_ge(*kv_made.at(c + 1))
                    if c:
                        dve.wait_ge(*decayed)
                        link(dve, K.dve_step, vv.tensor_tensor(Sd[:], Sd[:], bank(slice(0, P), 7), ALU.add))
                    else:
                        link(dve, K.dve_step, vv.tensor_copy(Sd[:], bank(slice(0, P), 7)))
                    dve.wait_ge(*st_made.at(c + 1))
                    vv.tensor_tensor(S[:], Sd[:], bank(slice(0, P), 4), ALU.add).then_inc(*st_ready.one())
            output(N_RC - 1)


def rwkv_output(K, y, v, g, bon, ln, tmp):
    nc, I = K.nc, K.ins
    n = 2 * RW_HEADS
    with ExitStack() as ctx:
        def sb(name, shape):
            return ctx.enter_context(nc.sbuf_tensor(name, shape, F32))
        st = sb("rw_st", [P, 4, n, 1])
        given, sq_in, sq_done = K.sig("rows_given"), K.sig("exp_asked"), K.sig("exp_done")
        block = ctx.enter_context(nc.Block())
        heads = lambda ap: ap.rearrange("p (h d) -> p h d", d=HD)
        Y = heads(y[:].rearrange("p t f -> p (t f)"))
        V = heads(v[:].rearrange("p t f -> p (t f)"))
        TMP = heads(tmp[:])
        wide = lambda i: st[:, i].to_broadcast([P, n, HD])

        @block.sync
        def _(sp):
            sp.dma_start(ln[:, 0], I["c_ln_g_2"].to_broadcast([P, D])).then_inc(*given.dma())
            sp.dma_start(ln[:, 1], I["c_ln_b_2"].to_broadcast([P, D])).then_inc(*given.dma())

        @block.scalar
        def _(act):
            act.wait_ge(*sq_in.at(1))
            nc.scalar.activation(TMP, Y, ACT.Square).then_inc(*sq_done.one())
            act.wait_ge(*sq_in.at(2))
            nc.scalar.activation(st[:, 2], st[:, 1], ACT.Sqrt, bias=K.eps[:, 2:3], scale=1.0 / HD).then_inc(*sq_done.one())

        @block.vector
        def _(dve):
            vv = nc.vector
            do = lambda ins: link(dve, K.dve_step, ins)
            do(vv.reduce_sum(st[:, 0], Y, AX))
            do(vv.tensor_scalar(st[:, 0], st[:, 0], 1.0 / HD, None, ALU.mult))
            vv.tensor_tensor(Y, Y, wide(0), ALU.subtract).then_inc(*sq_in.one())
            dve.wait_ge(*sq_done.at(1))
            vv.reduce_sum(st[:, 1], TMP, AX).then_inc(*sq_in.one())
            dve.wait_ge(*sq_done.at(2))
            do(vv.reciprocal(st[:, 3], st[:, 2]))
            do(vv.tensor_tensor(Y, Y, wide(3), ALU.mult))
            dve.wait_ge(*given.at(32))
            for j, op in ((0, ALU.mult), (1, ALU.add)):
                row = ln[:, j:j + 1].to_broadcast([P, 2, D])
                do(vv.tensor_tensor(y[:], y[:], row, op))
            do(vv.tensor_tensor(TMP, V, bon[:].rearrange("p t (h a) -> p (t h) a", a=1).to_broadcast([P, n, HD]), ALU.mult))
            do(vv.tensor_tensor(Y, Y, TMP, ALU.add))
            do(vv.tensor_tensor(y[:], y[:], g[:], ALU.mult))


def second_block(K, scratch):
    H, X = K.h[:, :, 0:SEQ], K.xn[:, :, 0:SEQ]
    for layer in range(2):
        gain = lambda j: K.col("norm_gains_2", (6 * layer + j) * KT, KT)
        ffn(K, *[K.ins[f"ffn1_w_{w}_2"][layer] for w in ("gate", "up", "down")], gain(0), gain(1))
        if layer == 0:
            nsa_ssd(K, gain(2))
        else:
            rwkv(K, scratch, gain(2))
        rms_norm(K, X, X, gain(3), add_to=H)
        ffn(K, *[K.ins[f"ffn2_w_{w}_2"][layer] for w in ("gate", "up", "down")], gain(4), gain(5))


def token_model_kernel(nc, ins, out, gates_dram, scratch):
    K = Core(nc, ins)
    load_all(K)
    first_block(K, gates_dram)
    second_block(K, scratch)
    store_tokens(K, out)


def first_block(K, gates_dram):
    rms_norm(K, K.h[:], K.xn[:], K.col("a_norm", 0, KT))
    pool_mixer(K)
    rms_norm(K, K.h[:], K.xn[:], K.col("ffn_norm", 0, KT))
    moe(K, 0, gates_dram)
    with ExitStack() as ctx:
        kv = latent_kv(K, ctx)
        mla(K, kv)
    rms_norm(K, K.h[:], K.xn[:], K.col("ffn_norm", KT, KT))
    moe(K, 1, gates_dram)
    final_norm(K)


INS = ["x", "meta_tokens", "a_norm", "a_w", "a_scale", "b_norm", "b_w_dq", "b_q_norm", "b_w_uq", "b_w_o", "kv_norm",
       "w_dkv", "kv_lat_norm", "w_uk", "w_uv", "ffn_norm", "router_g", "router_g_bias", "router_e", "router_e_bias",
       "w_gate", "w_up", "w_down", "final_norm", "norm_gains_2", "ffn1_w_gate_2", "ffn1_w_up_2", "ffn1_w_down_2",
       "ffn2_w_gate_2", "ffn2_w_up_2", "ffn2_w_down_2", "ab_w_in_2", "a_cmp_pe_k_2", "a_cmp_w1_k_2", "a_cmp_w2_k_2",
       "a_cmp_pe_v_2", "a_cmp_w1_v_2", "a_cmp_w2_v_2", "b_conv_w_2", "b_conv_b_2", "b_dt_bias_2", "b_a_log_2",
       "b_d_skip_2", "b_norm_w_2", "ab_w_out_2", "c_mu_2", "c_w_r_2", "c_w_k_2", "c_w_v_2", "c_w_o_2", "c_w0_2",
       "c_w1_2", "c_w2_2", "c_a0_2", "c_a1_2", "c_a2_2", "c_g1_2", "c_g2_2", "c_k_k_2", "c_k_a_2", "c_r_k_2",
       "c_ln_g_2", "c_ln_b_2"]


def kernel(**inputs):
    import concourse.bacc as bacc
    from concourse.bass_utils import run_bass_kernel_spmd

    nc = bacc.Bacc("TRN2", target_bir_lowering=False, num_devices=1)
    arrays = {f"in_{n}": np.ascontiguousarray(inputs[n]) for n in INS}
    arrays["in_constants"] = constants()
    ins = {n[3:]: nc.dram_tensor(n, a.shape, F32, kind="ExternalInput").ap() for n, a in arrays.items()}
    out = nc.dram_tensor("out", (1, SEQ, D), F32, kind="ExternalOutput").ap()
    gates = nc.dram_tensor("gates", (N_EXP, L1), F32, kind="Internal").ap()
    scratch = nc.dram_tensor("scratch", (2, P, RC * RC), F32, kind="Internal").ap()
    token_model_kernel(nc, ins, out, gates, scratch)
    result = run_bass_kernel_spmd(nc, [arrays], core_ids=[0])
    return result.results[0]["out"]
```
